# Optimizing a Trainium2 kernel written in Bass

```python
import math
import jax, jax.numpy as jnp
from jax import lax
import numpy as np

D_MODEL = 1024
BATCH = 1
SEQ = 512
DEPTH = 2
DEC_BATCH = 8
DEC_SEQ = 8
PAST_LEN = 4096
PAGE_SIZE = 128

N_A_LAYERS = DEPTH // 2
N_B_LAYERS = DEPTH - N_A_LAYERS
SSM_GROUP_WIDTH = 16
SSM_GROUPS = D_MODEL // SSM_GROUP_WIDTH
SSM_STATE = 64
SSM_CHUNK = 128
DT_MIN = 0.001
DT_MAX = 0.1
N_HEADS = 16
HEAD_DIM = 64
N_KV = 4
HEADS_PER_KV = N_HEADS // N_KV
N_BRANCH = 3
CMP_BLOCK = 32
CMP_STRIDE = 16
CMP_HIDDEN = 256
SEL_BLOCK = 64
N_SELECT = 16
WINDOW = 512
Q_BLOCK = 128
ATTN_SCALE = HEAD_DIM ** -0.5
FORCE_SCORE = 1e4
NEG_INF = -1e30
TINY = 1e-30
N_EXPERT_GROUPS = 4
EXPERTS_PER_GROUP = 8
N_EXPERTS = N_EXPERT_GROUPS * EXPERTS_PER_GROUP
TOP_K_IN_GROUP = 2
D_EXPERT = 256
MOE_ROW_BLOCK = 128
DEEPNORM_ALPHA = (2 * DEPTH) ** 0.25
DEEPNORM_BETA = (8 * DEPTH) ** -0.25
LN_EPS = 1e-5

kernel_name = 'yoco_s5_nsa_hmoe_step'

def layer_norm(x, g, b):
    xf = x.astype(jnp.float32)
    mu = jnp.mean(xf, -1, keepdims=True)
    var = jnp.mean(jnp.square(xf - mu), -1, keepdims=True)
    y = (xf - mu) * lax.rsqrt(var + LN_EPS) * g.astype(jnp.float32) + b.astype(jnp.float32)
    return y.astype(x.dtype)

def deepnorm_residual(x, f, g, b):
    return layer_norm(DEEPNORM_ALPHA * x + f.astype(x.dtype), g, b)

def masked_softmax(s, mask):
    s = jnp.where(mask, s.astype(jnp.float32), NEG_INF)
    p = jnp.exp(s - jnp.max(s, -1, keepdims=True)) * mask
    return p / jnp.maximum(jnp.sum(p, -1, keepdims=True), TINY)

def _cmul(ar, ai, br, bi):
    return ar * br - ai * bi, ar * bi + ai * br

def _ssm_combine(e1, e2):
    a1r, a1i, b1r, b1i = e1
    a2r, a2i, b2r, b2i = e2
    ar, ai = _cmul(a2r, a2i, a1r, a1i)
    cr, ci = _cmul(a2r, a2i, b1r, b1i)
    return ar, ai, cr + b2r, ci + b2i

def s5_discretize(lam_re, lam_im, log_dt, b_re, b_im):
    lr, li = lam_re.astype(jnp.float32), lam_im.astype(jnp.float32)
    dt = jnp.exp(log_dt.astype(jnp.float32))[:, None]
    mag = jnp.exp(lr * dt)
    abar_re, abar_im = mag * jnp.cos(li * dt), mag * jnp.sin(li * dt)
    den = lr * lr + li * li
    nr = abar_re - 1.0
    z_re = (nr * lr + abar_im * li) / den
    z_im = (abar_im * lr - nr * li) / den
    bbar_re, bbar_im = _cmul(z_re[..., None], z_im[..., None],
                             b_re.astype(jnp.float32), b_im.astype(jnp.float32))
    return abar_re, abar_im, bbar_re, bbar_im

def s5_mixer(x, h0, w_in, lam_re, lam_im, log_dt, b_re, b_im, c_re, c_im, d_skip, w_glu):
    bsz, L, _ = x.shape
    u = x @ w_in
    abar_re, abar_im, bb_re, bb_im = s5_discretize(lam_re, lam_im, log_dt, b_re, b_im)
    cr_w, ci_w = c_re.astype(jnp.float32), c_im.astype(jnp.float32)
    chunk = SSM_CHUNK if L % SSM_CHUNK == 0 else L
    n_chunks = L // chunk
    uc = u.astype(jnp.float32).reshape(bsz, n_chunks, chunk, SSM_GROUPS, SSM_GROUP_WIDTH)
    uc = jnp.moveaxis(uc, 1, 0)

    def step(h, u_blk):
        hr, hi = h
        br = jnp.einsum('btgw,gpw->btgp', u_blk, bb_re)
        bi = jnp.einsum('btgw,gpw->btgp', u_blk, bb_im)
        ar_h, ai_h = _cmul(abar_re, abar_im, hr, hi)
        br = br.at[:, 0].add(ar_h)
        bi = bi.at[:, 0].add(ai_h)
        a_re_b = jnp.broadcast_to(abar_re, br.shape)
        a_im_b = jnp.broadcast_to(abar_im, bi.shape)
        _, _, sr, si = lax.associative_scan(_ssm_combine, (a_re_b, a_im_b, br, bi), axis=1)
        y = jnp.einsum('btgp,gwp->btgw', sr, cr_w) - jnp.einsum('btgp,gwp->btgw', si, ci_w)
        return (sr[:, -1], si[:, -1]), y

    h_init = (h0[..., 0].astype(jnp.float32), h0[..., 1].astype(jnp.float32))
    (hr, hi), yc = lax.scan(step, h_init, uc)
    y = jnp.moveaxis(yc, 0, 1).reshape(bsz, L, D_MODEL)
    y = y + d_skip.astype(jnp.float32) * u.astype(jnp.float32)
    g = jax.nn.gelu(y).astype(x.dtype)
    val, gate = jnp.split(g @ w_glu, 2, axis=-1)
    return val * jax.nn.sigmoid(gate), jnp.stack([hr, hi], axis=-1)

def shared_kv(h, kv_w):
    bsz, L, _ = h.shape
    return (h @ kv_w).reshape(bsz, L, N_BRANCH, 2, N_KV, HEAD_DIM)

def compress_blocks(rows, cmp_pe, cmp_w1, cmp_w2):
    bsz, T = rows.shape[:2]
    n_sub = T // CMP_STRIDE
    sub = rows[:, :n_sub * CMP_STRIDE].reshape(bsz, n_sub, CMP_STRIDE, 2, N_KV, HEAD_DIM)
    w1 = cmp_w1.reshape(2, CMP_BLOCK // CMP_STRIDE, CMP_STRIDE, HEAD_DIM, CMP_HIDDEN)
    lo = jnp.einsum('bnskgd,ksdh->bnkgh', sub, w1[:, 0])
    hi = jnp.einsum('bnskgd,ksdh->bnkgh', sub, w1[:, 1])
    pe_bias = jnp.einsum('kf,kfh->kh', cmp_pe.reshape(2, CMP_BLOCK * HEAD_DIM), cmp_w1)
    hid = jax.nn.gelu(lo[:, :-1] + hi[:, 1:] + pe_bias[:, None, :])
    return jnp.einsum('bnkgh,khd->bnkgd', hid, cmp_w2)

def kv_side_prompt(h, kv_w, cmp_pe, cmp_w1, cmp_w2):
    kv = shared_kv(h, kv_w)
    return kv, compress_blocks(kv[:, :, 0], cmp_pe, cmp_w1, cmp_w2)

def kv_side_sample(h, cache_cmp_kv, cache_win_kv, page_table, kv_w, cmp_pe, cmp_w1, cmp_w2):
    kv_new = shared_kv(h, kv_w)
    db = h.shape[0]
    past = page_table.shape[1] * cache_cmp_kv.shape[1]
    past_cmp = cache_cmp_kv[page_table].reshape((db, past) + cache_cmp_kv.shape[2:])
    full_cmp = jnp.concatenate([past_cmp, kv_new[:, :, 0].astype(past_cmp.dtype)], axis=1)
    ckv = compress_blocks(full_cmp, cmp_pe, cmp_w1, cmp_w2)
    win_all = jnp.concatenate([cache_win_kv, kv_new[:, :, 2].astype(cache_win_kv.dtype)], axis=1)
    return kv_new, ckv, win_all

def gather_paged(pool, page_table, new_rows, tok):
    db = page_table.shape[0]
    page = pool.shape[1]
    past = page_table.shape[1] * page
    n_new = new_rows.shape[1]
    b = jnp.arange(db).reshape((db,) + (1,) * (tok.ndim - 1))
    g = jnp.arange(N_KV)[:, None]
    tp = jnp.minimum(tok, past - 1)
    phys = page_table[b, tp // page]
    from_past = pool[phys, tp % page, :, g]
    from_new = new_rows[b, jnp.clip(tok - past, 0, n_new - 1), :, g]
    return jnp.where((tok < past)[..., None, None], from_past, from_new.astype(from_past.dtype))

def query_side(x, w_qg):
    bsz, L, _ = x.shape
    qg = x @ w_qg
    q = qg[..., :N_HEADS * HEAD_DIM].reshape(bsz, L, N_KV, HEADS_PER_KV, HEAD_DIM)
    gates = jax.nn.sigmoid(qg[..., N_HEADS * HEAD_DIM:].astype(jnp.float32))
    return q, gates.reshape(bsz, L, N_KV, HEADS_PER_KV, N_BRANCH)

def cmp_attend(q, q_pos, ckv):
    n_cmp = ckv.shape[1]
    c_end = jnp.arange(n_cmp) * CMP_STRIDE + CMP_BLOCK - 1
    mask = (c_end[None, :] <= q_pos[:, None])[None, :, None, None, :]
    s = jnp.einsum('blgnd,bcgd->blgnc', q, ckv[:, :, 0]) * ATTN_SCALE
    p = masked_softmax(s, mask)
    o = jnp.einsum('blgnc,bcgd->blgnd', p.astype(ckv.dtype), ckv[:, :, 1])
    return o, p

def select_blocks(p_cmp, q_pos, n_sel):
    pg = jnp.moveaxis(jnp.sum(p_cmp, axis=3), -1, 0)
    c = jnp.arange(pg.shape[0])
    j_first = (c * CMP_STRIDE) // SEL_BLOCK
    j_last = (c * CMP_STRIDE + CMP_BLOCK - 1) // SEL_BLOCK
    spill = (j_last != j_first).astype(pg.dtype)[:, None, None, None]
    ps = (jax.ops.segment_sum(pg, j_first, num_segments=n_sel)
          + jax.ops.segment_sum(pg * spill, j_last, num_segments=n_sel))
    ps = jnp.moveaxis(ps, 0, -1)
    j = jnp.arange(n_sel)
    valid = (j[None, :] * SEL_BLOCK <= q_pos[:, None])[None, :, None, :]
    forced = ((j[None, :] == (q_pos // SEL_BLOCK)[:, None]) | (j[None, :] == 0))[None, :, None, :]
    score = jnp.where(valid, ps + FORCE_SCORE * forced.astype(ps.dtype), -1.0)
    _, idx = lax.top_k(score, min(N_SELECT, n_sel))
    return idx

def block_tokens(blk):
    tok = blk[..., None] * SEL_BLOCK + jnp.arange(SEL_BLOCK)
    return tok.reshape(blk.shape[:-1] + (-1,))

def slc_attend(q, q_pos, tok, k_rows, v_rows):
    s = jnp.einsum('...gnd,...gkd->...gnk', q, k_rows) * ATTN_SCALE
    mask = (tok <= q_pos[..., None, None])[..., None, :]
    p = masked_softmax(s, mask)
    return jnp.einsum('...gnk,...gkd->...gnd', p.astype(v_rows.dtype), v_rows)

def win_attend(q, q_pos, k_pos, k, v):
    dist = q_pos[:, None] - k_pos[None, :]
    mask = ((dist >= 0) & (dist < WINDOW) & (k_pos[None, :] >= 0))[None, :, None, None, :]
    s = jnp.einsum('blgnd,bkgd->blgnk', q, k) * ATTN_SCALE
    p = masked_softmax(s, mask)
    return jnp.einsum('blgnk,bkgd->blgnd', p.astype(v.dtype), v)

def nsa_merge(o_cmp, o_slc, o_win, gates, w_o):
    g = gates.astype(o_cmp.dtype)
    o = g[..., 0:1] * o_cmp + g[..., 1:2] * o_slc.astype(o_cmp.dtype) + g[..., 2:3] * o_win.astype(o_cmp.dtype)
    bsz, L = o.shape[:2]
    return o.reshape(bsz, L, N_HEADS * HEAD_DIM) @ w_o

def nsa_prompt(x, kv, ckv, w_qg, w_o):
    bsz, L, _ = x.shape
    q, gates = query_side(x, w_qg)
    q_pos = jnp.arange(L)
    o_cmp, p_cmp = cmp_attend(q, q_pos, ckv)
    blk = select_blocks(p_cmp, q_pos, -(-L // SEL_BLOCK))
    qb = min(Q_BLOCK, L)
    nqb = L // qb
    slc_k = jnp.swapaxes(kv[:, :, 1, 0], 1, 2)
    slc_v = jnp.swapaxes(kv[:, :, 1, 1], 1, 2)
    g_ix = jnp.arange(N_KV)[:, None]

    def slc_block(args):
        b, q_blk, p_blk, b_blk = args
        tok = block_tokens(b_blk)
        tc = jnp.minimum(tok, L - 1)
        return slc_attend(q_blk, p_blk, tok, slc_k[b, g_ix, tc], slc_v[b, g_ix, tc])

    o_slc = lax.map(slc_block, (jnp.repeat(jnp.arange(bsz), nqb),
                                q.reshape(bsz * nqb, qb, N_KV, HEADS_PER_KV, HEAD_DIM),
                                jnp.tile(q_pos.reshape(nqb, qb), (bsz, 1)),
                                blk.reshape(bsz * nqb, qb, N_KV, -1))).reshape(q.shape)
    win = jnp.pad(kv[:, :, 2], ((0, 0), (WINDOW, 0), (0, 0), (0, 0), (0, 0)))

    def win_block(c):
        start = c * qb
        kw = lax.dynamic_slice_in_dim(win, start, qb + WINDOW, axis=1)
        q_blk = lax.dynamic_slice_in_dim(q, start, qb, axis=1)
        return win_attend(q_blk, start + jnp.arange(qb), start - WINDOW + jnp.arange(qb + WINDOW),
                          kw[:, :, 0], kw[:, :, 1])

    o_win = jnp.moveaxis(lax.map(win_block, jnp.arange(nqb)), 0, 1).reshape(q.shape)
    return nsa_merge(o_cmp, o_slc, o_win, gates, w_o)

def nsa_sample(x, kv_new, ckv, win_all, cache_slc_kv, page_table, w_qg, w_o):
    n_new = x.shape[1]
    past = page_table.shape[1] * cache_slc_kv.shape[1]
    total = past + n_new
    q, gates = query_side(x, w_qg)
    q_pos = past + jnp.arange(n_new)
    o_cmp, p_cmp = cmp_attend(q, q_pos, ckv)
    blk = select_blocks(p_cmp, q_pos, -(-total // SEL_BLOCK))
    tok = block_tokens(blk)
    rows = gather_paged(cache_slc_kv, page_table, kv_new[:, :, 1], tok)
    o_slc = slc_attend(q, q_pos, tok, rows[..., 0, :], rows[..., 1, :])
    n_win = win_all.shape[1]
    k_pos = past - (n_win - n_new) + jnp.arange(n_win)
    o_win = win_attend(q, q_pos, k_pos, win_all[:, :, 0], win_all[:, :, 1])
    return nsa_merge(o_cmp, o_slc, o_win, gates, w_o)

def hier_moe(x, w_group, w_expert, w_gate_up, w_down):
    shp = x.shape
    xt = x.reshape(-1, shp[-1])
    T = xt.shape[0]
    lg = (xt @ w_group).astype(jnp.float32)
    g_top, g_sel = lax.top_k(lg, 1)
    g_w = jnp.exp(g_top[:, 0] - jax.nn.logsumexp(lg, axis=-1))
    le = (xt @ w_expert).astype(jnp.float32).reshape(T, N_EXPERT_GROUPS, EXPERTS_PER_GROUP)
    le_g = le[jnp.arange(T), g_sel[:, 0]]
    e_top, e_loc = lax.top_k(le_g, TOP_K_IN_GROUP)
    w = g_w[:, None] * jax.nn.softmax(e_top, axis=-1)
    e_id = g_sel * EXPERTS_PER_GROUP + e_loc
    n_asg = T * TOP_K_IN_GROUP
    e_flat = e_id.reshape(-1)
    tok_flat = jnp.repeat(jnp.arange(T), TOP_K_IN_GROUP)
    order = jnp.argsort(e_flat)
    e_s, tok_s, w_s = e_flat[order], tok_flat[order], w.reshape(-1)[order]
    counts = jax.ops.segment_sum(jnp.ones((n_asg,), jnp.int32), e_flat, num_segments=N_EXPERTS)
    starts = jnp.cumsum(counts) - counts
    padded = (counts + MOE_ROW_BLOCK - 1) // MOE_ROW_BLOCK * MOE_ROW_BLOCK
    pends = jnp.cumsum(padded)
    dest = (pends - padded)[e_s] + jnp.arange(n_asg) - starts[e_s]
    n_blocks = -(-n_asg // MOE_ROW_BLOCK) + N_EXPERTS
    n_rows = n_blocks * MOE_ROW_BLOCK
    row_tok = jnp.zeros((n_rows,), jnp.int32).at[dest].set(tok_s)
    row_w = jnp.zeros((n_rows,), jnp.float32).at[dest].set(w_s)
    blk_e = jnp.minimum(jnp.searchsorted(pends, jnp.arange(n_blocks) * MOE_ROW_BLOCK, side='right'),
                        N_EXPERTS - 1)

    def expert_block(args):
        e, toks = args
        gate, up = jnp.split(xt[toks] @ w_gate_up[e], 2, axis=-1)
        return (jax.nn.silu(gate) * up) @ w_down[e]

    yb = lax.map(expert_block, (blk_e, row_tok.reshape(n_blocks, MOE_ROW_BLOCK)))
    out = jnp.zeros((T, shp[-1]), x.dtype).at[row_tok].add(
        yb.reshape(n_rows, shp[-1]) * row_w[:, None].astype(x.dtype))
    return out.reshape(shp)

def setup_inputs(seed: int = 0) -> dict:
    key = jax.random.key(seed)
    ks = iter(jax.random.split(key, 40))

    def nrm(shape, scale):
        return jax.random.normal(next(ks), shape, jnp.float32) * scale

    n_pages = PAST_LEN // PAGE_SIZE
    n_pool = (5 * DEC_BATCH * n_pages + 3) // 4
    win_buf = min(WINDOW, PAST_LEN)
    x_prompt = nrm((BATCH, SEQ, D_MODEL), 1.0)
    x_sample = nrm((DEC_BATCH, DEC_SEQ, D_MODEL), 1.0)
    state_ssm = nrm((N_A_LAYERS, DEC_BATCH, SSM_GROUPS, SSM_STATE, 2), 0.3)
    cache_cmp_kv = nrm((n_pool, PAGE_SIZE, 2, N_KV, HEAD_DIM), 1.0)
    cache_slc_kv = nrm((n_pool, PAGE_SIZE, 2, N_KV, HEAD_DIM), 1.0)
    cache_win_kv = nrm((DEC_BATCH, win_buf, 2, N_KV, HEAD_DIM), 1.0)
    page_table = jax.random.permutation(next(ks), n_pool)[:DEC_BATCH * n_pages]
    page_table = page_table.reshape(DEC_BATCH, n_pages).astype(jnp.int32)
    a_w_in = nrm((N_A_LAYERS, D_MODEL, D_MODEL), D_MODEL ** -0.5)
    a_lambda_re = -0.5 + nrm((N_A_LAYERS, SSM_GROUPS, SSM_STATE), 0.01)
    a_lambda_im = math.pi * jnp.arange(SSM_STATE, dtype=jnp.float32) + nrm((N_A_LAYERS, SSM_GROUPS, SSM_STATE), 0.01)
    a_log_dt = math.log(DT_MIN) + jax.random.uniform(next(ks), (N_A_LAYERS, SSM_GROUPS), jnp.float32) * (math.log(DT_MAX) - math.log(DT_MIN))
    a_b_re = nrm((N_A_LAYERS, SSM_GROUPS, SSM_STATE, SSM_GROUP_WIDTH), (2 * SSM_GROUP_WIDTH) ** -0.5)
    a_b_im = nrm((N_A_LAYERS, SSM_GROUPS, SSM_STATE, SSM_GROUP_WIDTH), (2 * SSM_GROUP_WIDTH) ** -0.5)
    a_c_re = nrm((N_A_LAYERS, SSM_GROUPS, SSM_GROUP_WIDTH, SSM_STATE), SSM_STATE ** -0.5)
    a_c_im = nrm((N_A_LAYERS, SSM_GROUPS, SSM_GROUP_WIDTH, SSM_STATE), SSM_STATE ** -0.5)
    a_d = nrm((N_A_LAYERS, D_MODEL), 1.0)
    a_w_glu = jnp.concatenate([nrm((N_A_LAYERS, D_MODEL, D_MODEL), DEEPNORM_BETA * D_MODEL ** -0.5),
                               nrm((N_A_LAYERS, D_MODEL, D_MODEL), D_MODEL ** -0.5)], axis=-1)
    kv_w = nrm((D_MODEL, N_BRANCH * 2 * N_KV * HEAD_DIM), D_MODEL ** -0.5)
    cmp_pe = nrm((2, CMP_BLOCK, HEAD_DIM), 0.02)
    cmp_w1 = nrm((2, CMP_BLOCK * HEAD_DIM, CMP_HIDDEN), (CMP_BLOCK * HEAD_DIM) ** -0.5)
    cmp_w2 = nrm((2, CMP_HIDDEN, HEAD_DIM), CMP_HIDDEN ** -0.5)
    b_w_qg = nrm((N_B_LAYERS, D_MODEL, N_HEADS * HEAD_DIM + N_HEADS * N_BRANCH), D_MODEL ** -0.5)
    b_w_o = nrm((N_B_LAYERS, N_HEADS * HEAD_DIM, D_MODEL), DEEPNORM_BETA * (N_HEADS * HEAD_DIM) ** -0.5)
    moe_w_group = nrm((DEPTH, D_MODEL, N_EXPERT_GROUPS), D_MODEL ** -0.5)
    moe_w_expert = nrm((DEPTH, D_MODEL, N_EXPERTS), D_MODEL ** -0.5)
    moe_w_gate_up = nrm((DEPTH, N_EXPERTS, D_MODEL, 2 * D_EXPERT), D_MODEL ** -0.5)
    moe_w_down = nrm((DEPTH, N_EXPERTS, D_EXPERT, D_MODEL), DEEPNORM_BETA * D_EXPERT ** -0.5)
    ln_g = 1.0 + nrm((DEPTH, 2, D_MODEL), 0.02)
    ln_b = nrm((DEPTH, 2, D_MODEL), 0.02)
    return {'x_prompt': x_prompt, 'x_sample': x_sample, 'state_ssm': state_ssm,
            'cache_cmp_kv': cache_cmp_kv, 'cache_slc_kv': cache_slc_kv, 'cache_win_kv': cache_win_kv,
            'page_table': page_table,
            'a_w_in': a_w_in, 'a_lambda_re': a_lambda_re, 'a_lambda_im': a_lambda_im, 'a_log_dt': a_log_dt,
            'a_b_re': a_b_re, 'a_b_im': a_b_im, 'a_c_re': a_c_re, 'a_c_im': a_c_im, 'a_d': a_d,
            'a_w_glu': a_w_glu, 'kv_w': kv_w, 'cmp_pe': cmp_pe, 'cmp_w1': cmp_w1, 'cmp_w2': cmp_w2,
            'b_w_qg': b_w_qg, 'b_w_o': b_w_o, 'moe_w_group': moe_w_group, 'moe_w_expert': moe_w_expert,
            'moe_w_gate_up': moe_w_gate_up, 'moe_w_down': moe_w_down, 'ln_g': ln_g, 'ln_b': ln_b}

def reference(x_prompt, x_sample, state_ssm, cache_cmp_kv, cache_slc_kv, cache_win_kv, page_table,
              a_w_in, a_lambda_re, a_lambda_im, a_log_dt, a_b_re, a_b_im, a_c_re, a_c_im, a_d, a_w_glu,
              kv_w, cmp_pe, cmp_w1, cmp_w2, b_w_qg, b_w_o,
              moe_w_group, moe_w_expert, moe_w_gate_up, moe_w_down, ln_g, ln_b):
    xp, xs = x_prompt, x_sample
    ssm_p, ssm_s = [], []
    for layer in range(DEPTH):
        if layer < N_A_LAYERS:
            a_par = (a_w_in[layer], a_lambda_re[layer], a_lambda_im[layer], a_log_dt[layer],
                     a_b_re[layer], a_b_im[layer], a_c_re[layer], a_c_im[layer], a_d[layer], a_w_glu[layer])
            h0 = jnp.zeros((xp.shape[0], SSM_GROUPS, SSM_STATE, 2), jnp.float32)
            fp, hp = s5_mixer(xp, h0, *a_par)
            fs, hs = s5_mixer(xs, state_ssm[layer], *a_par)
            ssm_p.append(hp)
            ssm_s.append(hs.astype(state_ssm.dtype))
        else:
            if layer == N_A_LAYERS:
                kv_p, ckv_p = kv_side_prompt(xp, kv_w, cmp_pe, cmp_w1, cmp_w2)
                kv_s, ckv_s, win_s = kv_side_sample(xs, cache_cmp_kv, cache_win_kv, page_table,
                                                    kv_w, cmp_pe, cmp_w1, cmp_w2)
            bl = layer - N_A_LAYERS
            fp = nsa_prompt(xp, kv_p, ckv_p, b_w_qg[bl], b_w_o[bl])
            fs = nsa_sample(xs, kv_s, ckv_s, win_s, cache_slc_kv, page_table, b_w_qg[bl], b_w_o[bl])
        xp = deepnorm_residual(xp, fp, ln_g[layer, 0], ln_b[layer, 0])
        xs = deepnorm_residual(xs, fs, ln_g[layer, 0], ln_b[layer, 0])
        moe_par = (moe_w_group[layer], moe_w_expert[layer], moe_w_gate_up[layer], moe_w_down[layer])
        xp = deepnorm_residual(xp, hier_moe(xp, *moe_par), ln_g[layer, 1], ln_b[layer, 1])
        xs = deepnorm_residual(xs, hier_moe(xs, *moe_par), ln_g[layer, 1], ln_b[layer, 1])
    p_win = kv_p[:, -min(WINDOW, kv_p.shape[1]):, 2]
    s_win = win_s[:, -min(WINDOW, win_s.shape[1]):]
    return (xp, xs, jnp.stack(ssm_p), kv_p[:, :, 0], kv_p[:, :, 1], p_win,
            jnp.stack(ssm_s), kv_s[:, :, 0], kv_s[:, :, 1], s_win)


_drawn_inputs = setup_inputs


def setup_inputs(seed=0):
    import zlib

    import numpy as np

    out = dict(_drawn_inputs(seed))
    spreads = {}
    factors = {'cache_cmp_kv': 4.685, 'cache_slc_kv': 5.504, 'a_lambda_re': 4.1, 'cmp_pe': 6.815}
    for name, (base, spread) in spreads.items():
        noise = np.random.default_rng([zlib.crc32(name.encode()), seed]).standard_normal(out[name].shape)
        drawn = base * np.exp(spread * noise) if base else spread * noise
        out[name] = __import__('jax').numpy.asarray(drawn.astype(out[name].dtype))
    for name, factor in factors.items():
        out[name] = (out[name] * factor).astype(out[name].dtype)
    return out
```

```python
from contextlib import ExitStack

import numpy as np

import concourse.bass as bass
from concourse import mybir

F32 = mybir.dt.float32
BF16 = mybir.dt.bfloat16
I32 = mybir.dt.int32
U32 = mybir.dt.uint32
ALU = mybir.AluOpType
ACT = mybir.ActivationFunctionType
AX = mybir.AxisListType.X

P = 128
D = 1024
KT = D // P
SEQ = 512
DEC_B, DEC_S = 8, 8
TOK = SEQ + DEC_B * DEC_S
TILES = [(0, 128), (128, 128), (256, 128), (384, 128), (512, 64)]
NT = len(TILES)
PAST, PAGE = 4096, 128
N_POOL = 320
SG, SP_, SW, CH = 64, 64, 16, 8
NCP = SEQ // CH
NC_ = NCP + DEC_B
NH, HD, NKV, HPK = 16, 64, 4, 4
SCALE = HD ** -0.5
CMP_H = 256
NCMP_S = PAST // 16 - 1
NCMP_P = SEQ // 16 - 1
NSEL = 65
NEG = -1e30
TINY = 1e-30
NG, EPG, NE, DE = 4, 8, 32, 256
RB = 128
NBLK = (TOK * 2) // RB + NE
NROW = NBLK * RB
ALPHA = (2 * 2) ** 0.25
EPS = 1e-5
ARENA = 52000

TWO_PI = 2 * np.pi
C1 = 6.28125
C2 = float(np.float32(np.round((TWO_PI - C1) * 2 ** 22) / 2 ** 22))
C3 = float(np.float32(TWO_PI - C1 - C2))
INV_2PI = float(np.float32(1 / TWO_PI))
MAGIC = 12582912.0


def bc(ap, shape):
    return ap.to_broadcast(shape)


class Link:

    def __init__(self, eng, sem, base=0):
        self.eng, self.sem, self.n, self.count = eng, sem, base, 0

    def __call__(self, ins):
        ins.then_inc(self.sem, 1)
        self.n = self.n + 1
        self.count += 1
        self.eng.wait_ge(self.sem, self.n)


class Scope:

    spent = []

    def __init__(self, nc, name):
        self.nc, self.name, self.ctx = nc, name, ExitStack()

    def __enter__(self):
        self.ctx.__enter__()
        return self

    def __exit__(self, *a):
        return self.ctx.__exit__(*a)

    def sb(self, name, shape, dt=F32):
        return self.ctx.enter_context(self.nc.sbuf_tensor(f"{self.name}_{name}", shape, dt))

    def banks(self, n=8, dt=F32):
        return [self.ctx.enter_context(self.nc.psum_tensor(f"{self.name}_bank{i}", [P, 512], dt)) for i in range(n)]

    def sem(self, name):
        handle = self.nc.alloc_semaphore(name=f"{self.name}_{name}")
        Scope.spent.append(handle)
        return handle


def recycle(nc):
    with nc.Block() as block:
        @block.gpsimd
        def _(pool):
            nc.clear_and_free_semaphores(Scope.spent)
    Scope.spent = []


def constants(nc, ident, jmat, eps):
    with Scope(nc, "const") as s:
        zeroed, made = s.sem("zeroed"), s.sem("made")
        with nc.Block() as block:
            @block.gpsimd
            def _(pool):
                pool.memset(ident[:, :], 0.0).then_inc(zeroed, 1)
                pool.memset(jmat[:, :], 0.0).then_inc(zeroed, 1)
                pool.memset(eps[:, :], EPS).then_inc(zeroed, 1)
                pool.wait_ge(zeroed, 3)
                pool.affine_select(out=ident[:, :], in_=ident[:, :], compare_op=ALU.not_equal, fill=1.0,
                                   base=0, pattern=[[-1, P]], channel_multiplier=1).then_inc(made, 1)
                pool.affine_select(out=jmat[:, 0:64], in_=jmat[:, 0:64], compare_op=ALU.not_equal, fill=-1.0,
                                   base=-64, pattern=[[-1, 64]], channel_multiplier=1).then_inc(made, 1)
                pool.affine_select(out=jmat[:, 64:P], in_=jmat[:, 64:P], compare_op=ALU.not_equal, fill=1.0,
                                   base=0, pattern=[[-1, 64]], channel_multiplier=1).then_inc(made, 1)
                pool.wait_ge(made, 3)


def s5_parameters(nc, A, ident, jmat, tab, x1, x2, y1, y2, R):
    with Scope(nc, "par") as s:
        at = [5376]

        def place(name, shape):
            at[0] += int(np.prod(shape[1:]))
            return R(at[0] - int(np.prod(shape[1:])), *shape[1:], np_=64)

        lr, li = place("lr", [64, 64]), place("li", [64, 64])
        ldt, dt = place("ldt", [64, 1]), place("dt", [64, 1])
        b_in, bb = place("b_in", [64, 2, 1024]), place("bb", [64, 2, 1024])
        c_in = place("c_in", [64, 16, 2, 64])
        tmp = place("tmp", [64, 1024])
        a1, th = place("a1", [64, 64]), place("th", [64, 64])
        rnd = place("rnd", [64, 9, 64])
        ang = place("ang", [64, 9, 64])
        sn, sh, mag = place("sn", [64, 9, 64]), place("sh", [64, 9, 64]), place("mag", [64, 9, 64])
        t20 = place("t20", [64, 20, 2, 64])
        den, rden, nr, t1, t2, zr, zi = (place(n, [64, 64]) for n in ("den", "rden", "nr", "t1", "t2", "zr", "zi"))
        bank = s.banks()
        loaded, dt_ready, a_ready, ang_ready, trig = (s.sem(n) for n in ("loaded", "dt_ready", "a_ready", "ang_ready", "trig"))
        dve, t20_ready, bb_ready, turned, moved, jdone = (s.sem(n) for n in ("dve", "t20_ready", "bb_ready", "turned", "moved", "jdone"))
        LOADS = [(lr[:, :], A["a_lambda_re"][0]), (li[:, :], A["a_lambda_im"][0]),
                 (ldt[:, :], A["a_log_dt"].rearrange("o g -> g o")),
                 (b_in[:, 0, :], A["a_b_re"][0].rearrange("g p w -> g (p w)")),
                 (b_in[:, 1, :], A["a_b_im"][0].rearrange("g p w -> g (p w)")),
                 (c_in[:, :, 0, :], A["a_c_re"][0]),
                 (c_in[:, :, 1, :], A["a_c_im"][0])]
        with nc.Block() as block:
            @block.sync
            def _(sp):
                for dst, src in LOADS:
                    sp.dma_start(dst, src).then_inc(loaded, 16)

            @block.scalar
            def _(act):
                act.wait_ge(loaded, 16 * len(LOADS))
                nc.scalar.activation(dt[:, :], ldt[:, :], ACT.Exp).then_inc(dt_ready, 1)
                act.wait_ge(a_ready, 1)
                for k in range(9):
                    nc.scalar.activation(mag[:, k, :], a1[:, :], ACT.Exp, scale=float(k)).then_inc(trig, 1)
                act.wait_ge(ang_ready, 1)
                nc.scalar.activation(sn[:, :, :], ang[:, :, :], ACT.Sin).then_inc(trig, 1)
                nc.scalar.activation(sh[:, :, :], ang[:, :, :], ACT.Sin, scale=0.5).then_inc(trig, 1)

            @block.vector
            def _(v):
                link = Link(v, dve)
                v.wait_ge(dt_ready, 1)
                v.tensor_scalar(a1[:, :], lr[:, :], dt[:, 0:1], None, ALU.mult).then_inc(a_ready, 1)
                link(v.tensor_scalar(th[:, :], li[:, :], dt[:, 0:1], None, ALU.mult))

                def reduce_angle(a, n):
                    link(v.tensor_scalar(n, a, INV_2PI, MAGIC, ALU.mult, ALU.add))
                    link(v.tensor_scalar(n, n, MAGIC, None, ALU.subtract))
                    for c in (C1, C2, C3):
                        link(v.scalar_tensor_tensor(out=a, in0=n, scalar=-c, in1=a, op0=ALU.mult, op1=ALU.add))

                reduce_angle(th[:, :], rnd[:, 0, :])
                for k in range(9):
                    ins = v.tensor_scalar(ang[:, k, :], th[:, :], float(k), None, ALU.mult)
                link(ins)
                reduce_angle(ang[:, :, :], rnd[:, :, :])
                v.engine_nop().then_inc(ang_ready, 1)
                link(v.tensor_tensor(t1[:, :], lr[:, :], lr[:, :], ALU.mult))
                link(v.tensor_tensor(t2[:, :], li[:, :], li[:, :], ALU.mult))
                link(v.tensor_tensor(den[:, :], t1[:, :], t2[:, :], ALU.add))
                link(v.reciprocal(rden[:, :], den[:, :]))
                v.wait_ge(trig, 11)
                link(v.tensor_tensor(sh[:, :, :], sh[:, :, :], sh[:, :, :], ALU.mult))
                link(v.tensor_scalar(sh[:, :, :], sh[:, :, :], -2.0, 1.0, ALU.mult, ALU.add))
                for ri in range(2):
                    v.tensor_tensor(t20[:, 0:9, ri, :], mag[:, :, :], sh[:, :, :], ALU.mult)
                    v.tensor_tensor(t20[:, 9:18, ri, :], mag[:, :, :], sn[:, :, :], ALU.mult)
                    v.tensor_copy(t20[:, 18, ri, :], ang[:, 8, :])
                    ins = v.tensor_copy(t20[:, 19, ri, :], mag[:, 8, :])
                link(ins)
                v.engine_nop().then_inc(t20_ready, 1)
                ai = t20[:, 10, 0, :]
                link(v.tensor_scalar(nr[:, :], t20[:, 1, 0, :], 1.0, None, ALU.subtract))
                link(v.tensor_tensor(t1[:, :], nr[:, :], lr[:, :], ALU.mult))
                link(v.tensor_tensor(t2[:, :], ai, li[:, :], ALU.mult))
                link(v.tensor_tensor(t1[:, :], t1[:, :], t2[:, :], ALU.add))
                link(v.tensor_tensor(zr[:, :], t1[:, :], rden[:, :], ALU.mult))
                link(v.tensor_tensor(t1[:, :], ai, lr[:, :], ALU.mult))
                link(v.tensor_tensor(t2[:, :], nr[:, :], li[:, :], ALU.mult))
                link(v.tensor_tensor(t1[:, :], t1[:, :], t2[:, :], ALU.subtract))
                link(v.tensor_tensor(zi[:, :], t1[:, :], rden[:, :], ALU.mult))
                zrb, zib = (bc(z[:, :].unsqueeze(2), [64, 64, 16]) for z in (zr, zi))
                pw = "g (p w) -> g p w"
                br, bi = (b_in[:, i, :].rearrange(pw, w=16) for i in range(2))
                b0, b1 = (bb[:, i, :].rearrange(pw, w=16) for i in range(2))
                tm = tmp[:, :].rearrange(pw, w=16)
                v.tensor_tensor(b0, br, zrb, ALU.mult)
                link(v.tensor_tensor(tm, bi, zib, ALU.mult))
                link(v.tensor_tensor(b0, b0, tm, ALU.subtract))
                v.tensor_tensor(b1, bi, zrb, ALU.mult)
                link(v.tensor_tensor(tm, br, zib, ALU.mult))
                link(v.tensor_tensor(b1, b1, tm, ALU.add))
                link(v.tensor_scalar(c_in[:, :, 1, :], c_in[:, :, 1, :], -1.0, None, ALU.mult))
                v.engine_nop().then_inc(bb_ready, 1)
                for i in range(3):
                    v.wait_ge(turned, i + 1)
                    n = 8 if i < 2 else 4
                    v.tensor_copy(tab[:, 8 * i:8 * i + n, :].rearrange("p k g -> p (k g)"),
                                  bank[i][:, 0:64 * n]).then_inc(moved, 1)
                for i in range(4):
                    dst = x1 if i < 2 else y1
                    h = i % 2
                    v.wait_ge(turned, 4 + i)
                    v.tensor_copy(dst[:, :, 8 * h:8 * h + 8],
                                  bank[3 + i][:, :].rearrange("p (w g) -> p g w", w=8)).then_inc(moved, 1)
                for i in range(4):
                    dst = x2 if i < 2 else y2
                    h = i % 2
                    v.wait_ge(jdone, i + 1)
                    v.tensor_copy(dst[:, 32 * h:32 * h + 32, :].rearrange("p g w -> p (g w)"),
                                  bank[i][:, :]).then_inc(moved, 1)
                v.wait_ge(moved, 11)

            @block.tensor
            def _(pe):
                pe.wait_ge(t20_ready, 1)
                for k in range(20):
                    ins = pe.transpose(bank[k // 8][:, 64 * (k % 8):64 * (k % 8) + 64],
                                       t20[:, k, :, :].rearrange("g r p -> g (r p)"), ident[0:64, 0:64])
                    if k in (7, 15, 19):
                        ins.then_inc(turned, 1)
                pe.wait_ge(bb_ready, 1)
                for which in range(2):
                    for w in range(16):
                        src = (bb[:, :, :].rearrange("g r (p w) -> g (r p) w", w=16)[:, :, w] if which == 0 else
                               c_in[:, w, :, :].rearrange("g r p -> g (r p)"))
                        j = 2 * which + w // 8
                        ins = pe.transpose(bank[3 + j][:, 64 * (w % 8):64 * (w % 8) + 64], src, ident[0:64, 0:64])
                        if w % 8 == 7:
                            ins.then_inc(turned, 1)
                pe.wait_ge(moved, 7)
                for i in range(4):
                    src = (x1 if i < 2 else y1)[:, 32 * (i % 2):32 * (i % 2) + 32, :].rearrange("p g w -> p (g w)")
                    pe.matmul(bank[i][:, :], jmat[:, :], src, start=True, stop=True).then_inc(jdone, 1)


_INS = ['x_prompt', 'x_sample', 'state_ssm', 'cache_cmp_kv', 'cache_slc_kv', 'cache_win_kv', 'page_table',
        'a_w_in', 'a_lambda_re', 'a_lambda_im', 'a_log_dt', 'a_b_re', 'a_b_im', 'a_c_re', 'a_c_im', 'a_d', 'a_w_glu',
        'kv_w', 'cmp_pe', 'cmp_w1', 'cmp_w2', 'b_w_qg', 'b_w_o',
        'moe_w_group', 'moe_w_expert', 'moe_w_gate_up', 'moe_w_down', 'ln_g', 'ln_b']


class Region:

    def __init__(self, arena):
        self.arena = arena

    def __call__(self, off, *shape, dt=F32, np_=P):
        n = int(np.prod(shape))
        if dt is BF16:
            assert n % 2 == 0
            v = self.arena[0:np_, off:off + n // 2].bitcast(BF16)
        else:
            v = self.arena[0:np_, off:off + n]
            if dt is not F32:
                v = v.bitcast(dt)
        if len(shape) == 1:
            return v
        names = "abcdef"[:len(shape)]
        return v.rearrange(f"p ({' '.join(names)}) -> p {' '.join(names)}", **dict(zip(names[1:], shape[1:])))


class Split:

    def __init__(self, n, full, used):
        self.n, self.full, self.used = n, full, used

    def claim(self, pe, job):
        old = job - self.n
        if old >= 0:
            pe.wait_ge(self.used[old % 2], old // 2 + 1)
        return job % self.n

    def done(self, ins):
        ins.then_inc(self.full, 1)

    def all_used(self, eng, jobs):
        if jobs > 0:
            eng.wait_ge(self.used[0], (jobs + 1) // 2)
        if jobs > 1:
            eng.wait_ge(self.used[1], jobs // 2)


S5_TAB, S5_X1, S5_X2, S5_Y1, S5_Y2, S5_FREE = 0, 1280, 2304, 3328, 4352, 5376


def s5_inputs(nc, A, R, ident, u_dram):
    with Scope(nc, "inp") as s:
        w = R(5376, KT, D)
        xT = R(13568, KT, CH, NC_)
        uT = R(18176, KT, CH * NC_)
        xin = R(22784, 2, D)
        bank = s.banks()
        w_in, stored = s.sem("w_in"), s.sem("stored")
        x_in = [s.sem(f"x_in{i}") for i in range(2)]
        full, used = s.sem("full"), (s.sem("used_v"), s.sem("used_a"))
        ring = Split(8, full, used)
        NJ = 2 * NT
        half = CH * NC_ // 2

        def x_rows(i):
            if i < 4:
                return A["x_prompt"][0, 128 * i:128 * i + 128, :]
            return A["x_sample"].rearrange("b t d -> (b t) d")

        def turn_out(eng_copy, i, h):
            n = TILES[i][1]
            job = 2 * i + h
            src = bank[job % 8][:, :].rearrange("p (k t) -> p k t", k=4)[:, :, 0:n].rearrange("p k (c s) -> p k c s", s=CH)
            dst = xT[:, 4 * h:4 * h + 4, :, 16 * i:16 * i + n // CH].rearrange("p k s c -> p k c s")
            return [eng_copy(dst[:, k], src[:, k]) for k in range(4)][-1]

        with nc.Block() as block:
            @block.sync
            def _(sp):
                for i in range(NT):
                    if i >= 2:
                        sp.wait_ge(full, 2 * (i - 1))
                    sp.dma_start(xin[0:TILES[i][1], i % 2, :], x_rows(i)).then_inc(x_in[i % 2], 16)
                    if i == 1:
                        sp.dma_start(w[:, :, :], A["a_w_in"][0].rearrange("(k p) n -> p k n", p=P)).then_inc(w_in, 16)
                for m in range(KT):
                    ring.all_used(sp, NJ + 2 * m + 2)
                    sp.dma_start(u_dram[P * m:P * m + P, :], uT[:, m, :]).then_inc(stored, 16)
                sp.wait_ge(stored, 16 * KT)

            @block.tensor
            def _(pe):
                for i, (_, n) in enumerate(TILES):
                    pe.wait_ge(x_in[i % 2], 16 * (i // 2 + 1))
                    for h in range(2):
                        b = ring.claim(pe, 2 * i + h)
                        for k in range(4):
                            ins = pe.transpose(bank[b][:, P * k:P * k + n],
                                               xin[0:n, i % 2, P * (4 * h + k):P * (4 * h + k + 1)], ident[0:n, 0:n])
                        ring.done(ins)
                pe.wait_ge(w_in, 16)
                ring.all_used(pe, NJ)
                xf = xT[:, :, :, :].rearrange("p k s c -> p k (s c)")
                for m in range(KT):
                    for n in range(2):
                        b = ring.claim(pe, NJ + 2 * m + n)
                        for k in range(KT):
                            ins = pe.matmul(bank[b][:, 0:half], w[:, k, P * m:P * m + P],
                                            xf[:, k, half * n:half * n + half], start=(k == 0), stop=(k == KT - 1))
                        ring.done(ins)

            def empty(eng, copy, me):
                for i in range(NT):
                    eng.wait_ge(full, 2 * i + me + 1)
                    turn_out(copy, i, me).then_inc(used[me], 1)
                for m in range(KT):
                    job = NJ + 2 * m + me
                    eng.wait_ge(full, job + 1)
                    copy(uT[:, m, half * me:half * me + half], bank[job % 8][:, 0:half]).then_inc(used[me], 1)

            @block.vector
            def _(v):
                empty(v, v.tensor_copy, 0)

            @block.scalar
            def _(act):
                empty(act, nc.scalar.copy, 1)


def s5_matrices(nc, A, R, ident, toep, et, o):
    with Scope(nc, "mat") as s:
        tab = R(S5_TAB, 20, 64)
        x1, x2, y1, y2 = (R(off, SG, SW) for off in (S5_X1, S5_X2, S5_Y1, S5_Y2))
        e = R(5376, SG, CH, SW)
        kb = R(38144, SG, SW)
        tt = R(29952, CH, SG, SW)
        tv, tp = R(39168, 2, SG, SW), R(41216, 2, SG, SW)
        bank = s.banks()
        dve, pool_, e_ready, zeroed, shifted = (s.sem(n) for n in ("dve", "pool", "e_ready", "zeroed", "shifted"))
        full, used = s.sem("full"), (s.sem("used_v"), s.sem("used_a"))
        k_full, k_used = s.sem("k_full"), s.sem("k_used")
        ring = Split(6, full, used)

        def coef(row):
            return bc(tab[:, row, :].unsqueeze(2), [P, SG, SW])

        with nc.Block() as block:
            @block.vector
            def _(v):
                link = Link(v, dve)
                for st in range(CH):
                    k = CH - 1 - st
                    v.tensor_tensor(tv[:, 0], x1, coef(k), ALU.mult)
                    link(v.tensor_tensor(tv[:, 1], x2, coef(9 + k), ALU.mult))
                    link(v.tensor_tensor(e[:, :, st, :], tv[:, 0], tv[:, 1], ALU.add))
                v.engine_nop().then_inc(e_ready, 1)
                for h in range(2):
                    v.wait_ge(k_full, h + 1)
                    v.tensor_copy(kb[:, 32 * h:32 * h + 32, :].rearrange("p g w -> p (g w)"),
                                  bank[6 + h][:, :]).then_inc(k_used, 1)
                for j in range(0, 16, 2):
                    v.wait_ge(full, j + 1)
                    v.tensor_copy(et[:, 4 * j:4 * j + 4, :].rearrange("p g m -> p (g m)"),
                                  bank[j % 6][:, :]).then_inc(used[0], 1)
                v.wait_ge(full, 16)
                for t in range(0, CH, 2):
                    if t == 0:
                        v.wait_ge(shifted, 16 * CH)
                    ins = v.tensor_copy(toep[:, :, t, :], tt[:, t, :, :])
                link(ins)

            @block.scalar
            def _(act):
                for j in range(1, 16, 2):
                    act.wait_ge(full, j + 1)
                    nc.scalar.copy(et[:, 4 * j:4 * j + 4, :].rearrange("p g m -> p (g m)"),
                                   bank[j % 6][:, :]).then_inc(used[1], 1)
                act.wait_ge(full, 16)
                act.wait_ge(shifted, 16 * CH)
                for t in range(1, CH, 2):
                    nc.scalar.copy(toep[:, :, t, :], tt[:, t, :, :]).then_inc(used[1], 1)

            @block.tensor
            def _(pe):
                pe.wait_ge(e_ready, 1)
                for g in range(SG):
                    ins = pe.matmul(bank[6 + g // 32][:, SW * (g % 32):SW * (g % 32) + SW],
                                    e[:, g, :, :].rearrange("p s w -> p (s w)"), y1[:, g, :],
                                    start=True, stop=True)
                    if g % 32 == 31:
                        ins.then_inc(k_full, 1)
                for j in range(16):
                    b = ring.claim(pe, j)
                    for q in range(4):
                        ins = pe.transpose(bank[b][:, P * q:P * q + P],
                                           e[:, 4 * j + q, :, :].rearrange("p s w -> p (s w)"), ident[:, :])
                    ring.done(ins)

            @block.gpsimd
            def _(pool):
                pool.memset(tt[:, :, :, :], 0.0).then_inc(zeroed, 1)
                link = Link(pool, pool_)
                for t in range(CH):
                    k = t + 1
                    pool.tensor_tensor(tp[:, 0], y1, coef(k), ALU.mult)
                    link(pool.tensor_tensor(tp[:, 1], y2, coef(9 + k), ALU.mult))
                    link(pool.tensor_tensor(o[:, :, t, :], tp[:, 0], tp[:, 1], ALU.subtract))

            @block.sync
            def _(sp):
                sp.wait_ge(zeroed, 1)
                sp.wait_ge(k_used, 2)
                for t in range(CH):
                    n = SW * (t + 1)
                    sp.dma_start(tt[0:n, t, :, :], kb[P - n:P, :, :]).then_inc(shifted, 16)


def s5_chunks(nc, A, R, toep, et, u_dram, hs):
    with Scope(nc, "chk") as s:
        tab = R(S5_TAB, 20, 64)
        uc, v_, y_ = R(29952, SG, NC_), R(34560, SG, NC_), R(39168, SG, NC_)
        cos_, sin_ = R(43776, SG, NCP), R(47872, SG, NCP)
        cidx = R(S5_X1, NCP)
        sh = R(21760 - 4096, SG, NCP)
        bank = s.banks()
        h_in, uin, dve, idx = (s.sem(n) for n in ("h_in", "uin", "dve", "idx"))
        full, used, ang_ready, sins, et_used = (s.sem(n) for n in ("full", "used", "ang_ready", "sins", "et_used"))
        GB = 7
        NB = -(-SG // GB)
        jobs = [(m, q, list(range(GB * q, min(GB * q + GB, SG)))) for m in range(2) for q in range(NB)]

        def flat(x):
            return x.rearrange("p g c -> p (g c)")

        with nc.Block() as block:
            @block.sync
            def _(sp):
                sp.dma_start(hs, A["state_ssm"]).then_inc(h_in, 16)
                for st in range(CH):
                    sp.dma_start(uc[SW * st:SW * st + SW, :, :],
                                 u_dram.rearrange("(g w) (s c) -> w s g c", w=SW, s=CH)[:, st]).then_inc(uin, 16)
                sp.wait_ge(h_in, 16)

            @block.tensor
            def _(pe):
                pe.wait_ge(uin, 16 * CH)
                for j, (m, q, gs) in enumerate(jobs):
                    if j >= 8:
                        pe.wait_ge(used, j - 7)
                    for n, g in enumerate(gs):
                        lhs = et[:, g] if m == 0 else toep[:, g].rearrange("p t w -> p (t w)")
                        ins = pe.matmul(bank[j % 8][:, NC_ * n:NC_ * n + NC_], lhs, uc[:, g, :], start=True, stop=True)
                    ins.then_inc(full, 1)

            @block.scalar
            def _(act):
                for j, (m, q, gs) in enumerate(jobs):
                    act.wait_ge(full, j + 1)
                    dst = (v_, y_)[m]
                    nc.scalar.copy(flat(dst[:, gs[0]:gs[-1] + 1, :]), bank[j % 8][:, 0:NC_ * len(gs)]).then_inc(used, 1)
                act.wait_ge(ang_ready, 1)
                nc.scalar.activation(sh, cos_, ACT.Sin, scale=0.5).then_inc(sins, 1)
                nc.scalar.activation(sin_, cos_, ACT.Sin).then_inc(sins, 1)

            @block.gpsimd
            def _(pool):
                pool.iota(cidx, pattern=[[1, NCP]], base=0, channel_multiplier=0,
                          allow_small_or_imprecise_dtypes=True).then_inc(idx, 1)

            @block.vector
            def _(v):
                link = Link(v, dve)
                v.wait_ge(idx, 1)
                link(v.tensor_tensor(cos_, bc(tab[:, 18, :].unsqueeze(2), [P, SG, NCP]),
                                     bc(cidx.unsqueeze(1), [P, SG, NCP]), ALU.mult))
                link(v.tensor_scalar(sin_, cos_, INV_2PI, MAGIC, ALU.mult, ALU.add))
                link(v.tensor_scalar(sin_, sin_, MAGIC, None, ALU.subtract))
                for c in (C1, C2, C3):
                    link(v.scalar_tensor_tensor(out=cos_, in0=sin_, scalar=-c, in1=cos_, op0=ALU.mult, op1=ALU.add))
                v.engine_nop().then_inc(ang_ready, 1)
                v.wait_ge(sins, 2)
                link(v.tensor_tensor(cos_, sh, sh, ALU.mult))
                link(v.tensor_scalar(cos_, cos_, -2.0, 1.0, ALU.mult, ALU.add))


def s5_scan(nc, R, jmat, hs, ho):
    with Scope(nc, "scan") as s:
        tab = R(S5_TAB, 20, 64)
        v_ = R(34560, SG, NC_)
        cos_, sin_ = R(43776, SG, NCP), R(47872, SG, NCP)
        rho, gc, g_, t_ = R(5376, SG, NCP), R(9472, SG, NCP), R(13568, SG, NCP), R(17664, SG, NCP)
        hp = R(29952, SG, NC_)
        th = R(S5_X2, DEC_B, SG)
        bank = s.banks()
        dve, turned, gs_ready, rho_ready, pooled = (s.sem(n) for n in ("dve", "turned", "gs_ready", "rho_ready", "pooled"))
        h_read = s.sem("h_read")
        Q = 8
        with nc.Block() as block:
            @block.tensor
            def _(pe):
                for q in range(8):
                    pe.matmul(bank[q][:, :], jmat[:, :], v_[:, Q * q:Q * q + Q, 0:NCP], start=True, stop=True).then_inc(turned, 1)
                for q in range(8):
                    pe.wait_ge(gs_ready, q + 1)
                    pe.matmul(bank[q][:, :], jmat[:, :], t_[:, Q * q:Q * q + Q, :], start=True, stop=True).then_inc(turned, 1)
                pe.wait_ge(h_read, 1)
                pe.matmul(bank[0][:, :], jmat[:, :], hs.rearrange("p b g -> p (b g)"), start=True, stop=True).then_inc(turned, 1)

            @block.gpsimd
            def _(pool):
                pool.tensor_copy(rho, bc(tab[:, 19, :].unsqueeze(2), [P, SG, NCP])).then_inc(pooled, 1)
                pool.wait_ge(pooled, 1)
                pool.memset(rho[:, :, 0:1], 0.0).then_inc(rho_ready, 1)
                pool.memset(hp[:, :, 0:1], 0.0).then_inc(rho_ready, 1)
                pool.tensor_copy(hp[:, :, NCP:NC_], hs.rearrange("p b g -> p g b")).then_inc(rho_ready, 1)

            @block.vector
            def _(v):
                link = Link(v, dve)
                link(v.tensor_tensor(g_, v_[:, :, 0:NCP], cos_, ALU.mult))
                for q in range(8):
                    g8 = slice(Q * q, Q * q + Q)
                    v.wait_ge(turned, q + 1)
                    ins = v.tensor_tensor(t_[:, g8, :], bank[q][:, :].rearrange("p (g c) -> p g c", g=Q), sin_[:, g8, :], ALU.mult)
                link(ins)
                link(v.tensor_tensor(g_, g_, t_, ALU.subtract))
                v.wait_ge(rho_ready, 3)
                flat = "p g c -> p (g c)"
                link(v.tensor_tensor_scan(gc.rearrange(flat), rho.rearrange(flat), g_.rearrange(flat), 0.0, ALU.mult, ALU.add))
                for q in range(8):
                    g8 = slice(Q * q, Q * q + Q)
                    v.tensor_tensor(t_[:, g8, :], gc[:, g8, :], sin_[:, g8, :], ALU.mult).then_inc(gs_ready, 1)
                link(v.tensor_tensor(g_, gc, cos_, ALU.mult))
                for q in range(8):
                    g8 = slice(Q * q, Q * q + Q)
                    v.wait_ge(turned, 9 + q)
                    src = bank[q][:, :].rearrange("p (g c) -> p g c", g=Q)
                    v.tensor_tensor(hp[:, g8, 1:NCP], g_[:, g8, 0:NCP - 1], src[:, :, 0:NCP - 1], ALU.add)
                    last = v.tensor_tensor(ho[:, 8, g8], g_[:, g8, NCP - 1], src[:, :, NCP - 1], ALU.add)
                    if q == 0:
                        last.then_inc(h_read, 1)
                v.wait_ge(turned, 17)
                a8r, a8i = (bc(tab[:, r, :].unsqueeze(1), [P, DEC_B, SG]) for r in (8, 17))
                v.tensor_tensor(ho[:, 0:8, :], hs, a8r, ALU.mult)
                link(v.tensor_tensor(th, bank[0][:, :].rearrange("p (b g) -> p b g", b=DEC_B), a8i, ALU.mult))
                link(v.tensor_tensor(ho[:, 0:8, :], ho[:, 0:8, :], th, ALU.add))
                link(v.tensor_tensor(ho[:, 0:8, :], ho[:, 0:8, :], v_[:, :, NCP:NC_].rearrange("p g b -> p b g"), ALU.add))


def s5_outputs(nc, R, o, y_dram, ho, h_out):
    with Scope(nc, "out") as s:
        hp, y_ = R(29952, SG, NC_), R(39168, SG, NC_)
        bank = s.banks()
        full, used, stored = s.sem("full"), s.sem("used"), s.sem("stored")
        GB = 7
        NB = -(-SG // GB)
        with nc.Block() as block:
            @block.sync
            def _(sp):
                sp.dma_start(h_out, ho).then_inc(stored, 16)
                sp.wait_ge(used, NB)
                for st in range(CH):
                    sp.dma_start(y_dram.rearrange("(g w) (s c) -> w s g c", w=SW, s=CH)[:, st],
                                 y_[SW * st:SW * st + SW, :, :]).then_inc(stored, 16)
                sp.wait_ge(stored, 16 * (CH + 1))

            @block.tensor
            def _(pe):
                for q in range(NB):
                    if q >= 8:
                        pe.wait_ge(used, q - 7)
                    for n, g in enumerate(range(GB * q, min(GB * q + GB, SG))):
                        ins = pe.matmul(bank[q % 8][:, NC_ * n:NC_ * n + NC_], o[:, g].rearrange("p t w -> p (t w)"),
                                        hp[:, g, :], start=True, stop=True)
                    ins.then_inc(full, 1)

            @block.vector
            def _(v):
                for q in range(NB):
                    a, b = GB * q, min(GB * q + GB, SG)
                    v.wait_ge(full, q + 1)
                    yy = y_[:, a:b, :].rearrange("p g c -> p (g c)")
                    v.tensor_tensor(yy, bank[q % 8][:, 0:NC_ * (b - a)], yy, ALU.add).then_inc(used, 1)


X_OFF, XT_OFF, GB_OFF, FREE = 0, 5120, 9728, 11776


def glu(nc, A, R, x, u_dram, y_dram):
    with Scope(nc, "glu") as s:
        yT, uT = R(FREE, KT, CH, NC_), R(FREE + 4608, KT, CH, NC_)
        gT = R(FREE + 9216, KT, NC_, CH)
        w = R(FREE + 13824, KT, 2 * D)
        sg = R(FREE + 30208, 2, 512)
        fv = R(FREE + 31232, 2, 512)
        d = R(FREE + 32256, KT)
        bank = s.banks()
        names = ("x_in", "d_in", "w_in", "dve", "skip_ready", "g_ready", "full", "sig", "used", "fused")
        x_in, d_in, w_in, dve, skip_ready, g_ready, full, sig, used, fused = (s.sem(n) for n in names)
        y_in = [s.sem(f"y_in{h}") for h in range(2)]
        jobs = [(i, h) for i in range(NT) for h in range(2)]
        with nc.Block() as block:
            @block.sync
            def _(sp):
                sp.dma_start(d, A["a_d"]).then_inc(d_in, 16)
                for h in range(2):
                    ks = slice(4 * h, 4 * h + 4)
                    for dst, src in ((yT, y_dram), (uT, u_dram)):
                        sp.dma_start(dst[:, ks].rearrange("p k s c -> p k (s c)"),
                                     src.rearrange("(k p) t -> p k t", p=P)[:, ks]).then_inc(y_in[h], 16)
                for h in range(2):
                    sp.dma_start(w[:, 4 * h:4 * h + 4, :],
                                 A["a_w_glu"][0].rearrange("(k p) n -> p k n", p=P)[:, 4 * h:4 * h + 4]).then_inc(w_in, 16)
                sp.dma_start(x[:, 0:4, :], A["x_prompt"][0].rearrange("(i p) d -> p i d", p=P)).then_inc(x_in, 16)
                sp.dma_start(x[0:64, 4, :], A["x_sample"].rearrange("b t d -> (b t) d")).then_inc(x_in, 16)

            @block.vector
            def _(v):
                v.wait_ge(d_in, 16)
                for k in range(KT):
                    v.wait_ge(y_in[k // 4], 32)
                    v.scalar_tensor_tensor(out=yT[:, k].rearrange("p s c -> p (s c)"), in0=uT[:, k].rearrange("p s c -> p (s c)"),
                                           scalar=d[:, k:k + 1], in1=yT[:, k].rearrange("p s c -> p (s c)"),
                                           op0=ALU.mult, op1=ALU.add).then_inc(skip_ready, 1)
                v.wait_ge(x_in, 32)
                for j, (i, h) in enumerate(jobs):
                    n = TILES[i][1]
                    xs = x[0:n, i, 512 * h:512 * h + 512]
                    v.wait_ge(sig, j + 1)
                    v.tensor_tensor(fv[0:n, j % 2], bank[(2 * j) % 8][0:n, :], sg[0:n, j % 2], ALU.mult).then_inc(used, 1)
                    v.wait_ge(used, j + 1)
                    v.scalar_tensor_tensor(out=xs, in0=xs, scalar=ALPHA, in1=fv[0:n, j % 2],
                                           op0=ALU.mult, op1=ALU.add).then_inc(fused, 1)

            @block.scalar
            def _(act):
                for k in range(KT):
                    act.wait_ge(skip_ready, k + 1)
                    nc.scalar.activation(gT[:, k].rearrange("p c s -> p s c"), yT[:, k], ACT.Gelu_apprx_tanh).then_inc(g_ready, 1)
                for j, (i, h) in enumerate(jobs):
                    n = TILES[i][1]
                    act.wait_ge(full, j + 1)
                    if j >= 2:
                        act.wait_ge(used, j - 1)
                    nc.scalar.activation(sg[0:n, j % 2], bank[(2 * j + 1) % 8][0:n, :], ACT.Sigmoid).then_inc(sig, 1)

            @block.tensor
            def _(pe):
                pe.wait_ge(g_ready, KT)
                pe.wait_ge(w_in, 32)
                for j, (i, h) in enumerate(jobs):
                    t0, n = TILES[i]
                    if j >= 4:
                        pe.wait_ge(used, j - 3)
                    for part in range(2):
                        for k in range(KT):
                            ins = pe.matmul(bank[(2 * j + part) % 8][0:n, :],
                                            gT[:, k].rearrange("p c s -> p (c s)")[:, t0:t0 + n],
                                            w[:, k, D * part + 512 * h:D * part + 512 * h + 512],
                                            start=(k == 0), stop=(k == KT - 1))
                    ins.then_inc(full, 1)


def layer_norm(nc, A, R, name, layer, which, ident, x, outs=None, x_dram=None, turn=True):
    with Scope(nc, name) as s:
        xT = R(XT_OFF, KT, TOK)
        gb = R(GB_OFF, 2, D)
        st = R(FREE, NT, 2, 6)
        mv = R(FREE + 64, NT, 2)
        sd = R(FREE + 80, NT)
        rs = R(FREE + 88, NT)
        bank = s.banks()
        gb_in, dve, stats, root, inv, normed, scaled, shifted, full, used, stored = (
            s.sem(n) for n in ("gb_in", "dve", "stats", "root", "inv", "normed", "scaled", "shifted", "full", "used", "stored"))
        with nc.Block() as block:
            @block.sync
            def _(sp):
                sp.dma_start(gb[:, 0, :], A["ln_g"][layer, which].partition_broadcast(P)).then_inc(gb_in, 16)
                sp.dma_start(gb[:, 1, :], A["ln_b"][layer, which].partition_broadcast(P)).then_inc(gb_in, 16)
                n_st = 0
                for i, (t0, n) in enumerate(TILES):
                    sp.wait_ge(shifted, i + 1)
                    if x_dram is not None:
                        sp.dma_start(x_dram[t0:t0 + n, :], x[0:n, i, :]).then_inc(stored, 16)
                        n_st += 1
                    if outs is not None:
                        dst = outs[0][0, t0:t0 + n, :] if i < 4 else outs[1].rearrange("b t d -> (b t) d")
                        sp.dma_start(dst, x[0:n, i, :]).then_inc(stored, 16)
                        n_st += 1
                sp.wait_ge(stored, 16 * n_st)

            @block.vector
            def _(v):
                link = Link(v, dve)
                for i, (t0, n) in enumerate(TILES):
                    for h in range(2):
                        ins = v.bn_stats(st[0:n, i, h, :], x[0:n, i, 512 * h:512 * h + 512])
                    link(ins)
                    v.bn_aggr(mv[0:n, i, :], st[0:n, i].rearrange("p h k -> p (h k)")).then_inc(stats, 1)
                for i, (t0, n) in enumerate(TILES):
                    v.wait_ge(root, i + 1)
                    link(v.reciprocal(rs[0:n, i:i + 1], sd[0:n, i:i + 1]))
                    v.tensor_scalar(x[0:n, i, :], x[0:n, i, :], mv[0:n, i, 0:1], rs[0:n, i:i + 1],
                                    ALU.subtract, ALU.mult).then_inc(normed, 1)
                    if i == 0:
                        v.wait_ge(gb_in, 32)
                    v.wait_ge(normed, i + 1)
                    v.tensor_tensor(x[0:n, i, :], x[0:n, i, :], gb[0:n, 0, :], ALU.mult).then_inc(scaled, 1)

            @block.gpsimd
            def _(pool):
                for i, (t0, n) in enumerate(TILES):
                    pool.wait_ge(scaled, i + 1)
                    pool.tensor_tensor(x[0:n, i, :], x[0:n, i, :], gb[0:n, 1, :], ALU.add).then_inc(shifted, 1)

            @block.tensor
            def _(pe):
                if not turn:
                    return
                for i, (t0, n) in enumerate(TILES):
                    pe.wait_ge(shifted, i + 1)
                    for h in range(2):
                        j = 2 * i + h
                        if j >= 8:
                            pe.wait_ge(used, j - 7)
                        for k in range(4):
                            ins = pe.transpose(bank[j % 8][:, P * k:P * k + n],
                                               x[0:n, i, P * (4 * h + k):P * (4 * h + k) + P], ident[0:n, 0:n])
                        ins.then_inc(full, 1)

            @block.scalar
            def _(act):
                for i, (t0, n) in enumerate(TILES):
                    act.wait_ge(stats, i + 1)
                    nc.scalar.activation(sd[0:n, i:i + 1], mv[0:n, i, 1:2], ACT.Sqrt, bias=A["eps"][0:n, 0:1]).then_inc(root, 1)
                if not turn:
                    return
                for i, (t0, n) in enumerate(TILES):
                    for h in range(2):
                        j = 2 * i + h
                        act.wait_ge(full, j + 1)
                        nc.scalar.copy(xT[:, 4 * h:4 * h + 4, t0:t0 + n],
                                       bank[j % 8][:, :].rearrange("p (k t) -> p k t", k=4)[:, :, 0:n]).then_inc(used, 1)


RT_OFF = FREE + 0
BE_OFF = FREE + 48
DST_OFF = FREE + 96
WT_OFF = FREE + 112
MOE_FREE = FREE + 128
BIG = 1e30


def route(nc, A, R, name, layer, row_tok):
    with Scope(nc, name) as s:
        xT = R(XT_OFF, KT, TOK)
        rt, be = R(RT_OFF, NBLK, dt=I32), R(BE_OFF, NBLK, dt=I32)
        dst, wt = R(DST_OFF, NT, 2, dt=I32), R(WT_OFF, 2, NT)
        at = [MOE_FREE]

        def place(*shape, dt=F32):
            n = int(np.prod(shape))
            at[0] += n + n % 2
            return R(at[0] - n - n % 2, *shape, dt=dt)

        wr = place(KT, NG + NE)
        lg, le, le2 = place(NT, NG), place(NT, NE), place(NT, NE)
        ig, ie, ib = place(NT, NG), place(NT, NE), place(NBLK)
        keyg, keye = place(NT, NG), place(NT, NE)
        ohg, oh = place(NT, NG), place(2, NT, NE)
        top = place(3, NT)
        low, gsum, gw, dif, ed, inv = (place(NT) for _ in range(6))
        ex = place(NT, NG)
        both = place(NT, NE)
        tri, ones = place(P), place(P)
        total, nblk, pend, base, one32 = (place(NE) for _ in range(5))
        pos, sel = place(NT, NE), place(NT, NE)
        dstf = place(NT, 2)
        cmpb, bef = place(NBLK, NE), place(NBLK)
        tok = place(NT, dt=I32)
        zero = place(NBLK, dt=I32)
        bank = s.banks(3)
        w_in, made, zeroed, cleared, logit, dve, lmoved, exp_in, exp_out, ohs, ranked, dests, scattered, rt_in = (
            s.sem(n) for n in ("w_in", "made", "zeroed", "cleared", "logit", "dve", "lmoved", "exp_in", "exp_out", "ohs",
                               "ranked", "dests", "scattered", "rt_in"))
        with nc.Block() as block:
            @block.sync
            def _(sp):
                sp.dma_start(wr[:, :, 0:NG], A["moe_w_group"][layer].rearrange("(k p) n -> p k n", p=P)).then_inc(w_in, 16)
                sp.dma_start(wr[:, :, NG:], A["moe_w_expert"][layer].rearrange("(k p) n -> p k n", p=P)).then_inc(w_in, 16)
                sp.wait_ge(zeroed, 1)
                sp.dma_start(row_tok.rearrange("(p b) o -> p (b o)", p=P), zero).then_inc(cleared, 16)
                sp.wait_ge(scattered, 16 * 2 * NT)
                sp.dma_start(rt, row_tok.rearrange("(b r) o -> r (b o)", r=P), allow_slow_non_contiguous=True).then_inc(rt_in, 16)
                sp.wait_ge(rt_in, 16)

            @block.gpsimd
            def _(pool):
                pool.memset(zero, 0).then_inc(zeroed, 1)
                pool.iota(ig, pattern=[[0, NT], [1, NG]], base=-64, channel_multiplier=0,
                          allow_small_or_imprecise_dtypes=True).then_inc(made, 1)
                pool.iota(ie, pattern=[[0, NT], [1, NE]], base=-64, channel_multiplier=0,
                          allow_small_or_imprecise_dtypes=True).then_inc(made, 1)
                pool.iota(ib, pattern=[[1, NBLK]], base=0, channel_multiplier=0,
                          allow_small_or_imprecise_dtypes=True).then_inc(made, 1)
                pool.iota(tok, pattern=[[P, NT]], base=0, channel_multiplier=1).then_inc(made, 1)
                pool.memset(ones, 1.0).then_inc(made, 1)
                pool.memset(one32, 1.0).then_inc(made, 1)
                pool.memset(lg, 0.0).then_inc(made, 1)
                pool.memset(le, 0.0).then_inc(made, 1)
                pool.wait_ge(made, 8)
                pool.affine_select(out=tri, in_=ones, compare_op=ALU.is_gt, fill=0.0, base=0,
                                   pattern=[[1, P]], channel_multiplier=-1).then_inc(made, 1)
                pool.wait_ge(dests, 1)
                pool.wait_ge(cleared, 16)
                for i, (t0, n) in enumerate(TILES):
                    for k in range(2):
                        pool.indirect_dma_start(out=row_tok, out_offset=bass.IndirectOffsetOnAxis(ap=dst[0:n, i, k:k + 1], axis=0),
                                                in_=tok[0:n, i:i + 1], in_offset=None).then_inc(scattered, 16)
                pool.wait_ge(scattered, 16 * 2 * NT)

            @block.tensor
            def _(pe):
                pe.wait_ge(w_in, 32)
                for i, (t0, n) in enumerate(TILES):
                    for k in range(KT):
                        ins = pe.matmul(bank[0][0:n, 36 * i:36 * i + 36], xT[:, k, t0:t0 + n], wr[:, k, :],
                                        start=(k == 0), stop=(k == KT - 1))
                ins.then_inc(logit, 1)
                pe.wait_ge(ohs, 1)
                pe.wait_ge(made, 9)
                for i in range(NT):
                    for q in range(i + 1):
                        ins = pe.matmul(bank[1][:, NE * i:NE * i + NE], tri if q == i else ones, both[:, q, :],
                                        start=(q == 0), stop=(q == i))
                for q in range(NT):
                    ins = pe.matmul(bank[2][:, 0:NE], ones, both[:, q, :], start=(q == 0), stop=(q == NT - 1))
                ins.then_inc(ranked, 1)

            @block.scalar
            def _(act):
                act.wait_ge(exp_in, 1)
                nc.scalar.activation(ex, ex, ACT.Exp).then_inc(exp_out, 1)
                act.wait_ge(exp_in, 2)
                nc.scalar.activation(ed, dif, ACT.Exp).then_inc(exp_out, 1)

            @block.vector
            def _(v):
                link = Link(v, dve)

                def first_largest(vals, idx, key, one, most, n):
                    link(v.tensor_reduce(most, vals, AX, ALU.max))
                    link(v.tensor_tensor(key, vals, bc(most.unsqueeze(2), [P, NT, n]), ALU.is_equal))
                    link(v.tensor_tensor(key, key, idx, ALU.mult))
                    link(v.tensor_reduce(low, key, AX, ALU.min))
                    link(v.tensor_tensor(one, idx, bc(low.unsqueeze(2), [P, NT, n]), ALU.is_equal))

                v.wait_ge(made, 8)
                v.wait_ge(logit, 1)
                src = bank[0][:, 0:36 * NT].rearrange("p (i n) -> p i n", i=NT)
                for np_, sl in ((P, slice(0, 4)), (64, slice(4, 5))):
                    v.tensor_copy(lg[0:np_, sl], src[0:np_, sl, 0:NG])
                    ins = v.tensor_copy(le[0:np_, sl], src[0:np_, sl, NG:36])
                link(ins)
                first_largest(lg, ig, keyg, ohg, top[:, 2], NG)
                link(v.tensor_tensor(ex, lg, bc(top[:, 2].unsqueeze(2), [P, NT, NG]), ALU.subtract))
                v.engine_nop().then_inc(exp_in, 1)
                link(v.tensor_scalar(keyg, ohg, 1.0, BIG, ALU.subtract, ALU.mult))
                for i in range(NT):
                    ins = v.tensor_tensor(le2[:, i, :].rearrange("p (g e) -> p g e", g=NG), le[:, i, :].rearrange("p (g e) -> p g e", g=NG),
                                          bc(keyg[:, i, :].unsqueeze(2), [P, NG, EPG]), ALU.add)
                link(ins)
                first_largest(le2, ie, keye, oh[:, 0], top[:, 0], NE)
                flat = "p i e -> p (i e)"
                link(v.scalar_tensor_tensor(out=le2.rearrange(flat), in0=oh[:, 0].rearrange(flat), scalar=-2 * BIG,
                                            in1=le2.rearrange(flat), op0=ALU.mult, op1=ALU.add))
                first_largest(le2, ie, keye, oh[:, 1], top[:, 1], NE)
                link(v.tensor_tensor(dif, top[:, 1], top[:, 0], ALU.subtract))
                v.engine_nop().then_inc(exp_in, 1)
                link(v.tensor_tensor(both, oh[:, 0], oh[:, 1], ALU.add))
                link(v.memset(both[64:P, 4, :], 0.0))
                v.engine_nop().then_inc(ohs, 1)
                v.wait_ge(exp_out, 2)
                link(v.tensor_reduce(gsum, ex, AX, ALU.add))
                link(v.reciprocal(gw, gsum))
                link(v.tensor_scalar(dif, ed, 1.0, None, ALU.add))
                link(v.reciprocal(inv, dif))
                link(v.tensor_tensor(wt[:, 0], gw, inv, ALU.mult))
                link(v.tensor_tensor(wt[:, 1], wt[:, 0], ed, ALU.mult))
                v.wait_ge(ranked, 1)
                link(v.tensor_copy(total, bank[2][:, 0:NE]))
                link(v.tensor_scalar(nblk, total, 0.0, None, ALU.is_gt))
                for q in range(1, -(-TOK // RB)):
                    link(v.scalar_tensor_tensor(out=nblk, in0=total, scalar=float(RB * q), in1=nblk, op0=ALU.is_gt, op1=ALU.add))
                link(v.tensor_tensor_scan(pend, one32, nblk, 0.0, ALU.mult, ALU.add))
                link(v.tensor_tensor(base, pend, nblk, ALU.subtract))
                link(v.tensor_scalar(base, base, float(RB), None, ALU.mult))
                link(v.tensor_tensor(pos, bank[1][:, 0:NE * NT].rearrange("p (i e) -> p i e", i=NT),
                                     bc(base.unsqueeze(1), [P, NT, NE]), ALU.add))
                for k in range(2):
                    link(v.tensor_tensor(sel, oh[:, k], pos, ALU.mult))
                    link(v.tensor_reduce(dstf[:, :, k], sel, AX, ALU.add))
                link(v.tensor_copy(dst, dstf))
                v.engine_nop().then_inc(dests, 1)
                link(v.tensor_tensor(cmpb, bc(pend.unsqueeze(1), [P, NBLK, NE]), bc(ib.unsqueeze(2), [P, NBLK, NE]), ALU.is_le))
                link(v.tensor_reduce(bef, cmpb, AX, ALU.add))
                link(v.tensor_scalar(be, bef, float(NE - 1), None, ALU.min))


def experts(nc, A, R, name, layer, ident, x_dram, y_rows):
    with Scope(nc, name) as s:
        rt, be = R(RT_OFF, NBLK, dt=I32), R(BE_OFF, NBLK, dt=I32)
        at = [MOE_FREE]

        def place(*shape, dt=F32):
            n = int(np.prod(shape))
            at[0] += n
            return R(at[0] - n, *shape, dt=dt)

        wgu = [place(KT, 2 * DE) for _ in range(2)]
        wdn = [place(2, D) for _ in range(2)]
        xg = [place(D) for _ in range(2)]
        xgT = [place(KT, P) for _ in range(2)]
        idx = [place(2, dt=I32) for _ in range(2)]
        sg, h, hT = place(DE), place(DE), [place(2, P) for _ in range(2)]
        y = [place(D) for _ in range(2)]
        bank = s.banks()
        BX, BG, BH, BY = bank[0:2], bank[2:4], bank[4], bank[5:7]
        w_in = [s.sem(f"w_in{i}") for i in range(2)]
        x_in = [s.sem(f"x_in{i}") for i in range(2)]
        y_out = [s.sem(f"y_out{i}") for i in range(2)]
        gather_go = s.sem("gather_go")
        idx_ready, x_turned, xT_ready, gu_done, sg_ready, h_ready, h_turned, hT_ready, dn_done, y0_ready, y1_ready = (
            s.sem(n) for n in ("idx_ready", "x_turned", "xT_ready", "gu_done", "sg_ready", "h_ready", "h_turned", "hT_ready",
                               "dn_done", "y0_ready", "y1_ready"))
        PAIRS = NBLK // 2
        assert NBLK % 2 == 1

        def pairs(eng, body, first=0):
            for b in range(first, 2):
                body(b, b, True)
            with eng.Fori(1, PAIRS) as i:
                for b in range(2):
                    body(2 * i + b, b, False)
            body(NBLK - 1, 0, False)

        with nc.Block() as block:
            @block.sync
            def _(sp):
                def load(b, q, first):
                    e = sp.value_load(be[0:1, bass.ds(b, 1)] if not isinstance(b, int) else be[0:1, b:b + 1], min_val=0, max_val=NE - 1)
                    if not first:
                        sp.wait_ge(dn_done, b - 1)
                    sp.dma_start(wgu[q], A["moe_w_gate_up"][layer, bass.ds(e, 1)].rearrange("o (k p) n -> p (o k) n", p=P)).then_inc(w_in[q], 16)
                    sp.dma_start(wdn[q], A["moe_w_down"][layer, bass.ds(e, 1)].rearrange("o (k p) n -> p (o k) n", p=P)).then_inc(w_in[q], 16)
                pairs(sp, load)

            @block.gpsimd
            def _(pool):
                def gather(b, q, first):
                    if not first:
                        pool.wait_ge(x_turned, b - 1)
                    pool.tensor_copy(idx[q][:, 0:1], rt[:, bass.ds(b, 1)] if not isinstance(b, int) else rt[:, b:b + 1]).then_inc(idx_ready, 1)
                    pool.wait_ge(idx_ready, b + 1)
                    pool.sem_inc(gather_go, 1)
                    pool.indirect_dma_start(out=xg[q], out_offset=None, in_=x_dram,
                                            in_offset=bass.IndirectOffsetOnAxis(ap=idx[q][:, 0:1], axis=0)).then_inc(x_in[q], 16)
                pairs(pool, gather)

            @block.tensor
            def _(pe):
                def turns(b):
                    return b // 2 + 1

                def turn_x(b, q, use, first=False):
                    pe.wait_ge(x_in[q], 16 * use)
                    if not (isinstance(b, int) and b == 0):
                        pe.wait_ge(xT_ready, 2 * b)
                    for k in range(KT):
                        ins = pe.transpose(BX[k // 4][:, P * (k % 4):P * (k % 4) + P], xg[q][:, P * k:P * k + P], ident[:, :])
                    ins.then_inc(x_turned, 1)

                def gate_up(b, q, use, first=False):
                    pe.wait_ge(w_in[q], 32 * use)
                    pe.wait_ge(xT_ready, 2 * b + 2)
                    if not first:
                        pe.wait_ge(h_ready, b - 1)
                    for k in range(KT):
                        ins = pe.matmul(BG[q][:, :], xgT[q][:, k, :], wgu[q][:, k, :], start=(k == 0), stop=(k == KT - 1))
                    ins.then_inc(gu_done, 1)

                def turn_h(b, q, first=False):
                    pe.wait_ge(h_ready, b + 1)
                    if not (isinstance(b, int) and b == 0):
                        pe.wait_ge(hT_ready, b)
                    for k in range(2):
                        ins = pe.transpose(BH[:, P * k:P * k + P], h[:, P * k:P * k + P], ident[:, :])
                    ins.then_inc(h_turned, 1)

                def down(b, q, first=False):
                    pe.wait_ge(hT_ready, b + 1)
                    if not first:
                        pe.wait_ge(y0_ready, b)
                        pe.wait_ge(y1_ready, b)
                    for n in range(2):
                        for k in range(2):
                            ins = pe.matmul(BY[n][:, :], hT[q][:, k, :], wdn[q][:, k, 512 * n:512 * n + 512],
                                            start=(k == 0), stop=(k == 1))
                    ins.then_inc(dn_done, 1)

                turn_x(0, 0, 1)
                gate_up(0, 0, 1, True)
                turn_x(1, 1, 1)
                turn_h(0, 0)
                gate_up(1, 1, 1, True)
                turn_x(2, 0, 2)
                down(0, 0, True)
                turn_h(1, 1)
                with pe.Fori(1, PAIRS) as i:
                    gate_up(2 * i, 0, i + 1)
                    turn_x(2 * i + 1, 1, i + 1)
                    down(2 * i - 1, 1)
                    turn_h(2 * i, 0)
                    gate_up(2 * i + 1, 1, i + 1)
                    turn_x(2 * i + 2, 0, i + 2)
                    down(2 * i, 0)
                    turn_h(2 * i + 1, 1)
                last = NBLK - 1
                gate_up(last, 0, PAIRS + 1)
                down(last - 1, 1)
                turn_h(last, 0)
                down(last, 0)

            @block.vector
            def _(v):
                def rows(b, q):
                    v.wait_ge(x_turned, b + 1)
                    if not (isinstance(b, int) and b < 2):
                        v.wait_ge(gu_done, b - 1)
                    for half in range(2):
                        v.tensor_copy(xgT[q][:, 4 * half:4 * half + 4, :].rearrange("p k t -> p (k t)"),
                                      BX[half][:, :]).then_inc(xT_ready, 1)

                def gated(b, q):
                    v.wait_ge(sg_ready, b + 1)
                    if not (isinstance(b, int) and b == 0):
                        v.wait_ge(h_turned, b)
                    v.tensor_tensor(h, sg, BG[q][:, DE:2 * DE], ALU.mult).then_inc(h_ready, 1)

                def out(b, q, use):
                    v.wait_ge(dn_done, b + 1)
                    if not (isinstance(use, int) and use == 0):
                        v.wait_ge(y_out[q], 16 * use)
                    v.tensor_copy(y[q][:, 0:512], BY[0][:, :]).then_inc(y0_ready, 1)

                rows(0, 0)
                rows(1, 1)
                gated(0, 0)
                rows(2, 0)
                gated(1, 1)
                out(0, 0, 0)

                def pair(i):
                    rows(2 * i + 1, 1)
                    gated(2 * i, 0)
                    out(2 * i - 1, 1, i - 1)
                    rows(2 * i + 2, 0)
                    gated(2 * i + 1, 1)
                    out(2 * i, 0, i)

                pair(1)
                with v.Fori(2, PAIRS) as i:
                    pair(i)
                last = NBLK - 1
                gated(last, 0)
                out(last - 1, 1, PAIRS - 1)
                out(last, 0, PAIRS)

            @block.scalar
            def _(act):
                def silu(b, q):
                    act.wait_ge(gu_done, b + 1)
                    if not (isinstance(b, int) and b == 0):
                        act.wait_ge(h_ready, b)
                    nc.scalar.activation(sg, BG[q][:, 0:DE], ACT.Silu).then_inc(sg_ready, 1)

                def turned(b, q):
                    act.wait_ge(h_turned, b + 1)
                    if not (isinstance(b, int) and b < 2):
                        act.wait_ge(dn_done, b - 1)
                    nc.scalar.copy(hT[q].rearrange("p k t -> p (k t)"), BH[:, 0:2 * P]).then_inc(hT_ready, 1)

                def out(b, q, use):
                    act.wait_ge(dn_done, b + 1)
                    if not (isinstance(use, int) and use == 0):
                        act.wait_ge(y_out[q], 16 * use)
                    nc.scalar.copy(y[q][:, 512:D], BY[1][:, :]).then_inc(y1_ready, 1)
                    act.wait_ge(y0_ready, b + 1)
                    act.wait_ge(y1_ready, b + 1)
                    row = b * RB
                    act.dma_start(y_rows[row:row + RB, :] if isinstance(b, int) else y_rows[bass.ds(row, RB), :], y[q]).then_inc(y_out[q], 16)

                silu(0, 0)
                turned(0, 0)
                silu(1, 1)
                out(0, 0, 0)
                turned(1, 1)

                def pair(i):
                    silu(2 * i, 0)
                    out(2 * i - 1, 1, i - 1)
                    turned(2 * i, 0)
                    silu(2 * i + 1, 1)
                    out(2 * i, 0, i)
                    turned(2 * i + 1, 1)

                pair(1)
                with act.Fori(2, PAIRS) as i:
                    pair(i)
                last = NBLK - 1
                silu(last, 0)
                out(last - 1, 1, PAIRS - 1)
                turned(last, 0)
                out(last, 0, PAIRS)
                act.wait_ge(y_out[0], 16 * (PAIRS + 1))
                act.wait_ge(y_out[1], 16 * PAIRS)


def combine(nc, R, name, x, y_rows):
    with Scope(nc, name) as s:
        dst, wt = R(DST_OFF, NT, 2, dt=I32), R(WT_OFF, 2, NT)
        yg = R(MOE_FREE, NT, 2, D)
        y_in = [s.sem(f"y_in{i}") for i in range(NT)]
        dve = s.sem("dve")
        with nc.Block() as block:
            @block.gpsimd
            def _(pool):
                for i, (t0, n) in enumerate(TILES):
                    for k in range(2):
                        pool.indirect_dma_start(out=yg[0:n, i, k, :], out_offset=None, in_=y_rows,
                                                in_offset=bass.IndirectOffsetOnAxis(ap=dst[0:n, i, k:k + 1], axis=0)).then_inc(y_in[i], 16)
                for i in range(NT):
                    pool.wait_ge(y_in[i], 32)

            @block.vector
            def _(v):
                link = Link(v, dve)
                for i, (t0, n) in enumerate(TILES):
                    v.wait_ge(y_in[i], 32)
                    link(v.tensor_scalar(yg[0:n, i, 0, :], yg[0:n, i, 0, :], wt[0:n, 0, i:i + 1], None, ALU.mult))
                    link(v.scalar_tensor_tensor(out=yg[0:n, i, 0, :], in0=yg[0:n, i, 1, :], scalar=wt[0:n, 1, i:i + 1],
                                                in1=yg[0:n, i, 0, :], op0=ALU.mult, op1=ALU.add))
                    link(v.scalar_tensor_tensor(out=x[0:n, i, :], in0=x[0:n, i, :], scalar=ALPHA, in1=yg[0:n, i, 0, :],
                                                op0=ALU.mult, op1=ALU.add))


HR = 8192


def page_rows(nc, A, idx_cmp, idx_slc):
    with Scope(nc, "pages") as s:
        pt = A["page_table"]
        raw1, raw2 = s.sb("raw1", [P, 16], I32), s.sb("raw2", [P, 64], I32)
        pi, p8, p32 = s.sb("pi", [P, 1], I32), s.sb("p8", [P, 1], I32), s.sb("p32", [P, 1], I32)
        f8, f32_ = s.sb("f8", [P, 1]), s.sb("f32", [P, 1])
        p_in, made, dve = s.sem("p_in"), s.sem("made"), s.sem("dve")
        with nc.Block() as block:
            @block.sync
            def _(sp):
                with nc.allow_non_contiguous_dma(reason="page numbers, four bytes each"):
                    for g in range(16):
                        src = pt.rearrange("b (h g) -> g (b h)", g=16)[g].partition_broadcast(8)
                        sp.dma_start(raw1[8 * g:8 * g + 8, :], src).then_inc(p_in, 16)
                    for g in range(4):
                        src = pt.rearrange("b (j g) -> g (b j)", g=4)[g].partition_broadcast(32)
                        sp.dma_start(raw2[32 * g:32 * g + 32, :], src).then_inc(p_in, 16)

            @block.gpsimd
            def _(pool):
                pool.iota(pi[:, :], pattern=[[0, 1]], base=0, channel_multiplier=1).then_inc(made, 1)

            @block.vector
            def _(v):
                link = Link(v, dve)
                v.wait_ge(made, 1)
                link(v.tensor_scalar(p8[:, :], pi[:, :], 7, None, ALU.bitwise_and))
                link(v.tensor_scalar(p32[:, :], pi[:, :], 31, None, ALU.bitwise_and))
                link(v.tensor_copy(f8[:, :], p8[:, :]))
                link(v.tensor_copy(f32_[:, :], p32[:, :]))
                v.wait_ge(p_in, 16 * 20)
                link(v.tensor_scalar(idx_cmp[:, :], raw1[:, :], 8.0, f8[:, 0:1], ALU.mult, ALU.add))
                link(v.tensor_scalar(idx_slc[:, :], raw2[:, :], 32.0, f32_[:, 0:1], ALU.mult, ALU.add))


def compress_cache(nc, A, R, ident, idx_cmp, pe_bias, ck_dram, cv_dram):
    with Scope(nc, "cc") as s:
        raw = R(0, 2, HR)
        xt = [R(16384 + HR * i, 8, NKV, 256) for i in range(2)]
        w1 = R(32768, 2, 16, CMP_H)
        hid = [R(40960 + 2048 * i, 2, 2, 256) for i in range(2)]
        w2 = R(45056, 2, 2, HD)
        peT = R(45312, 2, 16)
        ck = R(45344, 2, 256)
        cv = R(45856, 2, 256)
        idx = R(46400, 2, dt=I32)
        bank = s.banks()
        BT, BM, BO = bank[0:3], bank[3:7], bank[7]
        names = ("w_in", "idx_ready", "turned", "moved_a", "moved_v", "mm_done", "hid_ready", "out_done", "out_moved", "pb", "zeroed")
        w_in, idx_ready, turned, moved_a, moved_v, mm_done, hid_ready, out_done, out_moved, pb, zeroed = (s.sem(n) for n in names)
        gather_go = s.sem("gather_go")
        raw_in = [s.sem(f"raw_in{i}") for i in range(2)]
        stored = [s.sem(f"stored{i}") for i in range(2)]
        cache = A["cache_cmp_kv"].rearrange("n (i s) k g d -> (n i) (s k g d)", s=16)
        with nc.Block() as block:
            @block.gpsimd
            def _(pool):
                def gather(b, first=False):
                    for h in range(2):
                        if not first:
                            pool.wait_ge(raw_in[h], 16 * b)
                        col = idx_cmp[:, h:h + 1] if first else idx_cmp[:, bass.ds(2 * b + h, 1)]
                        pool.tensor_copy(idx[:, h:h + 1], col).then_inc(idx_ready, 1)
                    pool.wait_ge(idx_ready, 2 * b + 2)
                    if not first:
                        pool.wait_ge(turned, 32 * b)
                        pool.sem_inc(gather_go, 1)
                    for h in range(2):
                        pool.indirect_dma_start(out=raw[:, h, :], out_offset=None, in_=cache,
                                                in_offset=bass.IndirectOffsetOnAxis(ap=idx[:, h:h + 1], axis=0)).then_inc(raw_in[h], 16)

                gather(0, True)
                with pool.Fori(1, DEC_B) as b:
                    gather(b)

            @block.sync
            def _(sp):
                sp.dma_start(w1, A["cmp_w1"].rearrange("k (t p) h -> p k t h", p=P)).then_inc(w_in, 16)
                sp.dma_start(w2, A["cmp_w2"].rearrange("k (m p) d -> p k m d", p=P)).then_inc(w_in, 16)
                sp.dma_start(peT, A["cmp_pe"]).then_inc(w_in, 16)
                with sp.Fori(0, DEC_B) as b:
                    sp.wait_ge(out_moved, 4 * b + 2)
                    sp.dma_start(ck_dram[bass.ds(b, 1)].rearrange("o p n -> p (o n)"), ck.rearrange("p a n -> p (a n)")).then_inc(stored[0], 16)
                    sp.wait_ge(out_moved, 4 * b + 4)
                    sp.dma_start(cv_dram[bass.ds(b, 1)].rearrange("o p n -> p (o n)"), cv.rearrange("p a n -> p (a n)")).then_inc(stored[1], 16)
                for i in range(2):
                    sp.wait_ge(stored[i], 16 * DEC_B)

            @block.tensor
            def _(pe):
                pe.wait_ge(w_in, 48)
                for kv in range(2):
                    for m in range(2):
                        for t in range(16):
                            ins = pe.matmul(BO[:, 2 * kv + m:2 * kv + m + 1], w1[:, kv, t, P * m:P * m + P],
                                            peT[:, kv, t:t + 1], start=(t == 0), stop=(t == 15))
                ins.then_inc(pb, 1)

                def turn(b, kv, after, steps=range(16)):
                    for st in steps:
                        if not (isinstance(after, int) and after + st < 3):
                            pe.wait_ge(moved_a, after + st - 2)
                            pe.wait_ge(moved_v, after + st - 2)
                        for gp in range(2):
                            for h in range(2):
                                o = 512 * st + 256 * kv + P * gp
                                ins = pe.transpose(BT[st % 3][:, 256 * gp + P * h:256 * gp + P * h + P],
                                                   raw[:, h, o:o + P], ident[:, :])
                        ins.then_inc(turned, 1)

                def product(b, kv, unit, first=False):
                    for gp in range(2):
                        for m in range(2):
                            n = 2 * gp + m
                            if not first:
                                pe.wait_ge(hid_ready, 4 * unit + n - 3)
                            for t in range(16):
                                sh = 1 if t >= 8 else 0
                                ins = pe.matmul(BM[n][:, 0:510], w1[:, kv, t, P * m:P * m + P],
                                                xt[kv][:, t % 8, 2 * gp:2 * gp + 2, sh:sh + 255], start=(t == 0), stop=(t == 15))
                            ins.then_inc(mm_done, 1)

                def outputs(b, kv, unit, first=False):
                    for gp in range(2):
                        pe.wait_ge(hid_ready, 4 * unit + 2 * gp + 2)
                        if not (first and gp == 0):
                            pe.wait_ge(out_moved, 2 * unit + gp)
                        for g2 in range(2):
                            if kv == 0:
                                for m in range(2):
                                    ins = pe.matmul(BO[64 * g2:64 * g2 + 64, 0:255], w2[:, kv, m, :],
                                                    hid[gp][:, m, g2, 0:255], start=(m == 0), stop=(m == 1))
                            else:
                                for h in range(2):
                                    c = P - h
                                    for m in range(2):
                                        ins = pe.matmul(BO[0:c, P * h + 64 * g2:P * h + 64 * g2 + 64],
                                                        hid[gp][:, m, g2, P * h:P * h + c], w2[:, kv, m, :],
                                                        start=(m == 0), stop=(m == 1))
                        ins.then_inc(out_done, 1)

                def ready(unit):
                    pe.wait_ge(moved_a, 16 * unit + 16)
                    pe.wait_ge(moved_v, 16 * unit + 16)

                pe.wait_ge(raw_in[0], 16)
                pe.wait_ge(raw_in[1], 16)
                turn(0, 0, 0)
                for b in range(1):
                    ready(0)
                    turn(0, 1, 16)
                    product(0, 0, 0, True)
                    outputs(0, 0, 0, True)
                    ready(1)
                    pe.wait_ge(raw_in[0], 32)
                    pe.wait_ge(raw_in[1], 32)
                    turn(1, 0, 32)
                    product(0, 1, 1)
                    outputs(0, 1, 1)
                with pe.Fori(1, DEC_B - 1) as b:
                    ready(2 * b)
                    turn(b, 1, 32 * b + 16)
                    product(b, 0, 2 * b)
                    outputs(b, 0, 2 * b)
                    ready(2 * b + 1)
                    pe.wait_ge(raw_in[0], 16 * b + 32)
                    pe.wait_ge(raw_in[1], 16 * b + 32)
                    turn(b + 1, 0, 32 * b + 32)
                    product(b, 1, 2 * b + 1)
                    outputs(b, 1, 2 * b + 1)
                u = 2 * DEC_B - 2
                ready(u)
                turn(DEC_B - 1, 1, 16 * u + 16)
                product(DEC_B - 1, 0, u)
                outputs(DEC_B - 1, 0, u)
                ready(u + 1)
                product(DEC_B - 1, 1, u + 1)
                outputs(DEC_B - 1, 1, u + 1)

            def moved_rows(copy, kv, st, g2, bnk):
                dst = xt[kv][64 * (st % 2):64 * (st % 2) + 64, st // 2].rearrange("p (q e) n -> p q e n", e=2)[:, :, g2, :]
                return copy(dst, bnk[64 * g2:64 * g2 + 64, :].rearrange("p (q n) -> p q n", q=2))

            def mover(eng, copy, sem_, g2, extra):
                def unit(u, kv, first=False):
                    for st in range(16):
                        eng.wait_ge(turned, 16 * u + st + 1)
                        if st == 0 and not first:
                            eng.wait_ge(mm_done, 4 * u - 4)
                        moved_rows(copy, kv, st, g2, BT[st % 3]).then_inc(sem_, 1)
                    
                return unit

            @block.scalar
            def _(act):
                unit = mover(act, nc.scalar.copy, moved_a, 0, None)

                def gelus(u, kv, first=False):
                    for gp in range(2):
                        for m in range(2):
                            act.wait_ge(mm_done, 4 * u + 2 * gp + m + 1)
                            if not first:
                                act.wait_ge(out_done, 2 * u + gp - 1)
                            nc.scalar.activation(hid[gp][:, m, :, 0:255], BM[2 * gp + m][:, 0:510].rearrange("p (a c) -> p a c", a=2),
                                                 ACT.Gelu_apprx_tanh, bias=pe_bias[:, 2 * kv + m:2 * kv + m + 1]).then_inc(hid_ready, 1)

                act.wait_ge(pb, 1)
                nc.scalar.copy(pe_bias[:, :], BO[:, 0:4]).then_inc(pb, 1)
                act.wait_ge(pb, 2)
                unit(0, 0, True)
                unit(1, 1, True)
                gelus(0, 0, True)
                unit(2, 0)
                gelus(1, 1)
                with act.Fori(1, DEC_B - 1) as b:
                    unit(2 * b + 1, 1)
                    gelus(2 * b, 0)
                    unit(2 * b + 2, 0)
                    gelus(2 * b + 1, 1)
                u = 2 * DEC_B - 2
                unit(u + 1, 1)
                gelus(u, 0)
                gelus(u + 1, 1)

            @block.vector
            def _(v):
                unit = mover(v, v.tensor_copy, moved_v, 1, None)

                def outs(u, kv, b, first=False):
                    for gp in range(2):
                        v.wait_ge(out_done, 2 * u + gp + 1)
                        if gp == 0 and not first:
                            v.wait_ge(stored[kv], 16 * b)
                        if kv == 0:
                            ins = v.tensor_copy(ck[:, gp, 0:255], BO[:, 0:255])
                        else:
                            for h in range(2):
                                c = P - h
                                ins = v.tensor_copy(cv[0:c, h, P * gp:P * gp + P], BO[0:c, P * h:P * h + P])
                        ins.then_inc(out_moved, 1)

                v.memset(ck[:, :, 255:256], 0.0)
                v.memset(cv[96:P, 1, :], 0.0).then_inc(zeroed, 1)
                v.wait_ge(zeroed, 1)
                v.wait_ge(pb, 2)
                unit(0, 0, True)
                unit(1, 1, True)
                outs(0, 0, 0, True)
                unit(2, 0)
                outs(1, 1, 0, True)
                with v.Fori(1, DEC_B - 1) as b:
                    unit(2 * b + 1, 1)
                    outs(2 * b, 0, b)
                    unit(2 * b + 2, 0)
                    outs(2 * b + 1, 1, b)
                b = DEC_B - 1
                unit(2 * b + 1, 1)
                outs(2 * b, 0, b)
                outs(2 * b + 1, 1, b)


KV_OFF = 9728
Q_OFF = KV_OFF + NT * 1536
GT_OFF = Q_OFF + 8 * TOK
A_FREE = GT_OFF + NT * 48 + 16


def projections(nc, A, R, outs, gate_dram):
    with Scope(nc, "proj") as s:
        xT = R(XT_OFF, KT, TOK)
        kv, q = R(KV_OFF, NT, 3, 512), R(Q_OFF, 8, TOK)
        gates = R(GT_OFF, NT, 48)
        wkv = R(A_FREE, KT, 1536)
        wq = R(A_FREE + KT * 1536, KT, NH * HD + 48)
        bank = s.banks()
        wq_in, full, stored, gates_done = (s.sem(n) for n in ("wq_in", "full", "stored", "gates_done"))
        wkv_in = [s.sem(f"wkv_in{i}") for i in range(3)]
        used = (s.sem("used_v"), s.sem("used_a"))
        ring = Split(8, full, used)
        NKVJ = 3 * NT
        half = TOK // 2
        p_out, s_out = outs[0:3], outs[3:6]
        n_out = [0]
        with nc.Block() as block:
            @block.sync
            def _(sp):
                for br in range(3):
                    sp.dma_start(wkv[:, :, 512 * br:512 * br + 512],
                                 A["kv_w"].rearrange("(k p) n -> p k n", p=P)[:, :, 512 * br:512 * br + 512]).then_inc(wkv_in[br], 16)
                sp.dma_start(wq, A["b_w_qg"].rearrange("(k p) n -> p k n", p=P)).then_inc(wq_in, 16)
                for b in range(DEC_B):
                    sp.dma_start(s_out[2][b, 0:504].rearrange("t k g d -> t (k g d)"),
                                 A["cache_win_kv"][b, 8:512].rearrange("t k g d -> t (k g d)")).then_inc(stored, 16)
                n = DEC_B
                for br in range(3):
                    for i in range(NT):
                        ring.all_used(sp, NT * br + i + 1)
                        flat = "t k g d -> t (k g d)"
                        if i < 4:
                            dst = p_out[br][0, P * i:P * i + P].rearrange(flat)
                            sp.dma_start(dst, kv[:, i, br, :]).then_inc(stored, 16)
                            n += 1
                        elif br < 2:
                            sp.dma_start(s_out[br].rearrange("b t k g d -> (b t) (k g d)"), kv[0:64, i, br, :]).then_inc(stored, 16)
                            n += 1
                        else:
                            for b in range(DEC_B):
                                sp.dma_start(s_out[2][b, 504:512].rearrange(flat), kv[8 * b:8 * b + 8, i, br, :]).then_inc(stored, 16)
                                n += 1
                sp.wait_ge(gates_done, NT)
                sp.dma_start(gate_dram, gates[0:64, 4, :]).then_inc(stored, 16)
                sp.wait_ge(stored, 16 * (n + 1))

            @block.tensor
            def _(pe):
                for br in range(3):
                    pe.wait_ge(wkv_in[br], 16)
                    for i, (t0, n) in enumerate(TILES):
                        b = ring.claim(pe, NT * br + i)
                        for k in range(KT):
                            ins = pe.matmul(bank[b][0:n, :], xT[:, k, t0:t0 + n], wkv[:, k, 512 * br:512 * br + 512],
                                            start=(k == 0), stop=(k == KT - 1))
                        ring.done(ins)
                pe.wait_ge(wq_in, 16)
                for m in range(8):
                    for h in range(2):
                        b = ring.claim(pe, NKVJ + 2 * m + h)
                        for k in range(KT):
                            ins = pe.matmul(bank[b][:, 0:half], wq[:, k, P * m:P * m + P], xT[:, k, half * h:half * h + half],
                                            start=(k == 0), stop=(k == KT - 1))
                        ring.done(ins)
                b = ring.claim(pe, NKVJ + 16)
                for i, (t0, n) in enumerate(TILES):
                    for k in range(KT):
                        ins = pe.matmul(bank[b][0:n, 48 * i:48 * i + 48], xT[:, k, t0:t0 + n], wq[:, k, NH * HD:],
                                        start=(k == 0), stop=(k == KT - 1))
                ring.done(ins)

            def empty(eng, copy, me):
                for j in range(me, NKVJ, 2):
                    br, i = j // NT, j % NT
                    n = TILES[i][1]
                    eng.wait_ge(full, j + 1)
                    copy(kv[0:n, i, br, :], bank[j % 8][0:n, :]).then_inc(used[me], 1)
                for j in range(NKVJ + (NKVJ + me) % 2, NKVJ + 16, 2):
                    m, h = (j - NKVJ) // 2, (j - NKVJ) % 2
                    eng.wait_ge(full, j + 1)
                    copy(q[:, m, half * h:half * h + half], bank[j % 8][:, 0:half]).then_inc(used[me], 1)

            @block.vector
            def _(v):
                empty(v, v.tensor_copy, 0)

            @block.scalar
            def _(act):
                empty(act, nc.scalar.copy, 1)
                j = NKVJ + 16
                act.wait_ge(full, j + 1)
                for i, (t0, n) in enumerate(TILES):
                    nc.scalar.activation(gates[0:n, i, :], bank[j % 8][0:n, 48 * i:48 * i + 48], ACT.Sigmoid).then_inc(gates_done, 1)


def compress_prompt(nc, A, R, ident, pe_bias, rows, ckp, cvp):
    with Scope(nc, "cp") as s:
        NS = 32
        raw = R(A_FREE, HR, np_=NS)
        xt = R(A_FREE + HR, 2, 8, NKV, NS)
        w1 = R(A_FREE + HR + 2048, 2, 16, CMP_H)
        w2 = R(A_FREE + 2 * HR + 2048, 2, 2, HD)
        hid = R(A_FREE + 2 * HR + 2304, 2, 2, NKV, NS)
        bank = s.banks()
        raw_in, w_in, turned, moved_a, moved_v, mm_done, hid_ready, out_done, dve = (
            s.sem(n) for n in ("raw_in", "w_in", "turned", "moved_a", "moved_v", "mm_done", "hid_ready", "out_done", "dve"))
        with nc.Block() as block:
            @block.sync
            def _(sp):
                sp.dma_start(raw, rows[0].rearrange("(n s) k g d -> n (s k g d)", s=16)).then_inc(raw_in, 16)
                sp.dma_start(w1, A["cmp_w1"].rearrange("k (t p) h -> p k t h", p=P)).then_inc(w_in, 16)
                sp.dma_start(w2, A["cmp_w2"].rearrange("k (m p) d -> p k m d", p=P)).then_inc(w_in, 16)

            @block.tensor
            def _(pe):
                pe.wait_ge(raw_in, 16)
                for kv in range(2):
                    for q in range(2):
                        for st in range(8 * q, 8 * q + 8):
                            for gp in range(2):
                                o = 512 * st + 256 * kv + P * gp
                                c = 64 * (st % 8) + NS * gp
                                ins = pe.transpose(bank[2 * kv + q][:, c:c + NS], raw[:, o:o + P], ident[0:NS, 0:NS])
                        ins.then_inc(turned, 1)
                pe.wait_ge(w_in, 32)
                pe.wait_ge(moved_a, 64)
                pe.wait_ge(moved_v, 64)
                for kv in range(2):
                    for m in range(2):
                        for t in range(16):
                            sh = 1 if t >= 8 else 0
                            ins = pe.matmul(bank[4 + 2 * kv + m][:, 0:NKV * 31], w1[:, kv, t, P * m:P * m + P],
                                            xt[:, kv, t % 8, :, sh:sh + 31], start=(t == 0), stop=(t == 15))
                        ins.then_inc(mm_done, 1)
                pe.wait_ge(hid_ready, 4)
                for g in range(NKV):
                    for m in range(2):
                        pe.matmul(bank[0][64 * (g % 2):64 * (g % 2) + 64, 32 * (g // 2):32 * (g // 2) + 31], w2[:, 0, m, :],
                                  hid[:, 0, m, g, 0:31], start=(m == 0), stop=(m == 1))
                for g in range(NKV):
                    for m in range(2):
                        ins = pe.matmul(bank[1][0:31, 64 * g:64 * g + 64], hid[:, 1, m, g, 0:31], w2[:, 1, m, :],
                                        start=(m == 0), stop=(m == 1))
                ins.then_inc(out_done, 1)

            def move(eng, copy, sem_, g2):
                for kv in range(2):
                    for q in range(2):
                        eng.wait_ge(turned, 2 * kv + q + 1)
                        for st in range(8 * q, 8 * q + 8):
                            for gp in range(2):
                                c = 64 * (st % 8) + NS * gp
                                copy(xt[64 * (st % 2):64 * (st % 2) + 64, kv, st // 2, 2 * gp + g2, :],
                                     bank[2 * kv + q][64 * g2:64 * g2 + 64, c:c + NS]).then_inc(sem_, 1)

            @block.scalar
            def _(act):
                move(act, nc.scalar.copy, moved_a, 0)
                for kv in range(2):
                    for m in range(2):
                        act.wait_ge(mm_done, 2 * kv + m + 1)
                        nc.scalar.activation(hid[:, kv, m, :, 0:31], bank[4 + 2 * kv + m][:, 0:NKV * 31].rearrange("p (g c) -> p g c", g=NKV),
                                             ACT.Gelu_apprx_tanh, bias=pe_bias[:, 2 * kv + m:2 * kv + m + 1]).then_inc(hid_ready, 1)

            @block.vector
            def _(v):
                move(v, v.tensor_copy, moved_v, 1)
                v.wait_ge(out_done, 1)
                v.tensor_copy(ckp[:, :, 0:31], bank[0][:, 0:64].rearrange("p (q c) -> p q c", q=2)[:, :, 0:31]).then_inc(dve, 1)
                v.tensor_copy(cvp[0:31, :], bank[1][0:31, 0:256]).then_inc(dve, 1)


def attention_masks(nc, R, cm, cma, cm01, nmask, wmask, hsum, forced):
    with Scope(nc, "masks") as s:
        ones = s.sb("ones", [P, P])
        pi, l_i, lf, li8, nm8 = s.sb("pi", [P, 1], I32), s.sb("l_i", [P, 1], I32), s.sb("lf", [P, 1]), s.sb("li8", [P, 8]), s.sb("nm8", [P, 8])
        qi, qf, cid, gl = s.sb("qi", [P, P], I32), s.sb("qf", [P, P]), s.sb("cid", [P, 1], I32), s.sb("gl", [P, 1])
        made, dve = s.sem("made"), s.sem("dve")
        with nc.Block() as block:
            @block.gpsimd
            def _(pool):
                pool.memset(ones[:, :], 0.0).then_inc(made, 1)
                pool.memset(cma, 0.0).then_inc(made, 1)
                pool.memset(cm01, 1.0).then_inc(made, 1)
                pool.iota(pi[:, :], pattern=[[0, 1]], base=0, channel_multiplier=1).then_inc(made, 1)
                pool.iota(li8[:, :], pattern=[[1, 8]], base=0, channel_multiplier=0, allow_small_or_imprecise_dtypes=True).then_inc(made, 1)
                pool.iota(qi[:, :], pattern=[[1, P]], base=0, channel_multiplier=0).then_inc(made, 1)
                pool.wait_ge(made, 6)
                pool.affine_select(out=cm, in_=ones[:, :], compare_op=ALU.is_ge, fill=NEG, base=0,
                                   pattern=[[-1, P]], channel_multiplier=1).then_inc(made, 1)
                pool.affine_select(out=cma, in_=cma, compare_op=ALU.is_ge, fill=NEG, base=-31,
                                   pattern=[[P, 4], [-16, 31]], channel_multiplier=1).then_inc(made, 1)
                pool.affine_select(out=cm01, in_=cm01, compare_op=ALU.is_ge, fill=0.0, base=-31,
                                   pattern=[[P, 4], [-16, 31]], channel_multiplier=1).then_inc(made, 1)

            @block.vector
            def _(v):
                link = Link(v, dve)
                v.wait_ge(made, 6)
                link(v.tensor_scalar(l_i[:, :], pi[:, :], 7, None, ALU.bitwise_and))
                link(v.tensor_copy(lf[:, :], l_i[:, :]))
                link(v.tensor_scalar(nm8[:, :], li8[:, :], lf[:, 0:1], NEG, ALU.is_gt, ALU.mult))
                link(v.tensor_scalar(wmask, li8[:, :], lf[:, 0:1], NEG, ALU.is_le, ALU.mult))
                link(v.memset(nmask, NEG))
                for b in range(DEC_B):
                    ins = v.tensor_copy(nmask[:, b, 8 * b:8 * b + 8], nm8[:, :])
                link(ins)
                link(v.tensor_scalar(qi[:, :], qi[:, :], 103, None, ALU.bitwise_and))
                link(v.tensor_scalar(cid[:, :], pi[:, :], 103, None, ALU.bitwise_and))
                link(v.tensor_copy(qf[:, :], qi[:, :]))
                link(v.tensor_copy(gl[:, :], cid[:, :]))
                link(v.tensor_scalar(hsum, qf[:, :], gl[:, 0:1], None, ALU.is_equal))
                link(v.memset(forced, 0.0))
                link(v.memset(forced[:, 0:1], 1e4))
                link(v.memset(forced[:, 64:65], 1e4))


def prompt_attention(nc, A, R, ident, ckp, cvp, cm, cma, cm01, kt_s, oT):
    with Scope(nc, "pa") as s:
        kv, q = R(KV_OFF, NT, 3, 512), R(Q_OFF, 8, TOK)
        gates = R(GT_OFF, NT, 16, 3)
        kt = R(A_FREE, 2, 2, SEQ)
        p_ = [R(A_FREE + 2048 + 1024 * i, 2, 512) for i in range(2)]
        pT = [R(A_FREE + 4096 + 1024 * i, 2, 512) for i in range(2)]
        o = R(A_FREE + 6144, 4, NH, HD)
        mx, sm, cf = R(A_FREE + 10240, 2, 2), R(A_FREE + 10244, 2, 2), R(A_FREE + 10248, 2, 2)
        ob = R(A_FREE + 10256, 2, 2, HD)
        pc = R(A_FREE + 10512, NH, 32)
        pcT = R(A_FREE + 11024, NH, P)
        mc, sc = R(A_FREE + 13072, NH), R(A_FREE + 13088, NH)
        tc = R(A_FREE + 13104, NH, HD)
        psS = [s.ctx.enter_context(nc.psum_tensor(f"pa_s{i}", [P, 2, 512], F32)) for i in range(2)]
        psT = [s.ctx.enter_context(nc.psum_tensor(f"pa_t{i}", [P, 512], F32)) for i in range(2)]
        psO = [s.ctx.enter_context(nc.psum_tensor(f"pa_o{i}", [P, 512], F32)) for i in range(2)]
        dve, k_turned, k_moved, s_done, c_exp_in, c_exp, c_ready, c_turned, c_moved, c_out, c_gated = (
            s.sem(n) for n in ("dve", "k_turned", "k_moved", "s_done", "c_exp_in", "c_exp", "c_ready", "c_turned", "c_moved", "c_out", "c_gated"))
        s_full, max_ready, p_ready, t_full, t_used, o_full, o_used, o_turned, o_moved = (
            s.sem(n) for n in ("s_full", "max_ready", "p_ready", "t_full", "t_used", "o_full", "o_used", "o_turned", "o_moved"))
        units = [(br, i, m, g2) for i in range(4) for br in range(2) for m in range(0, 8, 2) for g2 in range(2)]

        def head(m, g2):
            return (2 * (m // 4) + g2) * HPK + m % 4

        with nc.Block() as block:
            @block.tensor
            def _(pe):
                for j in range(4):
                    br, gp = j // 2, j % 2
                    for i in range(4):
                        ins = pe.transpose(psS[j // 2][:, j % 2, P * i:P * i + P], kv[:, i, 1 + br, P * gp:P * gp + P], ident[:, :])
                    ins.then_inc(k_turned, 1)
                for j in range(4):
                    br, gp = j // 2, j % 2
                    ins = pe.transpose(psO[0][:, 64 * j:64 * j + 64], kv[0:64, 4, 1 + br, P * gp:P * gp + P], ident[0:64, 0:64])
                ins.then_inc(k_turned, 1)
                for i in range(4):
                    if i == 0:
                        pe.wait_ge(k_moved, 5)
                    else:
                        pe.wait_ge(c_exp_in, i)
                    for m in range(8):
                        for g2 in range(2):
                            r = slice(64 * g2, 64 * g2 + 64)
                            ins = pe.matmul(psS[0][:, g2, 32 * m:32 * m + 31], q[r, m, P * i:P * i + P], ckp[r, m // 4, 0:31],
                                            start=True, stop=True)
                    ins.then_inc(s_done, 1)
                    pe.wait_ge(c_ready, i + 1)
                    for j in range(4):
                        if 4 * i + j >= 2:
                            pe.wait_ge(c_moved, 4 * i + j - 1)
                        for n in range(4):
                            ins = pe.transpose(psT[j % 2][0:31, P * n:P * n + P], pc[:, 4 * j + n, 0:31], ident[:, :])
                        ins.then_inc(c_turned, 1)
                    pe.wait_ge(c_moved, 4 * i + 4)
                    if i >= 1:
                        pe.wait_ge(c_gated, i)
                    for h in range(NH):
                        ins = pe.matmul(psO[h // 8][:, HD * (h % 8):HD * (h % 8) + HD], pcT[0:31, h, :],
                                        cvp[0:31, HD * (h // HPK):HD * (h // HPK) + HD], start=True, stop=True)
                    ins.then_inc(c_out, 1)

                def scores(u):
                    br, i, m, g2 = units[u]
                    r = slice(64 * g2, 64 * g2 + 64)
                    if u >= 2:
                        pe.wait_ge(p_ready, 2 * (u - 1))
                    n = P * (i + 1)
                    for e in range(2):
                        ins = pe.matmul(psS[u % 2][:, e, 0:n], q[r, m + e, P * i:P * i + P], kt[r, br, m // 4, 0:n], start=True, stop=True)
                    ins.then_inc(s_full, 1)

                def outputs(u):
                    br, i, m, g2 = units[u]
                    g = 2 * (m // 4) + g2
                    pe.wait_ge(p_ready, 2 * u + 2)
                    for e in range(2):
                        if 2 * u + e >= 2:
                            pe.wait_ge(t_used, 2 * u + e - 1)
                        for k in range(i + 1):
                            ins = pe.transpose(psT[e][:, P * k:P * k + P], p_[u % 2][:, e, P * k:P * k + P], ident[:, :])
                        ins.then_inc(t_full, 1)
                    if u >= 2:
                        pe.wait_ge(o_used, u - 1)
                    for e in range(2):
                        pe.wait_ge(t_used, 2 * u + e + 1)
                        for k in range(i + 1):
                            ins = pe.matmul(psO[u % 2][:, HD * e:HD * e + HD], pT[u % 2][:, e, P * k:P * k + P],
                                            kv[:, k, 1 + br, 256 + HD * g:256 + HD * g + HD], start=(k == 0), stop=(k == i))
                    ins.then_inc(o_full, 1)

                pe.wait_ge(c_exp_in, 4)
                pe.wait_ge(c_gated, 4)
                scores(0)
                for u in range(len(units)):
                    if u + 1 < len(units):
                        scores(u + 1)
                    outputs(u)
                pe.wait_ge(o_used, len(units))
                for i in range(4):
                    for h in range(2):
                        j = 2 * i + h
                        if j >= 2:
                            pe.wait_ge(o_moved, j - 1)
                        for k in range(4):
                            a = P * (4 * h + k)
                            ins = pe.transpose(psT[j % 2][:, P * k:P * k + P],
                                               o[:, i].rearrange("p h d -> p (h d)")[:, a:a + P], ident[:, :])
                        ins.then_inc(o_turned, 1)

            def turned_out(act, u):
                n = P * (units[u][1] + 1)
                for e in range(2):
                    act.wait_ge(t_full, 2 * u + e + 1)
                    if u >= 2:
                        act.wait_ge(o_full, u - 1)
                    nc.scalar.copy(pT[u % 2][:, e, 0:n], psT[e][:, 0:n]).then_inc(t_used, 1)

            @block.scalar
            def _(act):
                for i in range(4):
                    act.wait_ge(c_exp_in, i + 1)
                    nc.scalar.activation(pc[:, :, 0:31], pc[:, :, 0:31], ACT.Exp, scale=SCALE).then_inc(c_exp, 1)
                for u, (br, i, m, g2) in enumerate(units):
                    n = P * (i + 1)
                    act.wait_ge(max_ready, u + 1)
                    if u >= 2:
                        act.wait_ge(t_full, 2 * u - 2)
                    for e in range(2):
                        nc.scalar.activation(p_[u % 2][:, e, 0:n], psS[u % 2][:, e, 0:n], ACT.Exp, bias=mx[:, u % 2, e:e + 1],
                                             scale=SCALE, accum_out=sm[:, u % 2, e:e + 1]).then_inc(p_ready, 1)
                    if u >= 1:
                        turned_out(act, u - 1)
                turned_out(act, len(units) - 1)
                for j in range(8):
                    act.wait_ge(o_turned, j + 1)
                    nc.scalar.copy(oT[:, 4 * (j % 2):4 * (j % 2) + 4, P * (j // 2):P * (j // 2) + P],
                                   psT[j % 2][:, :].rearrange("p (k t) -> p k t", k=4)).then_inc(o_moved, 1)

            @block.vector
            def _(v):
                link = Link(v, dve)
                for j in range(4):
                    v.wait_ge(k_turned, j + 1)
                    v.tensor_copy(kt[:, j // 2, j % 2, :], psS[j // 2][:, j % 2, :]).then_inc(k_moved, 1)
                v.wait_ge(k_turned, 5)
                v.tensor_copy(kt_s.rearrange("p a b t -> p (a b t)"), psO[0][:, 0:256]).then_inc(k_moved, 1)
                for i in range(4):
                    v.wait_ge(s_done, i + 1)
                    if i >= 1:
                        v.wait_ge(c_turned, 4 * i)
                    for gp in range(2):
                        for g2 in range(2):
                            h = head(4 * gp, g2)
                            s31 = psS[0][:, g2, 0:256].rearrange("p (h c) -> p h c", h=8)[:, 4 * gp:4 * gp + 4, 0:31]
                            ins = v.tensor_tensor(pc[:, h:h + 4, 0:31], s31, bc(cma[:, i, :].unsqueeze(1), [P, 4, 31]), ALU.add)
                    link(ins)
                    link(v.tensor_reduce(mc, pc[:, :, 0:31], AX, ALU.max))
                    v.tensor_tensor(pc[:, :, 0:31], pc[:, :, 0:31], bc(mc.unsqueeze(2), [P, NH, 31]), ALU.subtract).then_inc(c_exp_in, 1)
                    v.wait_ge(c_exp, i + 1)
                    link(v.tensor_tensor(pc[:, :, 0:31], pc[:, :, 0:31], bc(cm01[:, i, :].unsqueeze(1), [P, NH, 31]), ALU.mult))
                    v.engine_nop().then_inc(c_ready, 1)
                    link(v.tensor_reduce(sc, pc[:, :, 0:31], AX, ALU.add))
                    link(v.tensor_scalar(sc, sc, TINY, None, ALU.max))
                    link(v.reciprocal(sc, sc))
                    link(v.tensor_tensor(sc, sc, gates[:, i, :, 0], ALU.mult))
                    for j in range(4):
                        v.wait_ge(c_turned, 4 * i + j + 1)
                        if j == 0 and i >= 1:
                            v.wait_ge(c_out, i)
                        v.tensor_copy(pcT[0:31, 4 * j:4 * j + 4, :], psT[j % 2][0:31, :].rearrange("p (h t) -> p h t", h=4)).then_inc(c_moved, 1)
                    v.wait_ge(c_out, i + 1)
                    for h in range(2):
                        ins = v.tensor_tensor(o[:, i, 8 * h:8 * h + 8, :], psO[h][:, :].rearrange("p (h d) -> p h d", h=8),
                                              bc(sc[:, 8 * h:8 * h + 8].unsqueeze(2), [P, 8, HD]), ALU.mult)
                    ins.then_inc(c_gated, 1)
                v.wait_ge(c_gated, 4)

                def merge(u):
                    br, i, m, g2 = units[u]
                    h = head(m, g2)
                    v.wait_ge(p_ready, 2 * u + 2)
                    link(v.reciprocal(cf[:, u % 2, :], sm[:, u % 2, :]))
                    link(v.tensor_tensor(cf[:, u % 2, :], cf[:, u % 2, :], gates[:, i, h:h + 2, 1 + br], ALU.mult))
                    v.wait_ge(o_full, u + 1)
                    link(v.tensor_tensor(ob[:, u % 2], psO[u % 2][:, 0:2 * HD].rearrange("p (e d) -> p e d", e=2),
                                         bc(cf[:, u % 2, :].unsqueeze(2), [P, 2, HD]), ALU.mult))
                    v.tensor_tensor(o[:, i, h:h + 2, :], o[:, i, h:h + 2, :], ob[:, u % 2], ALU.add).then_inc(o_used, 1)

                for u, (br, i, m, g2) in enumerate(units):
                    n = P * (i + 1)
                    v.wait_ge(s_full, u + 1)
                    diag = psS[u % 2][:, :, P * i:n]
                    link(v.tensor_tensor(diag, diag, bc(cm.unsqueeze(1), [P, 2, P]), ALU.add))
                    if u >= 2:
                        v.wait_ge(p_ready, 2 * u - 2)
                    link(v.tensor_reduce(mx[:, u % 2, :], psS[u % 2][:, :, 0:n], AX, ALU.max))
                    v.tensor_scalar(mx[:, u % 2, :], mx[:, u % 2, :], -SCALE, None, ALU.mult).then_inc(max_ready, 1)
                    if u >= 1:
                        merge(u - 1)
                merge(len(units) - 1)


OT_OFF = KV_OFF
KV4_OFF = KV_OFF + 4 * 1536
QBD_OFF = XT_OFF + 1680
S_FREE = Q_OFF


def sample_queries(nc, R, gate_dram, gs):
    with Scope(nc, "sq") as s:
        q, qbd = R(Q_OFF, 8, TOK), R(QBD_OFF, DEC_B, 2, P)
        zeroed, done, g_in = s.sem("zeroed"), s.sem("done"), s.sem("g_in")
        with nc.Block() as block:
            @block.gpsimd
            def _(pool):
                pool.memset(qbd, 0.0).then_inc(zeroed, 1)

            @block.vector
            def _(v):
                v.wait_ge(zeroed, 1)
                for g in range(NKV):
                    gp, g2 = g // 2, g % 2
                    r = slice(64 * g2, 64 * g2 + 64)
                    dst = qbd[r, :, gp, 32 * g:32 * g + 32].rearrange("p b (n l) -> p b n l", n=HPK)
                    src = q[r, 4 * gp:4 * gp + 4, SEQ:TOK].rearrange("p n (b l) -> p b n l", b=DEC_B)
                    v.tensor_copy(dst, src).then_inc(done, 1)

            @block.sync
            def _(sp):
                for b in range(DEC_B):
                    src = gate_dram.rearrange("(b l) (h r) -> b h l r", b=DEC_B, r=3)[b]
                    sp.dma_start(gs[:, b, :], src).then_inc(g_in, 16)
                sp.wait_ge(g_in, 16 * DEC_B)


def sample_attention(nc, A, R, ident, idx_slc, ck_dram, cv_dram, kt_s, nmask, wmask, hsum, forced, gs, oT):
    with Scope(nc, "sa") as s:
        qbd, kv4 = R(QBD_OFF, DEC_B, 2, P), R(KV4_OFF, 3, 512)
        at = [S_FREE]

        def place(*shape, dt=F32):
            n = int(np.prod(shape))
            at[0] += n + n % 2
            return R(at[0] - n - n % 2, *shape, dt=dt)

        NJ = 8
        raw = [place(4, 512) for _ in range(NJ + 1)]
        sc = place(9 * 512 + 128)
        OLD, WIN = NJ * 512, NJ * 512 + 64
        kts = [place(2, 512) for _ in range(2)]
        pt = [place(512) for _ in range(2)]
        ptn = place(512)
        ck, cv = place(2, 256), place(2, 256)
        pc = place(256)
        qb = place(2, P)
        ps = place(66)
        sel = place(66)
        m8 = place(2, 8)
        mxs, sms, cf = place(4), place(4), place(4)
        ob, ob2 = place(HD), place(2, HD)
        idx = place(NJ, dt=I32)
        bank = s.banks()
        psK, psS, psT, O0, O1 = bank[0:2], bank[2:4], bank[4:6], bank[6], bank[7]
        names = ("idx_ready", "gather_go", "win_in", "ck_in", "dve", "qb_ready", "c_full", "cmax_ready", "c_exp", "p4_ready",
                 "hs_full", "k_turned", "k_moved_v", "k_moved_a", "s_full", "s_moved", "max_ready", "e_ready", "pn_ready",
                 "t_full", "t_moved_v", "t_moved_a", "pv_done", "o_done", "ob_ready", "ob_turned", "o_stored")
        (idx_ready, gather_go, win_in, ck_in, dve, qb_ready, c_full, cmax_ready, c_exp, p4_ready, hs_full, k_turned, k_moved_v,
         k_moved_a, s_full, s_moved, max_ready, e_ready, pn_ready, t_full, t_moved_v, t_moved_a, pv_done, o_done, ob_ready,
         ob_turned, o_stored) = (s.sem(n) for n in names)
        pad_ready, own_wait = s.sem("pad_ready"), s.sem("own_wait")
        raw_in = [s.sem(f"raw_in{j}") for j in range(NJ)]
        cache = A["cache_slc_kv"].rearrange("n (i s) k g d -> (n i) (s k g d)", s=4)

        def samples(eng, body):
            body(0, True)
            with eng.Fori(1, DEC_B) as b:
                body(b, False)

        def at_b(x, b, n=1):
            return x[:, n * b:n * b + n] if isinstance(b, int) else x[:, bass.ds(n * b, n)]

        def turned_k(j):
            return kts[j % 2]

        with nc.Block() as block:
            @block.gpsimd
            def _(pool):
                def body(b, first):
                    if not first:
                        for j in range(NJ):
                            pool.wait_ge(raw_in[j], 16 * b)
                    pool.tensor_copy(idx, at_b(idx_slc, b, NJ)).then_inc(idx_ready, 1)
                    pool.wait_ge(idx_ready, b + 1)
                    for j in range(NJ):
                        if not first:
                            pool.wait_ge(pv_done, NJ * b - NJ + j + 1)
                            pool.sem_inc(gather_go, 1)
                        pool.indirect_dma_start(out=raw[j].rearrange("p s n -> p (s n)"), out_offset=None, in_=cache,
                                                in_offset=bass.IndirectOffsetOnAxis(ap=idx[:, j:j + 1], axis=0)).then_inc(raw_in[j], 16)
                samples(pool, body)

            @block.sync
            def _(sp):
                def body(b, first):
                    if not first:
                        sp.wait_ge(o_done, b)
                    def row(x):
                        return x[b:b + 1] if isinstance(b, int) else x[bass.ds(b, 1)]
                    sp.dma_start(ck.rearrange("p a n -> p (a n)"), row(ck_dram).rearrange("o p n -> p (o n)")).then_inc(ck_in, 16)
                    sp.dma_start(cv.rearrange("p a n -> p (a n)"), row(cv_dram).rearrange("o p n -> p (o n)")).then_inc(ck_in, 16)
                    sp.dma_start(raw[NJ].rearrange("p s n -> p (s n)"),
                                 row(A["cache_win_kv"]).rearrange("o (p s) k g d -> p (o s k g d)", s=4)).then_inc(win_in, 16)
                samples(sp, body)

            @block.tensor
            def _(pe):
                def body(b, first):
                    pe.wait_ge(qb_ready, b + 1)
                    pe.wait_ge(ck_in, 32 * b + 32)
                    if not first:
                        pe.wait_ge(o_stored, b)
                    for gp in range(2):
                        ins = pe.matmul(O0[:, 0:255], qb[:, gp, :], ck[:, gp, 0:255], start=(gp == 0), stop=(gp == 1))
                    for br in range(2):
                        for gp in range(2):
                            ins = pe.matmul(O0[:, 320 + 64 * br:384 + 64 * br], qb[:, gp, :], kt_s[:, br, gp, :],
                                            start=(gp == 0), stop=(gp == 1))
                    ins.then_inc(c_full, 1)

                    def turn(j):
                        pe.wait_ge(raw_in[j], 16 * b + 16) if j < NJ else pe.wait_ge(win_in, 16 * b + 16)
                        if not (first and j == 0):
                            pe.wait_ge(k_moved_v, 9 * b + j)
                            pe.wait_ge(k_moved_a, 9 * b + j)
                        for gp in range(2):
                            for r in range(4):
                                ins = pe.transpose(psK[gp][:, P * r:P * r + P], raw[j][:, r, P * gp:P * gp + P], ident[:, :])
                            ins.then_inc(k_turned, 1)

                    def scores(j):
                        pe.wait_ge(k_moved_v, 9 * b + j + 1)
                        pe.wait_ge(k_moved_a, 9 * b + j + 1)
                        if not (first and j < 2):
                            pe.wait_ge(s_moved, 9 * b + j - 1)
                        for gp in range(2):
                            ins = pe.matmul(psS[j % 2][:, :], qb[:, gp, :], turned_k(j)[:, gp, :], start=(gp == 0), stop=(gp == 1))
                        ins.then_inc(s_full, 1)

                    turn(0)
                    pe.wait_ge(p4_ready, b + 1)
                    pe.matmul(O0[:, 256:320], hsum, ps[:, 0:64], start=True, stop=True).then_inc(hs_full, 1)
                    for j in range(9):
                        if j < 8:
                            turn(j + 1)
                        scores(j)

                    def turn_p(q):
                        if q == 0:
                            pe.wait_ge(pn_ready, b + 1)
                            pe.wait_ge(e_ready, 2 * b + 2)
                        if q >= 2 or not first:
                            if q % 2 == 0:
                                pe.wait_ge(t_moved_v, 5 * b + q // 2)
                            else:
                                pe.wait_ge(t_moved_a, 5 * b + q // 2)
                        for r in range(4):
                            if q == 0 and r >= 2:
                                o = (OLD, WIN + 512)[r - 2]
                                ins = pe.transpose(psT[0][0:64, P * r:P * r + P], sc[:, o:o + 64], ident[:, :])
                                continue
                            src = pc[:, P * r:P * r + P] if q == 0 else \
                                (sc[:, 512 * (q - 1) + P * r:512 * (q - 1) + P * r + P] if q < 9 else sc[:, WIN + P * r:WIN + P * r + P])
                            ins = pe.transpose(psT[q % 2][:, P * r:P * r + P], src, ident[:, :])
                        ins.then_inc(t_full, 1)

                    def values(q):
                        if q % 2 == 0:
                            pe.wait_ge(t_moved_v, 5 * b + q // 2 + 1)
                        else:
                            pe.wait_ge(t_moved_a, 5 * b + q // 2 + 1)
                        if q == 0:
                            for r in range(2):
                                pe.matmul(O1[:, 0:256], ptn[:, P * r:P * r + P], cv[:, r, :], start=(r == 0), stop=(r == 1))
                            return
                        out = O0[:, 0:256] if q < 9 else O1[:, 256:512]
                        j = q - 1
                        last = q >= 8
                        for r in range(4):
                            ins = pe.matmul(out, pt[q % 2][:, P * r:P * r + P], raw[j][:, r, 256:512],
                                            start=(r == 0 and q in (1, 9)), stop=False, skip_group_check=True)
                        if q < 9:
                            ins.then_inc(pv_done, 1)
                        if last:
                            o = 256 if q == 8 else 384
                            ins = pe.matmul(out, ptn[0:64, o:o + P], kv4[0:64, 1 + (q == 9), 256:512], start=False, stop=True,
                                            skip_group_check=True)
                        if q == 9:
                            ins.then_inc(o_done, 1)

                    turn_p(0)
                    for q in range(10):
                        if q < 9:
                            turn_p(q + 1)
                        values(q)
                    pe.wait_ge(ob_ready, b + 1)
                    pe.transpose(O0[:, 0:P], ob2.rearrange("p e d -> p (e d)"), ident[:, :]).then_inc(ob_turned, 1)
                samples(pe, body)

            @block.scalar
            def _(act):
                def body(b, first):
                    act.wait_ge(cmax_ready, b + 1)
                    nc.scalar.activation(pc[:, 0:255], O0[:, 0:255], ACT.Exp, bias=mxs[:, 0:1], scale=SCALE,
                                         accum_out=sms[:, 0:1]).then_inc(c_exp, 1)
                    for j in range(9):
                        act.wait_ge(k_turned, 18 * b + 2 * j + 2)
                        if not (first and j < 2):
                            act.wait_ge(s_full, 9 * b + j - 1)
                        nc.scalar.copy(turned_k(j)[:, 1, :], psK[1][:, :]).then_inc(k_moved_a, 1)
                    for w, (o, n) in enumerate(((0, 4160), (WIN, 576))):
                        act.wait_ge(max_ready, 2 * b + w + 1)
                        nc.scalar.activation(sc[:, o:o + n], sc[:, o:o + n], ACT.Exp, bias=mxs[:, 1 + w:2 + w], scale=SCALE,
                                             accum_out=sms[:, 1 + w:2 + w]).then_inc(e_ready, 1)
                    for q in range(1, 10, 2):
                        act.wait_ge(t_full, 10 * b + q + 1)
                        if q >= 3:
                            act.wait_ge(pv_done, NJ * b + q - 2)
                        elif not first:
                            act.wait_ge(o_done, b)
                        nc.scalar.copy(pt[1], psT[1][:, :]).then_inc(t_moved_a, 1)
                samples(act, body)

            @block.vector
            def _(v):
                NL = 23

                def body(b, first):
                    link = Link(v, dve, NL * b)
                    if not first:
                        v.wait_ge(s_full, 9 * b)
                    v.tensor_copy(qb.rearrange("p a n -> p (a n)"),
                                  (qbd[:, 0:1] if first else qbd[:, bass.ds(b, 1)]).rearrange("p o a n -> p (o a n)")).then_inc(qb_ready, 1)
                    v.wait_ge(c_full, b + 1)
                    link(v.tensor_reduce(mxs[:, 0:1], O0[:, 0:255], AX, ALU.max))
                    v.tensor_scalar(mxs[:, 0:1], mxs[:, 0:1], -SCALE, None, ALU.mult).then_inc(cmax_ready, 1)

                    def move_k(j):
                        v.wait_ge(k_turned, 18 * b + 2 * j + 1)
                        if not (first and j < 2):
                            v.wait_ge(s_full, 9 * b + j - 1)
                        v.tensor_copy(turned_k(j)[:, 0, :], psK[0][:, :]).then_inc(k_moved_v, 1)

                    move_k(0)
                    v.wait_ge(c_exp, b + 1)
                    link(v.reciprocal(cf[:, 0:1], sms[:, 0:1]))
                    link(v.tensor_scalar(pc[:, 0:255], pc[:, 0:255], cf[:, 0:1], None, ALU.mult))
                    v.sem_inc(pn_ready, 1)
                    link(v.tensor_reduce(ps[:, 0:64], pc.rearrange("p (j c) -> p j c", c=4), AX, ALU.add))
                    spill = pc.rearrange("p (j c) -> p j c", c=4)[:, 0:63, 3]
                    v.tensor_tensor(ps[:, 1:64], ps[:, 1:64], spill, ALU.add).then_inc(p4_ready, 1)
                    move_k(1)
                    v.wait_ge(hs_full, b + 1)
                    v.tensor_tensor(sel[:, 0:64], O0[:, 256:320], forced[:, 0:64], ALU.add)
                    link(v.tensor_copy(sel[:, 64:65], forced[:, 64:65]))
                    for i in range(2):
                        v.sem_inc(own_wait, 1)
                        link(v.max(m8[:, i, :], sel[:, 0:65]))
                        v.sem_inc(own_wait, 1)
                        link(v.match_replace(sel[:, 0:65], m8[:, i, :], sel[:, 0:65], -1e9))
                    link(v.tensor_scalar(sel[:, 0:65], sel[:, 0:65], -1e9, NEG, ALU.not_equal, ALU.mult))
                    for j in range(8):
                        if j < 7:
                            move_k(j + 2)
                        v.wait_ge(s_full, 9 * b + j + 1)
                        if j == 0 and not first:
                            v.wait_ge(t_full, 10 * b)
                        m = bc(bc(sel[:, 8 * j:8 * j + 8].unsqueeze(2), [P, 8, 16]).unsqueeze(1), [P, 4, 8, 16])
                        v.tensor_tensor(sc[:, 512 * j:512 * j + 512].rearrange("p (r j i) -> p r j i", r=4, j=8),
                                        psS[j % 2][:, :].rearrange("p (r j i) -> p r j i", r=4, j=8), m, ALU.add).then_inc(s_moved, 1)
                    nm = nmask[:, 0] if first else nmask[:, bass.ds(b, 1)].rearrange("p o n -> p (o n)")
                    v.tensor_tensor(sc[:, OLD:OLD + 64], O0[:, 320:384], nm, ALU.add)
                    link(v.tensor_tensor(sc[:, WIN + 512:WIN + 576], O0[:, 384:448], nm, ALU.add))
                    link(v.tensor_scalar(sc[:, OLD:OLD + 64], sc[:, OLD:OLD + 64], sel[:, 64:65], None, ALU.add))
                    v.wait_ge(s_moved, 9 * b + 8)
                    link(v.tensor_reduce(mxs[:, 1:2], sc[:, 0:4160], AX, ALU.max))
                    v.tensor_scalar(mxs[:, 1:2], mxs[:, 1:2], -SCALE, None, ALU.mult).then_inc(max_ready, 1)
                    v.wait_ge(s_full, 9 * b + 9)
                    link(v.tensor_copy(sc[:, WIN:WIN + 512], psS[0][:, :]))
                    v.sem_inc(s_moved, 1)
                    w8 = sc[:, WIN:WIN + 512].rearrange("p (r q) -> p r q", r=4)[:, :, 0:2]
                    link(v.tensor_tensor(w8, w8, wmask.rearrange("p (q r) -> p r q", r=4), ALU.add))
                    link(v.tensor_reduce(mxs[:, 2:3], sc[:, WIN:WIN + 576], AX, ALU.max))
                    v.tensor_scalar(mxs[:, 2:3], mxs[:, 2:3], -SCALE, None, ALU.mult).then_inc(max_ready, 1)
                    for q in range(0, 10, 2):
                        v.wait_ge(t_full, 10 * b + q + 1)
                        if q >= 4:
                            v.wait_ge(pv_done, NJ * b + q - 2)
                        elif not first:
                            v.wait_ge(o_done, b)
                        if q == 0:
                            v.tensor_copy(ptn[:, 0:256], psT[0][:, 0:256])
                            v.tensor_copy(ptn[0:64, 256:512], psT[0][0:64, 256:512]).then_inc(t_moved_v, 1)
                        else:
                            v.tensor_copy(pt[0], psT[0][:, :]).then_inc(t_moved_v, 1)
                    link(v.memset(sms[:, 0:1], 1.0))
                    v.wait_ge(e_ready, 2 * b + 2)
                    link(v.reciprocal(cf[:, 0:3], sms[:, 0:3]))
                    g3 = gs[:, 0] if first else gs[:, bass.ds(b, 1)].rearrange("p o n -> p (o n)")
                    link(v.tensor_tensor(cf[:, 0:3], cf[:, 0:3], g3, ALU.mult))
                    v.wait_ge(o_done, b + 1)
                    for br, src in ((0, O1[:, 0:256]), (1, O0[:, 0:256]), (2, O1[:, 256:512])):
                        for g in range(NKV):
                            r = slice(32 * g, 32 * g + 32)
                            x = src[r, HD * g:HD * g + HD]
                            if br == 0:
                                ins = v.tensor_scalar(ob[r, :], x, cf[r, 0:1], None, ALU.mult)
                            elif br == 1:
                                ins = v.scalar_tensor_tensor(out=ob[r, :], in0=x, scalar=cf[r, 1:2], in1=ob[r, :], op0=ALU.mult, op1=ALU.add)
                            else:
                                for e in range(2):
                                    ins = v.scalar_tensor_tensor(out=ob2[r, e, :], in0=x, scalar=cf[r, 2:3], in1=ob[r, :], op0=ALU.mult, op1=ALU.add)
                        link(ins)
                    v.sem_inc(ob_ready, 1)
                    v.wait_ge(ob_turned, b + 1)
                    for e in range(2):
                        r = slice(64 * e, 64 * e + 64)
                        col = oT[r, :, SEQ:SEQ + 8] if first else oT[r, :, bass.ds(8 * b + SEQ, 8)]
                        ins = v.tensor_copy(col, O0[r, 0:P].rearrange("p (m e l) -> p m e l", m=8, e=2)[:, :, e, :])
                    link(ins)
                    v.sem_inc(o_stored, 1)
                    used = link.count
                    assert used == NL, used
                v.memset(pc[:, 255:256], 0.0).then_inc(pad_ready, 1)
                v.wait_ge(pad_ready, 1)
                samples(v, body)


def attention_out(nc, A, R, x, oT):
    with Scope(nc, "ao") as s:
        w = R(A_FREE, KT, D)
        bank = s.banks()
        w_in, full, used = s.sem("w_in"), s.sem("full"), s.sem("used")
        with nc.Block() as block:
            @block.sync
            def _(sp):
                sp.dma_start(w, A["b_w_o"][0].rearrange("(k p) n -> p k n", p=P)).then_inc(w_in, 16)

            @block.tensor
            def _(pe):
                pe.wait_ge(w_in, 16)
                for i, (t0, n) in enumerate(TILES):
                    for h in range(2):
                        j = 2 * i + h
                        if j >= 8:
                            pe.wait_ge(used, j - 7)
                        for k in range(KT):
                            ins = pe.matmul(bank[j % 8][0:n, :], oT[:, k, t0:t0 + n], w[:, k, 512 * h:512 * h + 512],
                                            start=(k == 0), stop=(k == KT - 1))
                        ins.then_inc(full, 1)

            @block.vector
            def _(v):
                for i, (t0, n) in enumerate(TILES):
                    for h in range(2):
                        j = 2 * i + h
                        v.wait_ge(full, j + 1)
                        xs = x[0:n, i, 512 * h:512 * h + 512]
                        v.scalar_tensor_tensor(out=xs, in0=xs, scalar=ALPHA, in1=bank[j % 8][0:n, :], op0=ALU.mult, op1=ALU.add).then_inc(used, 1)


OUTS = {"y_prompt": [1, SEQ, D], "y_sample": [DEC_B, DEC_S, D], "h_last": [P, DEC_B + 1, SG],
        "p_cmp": [1, SEQ, 2, NKV, HD], "p_slc": [1, SEQ, 2, NKV, HD], "p_win": [1, SEQ, 2, NKV, HD],
        "s_cmp": [DEC_B, DEC_S, 2, NKV, HD], "s_slc": [DEC_B, DEC_S, 2, NKV, HD], "s_win": [DEC_B, SEQ, 2, NKV, HD]}


def build(nc, A, O):
    def dram(name, shape, dt=F32):
        return nc.dram_tensor(name, shape, dt).ap()

    Scope.spent = []
    with Scope(nc, "all") as s:
        ident, jmat = s.sb("ident", [P, P]), s.sb("jmat", [P, P])
        A["eps"] = s.sb("eps", [P, 1])
        idx_cmp, idx_slc = s.sb("idx_cmp", [P, 2 * DEC_B], I32), s.sb("idx_slc", [P, 8 * DEC_B], I32)
        pe_bias, gates_s = s.sb("pe_bias", [P, 4]), s.sb("gates_s", [P, DEC_B, 3])
        R = Region(s.sb("arena", [P, ARENA]))
        x = R(X_OFF, NT, D)
        ck_dram, cv_dram = dram("ck", [DEC_B, P, 512]), dram("cv", [DEC_B, P, 512])
        constants(nc, ident, jmat, A["eps"])
        page_rows(nc, A, idx_cmp, idx_slc)
        compress_cache(nc, A, R, ident, idx_cmp, pe_bias, ck_dram, cv_dram)
        recycle(nc)

        u_dram, s5_dram = dram("u", [D, TOK]), dram("s5_y", [D, TOK])
        tab, bx1, bx2, cy1, cy2 = (R(S5_TAB, 20, 64), *[R(off, SG, SW) for off in (S5_X1, S5_X2, S5_Y1, S5_Y2)])
        toep, et, o = R(5376, SG, CH, SW), R(13568, SG, P), R(21760, SG, CH, SW)
        ho, hs = R(S5_X1, DEC_B + 1, SG), R(S5_X2 + 512, DEC_B, SG)
        s5_inputs(nc, A, R, ident, u_dram)
        s5_parameters(nc, A, ident, jmat, tab, bx1, bx2, cy1, cy2, R)
        s5_matrices(nc, A, R, ident, toep, et, o)
        s5_chunks(nc, A, R, toep, et, u_dram, hs)
        s5_scan(nc, R, jmat, hs, ho)
        s5_outputs(nc, R, o, s5_dram, ho, O["h_last"])
        glu(nc, A, R, x, u_dram, s5_dram)
        for layer in range(2):
            recycle(nc)
            if layer == 1:
                attention(nc, A, O, R, x, ident, idx_slc, pe_bias, gates_s, ck_dram, cv_dram, dram("gates", [DEC_B * DEC_S, NH * 3]))
                recycle(nc)
            x_dram, row_tok, y_rows = dram(f"x{layer}", [TOK, D]), dram(f"row_tok{layer}", [NROW, 1], I32), dram(f"y_rows{layer}", [NROW, D])
            layer_norm(nc, A, R, f"ln_a{layer}", layer, 0, ident, x, x_dram=x_dram)
            route(nc, A, R, f"route{layer}", layer, row_tok)
            experts(nc, A, R, f"moe{layer}", layer, ident, x_dram, y_rows)
            combine(nc, R, f"comb{layer}", x, y_rows)
            layer_norm(nc, A, R, f"ln_b{layer}", layer, 1, ident, x,
                       outs=(O["y_prompt"], O["y_sample"]) if layer == 1 else None, turn=(layer == 0))


def attention(nc, A, O, R, x, ident, idx_slc, pe_bias, gates_s, ck_dram, cv_dram, gate_dram):
    at = [XT_OFF]

    def place(*shape):
        at[0] += int(np.prod(shape))
        return R(at[0] - int(np.prod(shape)), *shape)

    projections(nc, A, R, [O[n] for n in ("p_cmp", "p_slc", "p_win", "s_cmp", "s_slc", "s_win")], gate_dram)
    ck_p, cv_p = place(2, 32), place(256)
    causal, seen, seen01 = place(P), place(4, NCMP_P), place(4, NCMP_P)
    new_mask, win_mask, head_sum, forced = place(DEC_B, 64), place(8), place(P), place(66)
    new_keys = place(2, 2, 64)
    compress_prompt(nc, A, R, ident, pe_bias, O["p_cmp"], ck_p, cv_p)
    attention_masks(nc, R, causal, seen, seen01, new_mask, win_mask, head_sum, forced)
    oT = R(OT_OFF, KT, TOK)
    prompt_attention(nc, A, R, ident, ck_p, cv_p, causal, seen, seen01, new_keys, oT)
    sample_queries(nc, R, gate_dram, gates_s)
    sample_attention(nc, A, R, ident, idx_slc, ck_dram, cv_dram, new_keys, new_mask, win_mask, head_sum, forced, gates_s, oT)
    attention_out(nc, A, R, x, oT)


def kernel(**inputs):
    import numpy as _np
    import concourse.bacc as _bacc
    from concourse import mybir as _mybir
    from concourse.bass_utils import run_bass_kernel_spmd as _run

    nc = _bacc.Bacc("TRN2", target_bir_lowering=False, num_devices=1)
    given = {n: _np.asarray(inputs[n]) for n in _INS}
    given["state_ssm"] = given["state_ssm"][0].transpose(3, 2, 0, 1).reshape(P, DEC_B, SG)
    given["a_d"] = given["a_d"].reshape(KT, P).T
    given["cmp_pe"] = given["cmp_pe"].reshape(2, 16, P).transpose(2, 0, 1)
    w = given["b_w_qg"][0]
    wq = w[:, :D].reshape(D, 2, 2, HPK, HD).transpose(0, 1, 3, 2, 4).reshape(D, D)
    given["b_w_qg"] = _np.concatenate([wq, w[:, D:]], axis=1)
    arrays, A, O = {}, {}, {}
    for n in _INS:
        a = _np.ascontiguousarray(given[n])
        arrays[f"in_{n}"] = a
        A[n] = nc.dram_tensor(f"in_{n}", a.shape, _mybir.dt.from_np(a.dtype), kind="ExternalInput").ap()
    for n, shape in OUTS.items():
        O[n] = nc.dram_tensor(f"out_{n}", shape, _mybir.dt.float32, kind="ExternalOutput").ap()
    build(nc, A, O)
    r = _run(nc, [arrays], core_ids=[0])
    got = {n: r.results[0][f"out_{n}"] for n in OUTS}
    h = got["h_last"]
    p_state = _np.ascontiguousarray(h[:, DEC_B].reshape(2, SP_, SG).transpose(2, 1, 0))[None, None]
    s_state = _np.ascontiguousarray(h[:, :DEC_B].reshape(2, SP_, DEC_B, SG).transpose(2, 3, 1, 0))[None]
    return (got["y_prompt"], got["y_sample"], p_state, got["p_cmp"], got["p_slc"], got["p_win"],
            s_state, got["s_cmp"], got["s_slc"], got["s_win"])
```

```python
from contextlib import ExitStack

import numpy as np

import concourse.bass as bass
from concourse import mybir

F32 = mybir.dt.float32
BF16 = mybir.dt.bfloat16
I32 = mybir.dt.int32
U32 = mybir.dt.uint32
ALU = mybir.AluOpType
ACT = mybir.ActivationFunctionType
AX = mybir.AxisListType.X

P = 128
D = 1024
KT = D // P
SEQ = 512
DEC_B, DEC_S = 8, 8
TOK = SEQ + DEC_B * DEC_S
TILES = [(0, 128), (128, 128), (256, 128), (384, 128), (512, 64)]
NT = len(TILES)
PAST, PAGE = 4096, 128
N_POOL = 320
SG, SP_, SW, CH = 64, 64, 16, 8
NCP = SEQ // CH
NC_ = NCP + DEC_B
NH, HD, NKV, HPK = 16, 64, 4, 4
SCALE = HD ** -0.5
CMP_H = 256
NCMP_S = PAST // 16 - 1
NCMP_P = SEQ // 16 - 1
NSEL = 65
NEG = -1e30
TINY = 1e-30
NG, EPG, NE, DE = 4, 8, 32, 256
RB = 64
NMORE = (TOK * 2) // (RB + 1)
NBLK = NE + NMORE
NROW = NBLK * RB
ALPHA = (2 * 2) ** 0.25
EPS = 1e-5
ARENA = 52000

TWO_PI = 2 * np.pi
C1 = 6.28125
C2 = float(np.float32(np.round((TWO_PI - C1) * 2 ** 22) / 2 ** 22))
C3 = float(np.float32(TWO_PI - C1 - C2))
INV_2PI = float(np.float32(1 / TWO_PI))
MAGIC = 12582912.0


def bc(ap, shape):
    return ap.to_broadcast(shape)


class Link:

    def __init__(self, eng, sem, base=0):
        self.eng, self.sem, self.n, self.count = eng, sem, base, 0

    def __call__(self, ins):
        ins.then_inc(self.sem, 1)
        self.n = self.n + 1
        self.count += 1
        self.eng.wait_ge(self.sem, self.n)


class Scope:

    spent = []

    def __init__(self, nc, name):
        self.nc, self.name, self.ctx = nc, name, ExitStack()

    def __enter__(self):
        self.ctx.__enter__()
        return self

    def __exit__(self, *a):
        return self.ctx.__exit__(*a)

    def sb(self, name, shape, dt=F32):
        return self.ctx.enter_context(self.nc.sbuf_tensor(f"{self.name}_{name}", shape, dt))

    def banks(self, n=8, dt=F32):
        return [self.ctx.enter_context(self.nc.psum_tensor(f"{self.name}_bank{i}", [P, 512], dt)) for i in range(n)]

    @staticmethod
    def handles(nc, names):
        made = [nc.alloc_semaphore(name=n) for n in names]
        Scope.spent.extend(made)
        return made

    def sem(self, name):
        return Scope.handles(self.nc, [f"{self.name}_{name}"])[0]


def recycle(nc):
    with nc.Block() as block:
        @block.gpsimd
        def _(pool):
            nc.clear_and_free_semaphores(Scope.spent)
    Scope.spent = []


def constants(nc, ident, jmat, eps):
    with Scope(nc, "const") as s:
        zeroed, made = s.sem("zeroed"), s.sem("made")
        with nc.Block() as block:
            @block.gpsimd
            def _(pool):
                pool.memset(ident[:, :], 0.0).then_inc(zeroed, 1)
                pool.memset(jmat[:, :], 0.0).then_inc(zeroed, 1)
                pool.memset(eps[:, :], EPS).then_inc(zeroed, 1)
                pool.wait_ge(zeroed, 3)
                pool.affine_select(out=ident[:, :], in_=ident[:, :], compare_op=ALU.not_equal, fill=1.0,
                                   base=0, pattern=[[-1, P]], channel_multiplier=1).then_inc(made, 1)
                pool.affine_select(out=jmat[:, 0:64], in_=jmat[:, 0:64], compare_op=ALU.not_equal, fill=-1.0,
                                   base=-64, pattern=[[-1, 64]], channel_multiplier=1).then_inc(made, 1)
                pool.affine_select(out=jmat[:, 64:P], in_=jmat[:, 64:P], compare_op=ALU.not_equal, fill=1.0,
                                   base=0, pattern=[[-1, 64]], channel_multiplier=1).then_inc(made, 1)
                pool.wait_ge(made, 3)


def s5_parameters(nc, A, ident, jmat, tab, x1, x2, y1, y2, R):
    with Scope(nc, "par") as s:
        at = [5376]

        def place(name, shape):
            at[0] += int(np.prod(shape[1:]))
            return R(at[0] - int(np.prod(shape[1:])), *shape[1:], np_=64)

        lr, li = place("lr", [64, 64]), place("li", [64, 64])
        ldt, dt = place("ldt", [64, 1]), place("dt", [64, 1])
        b_in, bb = place("b_in", [64, 2, 1024]), place("bb", [64, 2, 1024])
        c_in = place("c_in", [64, 16, 2, 64])
        tmp = place("tmp", [64, 1024])
        a1, th = place("a1", [64, 64]), place("th", [64, 64])
        rnd = place("rnd", [64, 9, 64])
        ang = place("ang", [64, 9, 64])
        sn, sh, mag = place("sn", [64, 9, 64]), place("sh", [64, 9, 64]), place("mag", [64, 9, 64])
        t20 = place("t20", [64, 20, 2, 64])
        den, rden, nr, t1, t2, zr, zi = (place(n, [64, 64]) for n in ("den", "rden", "nr", "t1", "t2", "zr", "zi"))
        bank = s.banks()
        loaded, dt_ready, a_ready, ang_ready, trig = (s.sem(n) for n in ("loaded", "dt_ready", "a_ready", "ang_ready", "trig"))
        dve, t20_ready, bb_ready, turned, moved, jdone = (s.sem(n) for n in ("dve", "t20_ready", "bb_ready", "turned", "moved", "jdone"))
        LOADS = [(lr[:, :], A["a_lambda_re"][0]), (li[:, :], A["a_lambda_im"][0]),
                 (ldt[:, :], A["a_log_dt"].rearrange("o g -> g o")),
                 (b_in[:, 0, :], A["a_b_re"][0].rearrange("g p w -> g (p w)")),
                 (b_in[:, 1, :], A["a_b_im"][0].rearrange("g p w -> g (p w)")),
                 (c_in[:, :, 0, :], A["a_c_re"][0]),
                 (c_in[:, :, 1, :], A["a_c_im"][0])]
        with nc.Block() as block:
            @block.sync
            def _(sp):
                for dst, src in LOADS:
                    sp.dma_start(dst, src).then_inc(loaded, 16)

            @block.scalar
            def _(act):
                act.wait_ge(loaded, 16 * len(LOADS))
                nc.scalar.activation(dt[:, :], ldt[:, :], ACT.Exp).then_inc(dt_ready, 1)
                act.wait_ge(a_ready, 1)
                for k in range(9):
                    nc.scalar.activation(mag[:, k, :], a1[:, :], ACT.Exp, scale=float(k)).then_inc(trig, 1)
                act.wait_ge(ang_ready, 1)
                nc.scalar.activation(sn[:, :, :], ang[:, :, :], ACT.Sin).then_inc(trig, 1)
                nc.scalar.activation(sh[:, :, :], ang[:, :, :], ACT.Sin, scale=0.5).then_inc(trig, 1)

            @block.vector
            def _(v):
                link = Link(v, dve)
                v.wait_ge(dt_ready, 1)
                v.tensor_scalar(a1[:, :], lr[:, :], dt[:, 0:1], None, ALU.mult).then_inc(a_ready, 1)
                link(v.tensor_scalar(th[:, :], li[:, :], dt[:, 0:1], None, ALU.mult))

                def reduce_angle(a, n):
                    link(v.tensor_scalar(n, a, INV_2PI, MAGIC, ALU.mult, ALU.add))
                    link(v.tensor_scalar(n, n, MAGIC, None, ALU.subtract))
                    for c in (C1, C2, C3):
                        link(v.scalar_tensor_tensor(out=a, in0=n, scalar=-c, in1=a, op0=ALU.mult, op1=ALU.add))

                reduce_angle(th[:, :], rnd[:, 0, :])
                for k in range(9):
                    ins = v.tensor_scalar(ang[:, k, :], th[:, :], float(k), None, ALU.mult)
                link(ins)
                reduce_angle(ang[:, :, :], rnd[:, :, :])
                v.engine_nop().then_inc(ang_ready, 1)
                link(v.tensor_tensor(t1[:, :], lr[:, :], lr[:, :], ALU.mult))
                link(v.tensor_tensor(t2[:, :], li[:, :], li[:, :], ALU.mult))
                link(v.tensor_tensor(den[:, :], t1[:, :], t2[:, :], ALU.add))
                link(v.reciprocal(rden[:, :], den[:, :]))
                v.wait_ge(trig, 11)
                link(v.tensor_tensor(sh[:, :, :], sh[:, :, :], sh[:, :, :], ALU.mult))
                link(v.tensor_scalar(sh[:, :, :], sh[:, :, :], -2.0, 1.0, ALU.mult, ALU.add))
                for ri in range(2):
                    v.tensor_tensor(t20[:, 0:9, ri, :], mag[:, :, :], sh[:, :, :], ALU.mult)
                    v.tensor_tensor(t20[:, 9:18, ri, :], mag[:, :, :], sn[:, :, :], ALU.mult)
                    v.tensor_copy(t20[:, 18, ri, :], ang[:, 8, :])
                    ins = v.tensor_copy(t20[:, 19, ri, :], mag[:, 8, :])
                link(ins)
                v.engine_nop().then_inc(t20_ready, 1)
                ai = t20[:, 10, 0, :]
                link(v.tensor_scalar(nr[:, :], t20[:, 1, 0, :], 1.0, None, ALU.subtract))
                link(v.tensor_tensor(t1[:, :], nr[:, :], lr[:, :], ALU.mult))
                link(v.tensor_tensor(t2[:, :], ai, li[:, :], ALU.mult))
                link(v.tensor_tensor(t1[:, :], t1[:, :], t2[:, :], ALU.add))
                link(v.tensor_tensor(zr[:, :], t1[:, :], rden[:, :], ALU.mult))
                link(v.tensor_tensor(t1[:, :], ai, lr[:, :], ALU.mult))
                link(v.tensor_tensor(t2[:, :], nr[:, :], li[:, :], ALU.mult))
                link(v.tensor_tensor(t1[:, :], t1[:, :], t2[:, :], ALU.subtract))
                link(v.tensor_tensor(zi[:, :], t1[:, :], rden[:, :], ALU.mult))
                zrb, zib = (bc(z[:, :].unsqueeze(2), [64, 64, 16]) for z in (zr, zi))
                pw = "g (p w) -> g p w"
                br, bi = (b_in[:, i, :].rearrange(pw, w=16) for i in range(2))
                b0, b1 = (bb[:, i, :].rearrange(pw, w=16) for i in range(2))
                tm = tmp[:, :].rearrange(pw, w=16)
                v.tensor_tensor(b0, br, zrb, ALU.mult)
                link(v.tensor_tensor(tm, bi, zib, ALU.mult))
                link(v.tensor_tensor(b0, b0, tm, ALU.subtract))
                v.tensor_tensor(b1, bi, zrb, ALU.mult)
                link(v.tensor_tensor(tm, br, zib, ALU.mult))
                link(v.tensor_tensor(b1, b1, tm, ALU.add))
                link(v.tensor_scalar(c_in[:, :, 1, :], c_in[:, :, 1, :], -1.0, None, ALU.mult))
                v.engine_nop().then_inc(bb_ready, 1)
                for i in range(3):
                    v.wait_ge(turned, i + 1)
                    n = 8 if i < 2 else 4
                    v.tensor_copy(tab[:, 8 * i:8 * i + n, :].rearrange("p k g -> p (k g)"),
                                  bank[i][:, 0:64 * n]).then_inc(moved, 1)
                for i in range(4):
                    dst = x1 if i < 2 else y1
                    h = i % 2
                    v.wait_ge(turned, 4 + i)
                    v.tensor_copy(dst[:, :, 8 * h:8 * h + 8],
                                  bank[3 + i][:, :].rearrange("p (w g) -> p g w", w=8)).then_inc(moved, 1)
                for i in range(4):
                    dst = x2 if i < 2 else y2
                    h = i % 2
                    v.wait_ge(jdone, i + 1)
                    v.tensor_copy(dst[:, 32 * h:32 * h + 32, :].rearrange("p g w -> p (g w)"),
                                  bank[i][:, :]).then_inc(moved, 1)
                v.wait_ge(moved, 11)

            @block.tensor
            def _(pe):
                pe.wait_ge(t20_ready, 1)
                for k in range(20):
                    ins = pe.transpose(bank[k // 8][:, 64 * (k % 8):64 * (k % 8) + 64],
                                       t20[:, k, :, :].rearrange("g r p -> g (r p)"), ident[0:64, 0:64])
                    if k in (7, 15, 19):
                        ins.then_inc(turned, 1)
                pe.wait_ge(bb_ready, 1)
                for which in range(2):
                    for w in range(16):
                        src = (bb[:, :, :].rearrange("g r (p w) -> g (r p) w", w=16)[:, :, w] if which == 0 else
                               c_in[:, w, :, :].rearrange("g r p -> g (r p)"))
                        j = 2 * which + w // 8
                        ins = pe.transpose(bank[3 + j][:, 64 * (w % 8):64 * (w % 8) + 64], src, ident[0:64, 0:64])
                        if w % 8 == 7:
                            ins.then_inc(turned, 1)
                pe.wait_ge(moved, 7)
                for i in range(4):
                    src = (x1 if i < 2 else y1)[:, 32 * (i % 2):32 * (i % 2) + 32, :].rearrange("p g w -> p (g w)")
                    pe.matmul(bank[i][:, :], jmat[:, :], src, start=True, stop=True).then_inc(jdone, 1)


_INS = ['x_prompt', 'x_sample', 'state_ssm', 'cache_cmp_kv', 'cache_slc_kv', 'cache_win_kv', 'page_table',
        'a_w_in', 'a_lambda_re', 'a_lambda_im', 'a_log_dt', 'a_b_re', 'a_b_im', 'a_c_re', 'a_c_im', 'a_d', 'a_w_glu',
        'kv_w', 'cmp_pe', 'cmp_w1', 'cmp_w2', 'b_w_qg', 'b_w_o',
        'moe_w_group', 'moe_w_expert', 'moe_w_gate_up', 'moe_w_down', 'ln_g', 'ln_b']


class Region:

    def __init__(self, arena):
        self.arena = arena

    def __call__(self, off, *shape, dt=F32, np_=P):
        n = int(np.prod(shape))
        if dt is BF16:
            assert n % 2 == 0
            v = self.arena[0:np_, off:off + n // 2].bitcast(BF16)
        else:
            v = self.arena[0:np_, off:off + n]
            if dt is not F32:
                v = v.bitcast(dt)
        if len(shape) == 1:
            return v
        names = "abcdef"[:len(shape)]
        return v.rearrange(f"p ({' '.join(names)}) -> p {' '.join(names)}", **dict(zip(names[1:], shape[1:])))


class Split:

    def __init__(self, n, full, used):
        self.n, self.full, self.used = n, full, used

    def claim(self, pe, job):
        old = job - self.n
        if old >= 0:
            pe.wait_ge(self.used[old % 2], old // 2 + 1)
        return job % self.n

    def done(self, ins):
        ins.then_inc(self.full, 1)

    def all_used(self, eng, jobs):
        if jobs > 0:
            eng.wait_ge(self.used[0], (jobs + 1) // 2)
        if jobs > 1:
            eng.wait_ge(self.used[1], jobs // 2)


S5_TAB, S5_X1, S5_X2, S5_Y1, S5_Y2, S5_FREE = 0, 1280, 2304, 3328, 4352, 5376


def s5_inputs(nc, A, R, ident, u_dram):
    with Scope(nc, "inp") as s:
        w = R(5376, KT, D)
        xT = R(13568, KT, CH, NC_)
        uT = R(18176, KT, CH * NC_)
        xin = R(22784, 2, D)
        bank = s.banks()
        w_in, stored = s.sem("w_in"), s.sem("stored")
        x_in = [s.sem(f"x_in{i}") for i in range(2)]
        full, used = s.sem("full"), (s.sem("used_v"), s.sem("used_a"))
        ring = Split(8, full, used)
        NJ = 2 * NT
        half = CH * NC_ // 2

        def x_rows(i):
            if i < 4:
                return A["x_prompt"][0, 128 * i:128 * i + 128, :]
            return A["x_sample"].rearrange("b t d -> (b t) d")

        def turn_out(eng_copy, i, h):
            n = TILES[i][1]
            job = 2 * i + h
            src = bank[job % 8][:, :].rearrange("p (k t) -> p k t", k=4)[:, :, 0:n].rearrange("p k (c s) -> p k c s", s=CH)
            dst = xT[:, 4 * h:4 * h + 4, :, 16 * i:16 * i + n // CH].rearrange("p k s c -> p k c s")
            return [eng_copy(dst[:, k], src[:, k]) for k in range(4)][-1]

        with nc.Block() as block:
            @block.sync
            def _(sp):
                for i in range(NT):
                    if i >= 2:
                        sp.wait_ge(full, 2 * (i - 1))
                    sp.dma_start(xin[0:TILES[i][1], i % 2, :], x_rows(i)).then_inc(x_in[i % 2], 16)
                    if i == 1:
                        sp.dma_start(w[:, :, :], A["a_w_in"][0].rearrange("(k p) n -> p k n", p=P)).then_inc(w_in, 16)
                for m in range(KT):
                    ring.all_used(sp, NJ + 2 * m + 2)
                    sp.dma_start(u_dram[P * m:P * m + P, :], uT[:, m, :]).then_inc(stored, 16)
                sp.wait_ge(stored, 16 * KT)

            @block.tensor
            def _(pe):
                for i, (_, n) in enumerate(TILES):
                    pe.wait_ge(x_in[i % 2], 16 * (i // 2 + 1))
                    for h in range(2):
                        b = ring.claim(pe, 2 * i + h)
                        for k in range(4):
                            ins = pe.transpose(bank[b][:, P * k:P * k + n],
                                               xin[0:n, i % 2, P * (4 * h + k):P * (4 * h + k + 1)], ident[0:n, 0:n])
                        ring.done(ins)
                pe.wait_ge(w_in, 16)
                ring.all_used(pe, NJ)
                xf = xT[:, :, :, :].rearrange("p k s c -> p k (s c)")
                for m in range(KT):
                    for n in range(2):
                        b = ring.claim(pe, NJ + 2 * m + n)
                        for k in range(KT):
                            ins = pe.matmul(bank[b][:, 0:half], w[:, k, P * m:P * m + P],
                                            xf[:, k, half * n:half * n + half], start=(k == 0), stop=(k == KT - 1))
                        ring.done(ins)

            def empty(eng, copy, me):
                for i in range(NT):
                    eng.wait_ge(full, 2 * i + me + 1)
                    turn_out(copy, i, me).then_inc(used[me], 1)
                for m in range(KT):
                    job = NJ + 2 * m + me
                    eng.wait_ge(full, job + 1)
                    copy(uT[:, m, half * me:half * me + half], bank[job % 8][:, 0:half]).then_inc(used[me], 1)

            @block.vector
            def _(v):
                empty(v, v.tensor_copy, 0)

            @block.scalar
            def _(act):
                empty(act, nc.scalar.copy, 1)


def s5_matrices(nc, A, R, ident, toep, et, o):
    with Scope(nc, "mat") as s:
        tab = R(S5_TAB, 20, 64)
        x1, x2, y1, y2 = (R(off, SG, SW) for off in (S5_X1, S5_X2, S5_Y1, S5_Y2))
        e = R(5376, SG, CH, SW)
        kb = R(38144, SG, SW)
        tt = R(29952, CH, SG, SW)
        tv, tp = R(39168, 2, SG, SW), R(41216, 2, SG, SW)
        bank = s.banks()
        dve, pool_, e_ready, zeroed, shifted = (s.sem(n) for n in ("dve", "pool", "e_ready", "zeroed", "shifted"))
        full, used = s.sem("full"), (s.sem("used_v"), s.sem("used_a"))
        k_full, k_used = s.sem("k_full"), s.sem("k_used")
        ring = Split(6, full, used)

        def coef(row):
            return bc(tab[:, row, :].unsqueeze(2), [P, SG, SW])

        with nc.Block() as block:
            @block.vector
            def _(v):
                link = Link(v, dve)
                for st in range(CH):
                    k = CH - 1 - st
                    v.tensor_tensor(tv[:, 0], x1, coef(k), ALU.mult)
                    link(v.tensor_tensor(tv[:, 1], x2, coef(9 + k), ALU.mult))
                    link(v.tensor_tensor(e[:, :, st, :], tv[:, 0], tv[:, 1], ALU.add))
                v.engine_nop().then_inc(e_ready, 1)
                for h in range(2):
                    v.wait_ge(k_full, h + 1)
                    v.tensor_copy(kb[:, 32 * h:32 * h + 32, :].rearrange("p g w -> p (g w)"),
                                  bank[6 + h][:, :]).then_inc(k_used, 1)
                for j in range(0, 16, 2):
                    v.wait_ge(full, j + 1)
                    v.tensor_copy(et[:, 4 * j:4 * j + 4, :].rearrange("p g m -> p (g m)"),
                                  bank[j % 6][:, :]).then_inc(used[0], 1)
                v.wait_ge(full, 16)
                for t in range(0, CH, 2):
                    if t == 0:
                        v.wait_ge(shifted, 16 * CH)
                    ins = v.tensor_copy(toep[:, :, t, :], tt[:, t, :, :])
                link(ins)

            @block.scalar
            def _(act):
                for j in range(1, 16, 2):
                    act.wait_ge(full, j + 1)
                    nc.scalar.copy(et[:, 4 * j:4 * j + 4, :].rearrange("p g m -> p (g m)"),
                                   bank[j % 6][:, :]).then_inc(used[1], 1)
                act.wait_ge(full, 16)
                act.wait_ge(shifted, 16 * CH)
                for t in range(1, CH, 2):
                    nc.scalar.copy(toep[:, :, t, :], tt[:, t, :, :]).then_inc(used[1], 1)

            @block.tensor
            def _(pe):
                pe.wait_ge(e_ready, 1)
                for g in range(SG):
                    ins = pe.matmul(bank[6 + g // 32][:, SW * (g % 32):SW * (g % 32) + SW],
                                    e[:, g, :, :].rearrange("p s w -> p (s w)"), y1[:, g, :],
                                    start=True, stop=True)
                    if g % 32 == 31:
                        ins.then_inc(k_full, 1)
                for j in range(16):
                    b = ring.claim(pe, j)
                    for q in range(4):
                        ins = pe.transpose(bank[b][:, P * q:P * q + P],
                                           e[:, 4 * j + q, :, :].rearrange("p s w -> p (s w)"), ident[:, :])
                    ring.done(ins)

            @block.gpsimd
            def _(pool):
                pool.memset(tt[:, :, :, :], 0.0).then_inc(zeroed, 1)
                link = Link(pool, pool_)
                for t in range(CH):
                    k = t + 1
                    pool.tensor_tensor(tp[:, 0], y1, coef(k), ALU.mult)
                    link(pool.tensor_tensor(tp[:, 1], y2, coef(9 + k), ALU.mult))
                    link(pool.tensor_tensor(o[:, :, t, :], tp[:, 0], tp[:, 1], ALU.subtract))

            @block.sync
            def _(sp):
                sp.wait_ge(zeroed, 1)
                sp.wait_ge(k_used, 2)
                for t in range(CH):
                    n = SW * (t + 1)
                    sp.dma_start(tt[0:n, t, :, :], kb[P - n:P, :, :]).then_inc(shifted, 16)


def s5_chunks(nc, A, R, toep, et, u_dram, hs):
    with Scope(nc, "chk") as s:
        tab = R(S5_TAB, 20, 64)
        uc, v_, y_ = R(29952, SG, NC_), R(34560, SG, NC_), R(39168, SG, NC_)
        cos_, sin_ = R(43776, SG, NCP), R(47872, SG, NCP)
        cidx = R(S5_X1, NCP)
        sh = R(21760 - 4096, SG, NCP)
        bank = s.banks()
        h_in, uin, dve, idx = (s.sem(n) for n in ("h_in", "uin", "dve", "idx"))
        full, used, ang_ready, sins, et_used = (s.sem(n) for n in ("full", "used", "ang_ready", "sins", "et_used"))
        GB = 7
        NB = -(-SG // GB)
        jobs = [(m, q, list(range(GB * q, min(GB * q + GB, SG)))) for m in range(2) for q in range(NB)]

        def flat(x):
            return x.rearrange("p g c -> p (g c)")

        with nc.Block() as block:
            @block.sync
            def _(sp):
                sp.dma_start(hs, A["state_ssm"]).then_inc(h_in, 16)
                for st in range(CH):
                    sp.dma_start(uc[SW * st:SW * st + SW, :, :],
                                 u_dram.rearrange("(g w) (s c) -> w s g c", w=SW, s=CH)[:, st]).then_inc(uin, 16)
                sp.wait_ge(h_in, 16)

            @block.tensor
            def _(pe):
                pe.wait_ge(uin, 16 * CH)
                for j, (m, q, gs) in enumerate(jobs):
                    if j >= 8:
                        pe.wait_ge(used, j - 7)
                    for n, g in enumerate(gs):
                        lhs = et[:, g] if m == 0 else toep[:, g].rearrange("p t w -> p (t w)")
                        ins = pe.matmul(bank[j % 8][:, NC_ * n:NC_ * n + NC_], lhs, uc[:, g, :], start=True, stop=True)
                    ins.then_inc(full, 1)

            @block.scalar
            def _(act):
                for j, (m, q, gs) in enumerate(jobs):
                    act.wait_ge(full, j + 1)
                    dst = (v_, y_)[m]
                    nc.scalar.copy(flat(dst[:, gs[0]:gs[-1] + 1, :]), bank[j % 8][:, 0:NC_ * len(gs)]).then_inc(used, 1)
                act.wait_ge(ang_ready, 1)
                nc.scalar.activation(sh, cos_, ACT.Sin, scale=0.5).then_inc(sins, 1)
                nc.scalar.activation(sin_, cos_, ACT.Sin).then_inc(sins, 1)

            @block.gpsimd
            def _(pool):
                pool.iota(cidx, pattern=[[1, NCP]], base=0, channel_multiplier=0,
                          allow_small_or_imprecise_dtypes=True).then_inc(idx, 1)

            @block.vector
            def _(v):
                link = Link(v, dve)
                v.wait_ge(idx, 1)
                link(v.tensor_tensor(cos_, bc(tab[:, 18, :].unsqueeze(2), [P, SG, NCP]),
                                     bc(cidx.unsqueeze(1), [P, SG, NCP]), ALU.mult))
                link(v.tensor_scalar(sin_, cos_, INV_2PI, MAGIC, ALU.mult, ALU.add))
                link(v.tensor_scalar(sin_, sin_, MAGIC, None, ALU.subtract))
                for c in (C1, C2, C3):
                    link(v.scalar_tensor_tensor(out=cos_, in0=sin_, scalar=-c, in1=cos_, op0=ALU.mult, op1=ALU.add))
                v.engine_nop().then_inc(ang_ready, 1)
                v.wait_ge(sins, 2)
                link(v.tensor_tensor(cos_, sh, sh, ALU.mult))
                link(v.tensor_scalar(cos_, cos_, -2.0, 1.0, ALU.mult, ALU.add))


def s5_scan(nc, R, jmat, hs, ho):
    with Scope(nc, "scan") as s:
        tab = R(S5_TAB, 20, 64)
        v_ = R(34560, SG, NC_)
        cos_, sin_ = R(43776, SG, NCP), R(47872, SG, NCP)
        rho, gc, g_, t_ = R(5376, SG, NCP), R(9472, SG, NCP), R(13568, SG, NCP), R(17664, SG, NCP)
        hp = R(29952, SG, NC_)
        th = R(S5_X2, DEC_B, SG)
        bank = s.banks()
        dve, turned, gs_ready, rho_ready, pooled = (s.sem(n) for n in ("dve", "turned", "gs_ready", "rho_ready", "pooled"))
        h_read = s.sem("h_read")
        Q = 8
        with nc.Block() as block:
            @block.tensor
            def _(pe):
                for q in range(8):
                    pe.matmul(bank[q][:, :], jmat[:, :], v_[:, Q * q:Q * q + Q, 0:NCP], start=True, stop=True).then_inc(turned, 1)
                for q in range(8):
                    pe.wait_ge(gs_ready, q + 1)
                    pe.matmul(bank[q][:, :], jmat[:, :], t_[:, Q * q:Q * q + Q, :], start=True, stop=True).then_inc(turned, 1)
                pe.wait_ge(h_read, 1)
                pe.matmul(bank[0][:, :], jmat[:, :], hs.rearrange("p b g -> p (b g)"), start=True, stop=True).then_inc(turned, 1)

            @block.gpsimd
            def _(pool):
                pool.tensor_copy(rho, bc(tab[:, 19, :].unsqueeze(2), [P, SG, NCP])).then_inc(pooled, 1)
                pool.wait_ge(pooled, 1)
                pool.memset(rho[:, :, 0:1], 0.0).then_inc(rho_ready, 1)
                pool.memset(hp[:, :, 0:1], 0.0).then_inc(rho_ready, 1)
                pool.tensor_copy(hp[:, :, NCP:NC_], hs.rearrange("p b g -> p g b")).then_inc(rho_ready, 1)

            @block.vector
            def _(v):
                link = Link(v, dve)
                link(v.tensor_tensor(g_, v_[:, :, 0:NCP], cos_, ALU.mult))
                for q in range(8):
                    g8 = slice(Q * q, Q * q + Q)
                    v.wait_ge(turned, q + 1)
                    ins = v.tensor_tensor(t_[:, g8, :], bank[q][:, :].rearrange("p (g c) -> p g c", g=Q), sin_[:, g8, :], ALU.mult)
                link(ins)
                link(v.tensor_tensor(g_, g_, t_, ALU.subtract))
                v.wait_ge(rho_ready, 3)
                flat = "p g c -> p (g c)"
                link(v.tensor_tensor_scan(gc.rearrange(flat), rho.rearrange(flat), g_.rearrange(flat), 0.0, ALU.mult, ALU.add))
                for q in range(8):
                    g8 = slice(Q * q, Q * q + Q)
                    v.tensor_tensor(t_[:, g8, :], gc[:, g8, :], sin_[:, g8, :], ALU.mult).then_inc(gs_ready, 1)
                link(v.tensor_tensor(g_, gc, cos_, ALU.mult))
                for q in range(8):
                    g8 = slice(Q * q, Q * q + Q)
                    v.wait_ge(turned, 9 + q)
                    src = bank[q][:, :].rearrange("p (g c) -> p g c", g=Q)
                    v.tensor_tensor(hp[:, g8, 1:NCP], g_[:, g8, 0:NCP - 1], src[:, :, 0:NCP - 1], ALU.add)
                    last = v.tensor_tensor(ho[:, 8, g8], g_[:, g8, NCP - 1], src[:, :, NCP - 1], ALU.add)
                    if q == 0:
                        last.then_inc(h_read, 1)
                v.wait_ge(turned, 17)
                a8r, a8i = (bc(tab[:, r, :].unsqueeze(1), [P, DEC_B, SG]) for r in (8, 17))
                v.tensor_tensor(ho[:, 0:8, :], hs, a8r, ALU.mult)
                link(v.tensor_tensor(th, bank[0][:, :].rearrange("p (b g) -> p b g", b=DEC_B), a8i, ALU.mult))
                link(v.tensor_tensor(ho[:, 0:8, :], ho[:, 0:8, :], th, ALU.add))
                link(v.tensor_tensor(ho[:, 0:8, :], ho[:, 0:8, :], v_[:, :, NCP:NC_].rearrange("p g b -> p b g"), ALU.add))


def s5_outputs(nc, R, o, y_dram, ho, h_out):
    with Scope(nc, "out") as s:
        hp, y_ = R(29952, SG, NC_), R(39168, SG, NC_)
        bank = s.banks()
        full, used, stored = s.sem("full"), s.sem("used"), s.sem("stored")
        GB = 7
        NB = -(-SG // GB)
        with nc.Block() as block:
            @block.sync
            def _(sp):
                sp.dma_start(h_out, ho).then_inc(stored, 16)
                sp.wait_ge(used, NB)
                for st in range(CH):
                    sp.dma_start(y_dram.rearrange("(g w) (s c) -> w s g c", w=SW, s=CH)[:, st],
                                 y_[SW * st:SW * st + SW, :, :]).then_inc(stored, 16)
                sp.wait_ge(stored, 16 * (CH + 1))

            @block.tensor
            def _(pe):
                for q in range(NB):
                    if q >= 8:
                        pe.wait_ge(used, q - 7)
                    for n, g in enumerate(range(GB * q, min(GB * q + GB, SG))):
                        ins = pe.matmul(bank[q % 8][:, NC_ * n:NC_ * n + NC_], o[:, g].rearrange("p t w -> p (t w)"),
                                        hp[:, g, :], start=True, stop=True)
                    ins.then_inc(full, 1)

            @block.vector
            def _(v):
                for q in range(NB):
                    a, b = GB * q, min(GB * q + GB, SG)
                    v.wait_ge(full, q + 1)
                    yy = y_[:, a:b, :].rearrange("p g c -> p (g c)")
                    v.tensor_tensor(yy, bank[q % 8][:, 0:NC_ * (b - a)], yy, ALU.add).then_inc(used, 1)


X_OFF, XT_OFF, GB_OFF, FREE = 0, 5120, 9728, 11776


def glu(nc, A, R, x, u_dram, y_dram):
    with Scope(nc, "glu") as s:
        yT, uT = R(FREE, KT, CH, NC_), R(FREE + 4608, KT, CH, NC_)
        gT = R(FREE + 9216, KT, NC_, CH)
        w = R(FREE + 13824, KT, 2 * D)
        sg = R(FREE + 30208, 2, 512)
        fv = R(FREE + 31232, 2, 512)
        d = R(FREE + 32256, KT)
        bank = s.banks()
        names = ("x_in", "d_in", "w_in", "dve", "skip_ready", "g_ready", "full", "sig", "used", "fused")
        x_in, d_in, w_in, dve, skip_ready, g_ready, full, sig, used, fused = (s.sem(n) for n in names)
        y_in = [s.sem(f"y_in{h}") for h in range(2)]
        jobs = [(i, h) for i in range(NT) for h in range(2)]
        with nc.Block() as block:
            @block.sync
            def _(sp):
                sp.dma_start(d, A["a_d"]).then_inc(d_in, 16)
                for h in range(2):
                    ks = slice(4 * h, 4 * h + 4)
                    for dst, src in ((yT, y_dram), (uT, u_dram)):
                        sp.dma_start(dst[:, ks].rearrange("p k s c -> p k (s c)"),
                                     src.rearrange("(k p) t -> p k t", p=P)[:, ks]).then_inc(y_in[h], 16)
                for h in range(2):
                    sp.dma_start(w[:, 4 * h:4 * h + 4, :],
                                 A["a_w_glu"][0].rearrange("(k p) n -> p k n", p=P)[:, 4 * h:4 * h + 4]).then_inc(w_in, 16)
                sp.dma_start(x[:, 0:4, :], A["x_prompt"][0].rearrange("(i p) d -> p i d", p=P)).then_inc(x_in, 16)
                sp.dma_start(x[0:64, 4, :], A["x_sample"].rearrange("b t d -> (b t) d")).then_inc(x_in, 16)

            @block.vector
            def _(v):
                v.wait_ge(d_in, 16)
                for k in range(KT):
                    v.wait_ge(y_in[k // 4], 32)
                    v.scalar_tensor_tensor(out=yT[:, k].rearrange("p s c -> p (s c)"), in0=uT[:, k].rearrange("p s c -> p (s c)"),
                                           scalar=d[:, k:k + 1], in1=yT[:, k].rearrange("p s c -> p (s c)"),
                                           op0=ALU.mult, op1=ALU.add).then_inc(skip_ready, 1)
                v.wait_ge(x_in, 32)
                for j, (i, h) in enumerate(jobs):
                    n = TILES[i][1]
                    xs = x[0:n, i, 512 * h:512 * h + 512]
                    v.wait_ge(sig, j + 1)
                    v.tensor_tensor(fv[0:n, j % 2], bank[(2 * j) % 8][0:n, :], sg[0:n, j % 2], ALU.mult).then_inc(used, 1)
                    v.wait_ge(used, j + 1)
                    v.scalar_tensor_tensor(out=xs, in0=xs, scalar=ALPHA, in1=fv[0:n, j % 2],
                                           op0=ALU.mult, op1=ALU.add).then_inc(fused, 1)

            @block.scalar
            def _(act):
                for k in range(KT):
                    act.wait_ge(skip_ready, k + 1)
                    nc.scalar.activation(gT[:, k].rearrange("p c s -> p s c"), yT[:, k], ACT.Gelu_apprx_tanh).then_inc(g_ready, 1)
                for j, (i, h) in enumerate(jobs):
                    n = TILES[i][1]
                    act.wait_ge(full, j + 1)
                    if j >= 2:
                        act.wait_ge(used, j - 1)
                    nc.scalar.activation(sg[0:n, j % 2], bank[(2 * j + 1) % 8][0:n, :], ACT.Sigmoid).then_inc(sig, 1)

            @block.tensor
            def _(pe):
                pe.wait_ge(g_ready, KT)
                pe.wait_ge(w_in, 32)
                for j, (i, h) in enumerate(jobs):
                    t0, n = TILES[i]
                    if j >= 4:
                        pe.wait_ge(used, j - 3)
                    for part in range(2):
                        for k in range(KT):
                            ins = pe.matmul(bank[(2 * j + part) % 8][0:n, :],
                                            gT[:, k].rearrange("p c s -> p (c s)")[:, t0:t0 + n],
                                            w[:, k, D * part + 512 * h:D * part + 512 * h + 512],
                                            start=(k == 0), stop=(k == KT - 1))
                    ins.then_inc(full, 1)


def layer_norm(nc, A, R, name, layer, which, ident, x, outs=None, x_dram=None, turn=True, weights=None):
    with Scope(nc, name) as s:
        xT = R(XT_OFF, KT, TOK)
        gb = R(GB_OFF, 2, D)
        st = R(FREE, NT, 2, 6)
        mv = R(FREE + 64, NT, 2)
        sd = R(FREE + 80, NT)
        rs = R(FREE + 88, NT)
        bank = s.banks()
        gb_in, dve, stats, root, inv, normed, scaled, shifted, full, used, stored = (
            s.sem(n) for n in ("gb_in", "dve", "stats", "root", "inv", "normed", "scaled", "shifted", "full", "used", "stored"))
        with nc.Block() as block:
            @block.sync
            def _(sp):
                sp.dma_start(gb[:, 0, :], A["ln_g"][layer, which].partition_broadcast(P)).then_inc(gb_in, 16)
                sp.dma_start(gb[:, 1, :], A["ln_b"][layer, which].partition_broadcast(P)).then_inc(gb_in, 16)
                if weights is not None:
                    weights.load_first(sp)
                n_st = 0
                for i, (t0, n) in enumerate(TILES):
                    sp.wait_ge(shifted, i + 1)
                    if x_dram is not None:
                        sp.dma_start(x_dram[t0:t0 + n, :], x[0:n, i, :]).then_inc(stored, 16)
                        n_st += 1
                    if outs is not None:
                        dst = outs[0][0, t0:t0 + n, :] if i < 4 else outs[1].rearrange("b t d -> (b t) d")
                        sp.dma_start(dst, x[0:n, i, :]).then_inc(stored, 16)
                        n_st += 1
                sp.wait_ge(stored, 16 * n_st)

            @block.vector
            def _(v):
                link = Link(v, dve)
                for i, (t0, n) in enumerate(TILES):
                    for h in range(2):
                        ins = v.bn_stats(st[0:n, i, h, :], x[0:n, i, 512 * h:512 * h + 512])
                    link(ins)
                    v.bn_aggr(mv[0:n, i, :], st[0:n, i].rearrange("p h k -> p (h k)")).then_inc(stats, 1)
                for i, (t0, n) in enumerate(TILES):
                    v.wait_ge(root, i + 1)
                    link(v.reciprocal(rs[0:n, i:i + 1], sd[0:n, i:i + 1]))
                    v.tensor_scalar(x[0:n, i, :], x[0:n, i, :], mv[0:n, i, 0:1], rs[0:n, i:i + 1],
                                    ALU.subtract, ALU.mult).then_inc(normed, 1)
                    if i == 0:
                        v.wait_ge(gb_in, 32)
                    v.wait_ge(normed, i + 1)
                    v.tensor_tensor(x[0:n, i, :], x[0:n, i, :], gb[0:n, 0, :], ALU.mult).then_inc(scaled, 1)

            @block.gpsimd
            def _(pool):
                for i, (t0, n) in enumerate(TILES):
                    pool.wait_ge(scaled, i + 1)
                    pool.tensor_tensor(x[0:n, i, :], x[0:n, i, :], gb[0:n, 1, :], ALU.add).then_inc(shifted, 1)

            @block.tensor
            def _(pe):
                if not turn:
                    return
                for i, (t0, n) in enumerate(TILES):
                    pe.wait_ge(shifted, i + 1)
                    for h in range(2):
                        j = 2 * i + h
                        if j >= 8:
                            pe.wait_ge(used, j - 7)
                        for k in range(4):
                            ins = pe.transpose(bank[j % 8][:, P * k:P * k + n],
                                               x[0:n, i, P * (4 * h + k):P * (4 * h + k) + P], ident[0:n, 0:n])
                        ins.then_inc(full, 1)

            @block.scalar
            def _(act):
                for i, (t0, n) in enumerate(TILES):
                    act.wait_ge(stats, i + 1)
                    nc.scalar.activation(sd[0:n, i:i + 1], mv[0:n, i, 1:2], ACT.Sqrt, bias=A["eps"][0:n, 0:1]).then_inc(root, 1)
                if not turn:
                    return
                for i, (t0, n) in enumerate(TILES):
                    for h in range(2):
                        j = 2 * i + h
                        act.wait_ge(full, j + 1)
                        nc.scalar.copy(xT[:, 4 * h:4 * h + 4, t0:t0 + n],
                                       bank[j % 8][:, :].rearrange("p (k t) -> p k t", k=4)[:, :, 0:n]).then_inc(used, 1)


RT_OFF = FREE + 0
BE_OFF = FREE + 50
MORE_OFF = FREE + 70
DST_OFF = FREE + 96
WT_OFF = FREE + 112
NW = 4
W_SIZE = KT * 2 * DE + 2 * D
W_OFF = ARENA - NW * W_SIZE
MOE_FREE = FREE + 128
BIG = 1e30


def route(nc, A, R, name, layer, row_tok):
    with Scope(nc, name) as s:
        xT = R(XT_OFF, KT, TOK)
        rt = R(RT_OFF, NBLK, dt=I32, np_=RB)
        be, more = R(BE_OFF, NMORE, dt=I32), R(MORE_OFF, 1, dt=I32)
        dst, wt = R(DST_OFF, NT, 2, dt=I32), R(WT_OFF, 2, NT)
        at = [MOE_FREE]

        def place(*shape, dt=F32, np_=P):
            n = int(np.prod(shape))
            at[0] += n + n % 2
            return R(at[0] - n - n % 2, *shape, dt=dt, np_=np_)

        wr = place(KT, NG + NE)
        lg, le, le2 = place(NT, NG), place(NT, NE), place(NT, NE)
        ig, ie, ib, i64 = place(NT, NG), place(NT, NE), place(NMORE), place(NE)
        keyg, keye = place(NT, NG), place(NT, NE)
        ohg, oh = place(NT, NG), place(2, NT, NE)
        top = place(3, NT)
        low, gsum, gw, dif, ed, inv = (place(NT) for _ in range(6))
        ex = place(NT, NG)
        both = place(NT, NE)
        tri, ones = place(P), place(P)
        total, nblk, pend, base, one32 = (place(NE) for _ in range(5))
        rank, pos, sel, over = place(NT, NE), place(NT, NE), place(NT, NE), place(NT, NE)
        dstf = place(NT, 2)
        cmpb, bef = place(NMORE, NE), place(NMORE)
        tok = place(NT, dt=I32)
        zero = place(NBLK, dt=I32, np_=RB)
        assert at[0] <= W_OFF
        bank = s.banks(3)
        w_in, made, zeroed, cleared, logit, dve, lmoved, exp_in, exp_out, ohs, ranked, dests, scattered, rt_in = (
            s.sem(n) for n in ("w_in", "made", "zeroed", "cleared", "logit", "dve", "lmoved", "exp_in", "exp_out", "ohs",
                               "ranked", "dests", "scattered", "rt_in"))
        with nc.Block() as block:
            @block.sync
            def _(sp):
                sp.dma_start(wr[:, :, 0:NG], A["moe_w_group"][layer].rearrange("(k p) n -> p k n", p=P)).then_inc(w_in, 16)
                sp.dma_start(wr[:, :, NG:], A["moe_w_expert"][layer].rearrange("(k p) n -> p k n", p=P)).then_inc(w_in, 16)
                sp.wait_ge(zeroed, 1)
                sp.dma_start(row_tok.rearrange("(p b) o -> p (b o)", p=RB), zero).then_inc(cleared, 16)
                sp.wait_ge(scattered, 16 * 2 * NT)
                sp.dma_start(rt, row_tok.rearrange("(b r) o -> r (b o)", r=RB), allow_slow_non_contiguous=True).then_inc(rt_in, 16)
                sp.wait_ge(rt_in, 16)

            @block.gpsimd
            def _(pool):
                pool.memset(zero, 0).then_inc(zeroed, 1)
                pool.iota(ig, pattern=[[0, NT], [1, NG]], base=-64, channel_multiplier=0,
                          allow_small_or_imprecise_dtypes=True).then_inc(made, 1)
                pool.iota(ie, pattern=[[0, NT], [1, NE]], base=-64, channel_multiplier=0,
                          allow_small_or_imprecise_dtypes=True).then_inc(made, 1)
                pool.iota(ib, pattern=[[1, NMORE]], base=0, channel_multiplier=0,
                          allow_small_or_imprecise_dtypes=True).then_inc(made, 1)
                pool.iota(i64, pattern=[[RB, NE]], base=0, channel_multiplier=0,
                          allow_small_or_imprecise_dtypes=True).then_inc(made, 1)
                pool.iota(tok, pattern=[[P, NT]], base=0, channel_multiplier=1).then_inc(made, 1)
                pool.memset(ones, 1.0).then_inc(made, 1)
                pool.memset(one32, 1.0).then_inc(made, 1)
                pool.memset(lg, 0.0).then_inc(made, 1)
                pool.memset(le, 0.0).then_inc(made, 1)
                pool.wait_ge(made, 9)
                pool.affine_select(out=tri, in_=ones, compare_op=ALU.is_gt, fill=0.0, base=0,
                                   pattern=[[1, P]], channel_multiplier=-1).then_inc(made, 1)
                pool.wait_ge(dests, 1)
                pool.wait_ge(cleared, 16)
                for i, (t0, n) in enumerate(TILES):
                    for k in range(2):
                        pool.indirect_dma_start(out=row_tok, out_offset=bass.IndirectOffsetOnAxis(ap=dst[0:n, i, k:k + 1], axis=0),
                                                in_=tok[0:n, i:i + 1], in_offset=None).then_inc(scattered, 16)
                pool.wait_ge(scattered, 16 * 2 * NT)

            @block.tensor
            def _(pe):
                pe.wait_ge(w_in, 32)
                for i, (t0, n) in enumerate(TILES):
                    for k in range(KT):
                        ins = pe.matmul(bank[0][0:n, 36 * i:36 * i + 36], xT[:, k, t0:t0 + n], wr[:, k, :],
                                        start=(k == 0), stop=(k == KT - 1))
                ins.then_inc(logit, 1)
                pe.wait_ge(ohs, 1)
                pe.wait_ge(made, 10)
                for i in range(NT):
                    for q in range(i + 1):
                        ins = pe.matmul(bank[1][:, NE * i:NE * i + NE], tri if q == i else ones, both[:, q, :],
                                        start=(q == 0), stop=(q == i))
                for q in range(NT):
                    ins = pe.matmul(bank[2][:, 0:NE], ones, both[:, q, :], start=(q == 0), stop=(q == NT - 1))
                ins.then_inc(ranked, 1)

            @block.scalar
            def _(act):
                act.wait_ge(exp_in, 1)
                nc.scalar.activation(ex, ex, ACT.Exp).then_inc(exp_out, 1)
                act.wait_ge(exp_in, 2)
                nc.scalar.activation(ed, dif, ACT.Exp).then_inc(exp_out, 1)

            @block.vector
            def _(v):
                link = Link(v, dve)

                def first_largest(vals, idx, key, one, most, n):
                    link(v.tensor_reduce(most, vals, AX, ALU.max))
                    link(v.tensor_tensor(key, vals, bc(most.unsqueeze(2), [P, NT, n]), ALU.is_equal))
                    link(v.tensor_tensor(key, key, idx, ALU.mult))
                    link(v.tensor_reduce(low, key, AX, ALU.min))
                    link(v.tensor_tensor(one, idx, bc(low.unsqueeze(2), [P, NT, n]), ALU.is_equal))

                v.wait_ge(made, 9)
                v.wait_ge(logit, 1)
                src = bank[0][:, 0:36 * NT].rearrange("p (i n) -> p i n", i=NT)
                for np_, sl in ((P, slice(0, 4)), (64, slice(4, 5))):
                    v.tensor_copy(lg[0:np_, sl], src[0:np_, sl, 0:NG])
                    ins = v.tensor_copy(le[0:np_, sl], src[0:np_, sl, NG:36])
                link(ins)
                first_largest(lg, ig, keyg, ohg, top[:, 2], NG)
                link(v.tensor_tensor(ex, lg, bc(top[:, 2].unsqueeze(2), [P, NT, NG]), ALU.subtract))
                v.engine_nop().then_inc(exp_in, 1)
                link(v.tensor_scalar(keyg, ohg, 1.0, BIG, ALU.subtract, ALU.mult))
                for i in range(NT):
                    ins = v.tensor_tensor(le2[:, i, :].rearrange("p (g e) -> p g e", g=NG), le[:, i, :].rearrange("p (g e) -> p g e", g=NG),
                                          bc(keyg[:, i, :].unsqueeze(2), [P, NG, EPG]), ALU.add)
                link(ins)
                first_largest(le2, ie, keye, oh[:, 0], top[:, 0], NE)
                flat = "p i e -> p (i e)"
                link(v.scalar_tensor_tensor(out=le2.rearrange(flat), in0=oh[:, 0].rearrange(flat), scalar=-2 * BIG,
                                            in1=le2.rearrange(flat), op0=ALU.mult, op1=ALU.add))
                first_largest(le2, ie, keye, oh[:, 1], top[:, 1], NE)
                link(v.tensor_tensor(dif, top[:, 1], top[:, 0], ALU.subtract))
                v.engine_nop().then_inc(exp_in, 1)
                link(v.tensor_tensor(both, oh[:, 0], oh[:, 1], ALU.add))
                link(v.memset(both[64:P, 4, :], 0.0))
                v.engine_nop().then_inc(ohs, 1)
                v.wait_ge(exp_out, 2)
                link(v.tensor_reduce(gsum, ex, AX, ALU.add))
                link(v.reciprocal(gw, gsum))
                link(v.tensor_scalar(dif, ed, 1.0, None, ALU.add))
                link(v.reciprocal(inv, dif))
                link(v.tensor_tensor(wt[:, 0], gw, inv, ALU.mult))
                link(v.tensor_tensor(wt[:, 1], wt[:, 0], ed, ALU.mult))
                v.wait_ge(ranked, 1)
                link(v.tensor_copy(total, bank[2][:, 0:NE]))
                link(v.tensor_copy(rank, bank[1][:, 0:NE * NT].rearrange("p (i e) -> p i e", i=NT)))
                link(v.tensor_scalar(nblk, total, float(RB), None, ALU.is_gt))
                for q in range(2, -(-TOK // RB)):
                    link(v.scalar_tensor_tensor(out=nblk, in0=total, scalar=float(RB * q), in1=nblk, op0=ALU.is_gt, op1=ALU.add))
                link(v.tensor_tensor_scan(pend, one32, nblk, 0.0, ALU.mult, ALU.add))
                link(v.tensor_tensor(base, pend, nblk, ALU.subtract))
                link(v.tensor_scalar(base, base, float(RB), float(NE * RB - RB), ALU.mult, ALU.add))
                link(v.tensor_tensor(base, base, i64, ALU.subtract))
                link(v.tensor_scalar(over, rank, float(RB), None, ALU.is_ge))
                link(v.tensor_tensor(over, over, bc(base.unsqueeze(1), [P, NT, NE]), ALU.mult))
                link(v.tensor_tensor(pos, rank, bc(i64.unsqueeze(1), [P, NT, NE]), ALU.add))
                link(v.tensor_tensor(pos, pos, over, ALU.add))
                for k in range(2):
                    link(v.tensor_tensor(sel, oh[:, k], pos, ALU.mult))
                    link(v.tensor_reduce(dstf[:, :, k], sel, AX, ALU.add))
                link(v.tensor_copy(dst, dstf))
                v.engine_nop().then_inc(dests, 1)
                link(v.tensor_copy(more, pend[:, NE - 1:NE]))
                link(v.tensor_tensor(cmpb, bc(pend.unsqueeze(1), [P, NMORE, NE]), bc(ib.unsqueeze(2), [P, NMORE, NE]), ALU.is_le))
                link(v.tensor_reduce(bef, cmpb, AX, ALU.add))
                link(v.tensor_scalar(be, bef, float(NE - 1), None, ALU.min))


class Weights:

    def __init__(self, nc, A, R, layer):
        self.A, self.layer = A, layer
        self.gate_up = [R(W_OFF + W_SIZE * q, KT, 2 * DE) for q in range(NW)]
        self.down = [R(W_OFF + W_SIZE * q + KT * 2 * DE, 2, D) for q in range(NW)]
        self.loaded = Scope.handles(nc, [f"weights{layer}_{q}" for q in range(NW)])

    def load(self, sp, e, q):
        which = bass.ds(e, 1)
        sp.dma_start(self.gate_up[q], self.A["moe_w_gate_up"][self.layer, which].rearrange("o (k p) n -> p (o k) n", p=P)).then_inc(self.loaded[q], 16)
        sp.dma_start(self.down[q], self.A["moe_w_down"][self.layer, which].rearrange("o (k p) n -> p (o k) n", p=P)).then_inc(self.loaded[q], 16)

    def load_first(self, sp):
        for q in range(NW):
            self.load(sp, q, q)


def experts(nc, A, R, name, layer, ident, weights, x_dram, y_rows):
    with Scope(nc, name) as s:
        rt = R(RT_OFF, NBLK, dt=I32, np_=RB)
        at = [MOE_FREE]

        def place(*shape, dt=F32, np_=RB):
            n = int(np.prod(shape))
            at[0] += n
            return R(at[0] - n, *shape, dt=dt, np_=np_)

        xg = [place(D) for _ in range(2)]
        xgT = [place(KT, RB, np_=P) for _ in range(2)]
        idx = [place(2, dt=I32) for _ in range(2)]
        sg, h, hT = place(DE), place(DE), [place(2, RB, np_=P) for _ in range(2)]
        y = [place(D) for _ in range(2)]
        assert at[0] <= W_OFF
        bank = s.banks()
        BX, BG, BH, BY = bank[0:2], bank[2:4], bank[4], bank[5:7]
        x_in = [s.sem(f"x_in{i}") for i in range(2)]
        y_out = [s.sem(f"y_out{i}") for i in range(2)]
        gather_go, own_wait = s.sem("gather_go"), s.sem("own_wait")
        idx_ready, x_turned, xT_ready, gu_done, sg_ready, h_ready, h_turned, hT_ready, dn_done, y0_ready, y1_ready = (
            s.sem(n) for n in ("idx_ready", "x_turned", "xT_ready", "gu_done", "sg_ready", "h_ready", "h_turned", "hT_ready",
                               "dn_done", "y0_ready", "y1_ready"))
        TURNS = NE // NW

        def blocks(eng, body, last=False):
            for q in range(NW):
                body(0, q)
            with eng.Fori(1, TURNS - last) as i:
                for q in range(NW):
                    body(i, q)
            if last:
                for q in range(NW):
                    body(TURNS - 1, q)

        def after(eng, sem, n):
            if not isinstance(n, int) or n > 0:
                eng.wait_ge(sem, n)

        with nc.Block() as block:
            @block.sync
            def _(sp):
                with sp.Fori(1, TURNS) as i:
                    for q in range(NW):
                        sp.wait_ge(dn_done, NW * i + q - NW + 1)
                        weights.load(sp, NW * i + q, q)

            @block.gpsimd
            def _(pool):
                def gather(i, q):
                    b = NW * i + q
                    after(pool, x_turned, b - 1)
                    pool.tensor_copy(idx[q % 2][:, 0:1], rt[:, bass.ds(b, 1)]).then_inc(idx_ready, 1)
                    pool.wait_ge(idx_ready, b + 1)
                    pool.sem_inc(gather_go, 1)
                    pool.indirect_dma_start(out=xg[q % 2], out_offset=None, in_=x_dram,
                                            in_offset=bass.IndirectOffsetOnAxis(ap=idx[q % 2][:, 0:1], axis=0)).then_inc(x_in[q % 2], 16)
                blocks(pool, gather)

            @block.tensor
            def _(pe):
                def turn_x(i, q):
                    b = NW * i + q
                    pe.wait_ge(x_in[q % 2], 16 * (NW // 2 * i + q // 2 + 1))
                    after(pe, xT_ready, 2 * b)
                    pe.sem_inc(own_wait, 1)
                    for k in range(KT):
                        ins = pe.transpose(BX[k // 4][:, RB * (k % 4):RB * (k % 4) + RB], xg[q % 2][:, P * k:P * k + P], ident[0:RB, 0:RB])
                    ins.then_inc(x_turned, 1)

                def gate_up(i, q):
                    b = NW * i + q
                    pe.wait_ge(weights.loaded[q], 32 * i + 32)
                    pe.wait_ge(xT_ready, 2 * b + 2)
                    after(pe, h_ready, b - 1)
                    for k in range(KT):
                        ins = pe.matmul(BG[q % 2][0:RB, :], xgT[q % 2][:, k, :], weights.gate_up[q][:, k, :], start=(k == 0), stop=(k == KT - 1))
                    ins.then_inc(gu_done, 1)

                def turn_h(i, q):
                    b = NW * i + q
                    pe.wait_ge(h_ready, b + 1)
                    after(pe, hT_ready, b)
                    pe.sem_inc(own_wait, 1)
                    for k in range(2):
                        ins = pe.transpose(BH[:, RB * k:RB * k + RB], h[:, P * k:P * k + P], ident[0:RB, 0:RB])
                    ins.then_inc(h_turned, 1)

                def down(i, q):
                    b = NW * i + q
                    pe.wait_ge(hT_ready, b + 1)
                    after(pe, y0_ready, b)
                    after(pe, y1_ready, b)
                    for n in range(2):
                        for k in range(2):
                            ins = pe.matmul(BY[n][0:RB, :], hT[q % 2][:, k, :], weights.down[q][:, k, 512 * n:512 * n + 512],
                                            start=(k == 0), stop=(k == 1))
                    ins.then_inc(dn_done, 1)

                def body(i, q):
                    gate_up(i, q)
                    if not (isinstance(i, int) and i == TURNS - 1 and q == NW - 1):
                        turn_x(i + (q + 1) // NW, (q + 1) % NW)
                    if not (isinstance(i, int) and i == 0 and q == 0):
                        down(i - (q == 0), (q - 1) % NW)
                    turn_h(i, q)

                turn_x(0, 0)
                blocks(pe, body, last=True)
                down(TURNS - 1, NW - 1)

            @block.vector
            def _(v):
                def rows(i, q):
                    b = NW * i + q
                    v.wait_ge(x_turned, b + 1)
                    after(v, gu_done, b - 1)
                    for half in range(2):
                        v.tensor_copy(xgT[q % 2][:, 4 * half:4 * half + 4, :].rearrange("p k t -> p (k t)"),
                                      BX[half][:, 0:4 * RB]).then_inc(xT_ready, 1)

                def gated(i, q):
                    b = NW * i + q
                    v.wait_ge(sg_ready, b + 1)
                    after(v, h_turned, b)
                    v.tensor_tensor(h, sg, BG[q % 2][0:RB, DE:2 * DE], ALU.mult).then_inc(h_ready, 1)

                def out(i, q):
                    b = NW * i + q
                    v.wait_ge(dn_done, b + 1)
                    after(v, y_out[q % 2], 16 * (NW // 2 * i + q // 2))
                    v.tensor_copy(y[q % 2][:, 0:512], BY[0][0:RB, :]).then_inc(y0_ready, 1)

                def body(i, q):
                    if not (isinstance(i, int) and i == TURNS - 1 and q == NW - 1):
                        rows(i + (q + 1) // NW, (q + 1) % NW)
                    gated(i, q)
                    if not (isinstance(i, int) and i == 0 and q == 0):
                        out(i - (q == 0), (q - 1) % NW)

                rows(0, 0)
                blocks(v, body, last=True)
                out(TURNS - 1, NW - 1)

            @block.scalar
            def _(act):
                def silu(i, q):
                    b = NW * i + q
                    act.wait_ge(gu_done, b + 1)
                    after(act, h_ready, b)
                    nc.scalar.activation(sg, BG[q % 2][0:RB, 0:DE], ACT.Silu).then_inc(sg_ready, 1)

                def turned(i, q):
                    b = NW * i + q
                    act.wait_ge(h_turned, b + 1)
                    after(act, dn_done, b - 1)
                    nc.scalar.copy(hT[q % 2].rearrange("p k t -> p (k t)"), BH[:, 0:2 * RB]).then_inc(hT_ready, 1)

                def out(i, q):
                    b = NW * i + q
                    act.wait_ge(dn_done, b + 1)
                    after(act, y_out[q % 2], 16 * (NW // 2 * i + q // 2))
                    nc.scalar.copy(y[q % 2][:, 512:D], BY[1][0:RB, :]).then_inc(y1_ready, 1)
                    act.wait_ge(y0_ready, b + 1)
                    act.wait_ge(y1_ready, b + 1)
                    act.dma_start(y_rows[bass.ds(RB * b, RB), :], y[q % 2]).then_inc(y_out[q % 2], 16)

                def body(i, q):
                    silu(i, q)
                    if not (isinstance(i, int) and i == 0 and q == 0):
                        out(i - (q == 0), (q - 1) % NW)
                    turned(i, q)

                blocks(act, body)
                out(TURNS - 1, NW - 1)
                for q in range(2):
                    act.wait_ge(y_out[q], 16 * NE // 2)


def more_experts(nc, A, R, name, layer, ident, weights, x_dram, y_rows):
    with Scope(nc, name) as s:
        rt = R(RT_OFF, NBLK, dt=I32, np_=RB)
        be, more = R(BE_OFF, NMORE, dt=I32), R(MORE_OFF, 1, dt=I32)
        at = [MOE_FREE]

        def place(*shape, dt=F32, np_=RB):
            n = int(np.prod(shape))
            at[0] += n
            return R(at[0] - n, *shape, dt=dt, np_=np_)

        xg, xgT, idx = place(D), place(KT, RB, np_=P), place(2, dt=I32)
        sg, h, hT, y = place(DE), place(DE), place(2, RB, np_=P), place(D)
        bank = s.banks()
        BX, BG, BH, BY = bank[0:2], bank[2], bank[4], bank[5:7]
        w_in, x_in, y_out, gather_go, idx_ready, x_turned, xT_ready, gu_done, sg_ready, h_ready, h_turned, hT_ready, dn_done, y_ready = (
            s.sem(n) for n in ("w_in", "x_in", "y_out", "gather_go", "idx_ready", "x_turned", "xT_ready", "gu_done", "sg_ready",
                               "h_ready", "h_turned", "hT_ready", "dn_done", "y_ready"))

        own_wait = s.sem("own_wait")

        def if_more(eng, first, body):
            n = eng.value_load(more[0:1, 0:1], min_val=0, max_val=NMORE)
            with eng.If(n > 0):
                body(0, True)
                with eng.Fori(1, NMORE) as b:
                    body(b, False)
                if first is not None:
                    first()

        with nc.Block() as block:
            @block.sync
            def _(sp):
                def load(b, first):
                    e = sp.value_load(be[0:1, bass.ds(b, 1)], min_val=0, max_val=NE - 1)
                    if not first:
                        sp.wait_ge(dn_done, b)
                    sp.dma_start(weights.gate_up[0], A["moe_w_gate_up"][layer, bass.ds(e, 1)].rearrange("o (k p) n -> p (o k) n", p=P)).then_inc(w_in, 16)
                    sp.dma_start(weights.down[0], A["moe_w_down"][layer, bass.ds(e, 1)].rearrange("o (k p) n -> p (o k) n", p=P)).then_inc(w_in, 16)
                    sp.wait_ge(y_ready, 2 * b + 2)
                    sp.dma_start(y_rows[bass.ds(RB * (b + NE), RB), :], y).then_inc(y_out, 16)
                if_more(sp, lambda: sp.wait_ge(y_out, 16 * NMORE), load)

            @block.gpsimd
            def _(pool):
                def gather(b, first):
                    if not first:
                        pool.wait_ge(x_turned, b)
                    pool.tensor_copy(idx[:, 0:1], rt[:, bass.ds(b + NE, 1)]).then_inc(idx_ready, 1)
                    pool.wait_ge(idx_ready, b + 1)
                    pool.sem_inc(gather_go, 1)
                    pool.indirect_dma_start(out=xg, out_offset=None, in_=x_dram,
                                            in_offset=bass.IndirectOffsetOnAxis(ap=idx[:, 0:1], axis=0)).then_inc(x_in, 16)
                if_more(pool, None, gather)

            @block.tensor
            def _(pe):
                def body(b, first):
                    pe.wait_ge(x_in, 16 * b + 16)
                    if not first:
                        pe.wait_ge(xT_ready, 2 * b)
                    pe.sem_inc(own_wait, 1)
                    for k in range(KT):
                        ins = pe.transpose(BX[k // 4][:, RB * (k % 4):RB * (k % 4) + RB], xg[:, P * k:P * k + P], ident[0:RB, 0:RB])
                    ins.then_inc(x_turned, 1)
                    pe.wait_ge(w_in, 32 * b + 32)
                    pe.wait_ge(xT_ready, 2 * b + 2)
                    if not first:
                        pe.wait_ge(h_ready, b)
                    for k in range(KT):
                        ins = pe.matmul(BG[0:RB, :], xgT[:, k, :], weights.gate_up[0][:, k, :], start=(k == 0), stop=(k == KT - 1))
                    ins.then_inc(gu_done, 1)
                    pe.wait_ge(h_ready, b + 1)
                    if not first:
                        pe.wait_ge(hT_ready, b)
                    pe.sem_inc(own_wait, 1)
                    for k in range(2):
                        ins = pe.transpose(BH[:, RB * k:RB * k + RB], h[:, P * k:P * k + P], ident[0:RB, 0:RB])
                    ins.then_inc(h_turned, 1)
                    pe.wait_ge(hT_ready, b + 1)
                    if not first:
                        pe.wait_ge(y_ready, 2 * b)
                    for n in range(2):
                        for k in range(2):
                            ins = pe.matmul(BY[n][0:RB, :], hT[:, k, :], weights.down[0][:, k, 512 * n:512 * n + 512],
                                            start=(k == 0), stop=(k == 1))
                    ins.then_inc(dn_done, 1)
                if_more(pe, None, body)

            @block.vector
            def _(v):
                def body(b, first):
                    v.wait_ge(x_turned, b + 1)
                    if not first:
                        v.wait_ge(gu_done, b)
                    for half in range(2):
                        v.tensor_copy(xgT[:, 4 * half:4 * half + 4, :].rearrange("p k t -> p (k t)"),
                                      BX[half][:, 0:4 * RB]).then_inc(xT_ready, 1)
                    v.wait_ge(sg_ready, b + 1)
                    if not first:
                        v.wait_ge(h_turned, b)
                    v.tensor_tensor(h, sg, BG[0:RB, DE:2 * DE], ALU.mult).then_inc(h_ready, 1)
                    v.wait_ge(dn_done, b + 1)
                    if not first:
                        v.wait_ge(y_out, 16 * b)
                    for n in range(2):
                        v.tensor_copy(y[:, 512 * n:512 * n + 512], BY[n][0:RB, :]).then_inc(y_ready, 1)
                if_more(v, None, body)

            @block.scalar
            def _(act):
                def body(b, first):
                    act.wait_ge(gu_done, b + 1)
                    if not first:
                        act.wait_ge(h_ready, b)
                    nc.scalar.activation(sg, BG[0:RB, 0:DE], ACT.Silu).then_inc(sg_ready, 1)
                    act.wait_ge(h_turned, b + 1)
                    if not first:
                        act.wait_ge(dn_done, b)
                    nc.scalar.copy(hT.rearrange("p k t -> p (k t)"), BH[:, 0:2 * RB]).then_inc(hT_ready, 1)
                if_more(act, None, body)


def combine(nc, R, name, x, y_rows):
    with Scope(nc, name) as s:
        dst, wt = R(DST_OFF, NT, 2, dt=I32), R(WT_OFF, 2, NT)
        yg = R(MOE_FREE, NT, 2, D)
        y_in = [s.sem(f"y_in{i}") for i in range(NT)]
        dve = s.sem("dve")
        with nc.Block() as block:
            @block.gpsimd
            def _(pool):
                for i, (t0, n) in enumerate(TILES):
                    for k in range(2):
                        pool.indirect_dma_start(out=yg[0:n, i, k, :], out_offset=None, in_=y_rows,
                                                in_offset=bass.IndirectOffsetOnAxis(ap=dst[0:n, i, k:k + 1], axis=0)).then_inc(y_in[i], 16)
                for i in range(NT):
                    pool.wait_ge(y_in[i], 32)

            @block.vector
            def _(v):
                link = Link(v, dve)
                for i, (t0, n) in enumerate(TILES):
                    v.wait_ge(y_in[i], 32)
                    link(v.tensor_scalar(yg[0:n, i, 0, :], yg[0:n, i, 0, :], wt[0:n, 0, i:i + 1], None, ALU.mult))
                    link(v.scalar_tensor_tensor(out=yg[0:n, i, 0, :], in0=yg[0:n, i, 1, :], scalar=wt[0:n, 1, i:i + 1],
                                                in1=yg[0:n, i, 0, :], op0=ALU.mult, op1=ALU.add))
                    link(v.scalar_tensor_tensor(out=x[0:n, i, :], in0=x[0:n, i, :], scalar=ALPHA, in1=yg[0:n, i, 0, :],
                                                op0=ALU.mult, op1=ALU.add))


HR = 8192


def page_rows(nc, A, idx_cmp, idx_slc):
    with Scope(nc, "pages") as s:
        pt = A["page_table"]
        raw1, raw2 = s.sb("raw1", [P, 16], I32), s.sb("raw2", [P, 64], I32)
        pi, p8, p32 = s.sb("pi", [P, 1], I32), s.sb("p8", [P, 1], I32), s.sb("p32", [P, 1], I32)
        f8, f32_ = s.sb("f8", [P, 1]), s.sb("f32", [P, 1])
        p_in, made, dve = s.sem("p_in"), s.sem("made"), s.sem("dve")
        with nc.Block() as block:
            @block.sync
            def _(sp):
                with nc.allow_non_contiguous_dma(reason="page numbers, four bytes each"):
                    for g in range(16):
                        src = pt.rearrange("b (h g) -> g (b h)", g=16)[g].partition_broadcast(8)
                        sp.dma_start(raw1[8 * g:8 * g + 8, :], src).then_inc(p_in, 16)
                    for g in range(4):
                        src = pt.rearrange("b (j g) -> g (b j)", g=4)[g].partition_broadcast(32)
                        sp.dma_start(raw2[32 * g:32 * g + 32, :], src).then_inc(p_in, 16)

            @block.gpsimd
            def _(pool):
                pool.iota(pi[:, :], pattern=[[0, 1]], base=0, channel_multiplier=1).then_inc(made, 1)

            @block.vector
            def _(v):
                link = Link(v, dve)
                v.wait_ge(made, 1)
                link(v.tensor_scalar(p8[:, :], pi[:, :], 7, None, ALU.bitwise_and))
                link(v.tensor_scalar(p32[:, :], pi[:, :], 31, None, ALU.bitwise_and))
                link(v.tensor_copy(f8[:, :], p8[:, :]))
                link(v.tensor_copy(f32_[:, :], p32[:, :]))
                v.wait_ge(p_in, 16 * 20)
                link(v.tensor_scalar(idx_cmp[:, :], raw1[:, :], 8.0, f8[:, 0:1], ALU.mult, ALU.add))
                link(v.tensor_scalar(idx_slc[:, :], raw2[:, :], 32.0, f32_[:, 0:1], ALU.mult, ALU.add))


def compress_cache(nc, A, R, ident, idx_cmp, pe_bias, ck_dram, cv_dram, spare_rows):
    with Scope(nc, "cc") as s:
        raw = R(0, 2, HR)
        xt = [R(16384 + HR * i, 8, NKV, 256) for i in range(2)]
        w1 = R(32768, 2, 16, CMP_H)
        hid = [R(40960 + 2048 * i, 2, 2, 256) for i in range(2)]
        w2 = R(45056, 2, 2, HD)
        peT = R(45312, 2, 16)
        ck = R(45344, 2, 256)
        cv = R(45856, 2, 256)
        idx = R(46400, 2, dt=I32)
        zero = R(46402, D, np_=RB)
        spare_zeroed, spare_out = s.sem("spare_zeroed"), s.sem("spare_out")
        bank = s.banks()
        BT, BM, BO = bank[0:3], bank[3:7], bank[7]
        names = ("w_in", "idx_ready", "turned", "moved_a", "moved_v", "mm_done", "hid_ready", "out_done", "out_moved", "pb", "zeroed")
        w_in, idx_ready, turned, moved_a, moved_v, mm_done, hid_ready, out_done, out_moved, pb, zeroed = (s.sem(n) for n in names)
        gather_go = s.sem("gather_go")
        raw_in = [s.sem(f"raw_in{i}") for i in range(2)]
        stored = [s.sem(f"stored{i}") for i in range(2)]
        cache = A["cache_cmp_kv"].rearrange("n (i s) k g d -> (n i) (s k g d)", s=16)
        with nc.Block() as block:
            @block.gpsimd
            def _(pool):
                def gather(b, first=False):
                    for h in range(2):
                        if not first:
                            pool.wait_ge(raw_in[h], 16 * b)
                        col = idx_cmp[:, h:h + 1] if first else idx_cmp[:, bass.ds(2 * b + h, 1)]
                        pool.tensor_copy(idx[:, h:h + 1], col).then_inc(idx_ready, 1)
                    pool.wait_ge(idx_ready, 2 * b + 2)
                    if not first:
                        pool.wait_ge(turned, 32 * b)
                        pool.sem_inc(gather_go, 1)
                    for h in range(2):
                        pool.indirect_dma_start(out=raw[:, h, :], out_offset=None, in_=cache,
                                                in_offset=bass.IndirectOffsetOnAxis(ap=idx[:, h:h + 1], axis=0)).then_inc(raw_in[h], 16)

                gather(0, True)
                with pool.Fori(1, DEC_B) as b:
                    gather(b)

            @block.sync
            def _(sp):
                sp.dma_start(w1, A["cmp_w1"].rearrange("k (t p) h -> p k t h", p=P)).then_inc(w_in, 16)
                sp.dma_start(w2, A["cmp_w2"].rearrange("k (m p) d -> p k m d", p=P)).then_inc(w_in, 16)
                sp.dma_start(peT, A["cmp_pe"]).then_inc(w_in, 16)
                sp.wait_ge(spare_zeroed, 1)
                sp.dma_start(spare_rows.rearrange("(b r) n -> r b n", r=RB), bc(zero.unsqueeze(1), [RB, NMORE, D])).then_inc(spare_out, 16)
                with sp.Fori(0, DEC_B) as b:
                    sp.wait_ge(out_moved, 4 * b + 2)
                    sp.dma_start(ck_dram[bass.ds(b, 1)].rearrange("o p n -> p (o n)"), ck.rearrange("p a n -> p (a n)")).then_inc(stored[0], 16)
                    sp.wait_ge(out_moved, 4 * b + 4)
                    sp.dma_start(cv_dram[bass.ds(b, 1)].rearrange("o p n -> p (o n)"), cv.rearrange("p a n -> p (a n)")).then_inc(stored[1], 16)
                for i in range(2):
                    sp.wait_ge(stored[i], 16 * DEC_B)
                sp.wait_ge(spare_out, 16)

            @block.tensor
            def _(pe):
                pe.wait_ge(w_in, 48)
                for kv in range(2):
                    for m in range(2):
                        for t in range(16):
                            ins = pe.matmul(BO[:, 2 * kv + m:2 * kv + m + 1], w1[:, kv, t, P * m:P * m + P],
                                            peT[:, kv, t:t + 1], start=(t == 0), stop=(t == 15))
                ins.then_inc(pb, 1)

                def turn(b, kv, after, steps=range(16)):
                    for st in steps:
                        if not (isinstance(after, int) and after + st < 3):
                            pe.wait_ge(moved_a, after + st - 2)
                            pe.wait_ge(moved_v, after + st - 2)
                        for gp in range(2):
                            for h in range(2):
                                o = 512 * st + 256 * kv + P * gp
                                ins = pe.transpose(BT[st % 3][:, 256 * gp + P * h:256 * gp + P * h + P],
                                                   raw[:, h, o:o + P], ident[:, :])
                        ins.then_inc(turned, 1)

                def product(b, kv, unit, first=False):
                    for gp in range(2):
                        for m in range(2):
                            n = 2 * gp + m
                            if not first:
                                pe.wait_ge(hid_ready, 4 * unit + n - 3)
                            for t in range(16):
                                sh = 1 if t >= 8 else 0
                                ins = pe.matmul(BM[n][:, 0:510], w1[:, kv, t, P * m:P * m + P],
                                                xt[kv][:, t % 8, 2 * gp:2 * gp + 2, sh:sh + 255], start=(t == 0), stop=(t == 15))
                            ins.then_inc(mm_done, 1)

                def outputs(b, kv, unit, first=False):
                    for gp in range(2):
                        pe.wait_ge(hid_ready, 4 * unit + 2 * gp + 2)
                        if not (first and gp == 0):
                            pe.wait_ge(out_moved, 2 * unit + gp)
                        for g2 in range(2):
                            if kv == 0:
                                for m in range(2):
                                    ins = pe.matmul(BO[64 * g2:64 * g2 + 64, 0:255], w2[:, kv, m, :],
                                                    hid[gp][:, m, g2, 0:255], start=(m == 0), stop=(m == 1))
                            else:
                                for h in range(2):
                                    c = P - h
                                    for m in range(2):
                                        ins = pe.matmul(BO[0:c, P * h + 64 * g2:P * h + 64 * g2 + 64],
                                                        hid[gp][:, m, g2, P * h:P * h + c], w2[:, kv, m, :],
                                                        start=(m == 0), stop=(m == 1))
                        ins.then_inc(out_done, 1)

                def ready(unit):
                    pe.wait_ge(moved_a, 16 * unit + 16)
                    pe.wait_ge(moved_v, 16 * unit + 16)

                pe.wait_ge(raw_in[0], 16)
                pe.wait_ge(raw_in[1], 16)
                turn(0, 0, 0)
                for b in range(1):
                    ready(0)
                    turn(0, 1, 16)
                    product(0, 0, 0, True)
                    outputs(0, 0, 0, True)
                    ready(1)
                    pe.wait_ge(raw_in[0], 32)
                    pe.wait_ge(raw_in[1], 32)
                    turn(1, 0, 32)
                    product(0, 1, 1)
                    outputs(0, 1, 1)
                with pe.Fori(1, DEC_B - 1) as b:
                    ready(2 * b)
                    turn(b, 1, 32 * b + 16)
                    product(b, 0, 2 * b)
                    outputs(b, 0, 2 * b)
                    ready(2 * b + 1)
                    pe.wait_ge(raw_in[0], 16 * b + 32)
                    pe.wait_ge(raw_in[1], 16 * b + 32)
                    turn(b + 1, 0, 32 * b + 32)
                    product(b, 1, 2 * b + 1)
                    outputs(b, 1, 2 * b + 1)
                u = 2 * DEC_B - 2
                ready(u)
                turn(DEC_B - 1, 1, 16 * u + 16)
                product(DEC_B - 1, 0, u)
                outputs(DEC_B - 1, 0, u)
                ready(u + 1)
                product(DEC_B - 1, 1, u + 1)
                outputs(DEC_B - 1, 1, u + 1)

            def moved_rows(copy, kv, st, g2, bnk):
                dst = xt[kv][64 * (st % 2):64 * (st % 2) + 64, st // 2].rearrange("p (q e) n -> p q e n", e=2)[:, :, g2, :]
                return copy(dst, bnk[64 * g2:64 * g2 + 64, :].rearrange("p (q n) -> p q n", q=2))

            def mover(eng, copy, sem_, g2, extra):
                def unit(u, kv, first=False):
                    for st in range(16):
                        eng.wait_ge(turned, 16 * u + st + 1)
                        if st == 0 and not first:
                            eng.wait_ge(mm_done, 4 * u - 4)
                        moved_rows(copy, kv, st, g2, BT[st % 3]).then_inc(sem_, 1)
                    
                return unit

            @block.scalar
            def _(act):
                unit = mover(act, nc.scalar.copy, moved_a, 0, None)

                def gelus(u, kv, first=False):
                    for gp in range(2):
                        for m in range(2):
                            act.wait_ge(mm_done, 4 * u + 2 * gp + m + 1)
                            if not first:
                                act.wait_ge(out_done, 2 * u + gp - 1)
                            nc.scalar.activation(hid[gp][:, m, :, 0:255], BM[2 * gp + m][:, 0:510].rearrange("p (a c) -> p a c", a=2),
                                                 ACT.Gelu_apprx_tanh, bias=pe_bias[:, 2 * kv + m:2 * kv + m + 1]).then_inc(hid_ready, 1)

                act.wait_ge(pb, 1)
                nc.scalar.copy(pe_bias[:, :], BO[:, 0:4]).then_inc(pb, 1)
                act.wait_ge(pb, 2)
                unit(0, 0, True)
                unit(1, 1, True)
                gelus(0, 0, True)
                unit(2, 0)
                gelus(1, 1)
                with act.Fori(1, DEC_B - 1) as b:
                    unit(2 * b + 1, 1)
                    gelus(2 * b, 0)
                    unit(2 * b + 2, 0)
                    gelus(2 * b + 1, 1)
                u = 2 * DEC_B - 2
                unit(u + 1, 1)
                gelus(u, 0)
                gelus(u + 1, 1)

            @block.vector
            def _(v):
                unit = mover(v, v.tensor_copy, moved_v, 1, None)

                def outs(u, kv, b, first=False):
                    for gp in range(2):
                        v.wait_ge(out_done, 2 * u + gp + 1)
                        if gp == 0 and not first:
                            v.wait_ge(stored[kv], 16 * b)
                        if kv == 0:
                            ins = v.tensor_copy(ck[:, gp, 0:255], BO[:, 0:255])
                        else:
                            for h in range(2):
                                c = P - h
                                ins = v.tensor_copy(cv[0:c, h, P * gp:P * gp + P], BO[0:c, P * h:P * h + P])
                        ins.then_inc(out_moved, 1)

                v.memset(zero, 0.0).then_inc(spare_zeroed, 1)
                v.memset(ck[:, :, 255:256], 0.0)
                v.memset(cv[96:P, 1, :], 0.0).then_inc(zeroed, 1)
                v.wait_ge(zeroed, 1)
                v.wait_ge(pb, 2)
                unit(0, 0, True)
                unit(1, 1, True)
                outs(0, 0, 0, True)
                unit(2, 0)
                outs(1, 1, 0, True)
                with v.Fori(1, DEC_B - 1) as b:
                    unit(2 * b + 1, 1)
                    outs(2 * b, 0, b)
                    unit(2 * b + 2, 0)
                    outs(2 * b + 1, 1, b)
                b = DEC_B - 1
                unit(2 * b + 1, 1)
                outs(2 * b, 0, b)
                outs(2 * b + 1, 1, b)


KV_OFF = 9728
Q_OFF = KV_OFF + NT * 1536
GT_OFF = Q_OFF + 8 * TOK
A_FREE = GT_OFF + NT * 48 + 16


def projections(nc, A, R, outs, gate_dram):
    with Scope(nc, "proj") as s:
        xT = R(XT_OFF, KT, TOK)
        kv, q = R(KV_OFF, NT, 3, 512), R(Q_OFF, 8, TOK)
        gates = R(GT_OFF, NT, 48)
        wkv = R(A_FREE, KT, 1536)
        wq = R(A_FREE + KT * 1536, KT, NH * HD + 48)
        bank = s.banks()
        wq_in, full, stored, gates_done = (s.sem(n) for n in ("wq_in", "full", "stored", "gates_done"))
        wkv_in = [s.sem(f"wkv_in{i}") for i in range(3)]
        used = (s.sem("used_v"), s.sem("used_a"))
        ring = Split(8, full, used)
        NKVJ = 3 * NT
        half = TOK // 2
        p_out, s_out = outs[0:3], outs[3:6]
        n_out = [0]
        with nc.Block() as block:
            @block.sync
            def _(sp):
                for br in range(3):
                    sp.dma_start(wkv[:, :, 512 * br:512 * br + 512],
                                 A["kv_w"].rearrange("(k p) n -> p k n", p=P)[:, :, 512 * br:512 * br + 512]).then_inc(wkv_in[br], 16)
                sp.dma_start(wq, A["b_w_qg"].rearrange("(k p) n -> p k n", p=P)).then_inc(wq_in, 16)
                for b in range(DEC_B):
                    sp.dma_start(s_out[2][b, 0:504].rearrange("t k g d -> t (k g d)"),
                                 A["cache_win_kv"][b, 8:512].rearrange("t k g d -> t (k g d)")).then_inc(stored, 16)
                n = DEC_B
                for br in range(3):
                    for i in range(NT):
                        ring.all_used(sp, NT * br + i + 1)
                        flat = "t k g d -> t (k g d)"
                        if i < 4:
                            dst = p_out[br][0, P * i:P * i + P].rearrange(flat)
                            sp.dma_start(dst, kv[:, i, br, :]).then_inc(stored, 16)
                            n += 1
                        elif br < 2:
                            sp.dma_start(s_out[br].rearrange("b t k g d -> (b t) (k g d)"), kv[0:64, i, br, :]).then_inc(stored, 16)
                            n += 1
                        else:
                            for b in range(DEC_B):
                                sp.dma_start(s_out[2][b, 504:512].rearrange(flat), kv[8 * b:8 * b + 8, i, br, :]).then_inc(stored, 16)
                                n += 1
                sp.wait_ge(gates_done, NT)
                sp.dma_start(gate_dram, gates[0:64, 4, :]).then_inc(stored, 16)
                sp.wait_ge(stored, 16 * (n + 1))

            @block.tensor
            def _(pe):
                for br in range(3):
                    pe.wait_ge(wkv_in[br], 16)
                    for i, (t0, n) in enumerate(TILES):
                        b = ring.claim(pe, NT * br + i)
                        for k in range(KT):
                            ins = pe.matmul(bank[b][0:n, :], xT[:, k, t0:t0 + n], wkv[:, k, 512 * br:512 * br + 512],
                                            start=(k == 0), stop=(k == KT - 1))
                        ring.done(ins)
                pe.wait_ge(wq_in, 16)
                for m in range(8):
                    for h in range(2):
                        b = ring.claim(pe, NKVJ + 2 * m + h)
                        for k in range(KT):
                            ins = pe.matmul(bank[b][:, 0:half], wq[:, k, P * m:P * m + P], xT[:, k, half * h:half * h + half],
                                            start=(k == 0), stop=(k == KT - 1))
                        ring.done(ins)
                b = ring.claim(pe, NKVJ + 16)
                for i, (t0, n) in enumerate(TILES):
                    for k in range(KT):
                        ins = pe.matmul(bank[b][0:n, 48 * i:48 * i + 48], xT[:, k, t0:t0 + n], wq[:, k, NH * HD:],
                                        start=(k == 0), stop=(k == KT - 1))
                ring.done(ins)

            def empty(eng, copy, me):
                for j in range(me, NKVJ, 2):
                    br, i = j // NT, j % NT
                    n = TILES[i][1]
                    eng.wait_ge(full, j + 1)
                    copy(kv[0:n, i, br, :], bank[j % 8][0:n, :]).then_inc(used[me], 1)
                for j in range(NKVJ + (NKVJ + me) % 2, NKVJ + 16, 2):
                    m, h = (j - NKVJ) // 2, (j - NKVJ) % 2
                    eng.wait_ge(full, j + 1)
                    copy(q[:, m, half * h:half * h + half], bank[j % 8][:, 0:half]).then_inc(used[me], 1)

            @block.vector
            def _(v):
                empty(v, v.tensor_copy, 0)

            @block.scalar
            def _(act):
                empty(act, nc.scalar.copy, 1)
                j = NKVJ + 16
                act.wait_ge(full, j + 1)
                for i, (t0, n) in enumerate(TILES):
                    nc.scalar.activation(gates[0:n, i, :], bank[j % 8][0:n, 48 * i:48 * i + 48], ACT.Sigmoid).then_inc(gates_done, 1)


def compress_prompt(nc, A, R, ident, pe_bias, rows, ckp, cvp):
    with Scope(nc, "cp") as s:
        NS = 32
        raw = R(A_FREE, HR, np_=NS)
        xt = R(A_FREE + HR, 2, 8, NKV, NS)
        w1 = R(A_FREE + HR + 2048, 2, 16, CMP_H)
        w2 = R(A_FREE + 2 * HR + 2048, 2, 2, HD)
        hid = R(A_FREE + 2 * HR + 2304, 2, 2, NKV, NS)
        bank = s.banks()
        raw_in, w_in, turned, moved_a, moved_v, mm_done, hid_ready, out_done, dve = (
            s.sem(n) for n in ("raw_in", "w_in", "turned", "moved_a", "moved_v", "mm_done", "hid_ready", "out_done", "dve"))
        with nc.Block() as block:
            @block.sync
            def _(sp):
                sp.dma_start(raw, rows[0].rearrange("(n s) k g d -> n (s k g d)", s=16)).then_inc(raw_in, 16)
                sp.dma_start(w1, A["cmp_w1"].rearrange("k (t p) h -> p k t h", p=P)).then_inc(w_in, 16)
                sp.dma_start(w2, A["cmp_w2"].rearrange("k (m p) d -> p k m d", p=P)).then_inc(w_in, 16)

            @block.tensor
            def _(pe):
                pe.wait_ge(raw_in, 16)
                for kv in range(2):
                    for q in range(2):
                        for st in range(8 * q, 8 * q + 8):
                            for gp in range(2):
                                o = 512 * st + 256 * kv + P * gp
                                c = 64 * (st % 8) + NS * gp
                                ins = pe.transpose(bank[2 * kv + q][:, c:c + NS], raw[:, o:o + P], ident[0:NS, 0:NS])
                        ins.then_inc(turned, 1)
                pe.wait_ge(w_in, 32)
                pe.wait_ge(moved_a, 64)
                pe.wait_ge(moved_v, 64)
                for kv in range(2):
                    for m in range(2):
                        for t in range(16):
                            sh = 1 if t >= 8 else 0
                            ins = pe.matmul(bank[4 + 2 * kv + m][:, 0:NKV * 31], w1[:, kv, t, P * m:P * m + P],
                                            xt[:, kv, t % 8, :, sh:sh + 31], start=(t == 0), stop=(t == 15))
                        ins.then_inc(mm_done, 1)
                pe.wait_ge(hid_ready, 4)
                for g in range(NKV):
                    for m in range(2):
                        pe.matmul(bank[0][64 * (g % 2):64 * (g % 2) + 64, 32 * (g // 2):32 * (g // 2) + 31], w2[:, 0, m, :],
                                  hid[:, 0, m, g, 0:31], start=(m == 0), stop=(m == 1))
                for g in range(NKV):
                    for m in range(2):
                        ins = pe.matmul(bank[1][0:31, 64 * g:64 * g + 64], hid[:, 1, m, g, 0:31], w2[:, 1, m, :],
                                        start=(m == 0), stop=(m == 1))
                ins.then_inc(out_done, 1)

            def move(eng, copy, sem_, g2):
                for kv in range(2):
                    for q in range(2):
                        eng.wait_ge(turned, 2 * kv + q + 1)
                        for st in range(8 * q, 8 * q + 8):
                            for gp in range(2):
                                c = 64 * (st % 8) + NS * gp
                                copy(xt[64 * (st % 2):64 * (st % 2) + 64, kv, st // 2, 2 * gp + g2, :],
                                     bank[2 * kv + q][64 * g2:64 * g2 + 64, c:c + NS]).then_inc(sem_, 1)

            @block.scalar
            def _(act):
                move(act, nc.scalar.copy, moved_a, 0)
                for kv in range(2):
                    for m in range(2):
                        act.wait_ge(mm_done, 2 * kv + m + 1)
                        nc.scalar.activation(hid[:, kv, m, :, 0:31], bank[4 + 2 * kv + m][:, 0:NKV * 31].rearrange("p (g c) -> p g c", g=NKV),
                                             ACT.Gelu_apprx_tanh, bias=pe_bias[:, 2 * kv + m:2 * kv + m + 1]).then_inc(hid_ready, 1)

            @block.vector
            def _(v):
                move(v, v.tensor_copy, moved_v, 1)
                v.wait_ge(out_done, 1)
                v.tensor_copy(ckp[:, :, 0:31], bank[0][:, 0:64].rearrange("p (q c) -> p q c", q=2)[:, :, 0:31]).then_inc(dve, 1)
                v.tensor_copy(cvp[0:31, :], bank[1][0:31, 0:256]).then_inc(dve, 1)


def attention_masks(nc, R, cm, cma, cm01, nmask, wmask, hsum, forced):
    with Scope(nc, "masks") as s:
        ones = s.sb("ones", [P, P])
        pi, l_i, lf, li8, nm8 = s.sb("pi", [P, 1], I32), s.sb("l_i", [P, 1], I32), s.sb("lf", [P, 1]), s.sb("li8", [P, 8]), s.sb("nm8", [P, 8])
        qi, qf, cid, gl = s.sb("qi", [P, P], I32), s.sb("qf", [P, P]), s.sb("cid", [P, 1], I32), s.sb("gl", [P, 1])
        made, dve = s.sem("made"), s.sem("dve")
        with nc.Block() as block:
            @block.gpsimd
            def _(pool):
                pool.memset(ones[:, :], 0.0).then_inc(made, 1)
                pool.memset(cma, 0.0).then_inc(made, 1)
                pool.memset(cm01, 1.0).then_inc(made, 1)
                pool.iota(pi[:, :], pattern=[[0, 1]], base=0, channel_multiplier=1).then_inc(made, 1)
                pool.iota(li8[:, :], pattern=[[1, 8]], base=0, channel_multiplier=0, allow_small_or_imprecise_dtypes=True).then_inc(made, 1)
                pool.iota(qi[:, :], pattern=[[1, P]], base=0, channel_multiplier=0).then_inc(made, 1)
                pool.wait_ge(made, 6)
                pool.affine_select(out=cm, in_=ones[:, :], compare_op=ALU.is_ge, fill=NEG, base=0,
                                   pattern=[[-1, P]], channel_multiplier=1).then_inc(made, 1)
                pool.affine_select(out=cma, in_=cma, compare_op=ALU.is_ge, fill=NEG, base=-31,
                                   pattern=[[P, 4], [-16, 31]], channel_multiplier=1).then_inc(made, 1)
                pool.affine_select(out=cm01, in_=cm01, compare_op=ALU.is_ge, fill=0.0, base=-31,
                                   pattern=[[P, 4], [-16, 31]], channel_multiplier=1).then_inc(made, 1)

            @block.vector
            def _(v):
                link = Link(v, dve)
                v.wait_ge(made, 6)
                link(v.tensor_scalar(l_i[:, :], pi[:, :], 7, None, ALU.bitwise_and))
                link(v.tensor_copy(lf[:, :], l_i[:, :]))
                link(v.tensor_scalar(nm8[:, :], li8[:, :], lf[:, 0:1], NEG, ALU.is_gt, ALU.mult))
                link(v.tensor_scalar(wmask, li8[:, :], lf[:, 0:1], NEG, ALU.is_le, ALU.mult))
                link(v.memset(nmask, NEG))
                for b in range(DEC_B):
                    ins = v.tensor_copy(nmask[:, b, 8 * b:8 * b + 8], nm8[:, :])
                link(ins)
                link(v.tensor_scalar(qi[:, :], qi[:, :], 103, None, ALU.bitwise_and))
                link(v.tensor_scalar(cid[:, :], pi[:, :], 103, None, ALU.bitwise_and))
                link(v.tensor_copy(qf[:, :], qi[:, :]))
                link(v.tensor_copy(gl[:, :], cid[:, :]))
                link(v.tensor_scalar(hsum, qf[:, :], gl[:, 0:1], None, ALU.is_equal))
                link(v.memset(forced, 0.0))
                link(v.memset(forced[:, 0:1], 1e4))
                link(v.memset(forced[:, 64:65], 1e4))


def prompt_attention(nc, A, R, ident, ckp, cvp, cm, cma, cm01, kt_s, oT):
    with Scope(nc, "pa") as s:
        kv, q = R(KV_OFF, NT, 3, 512), R(Q_OFF, 8, TOK)
        gates = R(GT_OFF, NT, 16, 3)
        kt = R(A_FREE, 2, 2, SEQ)
        p_ = [R(A_FREE + 2048 + 1024 * i, 2, 512) for i in range(2)]
        pT = [R(A_FREE + 4096 + 1024 * i, 2, 512) for i in range(2)]
        o = R(A_FREE + 6144, 4, NH, HD)
        mx, sm, cf = R(A_FREE + 10240, 2, 2), R(A_FREE + 10244, 2, 2), R(A_FREE + 10248, 2, 2)
        ob = R(A_FREE + 10256, 2, 2, HD)
        pc = R(A_FREE + 10512, NH, 32)
        pcT = R(A_FREE + 11024, NH, P)
        mc, sc = R(A_FREE + 13072, NH), R(A_FREE + 13088, NH)
        tc = R(A_FREE + 13104, NH, HD)
        psS = [s.ctx.enter_context(nc.psum_tensor(f"pa_s{i}", [P, 2, 512], F32)) for i in range(2)]
        psT = [s.ctx.enter_context(nc.psum_tensor(f"pa_t{i}", [P, 512], F32)) for i in range(2)]
        psO = [s.ctx.enter_context(nc.psum_tensor(f"pa_o{i}", [P, 512], F32)) for i in range(2)]
        dve, k_turned, k_moved, s_done, c_exp_in, c_exp, c_ready, c_turned, c_moved, c_out, c_gated = (
            s.sem(n) for n in ("dve", "k_turned", "k_moved", "s_done", "c_exp_in", "c_exp", "c_ready", "c_turned", "c_moved", "c_out", "c_gated"))
        s_full, max_ready, p_ready, t_full, t_used, o_full, o_used, o_turned, o_moved = (
            s.sem(n) for n in ("s_full", "max_ready", "p_ready", "t_full", "t_used", "o_full", "o_used", "o_turned", "o_moved"))
        units = [(br, i, m, g2) for i in range(4) for br in range(2) for m in range(0, 8, 2) for g2 in range(2)]

        def head(m, g2):
            return (2 * (m // 4) + g2) * HPK + m % 4

        with nc.Block() as block:
            @block.tensor
            def _(pe):
                for j in range(4):
                    br, gp = j // 2, j % 2
                    for i in range(4):
                        ins = pe.transpose(psS[j // 2][:, j % 2, P * i:P * i + P], kv[:, i, 1 + br, P * gp:P * gp + P], ident[:, :])
                    ins.then_inc(k_turned, 1)
                for j in range(4):
                    br, gp = j // 2, j % 2
                    ins = pe.transpose(psO[0][:, 64 * j:64 * j + 64], kv[0:64, 4, 1 + br, P * gp:P * gp + P], ident[0:64, 0:64])
                ins.then_inc(k_turned, 1)
                for i in range(4):
                    if i == 0:
                        pe.wait_ge(k_moved, 5)
                    else:
                        pe.wait_ge(c_exp_in, i)
                    for m in range(8):
                        for g2 in range(2):
                            r = slice(64 * g2, 64 * g2 + 64)
                            ins = pe.matmul(psS[0][:, g2, 32 * m:32 * m + 31], q[r, m, P * i:P * i + P], ckp[r, m // 4, 0:31],
                                            start=True, stop=True)
                    ins.then_inc(s_done, 1)
                    pe.wait_ge(c_ready, i + 1)
                    for j in range(4):
                        if 4 * i + j >= 2:
                            pe.wait_ge(c_moved, 4 * i + j - 1)
                        for n in range(4):
                            ins = pe.transpose(psT[j % 2][0:31, P * n:P * n + P], pc[:, 4 * j + n, 0:31], ident[:, :])
                        ins.then_inc(c_turned, 1)
                    pe.wait_ge(c_moved, 4 * i + 4)
                    if i >= 1:
                        pe.wait_ge(c_gated, i)
                    for h in range(NH):
                        ins = pe.matmul(psO[h // 8][:, HD * (h % 8):HD * (h % 8) + HD], pcT[0:31, h, :],
                                        cvp[0:31, HD * (h // HPK):HD * (h // HPK) + HD], start=True, stop=True)
                    ins.then_inc(c_out, 1)

                def scores(u):
                    br, i, m, g2 = units[u]
                    r = slice(64 * g2, 64 * g2 + 64)
                    if u >= 2:
                        pe.wait_ge(p_ready, 2 * (u - 1))
                    n = P * (i + 1)
                    for e in range(2):
                        ins = pe.matmul(psS[u % 2][:, e, 0:n], q[r, m + e, P * i:P * i + P], kt[r, br, m // 4, 0:n], start=True, stop=True)
                    ins.then_inc(s_full, 1)

                def outputs(u):
                    br, i, m, g2 = units[u]
                    g = 2 * (m // 4) + g2
                    pe.wait_ge(p_ready, 2 * u + 2)
                    for e in range(2):
                        if 2 * u + e >= 2:
                            pe.wait_ge(t_used, 2 * u + e - 1)
                        for k in range(i + 1):
                            ins = pe.transpose(psT[e][:, P * k:P * k + P], p_[u % 2][:, e, P * k:P * k + P], ident[:, :])
                        ins.then_inc(t_full, 1)
                    if u >= 2:
                        pe.wait_ge(o_used, u - 1)
                    for e in range(2):
                        pe.wait_ge(t_used, 2 * u + e + 1)
                        for k in range(i + 1):
                            ins = pe.matmul(psO[u % 2][:, HD * e:HD * e + HD], pT[u % 2][:, e, P * k:P * k + P],
                                            kv[:, k, 1 + br, 256 + HD * g:256 + HD * g + HD], start=(k == 0), stop=(k == i))
                    ins.then_inc(o_full, 1)

                pe.wait_ge(c_exp_in, 4)
                pe.wait_ge(c_gated, 4)
                scores(0)
                for u in range(len(units)):
                    if u + 1 < len(units):
                        scores(u + 1)
                    outputs(u)
                pe.wait_ge(o_used, len(units))
                for i in range(4):
                    for h in range(2):
                        j = 2 * i + h
                        if j >= 2:
                            pe.wait_ge(o_moved, j - 1)
                        for k in range(4):
                            a = P * (4 * h + k)
                            ins = pe.transpose(psT[j % 2][:, P * k:P * k + P],
                                               o[:, i].rearrange("p h d -> p (h d)")[:, a:a + P], ident[:, :])
                        ins.then_inc(o_turned, 1)

            def turned_out(act, u):
                n = P * (units[u][1] + 1)
                for e in range(2):
                    act.wait_ge(t_full, 2 * u + e + 1)
                    if u >= 2:
                        act.wait_ge(o_full, u - 1)
                    nc.scalar.copy(pT[u % 2][:, e, 0:n], psT[e][:, 0:n]).then_inc(t_used, 1)

            @block.scalar
            def _(act):
                for i in range(4):
                    act.wait_ge(c_exp_in, i + 1)
                    nc.scalar.activation(pc[:, :, 0:31], pc[:, :, 0:31], ACT.Exp, scale=SCALE).then_inc(c_exp, 1)
                for u, (br, i, m, g2) in enumerate(units):
                    n = P * (i + 1)
                    act.wait_ge(max_ready, u + 1)
                    if u >= 2:
                        act.wait_ge(t_full, 2 * u - 2)
                    for e in range(2):
                        nc.scalar.activation(p_[u % 2][:, e, 0:n], psS[u % 2][:, e, 0:n], ACT.Exp, bias=mx[:, u % 2, e:e + 1],
                                             scale=SCALE, accum_out=sm[:, u % 2, e:e + 1]).then_inc(p_ready, 1)
                    if u >= 1:
                        turned_out(act, u - 1)
                turned_out(act, len(units) - 1)
                for j in range(8):
                    act.wait_ge(o_turned, j + 1)
                    nc.scalar.copy(oT[:, 4 * (j % 2):4 * (j % 2) + 4, P * (j // 2):P * (j // 2) + P],
                                   psT[j % 2][:, :].rearrange("p (k t) -> p k t", k=4)).then_inc(o_moved, 1)

            @block.vector
            def _(v):
                link = Link(v, dve)
                for j in range(4):
                    v.wait_ge(k_turned, j + 1)
                    v.tensor_copy(kt[:, j // 2, j % 2, :], psS[j // 2][:, j % 2, :]).then_inc(k_moved, 1)
                v.wait_ge(k_turned, 5)
                v.tensor_copy(kt_s.rearrange("p a b t -> p (a b t)"), psO[0][:, 0:256]).then_inc(k_moved, 1)
                for i in range(4):
                    v.wait_ge(s_done, i + 1)
                    if i >= 1:
                        v.wait_ge(c_turned, 4 * i)
                    for gp in range(2):
                        for g2 in range(2):
                            h = head(4 * gp, g2)
                            s31 = psS[0][:, g2, 0:256].rearrange("p (h c) -> p h c", h=8)[:, 4 * gp:4 * gp + 4, 0:31]
                            ins = v.tensor_tensor(pc[:, h:h + 4, 0:31], s31, bc(cma[:, i, :].unsqueeze(1), [P, 4, 31]), ALU.add)
                    link(ins)
                    link(v.tensor_reduce(mc, pc[:, :, 0:31], AX, ALU.max))
                    v.tensor_tensor(pc[:, :, 0:31], pc[:, :, 0:31], bc(mc.unsqueeze(2), [P, NH, 31]), ALU.subtract).then_inc(c_exp_in, 1)
                    v.wait_ge(c_exp, i + 1)
                    link(v.tensor_tensor(pc[:, :, 0:31], pc[:, :, 0:31], bc(cm01[:, i, :].unsqueeze(1), [P, NH, 31]), ALU.mult))
                    v.engine_nop().then_inc(c_ready, 1)
                    link(v.tensor_reduce(sc, pc[:, :, 0:31], AX, ALU.add))
                    link(v.tensor_scalar(sc, sc, TINY, None, ALU.max))
                    link(v.reciprocal(sc, sc))
                    link(v.tensor_tensor(sc, sc, gates[:, i, :, 0], ALU.mult))
                    for j in range(4):
                        v.wait_ge(c_turned, 4 * i + j + 1)
                        if j == 0 and i >= 1:
                            v.wait_ge(c_out, i)
                        v.tensor_copy(pcT[0:31, 4 * j:4 * j + 4, :], psT[j % 2][0:31, :].rearrange("p (h t) -> p h t", h=4)).then_inc(c_moved, 1)
                    v.wait_ge(c_out, i + 1)
                    for h in range(2):
                        ins = v.tensor_tensor(o[:, i, 8 * h:8 * h + 8, :], psO[h][:, :].rearrange("p (h d) -> p h d", h=8),
                                              bc(sc[:, 8 * h:8 * h + 8].unsqueeze(2), [P, 8, HD]), ALU.mult)
                    ins.then_inc(c_gated, 1)
                v.wait_ge(c_gated, 4)

                def merge(u):
                    br, i, m, g2 = units[u]
                    h = head(m, g2)
                    v.wait_ge(p_ready, 2 * u + 2)
                    link(v.reciprocal(cf[:, u % 2, :], sm[:, u % 2, :]))
                    link(v.tensor_tensor(cf[:, u % 2, :], cf[:, u % 2, :], gates[:, i, h:h + 2, 1 + br], ALU.mult))
                    v.wait_ge(o_full, u + 1)
                    link(v.tensor_tensor(ob[:, u % 2], psO[u % 2][:, 0:2 * HD].rearrange("p (e d) -> p e d", e=2),
                                         bc(cf[:, u % 2, :].unsqueeze(2), [P, 2, HD]), ALU.mult))
                    v.tensor_tensor(o[:, i, h:h + 2, :], o[:, i, h:h + 2, :], ob[:, u % 2], ALU.add).then_inc(o_used, 1)

                for u, (br, i, m, g2) in enumerate(units):
                    n = P * (i + 1)
                    v.wait_ge(s_full, u + 1)
                    diag = psS[u % 2][:, :, P * i:n]
                    link(v.tensor_tensor(diag, diag, bc(cm.unsqueeze(1), [P, 2, P]), ALU.add))
                    if u >= 2:
                        v.wait_ge(p_ready, 2 * u - 2)
                    link(v.tensor_reduce(mx[:, u % 2, :], psS[u % 2][:, :, 0:n], AX, ALU.max))
                    v.tensor_scalar(mx[:, u % 2, :], mx[:, u % 2, :], -SCALE, None, ALU.mult).then_inc(max_ready, 1)
                    if u >= 1:
                        merge(u - 1)
                merge(len(units) - 1)


OT_OFF = KV_OFF
KV4_OFF = KV_OFF + 4 * 1536
QBD_OFF = XT_OFF + 1680
S_FREE = Q_OFF


def sample_queries(nc, R, gate_dram, gs):
    with Scope(nc, "sq") as s:
        q, qbd = R(Q_OFF, 8, TOK), R(QBD_OFF, DEC_B, 2, P)
        zeroed, done, g_in = s.sem("zeroed"), s.sem("done"), s.sem("g_in")
        with nc.Block() as block:
            @block.gpsimd
            def _(pool):
                pool.memset(qbd, 0.0).then_inc(zeroed, 1)

            @block.vector
            def _(v):
                v.wait_ge(zeroed, 1)
                for g in range(NKV):
                    gp, g2 = g // 2, g % 2
                    r = slice(64 * g2, 64 * g2 + 64)
                    dst = qbd[r, :, gp, 32 * g:32 * g + 32].rearrange("p b (n l) -> p b n l", n=HPK)
                    src = q[r, 4 * gp:4 * gp + 4, SEQ:TOK].rearrange("p n (b l) -> p b n l", b=DEC_B)
                    v.tensor_copy(dst, src).then_inc(done, 1)

            @block.sync
            def _(sp):
                for b in range(DEC_B):
                    src = gate_dram.rearrange("(b l) (h r) -> b h l r", b=DEC_B, r=3)[b]
                    sp.dma_start(gs[:, b, :], src).then_inc(g_in, 16)
                sp.wait_ge(g_in, 16 * DEC_B)


def sample_attention(nc, A, R, ident, idx_slc, ck_dram, cv_dram, kt_s, nmask, wmask, hsum, forced, gs, oT):
    with Scope(nc, "sa") as s:
        qbd, kv4 = R(QBD_OFF, DEC_B, 2, P), R(KV4_OFF, 3, 512)
        at = [S_FREE]

        def place(*shape, dt=F32):
            n = int(np.prod(shape))
            at[0] += n + n % 2
            return R(at[0] - n - n % 2, *shape, dt=dt)

        NJ = 8
        raw = [place(4, 512) for _ in range(NJ + 1)]
        sc = place(9 * 512 + 128)
        OLD, WIN = NJ * 512, NJ * 512 + 64
        kts = [place(2, 512) for _ in range(2)]
        pt = [place(512) for _ in range(2)]
        ptn = place(512)
        ck, cv = place(2, 256), place(2, 256)
        pc = place(256)
        qb = place(2, P)
        ps = place(66)
        sel = place(66)
        m8 = place(2, 8)
        mxs, sms, cf = place(4), place(4), place(4)
        ob, ob2 = place(HD), place(2, HD)
        idx = place(NJ, dt=I32)
        bank = s.banks()
        psK, psS, psT, O0, O1 = bank[0:2], bank[2:4], bank[4:6], bank[6], bank[7]
        names = ("idx_ready", "gather_go", "win_in", "ck_in", "dve", "qb_ready", "c_full", "cmax_ready", "c_exp", "p4_ready",
                 "hs_full", "k_turned", "k_moved_v", "k_moved_a", "s_full", "s_moved", "max_ready", "e_ready", "pn_ready",
                 "t_full", "t_moved_v", "t_moved_a", "pv_done", "o_done", "ob_ready", "ob_turned", "o_stored")
        (idx_ready, gather_go, win_in, ck_in, dve, qb_ready, c_full, cmax_ready, c_exp, p4_ready, hs_full, k_turned, k_moved_v,
         k_moved_a, s_full, s_moved, max_ready, e_ready, pn_ready, t_full, t_moved_v, t_moved_a, pv_done, o_done, ob_ready,
         ob_turned, o_stored) = (s.sem(n) for n in names)
        pad_ready, own_wait = s.sem("pad_ready"), s.sem("own_wait")
        raw_in = [s.sem(f"raw_in{j}") for j in range(NJ)]
        cache = A["cache_slc_kv"].rearrange("n (i s) k g d -> (n i) (s k g d)", s=4)

        def samples(eng, body):
            body(0, True)
            with eng.Fori(1, DEC_B) as b:
                body(b, False)

        def at_b(x, b, n=1):
            return x[:, n * b:n * b + n] if isinstance(b, int) else x[:, bass.ds(n * b, n)]

        def turned_k(j):
            return kts[j % 2]

        with nc.Block() as block:
            @block.gpsimd
            def _(pool):
                def body(b, first):
                    if not first:
                        for j in range(NJ):
                            pool.wait_ge(raw_in[j], 16 * b)
                    pool.tensor_copy(idx, at_b(idx_slc, b, NJ)).then_inc(idx_ready, 1)
                    pool.wait_ge(idx_ready, b + 1)
                    for j in range(NJ):
                        if not first:
                            pool.wait_ge(pv_done, NJ * b - NJ + j + 1)
                            pool.sem_inc(gather_go, 1)
                        pool.indirect_dma_start(out=raw[j].rearrange("p s n -> p (s n)"), out_offset=None, in_=cache,
                                                in_offset=bass.IndirectOffsetOnAxis(ap=idx[:, j:j + 1], axis=0)).then_inc(raw_in[j], 16)
                samples(pool, body)

            @block.sync
            def _(sp):
                def body(b, first):
                    if not first:
                        sp.wait_ge(o_done, b)
                    def row(x):
                        return x[b:b + 1] if isinstance(b, int) else x[bass.ds(b, 1)]
                    sp.dma_start(ck.rearrange("p a n -> p (a n)"), row(ck_dram).rearrange("o p n -> p (o n)")).then_inc(ck_in, 16)
                    sp.dma_start(cv.rearrange("p a n -> p (a n)"), row(cv_dram).rearrange("o p n -> p (o n)")).then_inc(ck_in, 16)
                    sp.dma_start(raw[NJ].rearrange("p s n -> p (s n)"),
                                 row(A["cache_win_kv"]).rearrange("o (p s) k g d -> p (o s k g d)", s=4)).then_inc(win_in, 16)
                samples(sp, body)

            @block.tensor
            def _(pe):
                def body(b, first):
                    pe.wait_ge(qb_ready, b + 1)
                    pe.wait_ge(ck_in, 32 * b + 32)
                    if not first:
                        pe.wait_ge(o_stored, b)
                    for gp in range(2):
                        ins = pe.matmul(O0[:, 0:255], qb[:, gp, :], ck[:, gp, 0:255], start=(gp == 0), stop=(gp == 1))
                    for br in range(2):
                        for gp in range(2):
                            ins = pe.matmul(O0[:, 320 + 64 * br:384 + 64 * br], qb[:, gp, :], kt_s[:, br, gp, :],
                                            start=(gp == 0), stop=(gp == 1))
                    ins.then_inc(c_full, 1)

                    def turn(j):
                        pe.wait_ge(raw_in[j], 16 * b + 16) if j < NJ else pe.wait_ge(win_in, 16 * b + 16)
                        if not (first and j == 0):
                            pe.wait_ge(k_moved_v, 9 * b + j)
                            pe.wait_ge(k_moved_a, 9 * b + j)
                        for gp in range(2):
                            for r in range(4):
                                ins = pe.transpose(psK[gp][:, P * r:P * r + P], raw[j][:, r, P * gp:P * gp + P], ident[:, :])
                            ins.then_inc(k_turned, 1)

                    def scores(j):
                        pe.wait_ge(k_moved_v, 9 * b + j + 1)
                        pe.wait_ge(k_moved_a, 9 * b + j + 1)
                        if not (first and j < 2):
                            pe.wait_ge(s_moved, 9 * b + j - 1)
                        for gp in range(2):
                            ins = pe.matmul(psS[j % 2][:, :], qb[:, gp, :], turned_k(j)[:, gp, :], start=(gp == 0), stop=(gp == 1))
                        ins.then_inc(s_full, 1)

                    turn(0)
                    pe.wait_ge(p4_ready, b + 1)
                    pe.matmul(O0[:, 256:320], hsum, ps[:, 0:64], start=True, stop=True).then_inc(hs_full, 1)
                    for j in range(9):
                        if j < 8:
                            turn(j + 1)
                        scores(j)

                    def turn_p(q):
                        if q == 0:
                            pe.wait_ge(pn_ready, b + 1)
                            pe.wait_ge(e_ready, 2 * b + 2)
                        if q >= 2 or not first:
                            if q % 2 == 0:
                                pe.wait_ge(t_moved_v, 5 * b + q // 2)
                            else:
                                pe.wait_ge(t_moved_a, 5 * b + q // 2)
                        for r in range(4):
                            if q == 0 and r >= 2:
                                o = (OLD, WIN + 512)[r - 2]
                                ins = pe.transpose(psT[0][0:64, P * r:P * r + P], sc[:, o:o + 64], ident[:, :])
                                continue
                            src = pc[:, P * r:P * r + P] if q == 0 else \
                                (sc[:, 512 * (q - 1) + P * r:512 * (q - 1) + P * r + P] if q < 9 else sc[:, WIN + P * r:WIN + P * r + P])
                            ins = pe.transpose(psT[q % 2][:, P * r:P * r + P], src, ident[:, :])
                        ins.then_inc(t_full, 1)

                    def values(q):
                        if q % 2 == 0:
                            pe.wait_ge(t_moved_v, 5 * b + q // 2 + 1)
                        else:
                            pe.wait_ge(t_moved_a, 5 * b + q // 2 + 1)
                        if q == 0:
                            for r in range(2):
                                pe.matmul(O1[:, 0:256], ptn[:, P * r:P * r + P], cv[:, r, :], start=(r == 0), stop=(r == 1))
                            return
                        out = O0[:, 0:256] if q < 9 else O1[:, 256:512]
                        j = q - 1
                        last = q >= 8
                        for r in range(4):
                            ins = pe.matmul(out, pt[q % 2][:, P * r:P * r + P], raw[j][:, r, 256:512],
                                            start=(r == 0 and q in (1, 9)), stop=False, skip_group_check=True)
                        if q < 9:
                            ins.then_inc(pv_done, 1)
                        if last:
                            o = 256 if q == 8 else 384
                            ins = pe.matmul(out, ptn[0:64, o:o + P], kv4[0:64, 1 + (q == 9), 256:512], start=False, stop=True,
                                            skip_group_check=True)
                        if q == 9:
                            ins.then_inc(o_done, 1)

                    turn_p(0)
                    for q in range(10):
                        if q < 9:
                            turn_p(q + 1)
                        values(q)
                    pe.wait_ge(ob_ready, b + 1)
                    pe.transpose(O0[:, 0:P], ob2.rearrange("p e d -> p (e d)"), ident[:, :]).then_inc(ob_turned, 1)
                samples(pe, body)

            @block.scalar
            def _(act):
                def body(b, first):
                    act.wait_ge(cmax_ready, b + 1)
                    nc.scalar.activation(pc[:, 0:255], O0[:, 0:255], ACT.Exp, bias=mxs[:, 0:1], scale=SCALE,
                                         accum_out=sms[:, 0:1]).then_inc(c_exp, 1)
                    for j in range(9):
                        act.wait_ge(k_turned, 18 * b + 2 * j + 2)
                        if not (first and j < 2):
                            act.wait_ge(s_full, 9 * b + j - 1)
                        nc.scalar.copy(turned_k(j)[:, 1, :], psK[1][:, :]).then_inc(k_moved_a, 1)
                    for w, (o, n) in enumerate(((0, 4160), (WIN, 576))):
                        act.wait_ge(max_ready, 2 * b + w + 1)
                        nc.scalar.activation(sc[:, o:o + n], sc[:, o:o + n], ACT.Exp, bias=mxs[:, 1 + w:2 + w], scale=SCALE,
                                             accum_out=sms[:, 1 + w:2 + w]).then_inc(e_ready, 1)
                    for q in range(1, 10, 2):
                        act.wait_ge(t_full, 10 * b + q + 1)
                        if q >= 3:
                            act.wait_ge(pv_done, NJ * b + q - 2)
                        elif not first:
                            act.wait_ge(o_done, b)
                        nc.scalar.copy(pt[1], psT[1][:, :]).then_inc(t_moved_a, 1)
                samples(act, body)

            @block.vector
            def _(v):
                NL = 23

                def body(b, first):
                    link = Link(v, dve, NL * b)
                    if not first:
                        v.wait_ge(s_full, 9 * b)
                    v.tensor_copy(qb.rearrange("p a n -> p (a n)"),
                                  (qbd[:, 0:1] if first else qbd[:, bass.ds(b, 1)]).rearrange("p o a n -> p (o a n)")).then_inc(qb_ready, 1)
                    v.wait_ge(c_full, b + 1)
                    link(v.tensor_reduce(mxs[:, 0:1], O0[:, 0:255], AX, ALU.max))
                    v.tensor_scalar(mxs[:, 0:1], mxs[:, 0:1], -SCALE, None, ALU.mult).then_inc(cmax_ready, 1)

                    def move_k(j):
                        v.wait_ge(k_turned, 18 * b + 2 * j + 1)
                        if not (first and j < 2):
                            v.wait_ge(s_full, 9 * b + j - 1)
                        v.tensor_copy(turned_k(j)[:, 0, :], psK[0][:, :]).then_inc(k_moved_v, 1)

                    move_k(0)
                    v.wait_ge(c_exp, b + 1)
                    link(v.reciprocal(cf[:, 0:1], sms[:, 0:1]))
                    link(v.tensor_scalar(pc[:, 0:255], pc[:, 0:255], cf[:, 0:1], None, ALU.mult))
                    v.sem_inc(pn_ready, 1)
                    link(v.tensor_reduce(ps[:, 0:64], pc.rearrange("p (j c) -> p j c", c=4), AX, ALU.add))
                    spill = pc.rearrange("p (j c) -> p j c", c=4)[:, 0:63, 3]
                    v.tensor_tensor(ps[:, 1:64], ps[:, 1:64], spill, ALU.add).then_inc(p4_ready, 1)
                    move_k(1)
                    v.wait_ge(hs_full, b + 1)
                    v.tensor_tensor(sel[:, 0:64], O0[:, 256:320], forced[:, 0:64], ALU.add)
                    link(v.tensor_copy(sel[:, 64:65], forced[:, 64:65]))
                    for i in range(2):
                        v.sem_inc(own_wait, 1)
                        link(v.max(m8[:, i, :], sel[:, 0:65]))
                        v.sem_inc(own_wait, 1)
                        link(v.match_replace(sel[:, 0:65], m8[:, i, :], sel[:, 0:65], -1e9))
                    link(v.tensor_scalar(sel[:, 0:65], sel[:, 0:65], -1e9, NEG, ALU.not_equal, ALU.mult))
                    for j in range(8):
                        if j < 7:
                            move_k(j + 2)
                        v.wait_ge(s_full, 9 * b + j + 1)
                        if j == 0 and not first:
                            v.wait_ge(t_full, 10 * b)
                        m = bc(bc(sel[:, 8 * j:8 * j + 8].unsqueeze(2), [P, 8, 16]).unsqueeze(1), [P, 4, 8, 16])
                        v.tensor_tensor(sc[:, 512 * j:512 * j + 512].rearrange("p (r j i) -> p r j i", r=4, j=8),
                                        psS[j % 2][:, :].rearrange("p (r j i) -> p r j i", r=4, j=8), m, ALU.add).then_inc(s_moved, 1)
                    nm = nmask[:, 0] if first else nmask[:, bass.ds(b, 1)].rearrange("p o n -> p (o n)")
                    v.tensor_tensor(sc[:, OLD:OLD + 64], O0[:, 320:384], nm, ALU.add)
                    link(v.tensor_tensor(sc[:, WIN + 512:WIN + 576], O0[:, 384:448], nm, ALU.add))
                    link(v.tensor_scalar(sc[:, OLD:OLD + 64], sc[:, OLD:OLD + 64], sel[:, 64:65], None, ALU.add))
                    v.wait_ge(s_moved, 9 * b + 8)
                    link(v.tensor_reduce(mxs[:, 1:2], sc[:, 0:4160], AX, ALU.max))
                    v.tensor_scalar(mxs[:, 1:2], mxs[:, 1:2], -SCALE, None, ALU.mult).then_inc(max_ready, 1)
                    v.wait_ge(s_full, 9 * b + 9)
                    link(v.tensor_copy(sc[:, WIN:WIN + 512], psS[0][:, :]))
                    v.sem_inc(s_moved, 1)
                    w8 = sc[:, WIN:WIN + 512].rearrange("p (r q) -> p r q", r=4)[:, :, 0:2]
                    link(v.tensor_tensor(w8, w8, wmask.rearrange("p (q r) -> p r q", r=4), ALU.add))
                    link(v.tensor_reduce(mxs[:, 2:3], sc[:, WIN:WIN + 576], AX, ALU.max))
                    v.tensor_scalar(mxs[:, 2:3], mxs[:, 2:3], -SCALE, None, ALU.mult).then_inc(max_ready, 1)
                    for q in range(0, 10, 2):
                        v.wait_ge(t_full, 10 * b + q + 1)
                        if q >= 4:
                            v.wait_ge(pv_done, NJ * b + q - 2)
                        elif not first:
                            v.wait_ge(o_done, b)
                        if q == 0:
                            v.tensor_copy(ptn[:, 0:256], psT[0][:, 0:256])
                            v.tensor_copy(ptn[0:64, 256:512], psT[0][0:64, 256:512]).then_inc(t_moved_v, 1)
                        else:
                            v.tensor_copy(pt[0], psT[0][:, :]).then_inc(t_moved_v, 1)
                    link(v.memset(sms[:, 0:1], 1.0))
                    v.wait_ge(e_ready, 2 * b + 2)
                    link(v.reciprocal(cf[:, 0:3], sms[:, 0:3]))
                    g3 = gs[:, 0] if first else gs[:, bass.ds(b, 1)].rearrange("p o n -> p (o n)")
                    link(v.tensor_tensor(cf[:, 0:3], cf[:, 0:3], g3, ALU.mult))
                    v.wait_ge(o_done, b + 1)
                    for br, src in ((0, O1[:, 0:256]), (1, O0[:, 0:256]), (2, O1[:, 256:512])):
                        for g in range(NKV):
                            r = slice(32 * g, 32 * g + 32)
                            x = src[r, HD * g:HD * g + HD]
                            if br == 0:
                                ins = v.tensor_scalar(ob[r, :], x, cf[r, 0:1], None, ALU.mult)
                            elif br == 1:
                                ins = v.scalar_tensor_tensor(out=ob[r, :], in0=x, scalar=cf[r, 1:2], in1=ob[r, :], op0=ALU.mult, op1=ALU.add)
                            else:
                                for e in range(2):
                                    ins = v.scalar_tensor_tensor(out=ob2[r, e, :], in0=x, scalar=cf[r, 2:3], in1=ob[r, :], op0=ALU.mult, op1=ALU.add)
                        link(ins)
                    v.sem_inc(ob_ready, 1)
                    v.wait_ge(ob_turned, b + 1)
                    for e in range(2):
                        r = slice(64 * e, 64 * e + 64)
                        col = oT[r, :, SEQ:SEQ + 8] if first else oT[r, :, bass.ds(8 * b + SEQ, 8)]
                        ins = v.tensor_copy(col, O0[r, 0:P].rearrange("p (m e l) -> p m e l", m=8, e=2)[:, :, e, :])
                    link(ins)
                    v.sem_inc(o_stored, 1)
                    used = link.count
                    assert used == NL, used
                v.memset(pc[:, 255:256], 0.0).then_inc(pad_ready, 1)
                v.wait_ge(pad_ready, 1)
                samples(v, body)


def attention_out(nc, A, R, x, oT):
    with Scope(nc, "ao") as s:
        w = R(A_FREE, KT, D)
        bank = s.banks()
        w_in, full, used = s.sem("w_in"), s.sem("full"), s.sem("used")
        with nc.Block() as block:
            @block.sync
            def _(sp):
                sp.dma_start(w, A["b_w_o"][0].rearrange("(k p) n -> p k n", p=P)).then_inc(w_in, 16)

            @block.tensor
            def _(pe):
                pe.wait_ge(w_in, 16)
                for i, (t0, n) in enumerate(TILES):
                    for h in range(2):
                        j = 2 * i + h
                        if j >= 8:
                            pe.wait_ge(used, j - 7)
                        for k in range(KT):
                            ins = pe.matmul(bank[j % 8][0:n, :], oT[:, k, t0:t0 + n], w[:, k, 512 * h:512 * h + 512],
                                            start=(k == 0), stop=(k == KT - 1))
                        ins.then_inc(full, 1)

            @block.vector
            def _(v):
                for i, (t0, n) in enumerate(TILES):
                    for h in range(2):
                        j = 2 * i + h
                        v.wait_ge(full, j + 1)
                        xs = x[0:n, i, 512 * h:512 * h + 512]
                        v.scalar_tensor_tensor(out=xs, in0=xs, scalar=ALPHA, in1=bank[j % 8][0:n, :], op0=ALU.mult, op1=ALU.add).then_inc(used, 1)


OUTS = {"y_prompt": [1, SEQ, D], "y_sample": [DEC_B, DEC_S, D], "h_last": [P, DEC_B + 1, SG],
        "p_cmp": [1, SEQ, 2, NKV, HD], "p_slc": [1, SEQ, 2, NKV, HD], "p_win": [1, SEQ, 2, NKV, HD],
        "s_cmp": [DEC_B, DEC_S, 2, NKV, HD], "s_slc": [DEC_B, DEC_S, 2, NKV, HD], "s_win": [DEC_B, SEQ, 2, NKV, HD]}


def build(nc, A, O):
    def dram(name, shape, dt=F32):
        return nc.dram_tensor(name, shape, dt).ap()

    Scope.spent = []
    with Scope(nc, "all") as s:
        ident, jmat = s.sb("ident", [P, P]), s.sb("jmat", [P, P])
        A["eps"] = s.sb("eps", [P, 1])
        idx_cmp, idx_slc = s.sb("idx_cmp", [P, 2 * DEC_B], I32), s.sb("idx_slc", [P, 8 * DEC_B], I32)
        pe_bias, gates_s = s.sb("pe_bias", [P, 4]), s.sb("gates_s", [P, DEC_B, 3])
        R = Region(s.sb("arena", [P, ARENA]))
        x = R(X_OFF, NT, D)
        ck_dram, cv_dram = dram("ck", [DEC_B, P, 512]), dram("cv", [DEC_B, P, 512])
        y_rows = dram("y_rows", [NROW, D])
        constants(nc, ident, jmat, A["eps"])
        page_rows(nc, A, idx_cmp, idx_slc)
        compress_cache(nc, A, R, ident, idx_cmp, pe_bias, ck_dram, cv_dram, y_rows[NE * RB:NROW])
        recycle(nc)

        u_dram, s5_dram = dram("u", [D, TOK]), dram("s5_y", [D, TOK])
        tab, bx1, bx2, cy1, cy2 = (R(S5_TAB, 20, 64), *[R(off, SG, SW) for off in (S5_X1, S5_X2, S5_Y1, S5_Y2)])
        toep, et, o = R(5376, SG, CH, SW), R(13568, SG, P), R(21760, SG, CH, SW)
        ho, hs = R(S5_X1, DEC_B + 1, SG), R(S5_X2 + 512, DEC_B, SG)
        s5_inputs(nc, A, R, ident, u_dram)
        s5_parameters(nc, A, ident, jmat, tab, bx1, bx2, cy1, cy2, R)
        s5_matrices(nc, A, R, ident, toep, et, o)
        s5_chunks(nc, A, R, toep, et, u_dram, hs)
        s5_scan(nc, R, jmat, hs, ho)
        s5_outputs(nc, R, o, s5_dram, ho, O["h_last"])
        glu(nc, A, R, x, u_dram, s5_dram)
        for layer in range(2):
            recycle(nc)
            if layer == 1:
                attention(nc, A, O, R, x, ident, idx_slc, pe_bias, gates_s, ck_dram, cv_dram, dram("gates", [DEC_B * DEC_S, NH * 3]))
                recycle(nc)
            x_dram, row_tok = dram(f"x{layer}", [TOK, D]), dram(f"row_tok{layer}", [NROW, 1], I32)
            weights = Weights(nc, A, R, layer)
            layer_norm(nc, A, R, f"ln_a{layer}", layer, 0, ident, x, x_dram=x_dram, weights=weights)
            route(nc, A, R, f"route{layer}", layer, row_tok)
            experts(nc, A, R, f"moe{layer}", layer, ident, weights, x_dram, y_rows)
            more_experts(nc, A, R, f"more{layer}", layer, ident, weights, x_dram, y_rows)
            combine(nc, R, f"comb{layer}", x, y_rows)
            layer_norm(nc, A, R, f"ln_b{layer}", layer, 1, ident, x,
                       outs=(O["y_prompt"], O["y_sample"]) if layer == 1 else None, turn=(layer == 0))


def attention(nc, A, O, R, x, ident, idx_slc, pe_bias, gates_s, ck_dram, cv_dram, gate_dram):
    at = [XT_OFF]

    def place(*shape):
        at[0] += int(np.prod(shape))
        return R(at[0] - int(np.prod(shape)), *shape)

    projections(nc, A, R, [O[n] for n in ("p_cmp", "p_slc", "p_win", "s_cmp", "s_slc", "s_win")], gate_dram)
    ck_p, cv_p = place(2, 32), place(256)
    causal, seen, seen01 = place(P), place(4, NCMP_P), place(4, NCMP_P)
    new_mask, win_mask, head_sum, forced = place(DEC_B, 64), place(8), place(P), place(66)
    new_keys = place(2, 2, 64)
    compress_prompt(nc, A, R, ident, pe_bias, O["p_cmp"], ck_p, cv_p)
    attention_masks(nc, R, causal, seen, seen01, new_mask, win_mask, head_sum, forced)
    oT = R(OT_OFF, KT, TOK)
    prompt_attention(nc, A, R, ident, ck_p, cv_p, causal, seen, seen01, new_keys, oT)
    sample_queries(nc, R, gate_dram, gates_s)
    sample_attention(nc, A, R, ident, idx_slc, ck_dram, cv_dram, new_keys, new_mask, win_mask, head_sum, forced, gates_s, oT)
    attention_out(nc, A, R, x, oT)


def kernel(**inputs):
    import numpy as _np
    import concourse.bacc as _bacc
    from concourse import mybir as _mybir
    from concourse.bass_utils import run_bass_kernel_spmd as _run

    nc = _bacc.Bacc("TRN2", target_bir_lowering=False, num_devices=1)
    given = {n: _np.asarray(inputs[n]) for n in _INS}
    given["state_ssm"] = given["state_ssm"][0].transpose(3, 2, 0, 1).reshape(P, DEC_B, SG)
    given["a_d"] = given["a_d"].reshape(KT, P).T
    given["cmp_pe"] = given["cmp_pe"].reshape(2, 16, P).transpose(2, 0, 1)
    w = given["b_w_qg"][0]
    wq = w[:, :D].reshape(D, 2, 2, HPK, HD).transpose(0, 1, 3, 2, 4).reshape(D, D)
    given["b_w_qg"] = _np.concatenate([wq, w[:, D:]], axis=1)
    arrays, A, O = {}, {}, {}
    for n in _INS:
        a = _np.ascontiguousarray(given[n])
        arrays[f"in_{n}"] = a
        A[n] = nc.dram_tensor(f"in_{n}", a.shape, _mybir.dt.from_np(a.dtype), kind="ExternalInput").ap()
    for n, shape in OUTS.items():
        O[n] = nc.dram_tensor(f"out_{n}", shape, _mybir.dt.float32, kind="ExternalOutput").ap()
    build(nc, A, O)
    r = _run(nc, [arrays], core_ids=[0])
    got = {n: r.results[0][f"out_{n}"] for n in OUTS}
    h = got["h_last"]
    p_state = _np.ascontiguousarray(h[:, DEC_B].reshape(2, SP_, SG).transpose(2, 1, 0))[None, None]
    s_state = _np.ascontiguousarray(h[:, :DEC_B].reshape(2, SP_, DEC_B, SG).transpose(2, 3, 1, 0))[None]
    return (got["y_prompt"], got["y_sample"], p_state, got["p_cmp"], got["p_slc"], got["p_win"],
            s_state, got["s_cmp"], got["s_slc"], got["s_win"])
```

```python
from contextlib import ExitStack

import numpy as np

import concourse.bass as bass
from concourse import mybir

F32 = mybir.dt.float32
F32R = mybir.dt.float32r
BF16 = mybir.dt.bfloat16
I32 = mybir.dt.int32
U32 = mybir.dt.uint32
ALU = mybir.AluOpType
ACT = mybir.ActivationFunctionType
AX = mybir.AxisListType.X

P = 128
D = 1024
KT = D // P
SEQ = 512
DEC_B, DEC_S = 8, 8
TOK = SEQ + DEC_B * DEC_S
TILES = [(0, 128), (128, 128), (256, 128), (384, 128), (512, 64)]
NT = len(TILES)
PAST, PAGE = 4096, 128
N_POOL = 320
SG, SP_, SW, CH = 64, 64, 16, 8
NCP = SEQ // CH
NC_ = NCP + DEC_B
NH, HD, NKV, HPK = 16, 64, 4, 4
SCALE = HD ** -0.5
CMP_H = 256
NCMP_S = PAST // 16 - 1
NCMP_P = SEQ // 16 - 1
NSEL = 65
NEG = -1e30
TINY = 1e-30
NG, EPG, NE, DE = 4, 8, 32, 256
RB = 64
NMORE = (TOK * 2) // (RB + 1)
NBLK = NE + NMORE
NPAIR = NE // 2
NROW = NBLK * RB
ALPHA = (2 * 2) ** 0.25
EPS = 1e-5
ARENA = 52000

TWO_PI = 2 * np.pi
C1 = 6.28125
C2 = float(np.float32(np.round((TWO_PI - C1) * 2 ** 22) / 2 ** 22))
C3 = float(np.float32(TWO_PI - C1 - C2))
INV_2PI = float(np.float32(1 / TWO_PI))
MAGIC = 12582912.0


def bc(ap, shape):
    return ap.to_broadcast(shape)


class Link:

    def __init__(self, eng, sem, base=0):
        self.eng, self.sem, self.n, self.count = eng, sem, base, 0

    def __call__(self, ins):
        ins.then_inc(self.sem, 1)
        self.n = self.n + 1
        self.count += 1
        self.eng.wait_ge(self.sem, self.n)


class Scope:

    spent = []

    def __init__(self, nc, name):
        self.nc, self.name, self.ctx = nc, name, ExitStack()

    def __enter__(self):
        self.ctx.__enter__()
        return self

    def __exit__(self, *a):
        return self.ctx.__exit__(*a)

    def sb(self, name, shape, dt=F32):
        return self.ctx.enter_context(self.nc.sbuf_tensor(f"{self.name}_{name}", shape, dt))

    def banks(self, n=8, dt=F32):
        return [self.ctx.enter_context(self.nc.psum_tensor(f"{self.name}_bank{i}", [P, 512], dt)) for i in range(n)]

    @staticmethod
    def handles(nc, names):
        made = [nc.alloc_semaphore(name=n) for n in names]
        Scope.spent.extend(made)
        return made

    def sem(self, name):
        return Scope.handles(self.nc, [f"{self.name}_{name}"])[0]


def recycle(nc):
    with nc.Block() as block:
        @block.gpsimd
        def _(pool):
            nc.clear_and_free_semaphores(Scope.spent)
    Scope.spent = []


def constants(nc, ident, jmat, eps):
    with Scope(nc, "const") as s:
        zeroed, made = s.sem("zeroed"), s.sem("made")
        with nc.Block() as block:
            @block.gpsimd
            def _(pool):
                pool.memset(ident[:, :], 0.0).then_inc(zeroed, 1)
                pool.memset(jmat[:, :], 0.0).then_inc(zeroed, 1)
                pool.memset(eps[:, :], EPS).then_inc(zeroed, 1)
                pool.wait_ge(zeroed, 3)
                pool.affine_select(out=ident[:, :], in_=ident[:, :], compare_op=ALU.not_equal, fill=1.0,
                                   base=0, pattern=[[-1, P]], channel_multiplier=1).then_inc(made, 1)
                pool.affine_select(out=jmat[:, 0:64], in_=jmat[:, 0:64], compare_op=ALU.not_equal, fill=-1.0,
                                   base=-64, pattern=[[-1, 64]], channel_multiplier=1).then_inc(made, 1)
                pool.affine_select(out=jmat[:, 64:P], in_=jmat[:, 64:P], compare_op=ALU.not_equal, fill=1.0,
                                   base=0, pattern=[[-1, 64]], channel_multiplier=1).then_inc(made, 1)
                pool.wait_ge(made, 3)


def s5_parameters(nc, A, ident, jmat, tab, x1, x2, y1, y2, R):
    with Scope(nc, "par") as s:
        at = [5376]

        def place(name, shape):
            at[0] += int(np.prod(shape[1:]))
            return R(at[0] - int(np.prod(shape[1:])), *shape[1:], np_=64)

        lr, li = place("lr", [64, 64]), place("li", [64, 64])
        ldt, dt = place("ldt", [64, 1]), place("dt", [64, 1])
        b_in, bb = place("b_in", [64, 2, 1024]), place("bb", [64, 2, 1024])
        c_in = place("c_in", [64, 16, 2, 64])
        tmp = place("tmp", [64, 1024])
        a1, th = place("a1", [64, 64]), place("th", [64, 64])
        rnd = place("rnd", [64, 9, 64])
        ang = place("ang", [64, 9, 64])
        sn, sh, mag = place("sn", [64, 9, 64]), place("sh", [64, 9, 64]), place("mag", [64, 9, 64])
        t20 = place("t20", [64, 20, 2, 64])
        den, rden, nr, t1, t2, zr, zi = (place(n, [64, 64]) for n in ("den", "rden", "nr", "t1", "t2", "zr", "zi"))
        bank = s.banks()
        loaded, dt_ready, a_ready, ang_ready, trig = (s.sem(n) for n in ("loaded", "dt_ready", "a_ready", "ang_ready", "trig"))
        dve, t20_ready, bb_ready, turned, moved, jdone = (s.sem(n) for n in ("dve", "t20_ready", "bb_ready", "turned", "moved", "jdone"))
        LOADS = [(lr[:, :], A["a_lambda_re"][0]), (li[:, :], A["a_lambda_im"][0]),
                 (ldt[:, :], A["a_log_dt"].rearrange("o g -> g o")),
                 (b_in[:, 0, :], A["a_b_re"][0].rearrange("g p w -> g (p w)")),
                 (b_in[:, 1, :], A["a_b_im"][0].rearrange("g p w -> g (p w)")),
                 (c_in[:, :, 0, :], A["a_c_re"][0]),
                 (c_in[:, :, 1, :], A["a_c_im"][0])]
        with nc.Block() as block:
            @block.sync
            def _(sp):
                for dst, src in LOADS:
                    sp.dma_start(dst, src).then_inc(loaded, 16)

            @block.scalar
            def _(act):
                act.wait_ge(loaded, 16 * len(LOADS))
                nc.scalar.activation(dt[:, :], ldt[:, :], ACT.Exp).then_inc(dt_ready, 1)
                act.wait_ge(a_ready, 1)
                for k in range(9):
                    nc.scalar.activation(mag[:, k, :], a1[:, :], ACT.Exp, scale=float(k)).then_inc(trig, 1)
                act.wait_ge(ang_ready, 1)
                nc.scalar.activation(sn[:, :, :], ang[:, :, :], ACT.Sin).then_inc(trig, 1)
                nc.scalar.activation(sh[:, :, :], ang[:, :, :], ACT.Sin, scale=0.5).then_inc(trig, 1)

            @block.vector
            def _(v):
                link = Link(v, dve)
                v.wait_ge(dt_ready, 1)
                v.tensor_scalar(a1[:, :], lr[:, :], dt[:, 0:1], None, ALU.mult).then_inc(a_ready, 1)
                link(v.tensor_scalar(th[:, :], li[:, :], dt[:, 0:1], None, ALU.mult))

                def reduce_angle(a, n):
                    link(v.tensor_scalar(n, a, INV_2PI, MAGIC, ALU.mult, ALU.add))
                    link(v.tensor_scalar(n, n, MAGIC, None, ALU.subtract))
                    for c in (C1, C2, C3):
                        link(v.scalar_tensor_tensor(out=a, in0=n, scalar=-c, in1=a, op0=ALU.mult, op1=ALU.add))

                reduce_angle(th[:, :], rnd[:, 0, :])
                for k in range(9):
                    ins = v.tensor_scalar(ang[:, k, :], th[:, :], float(k), None, ALU.mult)
                link(ins)
                reduce_angle(ang[:, :, :], rnd[:, :, :])
                v.engine_nop().then_inc(ang_ready, 1)
                link(v.tensor_tensor(t1[:, :], lr[:, :], lr[:, :], ALU.mult))
                link(v.tensor_tensor(t2[:, :], li[:, :], li[:, :], ALU.mult))
                link(v.tensor_tensor(den[:, :], t1[:, :], t2[:, :], ALU.add))
                link(v.reciprocal(rden[:, :], den[:, :]))
                v.wait_ge(trig, 11)
                link(v.tensor_tensor(sh[:, :, :], sh[:, :, :], sh[:, :, :], ALU.mult))
                link(v.tensor_scalar(sh[:, :, :], sh[:, :, :], -2.0, 1.0, ALU.mult, ALU.add))
                for ri in range(2):
                    v.tensor_tensor(t20[:, 0:9, ri, :], mag[:, :, :], sh[:, :, :], ALU.mult)
                    v.tensor_tensor(t20[:, 9:18, ri, :], mag[:, :, :], sn[:, :, :], ALU.mult)
                    v.tensor_copy(t20[:, 18, ri, :], ang[:, 8, :])
                    ins = v.tensor_copy(t20[:, 19, ri, :], mag[:, 8, :])
                link(ins)
                v.engine_nop().then_inc(t20_ready, 1)
                ai = t20[:, 10, 0, :]
                link(v.tensor_scalar(nr[:, :], t20[:, 1, 0, :], 1.0, None, ALU.subtract))
                link(v.tensor_tensor(t1[:, :], nr[:, :], lr[:, :], ALU.mult))
                link(v.tensor_tensor(t2[:, :], ai, li[:, :], ALU.mult))
                link(v.tensor_tensor(t1[:, :], t1[:, :], t2[:, :], ALU.add))
                link(v.tensor_tensor(zr[:, :], t1[:, :], rden[:, :], ALU.mult))
                link(v.tensor_tensor(t1[:, :], ai, lr[:, :], ALU.mult))
                link(v.tensor_tensor(t2[:, :], nr[:, :], li[:, :], ALU.mult))
                link(v.tensor_tensor(t1[:, :], t1[:, :], t2[:, :], ALU.subtract))
                link(v.tensor_tensor(zi[:, :], t1[:, :], rden[:, :], ALU.mult))
                zrb, zib = (bc(z[:, :].unsqueeze(2), [64, 64, 16]) for z in (zr, zi))
                pw = "g (p w) -> g p w"
                br, bi = (b_in[:, i, :].rearrange(pw, w=16) for i in range(2))
                b0, b1 = (bb[:, i, :].rearrange(pw, w=16) for i in range(2))
                tm = tmp[:, :].rearrange(pw, w=16)
                v.tensor_tensor(b0, br, zrb, ALU.mult)
                link(v.tensor_tensor(tm, bi, zib, ALU.mult))
                link(v.tensor_tensor(b0, b0, tm, ALU.subtract))
                v.tensor_tensor(b1, bi, zrb, ALU.mult)
                link(v.tensor_tensor(tm, br, zib, ALU.mult))
                link(v.tensor_tensor(b1, b1, tm, ALU.add))
                link(v.tensor_scalar(c_in[:, :, 1, :], c_in[:, :, 1, :], -1.0, None, ALU.mult))
                v.engine_nop().then_inc(bb_ready, 1)
                for i in range(3):
                    v.wait_ge(turned, i + 1)
                    n = 8 if i < 2 else 4
                    v.tensor_copy(tab[:, 8 * i:8 * i + n, :].rearrange("p k g -> p (k g)"),
                                  bank[i][:, 0:64 * n]).then_inc(moved, 1)
                for i in range(4):
                    dst = x1 if i < 2 else y1
                    h = i % 2
                    v.wait_ge(turned, 4 + i)
                    v.tensor_copy(dst[:, :, 8 * h:8 * h + 8],
                                  bank[3 + i][:, :].rearrange("p (w g) -> p g w", w=8)).then_inc(moved, 1)
                for i in range(4):
                    dst = x2 if i < 2 else y2
                    h = i % 2
                    v.wait_ge(jdone, i + 1)
                    v.tensor_copy(dst[:, 32 * h:32 * h + 32, :].rearrange("p g w -> p (g w)"),
                                  bank[i][:, :]).then_inc(moved, 1)
                v.wait_ge(moved, 11)

            @block.tensor
            def _(pe):
                pe.wait_ge(t20_ready, 1)
                for k in range(20):
                    ins = pe.transpose(bank[k // 8][:, 64 * (k % 8):64 * (k % 8) + 64],
                                       t20[:, k, :, :].rearrange("g r p -> g (r p)"), ident[0:64, 0:64])
                    if k in (7, 15, 19):
                        ins.then_inc(turned, 1)
                pe.wait_ge(bb_ready, 1)
                for which in range(2):
                    for w in range(16):
                        src = (bb[:, :, :].rearrange("g r (p w) -> g (r p) w", w=16)[:, :, w] if which == 0 else
                               c_in[:, w, :, :].rearrange("g r p -> g (r p)"))
                        j = 2 * which + w // 8
                        ins = pe.transpose(bank[3 + j][:, 64 * (w % 8):64 * (w % 8) + 64], src, ident[0:64, 0:64])
                        if w % 8 == 7:
                            ins.then_inc(turned, 1)
                pe.wait_ge(moved, 7)
                for i in range(4):
                    src = (x1 if i < 2 else y1)[:, 32 * (i % 2):32 * (i % 2) + 32, :].rearrange("p g w -> p (g w)")
                    pe.matmul(bank[i][:, :], jmat[:, :], src, start=True, stop=True).then_inc(jdone, 1)


_INS = ['x_prompt', 'x_sample', 'state_ssm', 'cache_cmp_kv', 'cache_slc_kv', 'cache_win_kv', 'page_table',
        'a_w_in', 'a_lambda_re', 'a_lambda_im', 'a_log_dt', 'a_b_re', 'a_b_im', 'a_c_re', 'a_c_im', 'a_d', 'a_w_glu',
        'kv_w', 'cmp_pe', 'cmp_w1', 'cmp_w2', 'b_w_qg', 'b_w_o',
        'moe_w_group', 'moe_w_expert', 'moe_w_gate_up', 'moe_w_down', 'ln_g', 'ln_b']


class Region:

    def __init__(self, arena):
        self.arena = arena

    def __call__(self, off, *shape, dt=F32, np_=P):
        n = int(np.prod(shape))
        if dt is BF16:
            assert n % 2 == 0
            v = self.arena[0:np_, off:off + n // 2].bitcast(BF16)
        else:
            v = self.arena[0:np_, off:off + n]
            if dt is not F32:
                v = v.bitcast(dt)
        if len(shape) == 1:
            return v
        names = "abcdef"[:len(shape)]
        return v.rearrange(f"p ({' '.join(names)}) -> p {' '.join(names)}", **dict(zip(names[1:], shape[1:])))


class Split:

    def __init__(self, n, full, used):
        self.n, self.full, self.used = n, full, used

    def claim(self, pe, job):
        old = job - self.n
        if old >= 0:
            pe.wait_ge(self.used[old % 2], old // 2 + 1)
        return job % self.n

    def done(self, ins):
        ins.then_inc(self.full, 1)

    def all_used(self, eng, jobs):
        if jobs > 0:
            eng.wait_ge(self.used[0], (jobs + 1) // 2)
        if jobs > 1:
            eng.wait_ge(self.used[1], jobs // 2)


S5_TAB, S5_X1, S5_X2, S5_Y1, S5_Y2, S5_FREE = 0, 1280, 2304, 3328, 4352, 5376


def s5_inputs(nc, A, R, ident, u_dram):
    with Scope(nc, "inp") as s:
        w = R(5376, KT, D)
        xT = R(13568, KT, CH, NC_)
        uT = R(18176, KT, CH * NC_)
        xin = R(22784, 2, D)
        bank = s.banks()
        w_in, stored = s.sem("w_in"), s.sem("stored")
        x_in = [s.sem(f"x_in{i}") for i in range(2)]
        full, used = s.sem("full"), (s.sem("used_v"), s.sem("used_a"))
        ring = Split(8, full, used)
        NJ = 2 * NT
        half = CH * NC_ // 2

        def x_rows(i):
            if i < 4:
                return A["x_prompt"][0, 128 * i:128 * i + 128, :]
            return A["x_sample"].rearrange("b t d -> (b t) d")

        def turn_out(eng_copy, i, h):
            n = TILES[i][1]
            job = 2 * i + h
            src = bank[job % 8][:, :].rearrange("p (k t) -> p k t", k=4)[:, :, 0:n].rearrange("p k (c s) -> p k c s", s=CH)
            dst = xT[:, 4 * h:4 * h + 4, :, 16 * i:16 * i + n // CH].rearrange("p k s c -> p k c s")
            return [eng_copy(dst[:, k], src[:, k]) for k in range(4)][-1]

        with nc.Block() as block:
            @block.sync
            def _(sp):
                for i in range(NT):
                    if i >= 2:
                        sp.wait_ge(full, 2 * (i - 1))
                    sp.dma_start(xin[0:TILES[i][1], i % 2, :], x_rows(i)).then_inc(x_in[i % 2], 16)
                    if i == 1:
                        sp.dma_start(w[:, :, :], A["a_w_in"][0].rearrange("(k p) n -> p k n", p=P)).then_inc(w_in, 16)
                for m in range(KT):
                    ring.all_used(sp, NJ + 2 * m + 2)
                    sp.dma_start(u_dram[P * m:P * m + P, :], uT[:, m, :]).then_inc(stored, 16)
                sp.wait_ge(stored, 16 * KT)

            @block.tensor
            def _(pe):
                for i, (_, n) in enumerate(TILES):
                    pe.wait_ge(x_in[i % 2], 16 * (i // 2 + 1))
                    for h in range(2):
                        b = ring.claim(pe, 2 * i + h)
                        for k in range(4):
                            ins = pe.transpose(bank[b][:, P * k:P * k + n],
                                               xin[0:n, i % 2, P * (4 * h + k):P * (4 * h + k + 1)], ident[0:n, 0:n])
                        ring.done(ins)
                pe.wait_ge(w_in, 16)
                ring.all_used(pe, NJ)
                xf = xT[:, :, :, :].rearrange("p k s c -> p k (s c)")
                for m in range(KT):
                    for n in range(2):
                        b = ring.claim(pe, NJ + 2 * m + n)
                        for k in range(KT):
                            ins = pe.matmul(bank[b][:, 0:half], w[:, k, P * m:P * m + P],
                                            xf[:, k, half * n:half * n + half], start=(k == 0), stop=(k == KT - 1))
                        ring.done(ins)

            def empty(eng, copy, me):
                for i in range(NT):
                    eng.wait_ge(full, 2 * i + me + 1)
                    turn_out(copy, i, me).then_inc(used[me], 1)
                for m in range(KT):
                    job = NJ + 2 * m + me
                    eng.wait_ge(full, job + 1)
                    copy(uT[:, m, half * me:half * me + half], bank[job % 8][:, 0:half]).then_inc(used[me], 1)

            @block.vector
            def _(v):
                empty(v, v.tensor_copy, 0)

            @block.scalar
            def _(act):
                empty(act, nc.scalar.copy, 1)


def s5_matrices(nc, A, R, ident, toep, et, o):
    with Scope(nc, "mat") as s:
        tab = R(S5_TAB, 20, 64)
        x1, x2, y1, y2 = (R(off, SG, SW) for off in (S5_X1, S5_X2, S5_Y1, S5_Y2))
        e = R(5376, SG, CH, SW)
        kb = R(38144, SG, SW)
        tt = R(29952, CH, SG, SW)
        tv, tp = R(39168, 2, SG, SW), R(41216, 2, SG, SW)
        bank = s.banks()
        dve, pool_, e_ready, zeroed, shifted = (s.sem(n) for n in ("dve", "pool", "e_ready", "zeroed", "shifted"))
        full, used = s.sem("full"), (s.sem("used_v"), s.sem("used_a"))
        k_full, k_used = s.sem("k_full"), s.sem("k_used")
        ring = Split(6, full, used)

        def coef(row):
            return bc(tab[:, row, :].unsqueeze(2), [P, SG, SW])

        with nc.Block() as block:
            @block.vector
            def _(v):
                link = Link(v, dve)
                for st in range(CH):
                    k = CH - 1 - st
                    v.tensor_tensor(tv[:, 0], x1, coef(k), ALU.mult)
                    link(v.tensor_tensor(tv[:, 1], x2, coef(9 + k), ALU.mult))
                    link(v.tensor_tensor(e[:, :, st, :], tv[:, 0], tv[:, 1], ALU.add))
                v.engine_nop().then_inc(e_ready, 1)
                for h in range(2):
                    v.wait_ge(k_full, h + 1)
                    v.tensor_copy(kb[:, 32 * h:32 * h + 32, :].rearrange("p g w -> p (g w)"),
                                  bank[6 + h][:, :]).then_inc(k_used, 1)
                for j in range(0, 16, 2):
                    v.wait_ge(full, j + 1)
                    v.tensor_copy(et[:, 4 * j:4 * j + 4, :].rearrange("p g m -> p (g m)"),
                                  bank[j % 6][:, :]).then_inc(used[0], 1)
                v.wait_ge(full, 16)
                for t in range(0, CH, 2):
                    if t == 0:
                        v.wait_ge(shifted, 16 * CH)
                    ins = v.tensor_copy(toep[:, :, t, :], tt[:, t, :, :])
                link(ins)

            @block.scalar
            def _(act):
                for j in range(1, 16, 2):
                    act.wait_ge(full, j + 1)
                    nc.scalar.copy(et[:, 4 * j:4 * j + 4, :].rearrange("p g m -> p (g m)"),
                                   bank[j % 6][:, :]).then_inc(used[1], 1)
                act.wait_ge(full, 16)
                act.wait_ge(shifted, 16 * CH)
                for t in range(1, CH, 2):
                    nc.scalar.copy(toep[:, :, t, :], tt[:, t, :, :]).then_inc(used[1], 1)

            @block.tensor
            def _(pe):
                pe.wait_ge(e_ready, 1)
                for g in range(SG):
                    ins = pe.matmul(bank[6 + g // 32][:, SW * (g % 32):SW * (g % 32) + SW],
                                    e[:, g, :, :].rearrange("p s w -> p (s w)"), y1[:, g, :],
                                    start=True, stop=True)
                    if g % 32 == 31:
                        ins.then_inc(k_full, 1)
                for j in range(16):
                    b = ring.claim(pe, j)
                    for q in range(4):
                        ins = pe.transpose(bank[b][:, P * q:P * q + P],
                                           e[:, 4 * j + q, :, :].rearrange("p s w -> p (s w)"), ident[:, :])
                    ring.done(ins)

            @block.gpsimd
            def _(pool):
                pool.memset(tt[:, :, :, :], 0.0).then_inc(zeroed, 1)
                link = Link(pool, pool_)
                for t in range(CH):
                    k = t + 1
                    pool.tensor_tensor(tp[:, 0], y1, coef(k), ALU.mult)
                    link(pool.tensor_tensor(tp[:, 1], y2, coef(9 + k), ALU.mult))
                    link(pool.tensor_tensor(o[:, :, t, :], tp[:, 0], tp[:, 1], ALU.subtract))

            @block.sync
            def _(sp):
                sp.wait_ge(zeroed, 1)
                sp.wait_ge(k_used, 2)
                for t in range(CH):
                    n = SW * (t + 1)
                    sp.dma_start(tt[0:n, t, :, :], kb[P - n:P, :, :]).then_inc(shifted, 16)


def s5_chunks(nc, A, R, toep, et, u_dram, hs):
    with Scope(nc, "chk") as s:
        tab = R(S5_TAB, 20, 64)
        uc, v_, y_ = R(29952, SG, NC_), R(34560, SG, NC_), R(39168, SG, NC_)
        cos_, sin_ = R(43776, SG, NCP), R(47872, SG, NCP)
        cidx = R(S5_X1, NCP)
        sh = R(21760 - 4096, SG, NCP)
        bank = s.banks()
        h_in, uin, dve, idx = (s.sem(n) for n in ("h_in", "uin", "dve", "idx"))
        full, used, ang_ready, sins, et_used = (s.sem(n) for n in ("full", "used", "ang_ready", "sins", "et_used"))
        GB = 7
        NB = -(-SG // GB)
        jobs = [(m, q, list(range(GB * q, min(GB * q + GB, SG)))) for m in range(2) for q in range(NB)]

        def flat(x):
            return x.rearrange("p g c -> p (g c)")

        with nc.Block() as block:
            @block.sync
            def _(sp):
                sp.dma_start(hs, A["state_ssm"]).then_inc(h_in, 16)
                for st in range(CH):
                    sp.dma_start(uc[SW * st:SW * st + SW, :, :],
                                 u_dram.rearrange("(g w) (s c) -> w s g c", w=SW, s=CH)[:, st]).then_inc(uin, 16)
                sp.wait_ge(h_in, 16)

            @block.tensor
            def _(pe):
                pe.wait_ge(uin, 16 * CH)
                for j, (m, q, gs) in enumerate(jobs):
                    if j >= 8:
                        pe.wait_ge(used, j - 7)
                    for n, g in enumerate(gs):
                        lhs = et[:, g] if m == 0 else toep[:, g].rearrange("p t w -> p (t w)")
                        ins = pe.matmul(bank[j % 8][:, NC_ * n:NC_ * n + NC_], lhs, uc[:, g, :], start=True, stop=True)
                    ins.then_inc(full, 1)

            @block.scalar
            def _(act):
                for j, (m, q, gs) in enumerate(jobs):
                    act.wait_ge(full, j + 1)
                    dst = (v_, y_)[m]
                    nc.scalar.copy(flat(dst[:, gs[0]:gs[-1] + 1, :]), bank[j % 8][:, 0:NC_ * len(gs)]).then_inc(used, 1)
                act.wait_ge(ang_ready, 1)
                nc.scalar.activation(sh, cos_, ACT.Sin, scale=0.5).then_inc(sins, 1)
                nc.scalar.activation(sin_, cos_, ACT.Sin).then_inc(sins, 1)

            @block.gpsimd
            def _(pool):
                pool.iota(cidx, pattern=[[1, NCP]], base=0, channel_multiplier=0,
                          allow_small_or_imprecise_dtypes=True).then_inc(idx, 1)

            @block.vector
            def _(v):
                link = Link(v, dve)
                v.wait_ge(idx, 1)
                link(v.tensor_tensor(cos_, bc(tab[:, 18, :].unsqueeze(2), [P, SG, NCP]),
                                     bc(cidx.unsqueeze(1), [P, SG, NCP]), ALU.mult))
                link(v.tensor_scalar(sin_, cos_, INV_2PI, MAGIC, ALU.mult, ALU.add))
                link(v.tensor_scalar(sin_, sin_, MAGIC, None, ALU.subtract))
                for c in (C1, C2, C3):
                    link(v.scalar_tensor_tensor(out=cos_, in0=sin_, scalar=-c, in1=cos_, op0=ALU.mult, op1=ALU.add))
                v.engine_nop().then_inc(ang_ready, 1)
                v.wait_ge(sins, 2)
                link(v.tensor_tensor(cos_, sh, sh, ALU.mult))
                link(v.tensor_scalar(cos_, cos_, -2.0, 1.0, ALU.mult, ALU.add))


def s5_scan(nc, R, jmat, hs, ho):
    with Scope(nc, "scan") as s:
        tab = R(S5_TAB, 20, 64)
        v_ = R(34560, SG, NC_)
        cos_, sin_ = R(43776, SG, NCP), R(47872, SG, NCP)
        rho, gc, g_, t_ = R(5376, SG, NCP), R(9472, SG, NCP), R(13568, SG, NCP), R(17664, SG, NCP)
        hp = R(29952, SG, NC_)
        th = R(S5_X2, DEC_B, SG)
        bank = s.banks()
        dve, turned, gs_ready, rho_ready, pooled = (s.sem(n) for n in ("dve", "turned", "gs_ready", "rho_ready", "pooled"))
        h_read = s.sem("h_read")
        Q = 8
        with nc.Block() as block:
            @block.tensor
            def _(pe):
                for q in range(8):
                    pe.matmul(bank[q][:, :], jmat[:, :], v_[:, Q * q:Q * q + Q, 0:NCP], start=True, stop=True).then_inc(turned, 1)
                for q in range(8):
                    pe.wait_ge(gs_ready, q + 1)
                    pe.matmul(bank[q][:, :], jmat[:, :], t_[:, Q * q:Q * q + Q, :], start=True, stop=True).then_inc(turned, 1)
                pe.wait_ge(h_read, 1)
                pe.matmul(bank[0][:, :], jmat[:, :], hs.rearrange("p b g -> p (b g)"), start=True, stop=True).then_inc(turned, 1)

            @block.gpsimd
            def _(pool):
                pool.tensor_copy(rho, bc(tab[:, 19, :].unsqueeze(2), [P, SG, NCP])).then_inc(pooled, 1)
                pool.wait_ge(pooled, 1)
                pool.memset(rho[:, :, 0:1], 0.0).then_inc(rho_ready, 1)
                pool.memset(hp[:, :, 0:1], 0.0).then_inc(rho_ready, 1)
                pool.tensor_copy(hp[:, :, NCP:NC_], hs.rearrange("p b g -> p g b")).then_inc(rho_ready, 1)

            @block.vector
            def _(v):
                link = Link(v, dve)
                link(v.tensor_tensor(g_, v_[:, :, 0:NCP], cos_, ALU.mult))
                for q in range(8):
                    g8 = slice(Q * q, Q * q + Q)
                    v.wait_ge(turned, q + 1)
                    ins = v.tensor_tensor(t_[:, g8, :], bank[q][:, :].rearrange("p (g c) -> p g c", g=Q), sin_[:, g8, :], ALU.mult)
                link(ins)
                link(v.tensor_tensor(g_, g_, t_, ALU.subtract))
                v.wait_ge(rho_ready, 3)
                flat = "p g c -> p (g c)"
                link(v.tensor_tensor_scan(gc.rearrange(flat), rho.rearrange(flat), g_.rearrange(flat), 0.0, ALU.mult, ALU.add))
                for q in range(8):
                    g8 = slice(Q * q, Q * q + Q)
                    v.tensor_tensor(t_[:, g8, :], gc[:, g8, :], sin_[:, g8, :], ALU.mult).then_inc(gs_ready, 1)
                link(v.tensor_tensor(g_, gc, cos_, ALU.mult))
                for q in range(8):
                    g8 = slice(Q * q, Q * q + Q)
                    v.wait_ge(turned, 9 + q)
                    src = bank[q][:, :].rearrange("p (g c) -> p g c", g=Q)
                    v.tensor_tensor(hp[:, g8, 1:NCP], g_[:, g8, 0:NCP - 1], src[:, :, 0:NCP - 1], ALU.add)
                    last = v.tensor_tensor(ho[:, 8, g8], g_[:, g8, NCP - 1], src[:, :, NCP - 1], ALU.add)
                    if q == 0:
                        last.then_inc(h_read, 1)
                v.wait_ge(turned, 17)
                a8r, a8i = (bc(tab[:, r, :].unsqueeze(1), [P, DEC_B, SG]) for r in (8, 17))
                v.tensor_tensor(ho[:, 0:8, :], hs, a8r, ALU.mult)
                link(v.tensor_tensor(th, bank[0][:, :].rearrange("p (b g) -> p b g", b=DEC_B), a8i, ALU.mult))
                link(v.tensor_tensor(ho[:, 0:8, :], ho[:, 0:8, :], th, ALU.add))
                link(v.tensor_tensor(ho[:, 0:8, :], ho[:, 0:8, :], v_[:, :, NCP:NC_].rearrange("p g b -> p b g"), ALU.add))


def s5_outputs(nc, R, o, y_dram, ho, h_out):
    with Scope(nc, "out") as s:
        hp, y_ = R(29952, SG, NC_), R(39168, SG, NC_)
        bank = s.banks()
        full, used, stored = s.sem("full"), s.sem("used"), s.sem("stored")
        GB = 7
        NB = -(-SG // GB)
        with nc.Block() as block:
            @block.sync
            def _(sp):
                sp.dma_start(h_out, ho).then_inc(stored, 16)
                sp.wait_ge(used, NB)
                for st in range(CH):
                    sp.dma_start(y_dram.rearrange("(g w) (s c) -> w s g c", w=SW, s=CH)[:, st],
                                 y_[SW * st:SW * st + SW, :, :]).then_inc(stored, 16)
                sp.wait_ge(stored, 16 * (CH + 1))

            @block.tensor
            def _(pe):
                for q in range(NB):
                    if q >= 8:
                        pe.wait_ge(used, q - 7)
                    for n, g in enumerate(range(GB * q, min(GB * q + GB, SG))):
                        ins = pe.matmul(bank[q % 8][:, NC_ * n:NC_ * n + NC_], o[:, g].rearrange("p t w -> p (t w)"),
                                        hp[:, g, :], start=True, stop=True)
                    ins.then_inc(full, 1)

            @block.vector
            def _(v):
                for q in range(NB):
                    a, b = GB * q, min(GB * q + GB, SG)
                    v.wait_ge(full, q + 1)
                    yy = y_[:, a:b, :].rearrange("p g c -> p (g c)")
                    v.tensor_tensor(yy, bank[q % 8][:, 0:NC_ * (b - a)], yy, ALU.add).then_inc(used, 1)


X_OFF, XT_OFF, GB_OFF, FREE = 0, 5120, 9728, 11776


def glu(nc, A, R, x, u_dram, y_dram):
    with Scope(nc, "glu") as s:
        yT, uT = R(FREE, KT, CH, NC_), R(FREE + 4608, KT, CH, NC_)
        gT = R(FREE + 9216, KT, NC_, CH)
        w = R(FREE + 13824, KT, 2 * D)
        sg = R(FREE + 30208, 2, 512)
        fv = R(FREE + 31232, 2, 512)
        d = R(FREE + 32256, KT)
        bank = s.banks()
        names = ("x_in", "d_in", "w_in", "dve", "skip_ready", "g_ready", "full", "sig", "used", "fused")
        x_in, d_in, w_in, dve, skip_ready, g_ready, full, sig, used, fused = (s.sem(n) for n in names)
        y_in = [s.sem(f"y_in{h}") for h in range(2)]
        jobs = [(i, h) for i in range(NT) for h in range(2)]
        with nc.Block() as block:
            @block.sync
            def _(sp):
                sp.dma_start(d, A["a_d"]).then_inc(d_in, 16)
                for h in range(2):
                    ks = slice(4 * h, 4 * h + 4)
                    for dst, src in ((yT, y_dram), (uT, u_dram)):
                        sp.dma_start(dst[:, ks].rearrange("p k s c -> p k (s c)"),
                                     src.rearrange("(k p) t -> p k t", p=P)[:, ks]).then_inc(y_in[h], 16)
                for h in range(2):
                    sp.dma_start(w[:, 4 * h:4 * h + 4, :],
                                 A["a_w_glu"][0].rearrange("(k p) n -> p k n", p=P)[:, 4 * h:4 * h + 4]).then_inc(w_in, 16)
                sp.dma_start(x[:, 0:4, :], A["x_prompt"][0].rearrange("(i p) d -> p i d", p=P)).then_inc(x_in, 16)
                sp.dma_start(x[0:64, 4, :], A["x_sample"].rearrange("b t d -> (b t) d")).then_inc(x_in, 16)

            @block.vector
            def _(v):
                v.wait_ge(d_in, 16)
                for k in range(KT):
                    v.wait_ge(y_in[k // 4], 32)
                    v.scalar_tensor_tensor(out=yT[:, k].rearrange("p s c -> p (s c)"), in0=uT[:, k].rearrange("p s c -> p (s c)"),
                                           scalar=d[:, k:k + 1], in1=yT[:, k].rearrange("p s c -> p (s c)"),
                                           op0=ALU.mult, op1=ALU.add).then_inc(skip_ready, 1)
                v.wait_ge(x_in, 32)
                for j, (i, h) in enumerate(jobs):
                    n = TILES[i][1]
                    xs = x[0:n, i, 512 * h:512 * h + 512]
                    v.wait_ge(sig, j + 1)
                    v.tensor_tensor(fv[0:n, j % 2], bank[(2 * j) % 8][0:n, :], sg[0:n, j % 2], ALU.mult).then_inc(used, 1)
                    v.wait_ge(used, j + 1)
                    v.scalar_tensor_tensor(out=xs, in0=xs, scalar=ALPHA, in1=fv[0:n, j % 2],
                                           op0=ALU.mult, op1=ALU.add).then_inc(fused, 1)

            @block.scalar
            def _(act):
                for k in range(KT):
                    act.wait_ge(skip_ready, k + 1)
                    nc.scalar.activation(gT[:, k].rearrange("p c s -> p s c"), yT[:, k], ACT.Gelu_apprx_tanh).then_inc(g_ready, 1)
                for j, (i, h) in enumerate(jobs):
                    n = TILES[i][1]
                    act.wait_ge(full, j + 1)
                    if j >= 2:
                        act.wait_ge(used, j - 1)
                    nc.scalar.activation(sg[0:n, j % 2], bank[(2 * j + 1) % 8][0:n, :], ACT.Sigmoid).then_inc(sig, 1)

            @block.tensor
            def _(pe):
                pe.wait_ge(g_ready, KT)
                pe.wait_ge(w_in, 32)
                for j, (i, h) in enumerate(jobs):
                    t0, n = TILES[i]
                    if j >= 4:
                        pe.wait_ge(used, j - 3)
                    for part in range(2):
                        for k in range(KT):
                            ins = pe.matmul(bank[(2 * j + part) % 8][0:n, :],
                                            gT[:, k].rearrange("p c s -> p (c s)")[:, t0:t0 + n],
                                            w[:, k, D * part + 512 * h:D * part + 512 * h + 512],
                                            start=(k == 0), stop=(k == KT - 1))
                    ins.then_inc(full, 1)


def layer_norm(nc, A, R, name, layer, which, ident, x, outs=None, x_dram=None, turn=True, weights=None):
    with Scope(nc, name) as s:
        xT = R(XT_OFF, KT, TOK)
        gb = R(GB_OFF, 2, D)
        st = R(FREE, NT, 2, 6)
        mv = R(FREE + 64, NT, 2)
        sd = R(FREE + 80, NT)
        rs = R(FREE + 88, NT)
        bank = s.banks()
        gb_in, dve, stats, root, inv, normed, scaled, shifted, full, used, stored = (
            s.sem(n) for n in ("gb_in", "dve", "stats", "root", "inv", "normed", "scaled", "shifted", "full", "used", "stored"))
        with nc.Block() as block:
            @block.sync
            def _(sp):
                sp.dma_start(gb[:, 0, :], A["ln_g"][layer, which].partition_broadcast(P)).then_inc(gb_in, 16)
                sp.dma_start(gb[:, 1, :], A["ln_b"][layer, which].partition_broadcast(P)).then_inc(gb_in, 16)
                if weights is not None:
                    weights.load_first(sp)
                n_st = 0
                for i, (t0, n) in enumerate(TILES):
                    sp.wait_ge(shifted, i + 1)
                    if x_dram is not None:
                        sp.dma_start(x_dram[t0:t0 + n, :], x[0:n, i, :]).then_inc(stored, 16)
                        n_st += 1
                    if outs is not None:
                        dst = outs[0][0, t0:t0 + n, :] if i < 4 else outs[1].rearrange("b t d -> (b t) d")
                        sp.dma_start(dst, x[0:n, i, :]).then_inc(stored, 16)
                        n_st += 1
                sp.wait_ge(stored, 16 * n_st)

            @block.vector
            def _(v):
                link = Link(v, dve)
                for i, (t0, n) in enumerate(TILES):
                    for h in range(2):
                        ins = v.bn_stats(st[0:n, i, h, :], x[0:n, i, 512 * h:512 * h + 512])
                    link(ins)
                    v.bn_aggr(mv[0:n, i, :], st[0:n, i].rearrange("p h k -> p (h k)")).then_inc(stats, 1)
                for i, (t0, n) in enumerate(TILES):
                    v.wait_ge(root, i + 1)
                    link(v.reciprocal(rs[0:n, i:i + 1], sd[0:n, i:i + 1]))
                    v.tensor_scalar(x[0:n, i, :], x[0:n, i, :], mv[0:n, i, 0:1], rs[0:n, i:i + 1],
                                    ALU.subtract, ALU.mult).then_inc(normed, 1)
                    if i == 0:
                        v.wait_ge(gb_in, 32)
                    v.wait_ge(normed, i + 1)
                    v.tensor_tensor(x[0:n, i, :], x[0:n, i, :], gb[0:n, 0, :], ALU.mult).then_inc(scaled, 1)

            @block.gpsimd
            def _(pool):
                for i, (t0, n) in enumerate(TILES):
                    pool.wait_ge(scaled, i + 1)
                    pool.tensor_tensor(x[0:n, i, :], x[0:n, i, :], gb[0:n, 1, :], ALU.add).then_inc(shifted, 1)

            @block.tensor
            def _(pe):
                if not turn:
                    return
                for i, (t0, n) in enumerate(TILES):
                    pe.wait_ge(shifted, i + 1)
                    for h in range(2):
                        j = 2 * i + h
                        if j >= 8:
                            pe.wait_ge(used, j - 7)
                        for k in range(4):
                            ins = pe.transpose(bank[j % 8][:, P * k:P * k + n],
                                               x[0:n, i, P * (4 * h + k):P * (4 * h + k) + P], ident[0:n, 0:n])
                        ins.then_inc(full, 1)

            @block.scalar
            def _(act):
                for i, (t0, n) in enumerate(TILES):
                    act.wait_ge(stats, i + 1)
                    nc.scalar.activation(sd[0:n, i:i + 1], mv[0:n, i, 1:2], ACT.Sqrt, bias=A["eps"][0:n, 0:1]).then_inc(root, 1)
                if not turn:
                    return
                for i, (t0, n) in enumerate(TILES):
                    for h in range(2):
                        j = 2 * i + h
                        act.wait_ge(full, j + 1)
                        nc.scalar.copy(xT[:, 4 * h:4 * h + 4, t0:t0 + n],
                                       bank[j % 8][:, :].rearrange("p (k t) -> p k t", k=4)[:, :, 0:n]).then_inc(used, 1)


RT_OFF = FREE + 0
RT_MORE_OFF = FREE + NPAIR
BE_OFF = FREE + 50
MORE_OFF = FREE + 70
DST_OFF = FREE + 96
WT_OFF = FREE + 112
W_SIZE = KT * 2 * DE + 2 * D
W_OFF = ARENA - 4 * W_SIZE
MOE_FREE = FREE + 128
BIG = 1e30


def route(nc, R, name, weights, row_tok):
    with Scope(nc, name) as s:
        xT = R(XT_OFF, KT, TOK)
        rt, rt_more = R(RT_OFF, NPAIR, dt=I32), R(RT_MORE_OFF, NMORE, dt=I32, np_=RB)
        be, more = R(BE_OFF, NMORE, dt=I32), R(MORE_OFF, 1, dt=I32)
        dst, wt = R(DST_OFF, NT, 2, dt=I32), R(WT_OFF, 2, NT)
        at = [MOE_FREE]

        def place(*shape, dt=F32, np_=P):
            n = int(np.prod(shape))
            at[0] += n + n % 2
            return R(at[0] - n - n % 2, *shape, dt=dt, np_=np_)

        place(KT, NG + NE)
        wr = weights.router
        lg, le, le2 = place(NT, NG), place(NT, NE), place(NT, NE)
        ig, ie, ib, i64 = place(NT, NG), place(NT, NE), place(NMORE), place(NE)
        keyg, keye = place(NT, NG), place(NT, NE)
        ohg, oh = place(NT, NG), place(2, NT, NE)
        top = place(3, NT)
        low, gsum, gw, dif, ed, inv = (place(NT) for _ in range(6))
        ex = place(NT, NG)
        both = place(NT, NE)
        tri, ones = place(P), place(P)
        total, nblk, pend, base, one32 = (place(NE) for _ in range(5))
        rank, pos, sel, over = place(NT, NE), place(NT, NE), place(NT, NE), place(NT, NE)
        dstf = place(NT, 2)
        cmpb, bef = place(NMORE, NE), place(NMORE)
        tok = place(NT, dt=I32)
        zero = place(NBLK, dt=I32, np_=RB)
        assert at[0] <= W_OFF
        bank = s.banks(3)
        made, zeroed, cleared, logit, dve, lmoved, exp_in, exp_out, ohs, ranked, dests, scattered, rt_in = (
            s.sem(n) for n in ("made", "zeroed", "cleared", "logit", "dve", "lmoved", "exp_in", "exp_out", "ohs",
                               "ranked", "dests", "scattered", "rt_in"))
        with nc.Block() as block:
            @block.scalar
            def _(act):
                act.wait_ge(zeroed, 1)
                act.dma_start(row_tok.rearrange("(p b) o -> p (b o)", p=RB), zero).then_inc(cleared, 16)
                act.wait_ge(exp_in, 1)
                nc.scalar.activation(ex, ex, ACT.Exp).then_inc(exp_out, 1)
                act.wait_ge(exp_in, 2)
                nc.scalar.activation(ed, dif, ACT.Exp).then_inc(exp_out, 1)
                act.wait_ge(scattered, 16 * 2 * NT)
                act.dma_start(rt, row_tok[0:NE * RB].rearrange("(b r) o -> r (b o)", r=P), allow_slow_non_contiguous=True).then_inc(rt_in, 16)
                act.dma_start(rt_more, row_tok[NE * RB:NROW].rearrange("(b r) o -> r (b o)", r=RB), allow_slow_non_contiguous=True).then_inc(rt_in, 16)
                act.wait_ge(rt_in, 32)

            @block.gpsimd
            def _(pool):
                pool.memset(zero, 0).then_inc(zeroed, 1)
                pool.iota(ig, pattern=[[0, NT], [1, NG]], base=-64, channel_multiplier=0,
                          allow_small_or_imprecise_dtypes=True).then_inc(made, 1)
                pool.iota(ie, pattern=[[0, NT], [1, NE]], base=-64, channel_multiplier=0,
                          allow_small_or_imprecise_dtypes=True).then_inc(made, 1)
                pool.iota(ib, pattern=[[1, NMORE]], base=0, channel_multiplier=0,
                          allow_small_or_imprecise_dtypes=True).then_inc(made, 1)
                pool.iota(i64, pattern=[[RB, NE]], base=0, channel_multiplier=0,
                          allow_small_or_imprecise_dtypes=True).then_inc(made, 1)
                pool.iota(tok, pattern=[[P, NT]], base=0, channel_multiplier=1).then_inc(made, 1)
                pool.memset(ones, 1.0).then_inc(made, 1)
                pool.memset(one32, 1.0).then_inc(made, 1)
                pool.memset(lg, 0.0).then_inc(made, 1)
                pool.memset(le, 0.0).then_inc(made, 1)
                pool.wait_ge(made, 9)
                pool.affine_select(out=tri, in_=ones, compare_op=ALU.is_gt, fill=0.0, base=0,
                                   pattern=[[1, P]], channel_multiplier=-1).then_inc(made, 1)
                pool.wait_ge(dests, 1)
                pool.wait_ge(cleared, 16)
                for i, (t0, n) in enumerate(TILES):
                    for k in range(2):
                        pool.indirect_dma_start(out=row_tok, out_offset=bass.IndirectOffsetOnAxis(ap=dst[0:n, i, k:k + 1], axis=0),
                                                in_=tok[0:n, i:i + 1], in_offset=None).then_inc(scattered, 16)
                pool.wait_ge(scattered, 16 * 2 * NT)

            @block.tensor
            def _(pe):
                pe.wait_ge(weights.router_in, 32)
                for i, (t0, n) in enumerate(TILES):
                    for k in range(KT):
                        ins = pe.matmul(bank[0][0:n, 36 * i:36 * i + 36], xT[:, k, t0:t0 + n], wr[:, k, :],
                                        start=(k == 0), stop=(k == KT - 1))
                ins.then_inc(logit, 1)
                pe.wait_ge(ohs, 1)
                pe.wait_ge(made, 10)
                for i in range(NT):
                    for q in range(i + 1):
                        ins = pe.matmul(bank[1][:, NE * i:NE * i + NE], tri if q == i else ones, both[:, q, :],
                                        start=(q == 0), stop=(q == i))
                for q in range(NT):
                    ins = pe.matmul(bank[2][:, 0:NE], ones, both[:, q, :], start=(q == 0), stop=(q == NT - 1))
                ins.then_inc(ranked, 1)

            @block.vector
            def _(v):
                link = Link(v, dve)

                def first_largest(vals, idx, key, one, most, n):
                    link(v.tensor_reduce(most, vals, AX, ALU.max))
                    link(v.tensor_tensor(key, vals, bc(most.unsqueeze(2), [P, NT, n]), ALU.is_equal))
                    link(v.tensor_tensor(key, key, idx, ALU.mult))
                    link(v.tensor_reduce(low, key, AX, ALU.min))
                    link(v.tensor_tensor(one, idx, bc(low.unsqueeze(2), [P, NT, n]), ALU.is_equal))

                v.wait_ge(made, 9)
                v.wait_ge(logit, 1)
                src = bank[0][:, 0:36 * NT].rearrange("p (i n) -> p i n", i=NT)
                for np_, sl in ((P, slice(0, 4)), (64, slice(4, 5))):
                    v.tensor_copy(lg[0:np_, sl], src[0:np_, sl, 0:NG])
                    ins = v.tensor_copy(le[0:np_, sl], src[0:np_, sl, NG:36])
                link(ins)
                first_largest(lg, ig, keyg, ohg, top[:, 2], NG)
                link(v.tensor_tensor(ex, lg, bc(top[:, 2].unsqueeze(2), [P, NT, NG]), ALU.subtract))
                v.engine_nop().then_inc(exp_in, 1)
                link(v.tensor_scalar(keyg, ohg, 1.0, BIG, ALU.subtract, ALU.mult))
                for i in range(NT):
                    ins = v.tensor_tensor(le2[:, i, :].rearrange("p (g e) -> p g e", g=NG), le[:, i, :].rearrange("p (g e) -> p g e", g=NG),
                                          bc(keyg[:, i, :].unsqueeze(2), [P, NG, EPG]), ALU.add)
                link(ins)
                first_largest(le2, ie, keye, oh[:, 0], top[:, 0], NE)
                flat = "p i e -> p (i e)"
                link(v.scalar_tensor_tensor(out=le2.rearrange(flat), in0=oh[:, 0].rearrange(flat), scalar=-2 * BIG,
                                            in1=le2.rearrange(flat), op0=ALU.mult, op1=ALU.add))
                first_largest(le2, ie, keye, oh[:, 1], top[:, 1], NE)
                link(v.tensor_tensor(dif, top[:, 1], top[:, 0], ALU.subtract))
                v.engine_nop().then_inc(exp_in, 1)
                link(v.tensor_tensor(both, oh[:, 0], oh[:, 1], ALU.add))
                link(v.memset(both[64:P, 4, :], 0.0))
                v.engine_nop().then_inc(ohs, 1)
                v.wait_ge(exp_out, 2)
                link(v.tensor_reduce(gsum, ex, AX, ALU.add))
                link(v.reciprocal(gw, gsum))
                link(v.tensor_scalar(dif, ed, 1.0, None, ALU.add))
                link(v.reciprocal(inv, dif))
                link(v.tensor_tensor(wt[:, 0], gw, inv, ALU.mult))
                link(v.tensor_tensor(wt[:, 1], wt[:, 0], ed, ALU.mult))
                v.wait_ge(ranked, 1)
                link(v.tensor_copy(total, bank[2][:, 0:NE]))
                link(v.tensor_copy(rank, bank[1][:, 0:NE * NT].rearrange("p (i e) -> p i e", i=NT)))
                link(v.tensor_scalar(nblk, total, float(RB), None, ALU.is_gt))
                for q in range(2, -(-TOK // RB)):
                    link(v.scalar_tensor_tensor(out=nblk, in0=total, scalar=float(RB * q), in1=nblk, op0=ALU.is_gt, op1=ALU.add))
                link(v.tensor_tensor_scan(pend, one32, nblk, 0.0, ALU.mult, ALU.add))
                link(v.tensor_tensor(base, pend, nblk, ALU.subtract))
                link(v.tensor_scalar(base, base, float(RB), float(NE * RB - RB), ALU.mult, ALU.add))
                link(v.tensor_tensor(base, base, i64, ALU.subtract))
                link(v.tensor_scalar(over, rank, float(RB), None, ALU.is_ge))
                link(v.tensor_tensor(over, over, bc(base.unsqueeze(1), [P, NT, NE]), ALU.mult))
                link(v.tensor_tensor(pos, rank, bc(i64.unsqueeze(1), [P, NT, NE]), ALU.add))
                link(v.tensor_tensor(pos, pos, over, ALU.add))
                for k in range(2):
                    link(v.tensor_tensor(sel, oh[:, k], pos, ALU.mult))
                    link(v.tensor_reduce(dstf[:, :, k], sel, AX, ALU.add))
                link(v.tensor_copy(dst, dstf))
                v.engine_nop().then_inc(dests, 1)
                link(v.tensor_copy(more, pend[:, NE - 1:NE]))
                link(v.tensor_tensor(cmpb, bc(pend.unsqueeze(1), [P, NMORE, NE]), bc(ib.unsqueeze(2), [P, NMORE, NE]), ALU.is_le))
                link(v.tensor_reduce(bef, cmpb, AX, ALU.add))
                link(v.tensor_scalar(be, bef, float(NE - 1), None, ALU.min))


class Weights:

    def __init__(self, nc, A, R, layer):
        self.A, self.layer = A, layer
        self.router = R(MOE_FREE, KT, NG + NE)
        self.gate_up = [[R(W_OFF + W_SIZE * (2 * q + e), KT, 2 * DE) for e in range(2)] for q in range(2)]
        self.down = [[R(W_OFF + W_SIZE * (2 * q + e) + KT * 2 * DE, 2, D) for e in range(2)] for q in range(2)]
        self.router_in, *ins = Scope.handles(nc, [f"{n}{layer}_in" for n in ("router", "gate_up_a", "gate_up_b", "down_a", "down_b")])
        self.gate_up_in, self.down_in = ins[0:2], ins[2:4]

    def load_gate_up(self, sp, pair, q):
        for e in range(2):
            src = self.A["moe_w_gate_up"][self.layer, bass.ds(2 * pair + e, 1)].rearrange("o (k p) n -> p (o k) n", p=P)
            sp.dma_start(self.gate_up[q][e], src).then_inc(self.gate_up_in[q], 16)

    def load_down(self, sp, pair, q):
        for e in range(2):
            src = self.A["moe_w_down"][self.layer, bass.ds(2 * pair + e, 1)].rearrange("o (k p) n -> p (o k) n", p=P)
            sp.dma_start(self.down[q][e], src).then_inc(self.down_in[q], 16)

    def load_first(self, sp):
        A, layer = self.A, self.layer
        sp.dma_start(self.router[:, :, 0:NG], A["moe_w_group"][layer].rearrange("(k p) n -> p k n", p=P)).then_inc(self.router_in, 16)
        sp.dma_start(self.router[:, :, NG:], A["moe_w_expert"][layer].rearrange("(k p) n -> p k n", p=P)).then_inc(self.router_in, 16)
        self.load_gate_up(sp, 0, 0)
        self.load_down(sp, 0, 0)


def experts(nc, R, name, ident, weights, x_dram, y_rows):
    with Scope(nc, name) as s:
        rt = R(RT_OFF, NPAIR, dt=I32)
        at = [MOE_FREE]

        def place(*shape, dt=F32):
            n = int(np.prod(shape))
            at[0] += n
            return R(at[0] - n, *shape, dt=dt)

        xg = [place(D) for _ in range(2)]
        xgT = [place(KT, P) for _ in range(2)]
        idx = [place(2, dt=I32) for _ in range(2)]
        sg, h, hT = place(DE), place(DE), [place(2, P) for _ in range(2)]
        y = [place(D) for _ in range(2)]
        assert at[0] <= W_OFF
        bank = s.banks()
        BX, BG, BH, BY = bank[0:2], bank[2:4], bank[4], bank[5:7]
        x_in = [s.sem(f"x_in{i}") for i in range(2)]
        y_out = [s.sem(f"y_out{i}") for i in range(2)]
        gather_go, own_wait = s.sem("gather_go"), s.sem("own_wait")
        idx_ready, x_turned, xT_ready, gu_done, sg_ready, h_ready, h_turned, hT_ready, dn_done, y0_ready, y1_ready = (
            s.sem(n) for n in ("idx_ready", "x_turned", "xT_ready", "gu_done", "sg_ready", "h_ready", "h_turned", "hT_ready",
                               "dn_done", "y0_ready", "y1_ready"))
        TURNS = NPAIR // 2

        def pairs(eng, body, last=False):
            for q in range(2):
                body(0, q)
            with eng.Fori(1, TURNS - last) as i:
                for q in range(2):
                    body(i, q)
            if last:
                for q in range(2):
                    body(TURNS - 1, q)

        def after(eng, sem, n):
            if not isinstance(n, int) or n > 0:
                eng.wait_ge(sem, n)

        with nc.Block() as block:
            @block.sync
            def _(sp):
                weights.load_gate_up(sp, 1, 1)
                weights.load_down(sp, 1, 1)
                with sp.Fori(1, TURNS) as i:
                    for q in range(2):
                        j = 2 * i + q
                        sp.wait_ge(gu_done, j - 1)
                        weights.load_gate_up(sp, j, q)
                        sp.wait_ge(dn_done, j - 1)
                        weights.load_down(sp, j, q)

            @block.gpsimd
            def _(pool):
                def gather(i, q):
                    j = 2 * i + q
                    after(pool, x_turned, j - 1)
                    pool.tensor_copy(idx[q][:, 0:1], rt[:, bass.ds(j, 1)]).then_inc(idx_ready, 1)
                    pool.wait_ge(idx_ready, j + 1)
                    pool.sem_inc(gather_go, 1)
                    pool.indirect_dma_start(out=xg[q], out_offset=None, in_=x_dram,
                                            in_offset=bass.IndirectOffsetOnAxis(ap=idx[q][:, 0:1], axis=0)).then_inc(x_in[q], 16)
                pairs(pool, gather)

            @block.tensor
            def _(pe):
                def turn_x(i, q):
                    j = 2 * i + q
                    pe.wait_ge(x_in[q], 16 * i + 16)
                    after(pe, xT_ready, 2 * j)
                    pe.sem_inc(own_wait, 1)
                    for k in range(KT):
                        ins = pe.transpose(BX[k // 4][:, P * (k % 4):P * (k % 4) + P], xg[q][:, P * k:P * k + P], ident[:, :])
                    ins.then_inc(x_turned, 1)

                def gate_up(i, q):
                    j = 2 * i + q
                    pe.wait_ge(weights.gate_up_in[q], 32 * i + 32)
                    pe.wait_ge(xT_ready, 2 * j + 2)
                    after(pe, h_ready, j - 1)
                    for k in range(KT):
                        for e in range(2):
                            r = slice(RB * e, RB * e + RB)
                            ins = pe.matmul(BG[q][r, :], xgT[q][:, k, r], weights.gate_up[q][e][:, k, :], start=(k == 0), stop=(k == KT - 1))
                    ins.then_inc(gu_done, 1)

                def turn_h(i, q):
                    j = 2 * i + q
                    pe.wait_ge(h_ready, j + 1)
                    after(pe, hT_ready, j)
                    pe.sem_inc(own_wait, 1)
                    for k in range(2):
                        ins = pe.transpose(BH[:, P * k:P * k + P], h[:, P * k:P * k + P], ident[:, :])
                    ins.then_inc(h_turned, 1)

                def down(i, q):
                    j = 2 * i + q
                    pe.wait_ge(weights.down_in[q], 32 * i + 32)
                    pe.wait_ge(hT_ready, j + 1)
                    after(pe, y0_ready, j)
                    after(pe, y1_ready, j)
                    for n in range(2):
                        for k in range(2):
                            for e in range(2):
                                r = slice(RB * e, RB * e + RB)
                                ins = pe.matmul(BY[n][r, :], hT[q][:, k, r], weights.down[q][e][:, k, 512 * n:512 * n + 512],
                                                start=(k == 0), stop=(k == 1))
                    ins.then_inc(dn_done, 1)

                def body(i, q):
                    gate_up(i, q)
                    if not (isinstance(i, int) and i == TURNS - 1 and q == 1):
                        turn_x(i + q, 1 - q)
                    turn_h(i, q)
                    down(i, q)

                turn_x(0, 0)
                pairs(pe, body, last=True)

            @block.vector
            def _(v):
                def rows(i, q):
                    j = 2 * i + q
                    v.wait_ge(x_turned, j + 1)
                    after(v, gu_done, j - 1)
                    for half in range(2):
                        v.tensor_copy(xgT[q][:, 4 * half:4 * half + 4, :].rearrange("p k t -> p (k t)"),
                                      BX[half][:, :]).then_inc(xT_ready, 1)

                def body(i, q):
                    j = 2 * i + q
                    v.wait_ge(sg_ready, j + 1)
                    after(v, h_turned, j)
                    v.tensor_tensor(h, sg, BG[q][:, DE:2 * DE], ALU.mult).then_inc(h_ready, 1)
                    if not (isinstance(i, int) and i == TURNS - 1 and q == 1):
                        rows(i + q, 1 - q)
                    v.wait_ge(dn_done, j + 1)
                    after(v, y_out[q], 16 * i)
                    v.tensor_copy(y[q][:, 0:512], BY[0][:, :]).then_inc(y0_ready, 1)

                rows(0, 0)
                pairs(v, body, last=True)

            @block.scalar
            def _(act):
                def body(i, q):
                    j = 2 * i + q
                    act.wait_ge(gu_done, j + 1)
                    after(act, h_ready, j)
                    nc.scalar.activation(sg, BG[q][:, 0:DE], ACT.Silu).then_inc(sg_ready, 1)
                    act.wait_ge(h_turned, j + 1)
                    after(act, dn_done, j - 1)
                    nc.scalar.copy(hT[q].rearrange("p k t -> p (k t)"), BH[:, 0:2 * P]).then_inc(hT_ready, 1)
                    act.wait_ge(dn_done, j + 1)
                    after(act, y_out[q], 16 * i)
                    nc.scalar.copy(y[q][:, 512:D], BY[1][:, :]).then_inc(y1_ready, 1)
                    act.wait_ge(y0_ready, j + 1)
                    act.wait_ge(y1_ready, j + 1)
                    act.dma_start(y_rows[bass.ds(P * j, P), :], y[q]).then_inc(y_out[q], 16)

                pairs(act, body)
                for q in range(2):
                    act.wait_ge(y_out[q], 16 * TURNS)


def more_experts(nc, A, R, name, layer, ident, weights, x_dram, y_rows):
    with Scope(nc, name) as s:
        rt_more = R(RT_MORE_OFF, NMORE, dt=I32, np_=RB)
        be, more = R(BE_OFF, NMORE, dt=I32), R(MORE_OFF, 1, dt=I32)
        at = [MOE_FREE]

        def place(*shape, dt=F32, np_=RB):
            n = int(np.prod(shape))
            at[0] += n
            return R(at[0] - n, *shape, dt=dt, np_=np_)

        xg, xgT, idx = place(D), place(KT, RB, np_=P), place(2, dt=I32)
        sg, h, hT, y = place(DE), place(DE), place(2, RB, np_=P), place(D)
        bank = s.banks()
        BX, BG, BH, BY = bank[0:2], bank[2], bank[4], bank[5:7]
        w_in, x_in, y_out, gather_go, idx_ready, x_turned, xT_ready, gu_done, sg_ready, h_ready, h_turned, hT_ready, dn_done, y_ready = (
            s.sem(n) for n in ("w_in", "x_in", "y_out", "gather_go", "idx_ready", "x_turned", "xT_ready", "gu_done", "sg_ready",
                               "h_ready", "h_turned", "hT_ready", "dn_done", "y_ready"))

        own_wait = s.sem("own_wait")

        def if_more(eng, first, body):
            n = eng.value_load(more[0:1, 0:1], min_val=0, max_val=NMORE)
            with eng.If(n > 0):
                body(0, True)
                with eng.Fori(1, NMORE) as b:
                    body(b, False)
                if first is not None:
                    first()

        with nc.Block() as block:
            @block.sync
            def _(sp):
                def load(b, first):
                    e = sp.value_load(be[0:1, bass.ds(b, 1)], min_val=0, max_val=NE - 1)
                    if not first:
                        sp.wait_ge(dn_done, b)
                    sp.dma_start(weights.gate_up[0][0], A["moe_w_gate_up"][layer, bass.ds(e, 1)].rearrange("o (k p) n -> p (o k) n", p=P)).then_inc(w_in, 16)
                    sp.dma_start(weights.down[0][0], A["moe_w_down"][layer, bass.ds(e, 1)].rearrange("o (k p) n -> p (o k) n", p=P)).then_inc(w_in, 16)
                    sp.wait_ge(y_ready, 2 * b + 2)
                    sp.dma_start(y_rows[bass.ds(RB * (b + NE), RB), :], y).then_inc(y_out, 16)
                if_more(sp, lambda: sp.wait_ge(y_out, 16 * NMORE), load)

            @block.gpsimd
            def _(pool):
                def gather(b, first):
                    if not first:
                        pool.wait_ge(x_turned, b)
                    pool.tensor_copy(idx[:, 0:1], rt_more[:, bass.ds(b, 1)]).then_inc(idx_ready, 1)
                    pool.wait_ge(idx_ready, b + 1)
                    pool.sem_inc(gather_go, 1)
                    pool.indirect_dma_start(out=xg, out_offset=None, in_=x_dram,
                                            in_offset=bass.IndirectOffsetOnAxis(ap=idx[:, 0:1], axis=0)).then_inc(x_in, 16)
                if_more(pool, None, gather)

            @block.tensor
            def _(pe):
                def body(b, first):
                    pe.wait_ge(x_in, 16 * b + 16)
                    if not first:
                        pe.wait_ge(xT_ready, 2 * b)
                    pe.sem_inc(own_wait, 1)
                    for k in range(KT):
                        ins = pe.transpose(BX[k // 4][:, RB * (k % 4):RB * (k % 4) + RB], xg[:, P * k:P * k + P], ident[0:RB, 0:RB])
                    ins.then_inc(x_turned, 1)
                    pe.wait_ge(w_in, 32 * b + 32)
                    pe.wait_ge(xT_ready, 2 * b + 2)
                    if not first:
                        pe.wait_ge(h_ready, b)
                    for k in range(KT):
                        ins = pe.matmul(BG[0:RB, :], xgT[:, k, :], weights.gate_up[0][0][:, k, :], start=(k == 0), stop=(k == KT - 1))
                    ins.then_inc(gu_done, 1)
                    pe.wait_ge(h_ready, b + 1)
                    if not first:
                        pe.wait_ge(hT_ready, b)
                    pe.sem_inc(own_wait, 1)
                    for k in range(2):
                        ins = pe.transpose(BH[:, RB * k:RB * k + RB], h[:, P * k:P * k + P], ident[0:RB, 0:RB])
                    ins.then_inc(h_turned, 1)
                    pe.wait_ge(hT_ready, b + 1)
                    if not first:
                        pe.wait_ge(y_ready, 2 * b)
                    for n in range(2):
                        for k in range(2):
                            ins = pe.matmul(BY[n][0:RB, :], hT[:, k, :], weights.down[0][0][:, k, 512 * n:512 * n + 512],
                                            start=(k == 0), stop=(k == 1))
                    ins.then_inc(dn_done, 1)
                if_more(pe, None, body)

            @block.vector
            def _(v):
                def body(b, first):
                    v.wait_ge(x_turned, b + 1)
                    if not first:
                        v.wait_ge(gu_done, b)
                    for half in range(2):
                        v.tensor_copy(xgT[:, 4 * half:4 * half + 4, :].rearrange("p k t -> p (k t)"),
                                      BX[half][:, 0:4 * RB]).then_inc(xT_ready, 1)
                    v.wait_ge(sg_ready, b + 1)
                    if not first:
                        v.wait_ge(h_turned, b)
                    v.tensor_tensor(h, sg, BG[0:RB, DE:2 * DE], ALU.mult).then_inc(h_ready, 1)
                    v.wait_ge(dn_done, b + 1)
                    if not first:
                        v.wait_ge(y_out, 16 * b)
                    for n in range(2):
                        v.tensor_copy(y[:, 512 * n:512 * n + 512], BY[n][0:RB, :]).then_inc(y_ready, 1)
                if_more(v, None, body)

            @block.scalar
            def _(act):
                def body(b, first):
                    act.wait_ge(gu_done, b + 1)
                    if not first:
                        act.wait_ge(h_ready, b)
                    nc.scalar.activation(sg, BG[0:RB, 0:DE], ACT.Silu).then_inc(sg_ready, 1)
                    act.wait_ge(h_turned, b + 1)
                    if not first:
                        act.wait_ge(dn_done, b)
                    nc.scalar.copy(hT.rearrange("p k t -> p (k t)"), BH[:, 0:2 * RB]).then_inc(hT_ready, 1)
                if_more(act, None, body)


def combine(nc, R, name, x, y_rows):
    with Scope(nc, name) as s:
        dst, wt = R(DST_OFF, NT, 2, dt=I32), R(WT_OFF, 2, NT)
        yg = R(MOE_FREE, NT, 2, D)
        y_in = [s.sem(f"y_in{i}") for i in range(NT)]
        dve = s.sem("dve")
        with nc.Block() as block:
            @block.gpsimd
            def _(pool):
                for i, (t0, n) in enumerate(TILES):
                    for k in range(2):
                        pool.indirect_dma_start(out=yg[0:n, i, k, :], out_offset=None, in_=y_rows,
                                                in_offset=bass.IndirectOffsetOnAxis(ap=dst[0:n, i, k:k + 1], axis=0)).then_inc(y_in[i], 16)
                for i in range(NT):
                    pool.wait_ge(y_in[i], 32)

            @block.vector
            def _(v):
                link = Link(v, dve)
                for i, (t0, n) in enumerate(TILES):
                    v.wait_ge(y_in[i], 32)
                    link(v.tensor_scalar(yg[0:n, i, 0, :], yg[0:n, i, 0, :], wt[0:n, 0, i:i + 1], None, ALU.mult))
                    link(v.scalar_tensor_tensor(out=yg[0:n, i, 0, :], in0=yg[0:n, i, 1, :], scalar=wt[0:n, 1, i:i + 1],
                                                in1=yg[0:n, i, 0, :], op0=ALU.mult, op1=ALU.add))
                    link(v.scalar_tensor_tensor(out=x[0:n, i, :], in0=x[0:n, i, :], scalar=ALPHA, in1=yg[0:n, i, 0, :],
                                                op0=ALU.mult, op1=ALU.add))


HR = 4096


def page_rows(nc, A, idx_cmp, idx_slc):
    with Scope(nc, "pages") as s:
        pt = A["page_table"]
        raw1, raw2 = s.sb("raw1", [P, 16], I32), s.sb("raw2", [P, 64], I32)
        pi, p8, p32 = s.sb("pi", [P, 1], I32), s.sb("p8", [P, 1], I32), s.sb("p32", [P, 1], I32)
        f8, f32_, part = s.sb("f8", [P, 1]), s.sb("f32", [P, 1]), s.sb("part", [P, 2])
        p_in, made, dve = s.sem("p_in"), s.sem("made"), s.sem("dve")
        with nc.Block() as block:
            @block.sync
            def _(sp):
                with nc.allow_non_contiguous_dma(reason="page numbers, four bytes each"):
                    for g in range(16):
                        src = pt.rearrange("b (h g) -> g (b h)", g=16)[g].partition_broadcast(8)
                        sp.dma_start(raw1[8 * g:8 * g + 8, :], src).then_inc(p_in, 16)
                    for g in range(4):
                        src = pt.rearrange("b (j g) -> g (b j)", g=4)[g].partition_broadcast(32)
                        sp.dma_start(raw2[32 * g:32 * g + 32, :], src).then_inc(p_in, 16)

            @block.gpsimd
            def _(pool):
                pool.iota(pi[:, :], pattern=[[0, 1]], base=0, channel_multiplier=1).then_inc(made, 1)

            @block.vector
            def _(v):
                link = Link(v, dve)
                v.wait_ge(made, 1)
                link(v.tensor_scalar(p8[:, :], pi[:, :], 7, None, ALU.bitwise_and))
                link(v.tensor_scalar(p32[:, :], pi[:, :], 31, None, ALU.bitwise_and))
                link(v.tensor_copy(f8[:, :], p8[:, :]))
                link(v.tensor_copy(f32_[:, :], p32[:, :]))
                v.wait_ge(p_in, 16 * 20)
                link(v.tensor_scalar(part[:, 0:1], f8[:, :], 2.0, None, ALU.mult))
                link(v.tensor_scalar(part[:, 1:2], part[:, 0:1], 1.0, None, ALU.add))
                for i in range(2):
                    v.tensor_scalar(idx_cmp[:, :].rearrange("p (b s h) -> p b s h", s=2, h=2)[:, :, i, :],
                                    raw1[:, :].rearrange("p (b h) -> p b h", h=2), 16.0, part[:, i:i + 1], ALU.mult, ALU.add)
                link(v.tensor_scalar(idx_slc[:, :], raw2[:, :], 32.0, f32_[:, 0:1], ALU.mult, ALU.add))


def compress_cache(nc, A, ident, idx_cmp, pe_bias, ck_dram, cv_dram, spare_rows):
    with Scope(nc, "cc") as s:
        raw = Region(s.sb("raw", [P, 4 * HR]))(0, 2, 2, HR)
        w1 = raw[:, 1].rearrange("p h (j t c) -> p (h j) t c", j=1, t=16)
        w1_hi, w1_lo = s.sb("w1_hi", [P, 2, 16, CMP_H], F32R), s.sb("w1_lo", [P, 2, 16, CMP_H], F32R)
        NR = 4
        hi, lo = s.sb("hi", [P, NR, NKV, 258], F32R), s.sb("lo", [P, NR, NKV, 258], F32R)
        hid = [s.sb(f"hid{i}", [P, 2, 2, 256]) for i in range(2)]
        w2 = s.sb("w2", [P, 2, 2, HD])
        peT = s.sb("peT", [P, 2, 16])
        ck, cv = s.sb("ck", [P, 2, 256]), s.sb("cv", [P, 2, 256])
        idx = s.sb("idx", [P, 4], I32)
        zero, zero_pair = s.sb("zero", [RB, D]), s.sb("zero_pair", [P, 2])
        bank = s.banks()
        BT, BM, BO = bank[0:2], bank[3:7], bank[7]
        names = ("w_in", "w2_in", "idx_ready", "turned", "hi_moved", "lo_moved", "mm_done", "hid_ready", "out_done", "out_moved", "pb",
                 "zeroed", "w_hi", "w_split", "gather_go", "own_wait", "spare_zeroed", "spare_out")
        (w_in, w2_in, idx_ready, turned, hi_moved, lo_moved, mm_done, hid_ready, out_done, out_moved, pb,
         zeroed, w_hi, w_split, gather_go, own_wait, spare_zeroed, spare_out) = (s.sem(n) for n in names)
        raw_in = [s.sem(f"raw_in{i}") for i in range(4)]
        stored = [s.sem(f"stored{i}") for i in range(2)]
        cache = A["cache_cmp_kv"].rearrange("n (i s) k g d -> (n i) (s k g d)", s=8)
        AHEAD = NR - 1
        with nc.Block() as block:
            @block.gpsimd
            def _(pool):
                def gather(b, first=False):
                    for i in range(4):
                        if not first:
                            pool.wait_ge(raw_in[i], 16 * b)
                    col = idx_cmp[:, 0:4] if first else idx_cmp[:, bass.ds(4 * b, 4)]
                    pool.tensor_copy(idx[:, :], col).then_inc(idx_ready, 1)
                    pool.wait_ge(idx_ready, b + 1)
                    for part in range(2):
                        if first and part == 1:
                            pool.wait_ge(w_split, 1)
                        if not first:
                            pool.wait_ge(turned, 32 * b - 8 + 8 * part)
                            pool.sem_inc(gather_go, 1)
                        for h in range(2):
                            i = 2 * part + h
                            pool.indirect_dma_start(out=raw[:, part, h, :], out_offset=None, in_=cache,
                                                    in_offset=bass.IndirectOffsetOnAxis(ap=idx[:, i:i + 1], axis=0)).then_inc(raw_in[i], 16)

                pool.wait_ge(w_in, 16)
                gather(0, True)
                with pool.Fori(1, DEC_B) as b:
                    gather(b)

            @block.sync
            def _(sp):
                sp.dma_start(w1, A["cmp_w1"].rearrange("k (t p) h -> p k t h", p=P)).then_inc(w_in, 16)
                sp.dma_start(w2[:, :, :, :], A["cmp_w2"].rearrange("k (m p) d -> p k m d", p=P)).then_inc(w2_in, 16)
                sp.dma_start(peT[:, :, :], A["cmp_pe"]).then_inc(w2_in, 16)
                sp.wait_ge(spare_zeroed, 1)
                sp.wait_ge(raw_in[3], 16)
                sp.dma_start(spare_rows.rearrange("(b r) n -> r b n", r=RB), bc(zero[:, :].unsqueeze(1), [RB, NMORE, D])).then_inc(spare_out, 16)
                with sp.Fori(0, DEC_B) as b:
                    sp.wait_ge(out_moved, 4 * b + 2)
                    sp.dma_start(ck_dram[bass.ds(b, 1)].rearrange("o p n -> p (o n)"), ck[:, :, :].rearrange("p a n -> p (a n)")).then_inc(stored[0], 16)
                    sp.wait_ge(out_moved, 4 * b + 4)
                    sp.dma_start(cv_dram[bass.ds(b, 1)].rearrange("o p n -> p (o n)"), cv[:, :, :].rearrange("p a n -> p (a n)")).then_inc(stored[1], 16)
                for i in range(2):
                    sp.wait_ge(stored[i], 16 * DEC_B)
                sp.wait_ge(spare_out, 16)

            @block.tensor
            def _(pe):
                pe.wait_ge(w_in, 16)
                pe.wait_ge(w2_in, 32)
                for kv in range(2):
                    for m in range(2):
                        for t in range(16):
                            ins = pe.matmul(BO[:, 2 * kv + m:2 * kv + m + 1], w1[:, kv, t, P * m:P * m + P],
                                            peT[:, kv, t:t + 1], start=(t == 0), stop=(t == 15))
                ins.then_inc(pb, 1)

                def turn(kv, unit, st, sample):
                    job = 16 * unit + st
                    if st % 8 == 0:
                        for h in range(2):
                            pe.wait_ge(raw_in[2 * (st // 8) + h], 16 * sample + 16)
                    if not (isinstance(job, int) and job < 2):
                        pe.wait_ge(lo_moved, job - 1)
                    pe.sem_inc(own_wait, 1)
                    for gp in range(2):
                        for h in range(2):
                            o = 512 * (st % 8) + 256 * kv + P * gp
                            ins = pe.transpose(BT[st % 2][:, 256 * gp + P * h:256 * gp + P * h + P],
                                               raw[:, st // 8, h, o:o + P], ident[:, :])
                    ins.then_inc(turned, 1)

                def output(kv, unit, gp, first=False):
                    pe.wait_ge(hid_ready, 4 * unit + 2 * gp + 2)
                    if not first:
                        pe.wait_ge(out_moved, 2 * unit + gp)
                    for g2 in range(2):
                        if kv == 0:
                            for m in range(2):
                                ins = pe.matmul(BO[64 * g2:64 * g2 + 64, 0:255], w2[:, kv, m, :],
                                                hid[gp][:, m, g2, 0:255], start=(m == 0), stop=(m == 1))
                        else:
                            for h in range(2):
                                c = P - h
                                for m in range(2):
                                    ins = pe.matmul(BO[0:c, P * h + 64 * g2:P * h + 64 * g2 + 64],
                                                    hid[gp][:, m, g2, P * h:P * h + c], w2[:, kv, m, :],
                                                    start=(m == 0), stop=(m == 1))
                    ins.then_inc(out_done, 1)

                def product(kv, b, first=False, last=False):
                    unit = 2 * b + kv
                    for sp_ in range(8):
                        pe.wait_ge(lo_moved, 16 * unit + 2 * sp_ + 2)
                        r = sp_ % NR
                        nxt = sp_ + AHEAD
                        for n in range(4):
                            gp, m = n // 2, n % 2
                            if sp_ == 0 and not first:
                                pe.wait_ge(hid_ready, 4 * unit + n - 3)
                            for sh in range(2):
                                t = sp_ + 8 * sh
                                cols = slice(P * m, P * m + P)
                                heads, sub = slice(2 * gp, 2 * gp + 2), slice(sh, sh + 256)
                                for i, (w, x) in enumerate(((w1_hi, hi), (w1_hi, lo), (w1_lo, hi))):
                                    ins = pe.matmul(BM[n][:, :], w[:, kv, t, cols], x[:, r, heads, sub],
                                                    start=(sp_ == 0 and sh == 0 and i == 0), stop=(sp_ == 7 and sh == 1 and i == 2))
                            if sp_ == 7:
                                ins.then_inc(mm_done, 1)
                            if n % 2 == 0 and not (last and nxt >= 8):
                                st = 2 * (nxt % 8) + n // 2
                                turn(kv if nxt < 8 else 1 - kv, unit + nxt // 8, st, b + (nxt // 8 if kv else 0))
                            if n == 1 and sp_ < 2 and not first:
                                output(1 - kv, unit - 1, sp_, isinstance(unit, int) and unit == 1 and sp_ == 0)

                for st in range(2 * AHEAD):
                    turn(0, 0, st, 0)
                pe.wait_ge(w_split, 1)
                product(0, 0, first=True)
                product(1, 0)
                with pe.Fori(1, DEC_B - 1) as b:
                    product(0, b)
                    product(1, b)
                product(0, DEC_B - 1)
                product(1, DEC_B - 1, last=True)
                for gp in range(2):
                    output(1, 2 * DEC_B - 1, gp)

            def place_of(x, g2, st):
                return x[64 * (st % 2):64 * (st % 2) + 64, (st // 2) % NR].rearrange("p (q e) n -> p q e n", e=2)[:, :, g2, 0:256]

            def turned_rows(g2, st):
                return BT[st % 2][64 * g2:64 * g2 + 64, :].rearrange("p (q n) -> p q n", q=2)

            def next_steps(eng_unit, kv, last):
                def of(sp_):
                    nxt = sp_ + AHEAD
                    return [] if last and nxt >= 8 else [(eng_unit + nxt // 8, 2 * (nxt % 8) + i) for i in range(2)]
                return of

            @block.scalar
            def _(act):
                def move_hi(unit, st):
                    act.wait_ge(turned, 16 * unit + st + 1)
                    for g2 in range(2):
                        ins = nc.scalar.copy(place_of(hi, g2, st), turned_rows(g2, st))
                    ins.then_inc(hi_moved, 1)

                def unit(u, kv, first=False, last=False):
                    steps = next_steps(u, kv, last)
                    for sp_ in range(8):
                        nxt = steps(sp_)
                        for n in range(4):
                            if sp_ == 7:
                                gp, m = n // 2, n % 2
                                act.wait_ge(mm_done, 4 * u + n + 1)
                                if not first:
                                    act.wait_ge(out_done, 2 * u + gp - 1)
                                nc.scalar.activation(hid[gp][:, m, :, 0:255], BM[n][:, :].rearrange("p (a c) -> p a c", a=2)[:, :, 0:255],
                                                     ACT.Gelu_apprx_tanh, bias=pe_bias[:, 2 * kv + m:2 * kv + m + 1]).then_inc(hid_ready, 1)
                            if n % 2 == 0 and nxt:
                                move_hi(*nxt[n // 2])

                for st in range(2 * AHEAD):
                    move_hi(0, st)
                act.wait_ge(pb, 1)
                nc.scalar.copy(pe_bias[:, :], BO[:, 0:4]).then_inc(pb, 1)
                act.wait_ge(pb, 2)
                unit(0, 0, first=True)
                unit(1, 1)
                with act.Fori(1, DEC_B - 1) as b:
                    unit(2 * b, 0)
                    unit(2 * b + 1, 1)
                unit(2 * DEC_B - 2, 0)
                unit(2 * DEC_B - 1, 1, last=True)

            @block.vector
            def _(v):
                def move_lo(unit, st):
                    v.wait_ge(hi_moved, 16 * unit + st + 1)
                    for g2 in range(2):
                        ins = v.tensor_tensor(place_of(lo, g2, st), turned_rows(g2, st), place_of(hi, g2, st), ALU.subtract)
                    ins.then_inc(lo_moved, 1)

                def out(u, kv, gp, b, first=False):
                    v.wait_ge(out_done, 2 * u + gp + 1)
                    if gp == 0 and not first:
                        v.wait_ge(stored[kv], 16 * b)
                    if kv == 0:
                        ins = v.tensor_copy(ck[:, gp, 0:255], BO[:, 0:255])
                    else:
                        for h in range(2):
                            c = P - h
                            ins = v.tensor_copy(cv[0:c, h, P * gp:P * gp + P], BO[0:c, P * h:P * h + P])
                    ins.then_inc(out_moved, 1)

                def unit(b, kv, before=None, last=False):
                    u = 2 * b + kv
                    steps = next_steps(u, kv, last)
                    for sp_ in range(8):
                        nxt = steps(sp_)
                        if nxt:
                            move_lo(*nxt[0])
                        if sp_ < 2 and before is not None:
                            out(u - 1, 1 - kv, sp_, before[0], before[1])
                        if nxt:
                            move_lo(*nxt[1])

                v.memset(zero[:, :], 0.0).then_inc(spare_zeroed, 1)
                v.memset(zero_pair[:, :], 0.0).then_inc(spare_zeroed, 1)
                v.wait_ge(spare_zeroed, 2)
                v.memset(ck[:, :, 255:256], 0.0)
                v.tensor_copy(hi[:, :, :, 256:258], bc(zero_pair[:, :].unsqueeze(1).unsqueeze(1), [P, NR, NKV, 2]))
                v.tensor_copy(lo[:, :, :, 256:258], bc(zero_pair[:, :].unsqueeze(1).unsqueeze(1), [P, NR, NKV, 2]))
                v.memset(cv[96:P, 1, :], 0.0).then_inc(zeroed, 1)
                v.wait_ge(zeroed, 1)
                v.wait_ge(w_in, 16)
                v.tensor_copy(w1_hi[:, :, :, :], w1).then_inc(w_hi, 1)
                v.wait_ge(w_hi, 1)
                v.wait_ge(pb, 1)
                v.tensor_tensor(w1_lo[:, :, :, :], w1, w1_hi[:, :, :, :], ALU.subtract).then_inc(w_split, 1)
                for st in range(2 * AHEAD):
                    move_lo(0, st)
                v.wait_ge(pb, 2)
                unit(0, 0)
                unit(0, 1, (0, True))
                unit(1, 0, (0, True))
                unit(1, 1, (1, False))
                with v.Fori(2, DEC_B - 1) as b:
                    unit(b, 0, (b - 1, False))
                    unit(b, 1, (b, False))
                b = DEC_B - 1
                unit(b, 0, (b - 1, False))
                unit(b, 1, (b, False), last=True)
                for gp in range(2):
                    out(2 * b + 1, 1, gp, b)


KV_OFF = 9728
Q_OFF = KV_OFF + NT * 1536
GT_OFF = Q_OFF + 8 * TOK
A_FREE = GT_OFF + NT * 48 + 16


def projections(nc, A, R, outs, gate_dram):
    with Scope(nc, "proj") as s:
        xT = R(XT_OFF, KT, TOK)
        kv, q = R(KV_OFF, NT, 3, 512), R(Q_OFF, 8, TOK)
        gates = R(GT_OFF, NT, 48)
        wkv = R(A_FREE, KT, 1536)
        wq = R(A_FREE + KT * 1536, KT, NH * HD + 48)
        bank = s.banks()
        wq_in, full, stored, gates_done = (s.sem(n) for n in ("wq_in", "full", "stored", "gates_done"))
        wkv_in = [s.sem(f"wkv_in{i}") for i in range(3)]
        used = (s.sem("used_v"), s.sem("used_a"))
        ring = Split(8, full, used)
        NKVJ = 3 * NT
        half = TOK // 2
        p_out, s_out = outs[0:3], outs[3:6]
        n_out = [0]
        with nc.Block() as block:
            @block.sync
            def _(sp):
                for br in range(3):
                    sp.dma_start(wkv[:, :, 512 * br:512 * br + 512],
                                 A["kv_w"].rearrange("(k p) n -> p k n", p=P)[:, :, 512 * br:512 * br + 512]).then_inc(wkv_in[br], 16)
                sp.dma_start(wq, A["b_w_qg"].rearrange("(k p) n -> p k n", p=P)).then_inc(wq_in, 16)
                for b in range(DEC_B):
                    sp.dma_start(s_out[2][b, 0:504].rearrange("t k g d -> t (k g d)"),
                                 A["cache_win_kv"][b, 8:512].rearrange("t k g d -> t (k g d)")).then_inc(stored, 16)
                n = DEC_B
                for br in range(3):
                    for i in range(NT):
                        ring.all_used(sp, NT * br + i + 1)
                        flat = "t k g d -> t (k g d)"
                        if i < 4:
                            dst = p_out[br][0, P * i:P * i + P].rearrange(flat)
                            sp.dma_start(dst, kv[:, i, br, :]).then_inc(stored, 16)
                            n += 1
                        elif br < 2:
                            sp.dma_start(s_out[br].rearrange("b t k g d -> (b t) (k g d)"), kv[0:64, i, br, :]).then_inc(stored, 16)
                            n += 1
                        else:
                            for b in range(DEC_B):
                                sp.dma_start(s_out[2][b, 504:512].rearrange(flat), kv[8 * b:8 * b + 8, i, br, :]).then_inc(stored, 16)
                                n += 1
                sp.wait_ge(gates_done, NT)
                sp.dma_start(gate_dram, gates[0:64, 4, :]).then_inc(stored, 16)
                sp.wait_ge(stored, 16 * (n + 1))

            @block.tensor
            def _(pe):
                for br in range(3):
                    pe.wait_ge(wkv_in[br], 16)
                    for i, (t0, n) in enumerate(TILES):
                        b = ring.claim(pe, NT * br + i)
                        for k in range(KT):
                            ins = pe.matmul(bank[b][0:n, :], xT[:, k, t0:t0 + n], wkv[:, k, 512 * br:512 * br + 512],
                                            start=(k == 0), stop=(k == KT - 1))
                        ring.done(ins)
                pe.wait_ge(wq_in, 16)
                for m in range(8):
                    for h in range(2):
                        b = ring.claim(pe, NKVJ + 2 * m + h)
                        for k in range(KT):
                            ins = pe.matmul(bank[b][:, 0:half], wq[:, k, P * m:P * m + P], xT[:, k, half * h:half * h + half],
                                            start=(k == 0), stop=(k == KT - 1))
                        ring.done(ins)
                b = ring.claim(pe, NKVJ + 16)
                for i, (t0, n) in enumerate(TILES):
                    for k in range(KT):
                        ins = pe.matmul(bank[b][0:n, 48 * i:48 * i + 48], xT[:, k, t0:t0 + n], wq[:, k, NH * HD:],
                                        start=(k == 0), stop=(k == KT - 1))
                ring.done(ins)

            def empty(eng, copy, me):
                for j in range(me, NKVJ, 2):
                    br, i = j // NT, j % NT
                    n = TILES[i][1]
                    eng.wait_ge(full, j + 1)
                    copy(kv[0:n, i, br, :], bank[j % 8][0:n, :]).then_inc(used[me], 1)
                for j in range(NKVJ + (NKVJ + me) % 2, NKVJ + 16, 2):
                    m, h = (j - NKVJ) // 2, (j - NKVJ) % 2
                    eng.wait_ge(full, j + 1)
                    copy(q[:, m, half * h:half * h + half], bank[j % 8][:, 0:half]).then_inc(used[me], 1)

            @block.vector
            def _(v):
                empty(v, v.tensor_copy, 0)

            @block.scalar
            def _(act):
                empty(act, nc.scalar.copy, 1)
                j = NKVJ + 16
                act.wait_ge(full, j + 1)
                for i, (t0, n) in enumerate(TILES):
                    nc.scalar.activation(gates[0:n, i, :], bank[j % 8][0:n, 48 * i:48 * i + 48], ACT.Sigmoid).then_inc(gates_done, 1)


def compress_prompt(nc, A, R, ident, pe_bias, rows, ckp, cvp):
    with Scope(nc, "cp") as s:
        NS = 32
        raw = R(A_FREE, 2 * HR, np_=NS)
        xt = R(A_FREE + 2 * HR, 2, 8, NKV, NS)
        w1 = R(A_FREE + 2 * HR + 2048, 2, 16, CMP_H)
        w2 = R(A_FREE + 2 * 2 * HR + 2048, 2, 2, HD)
        hid = R(A_FREE + 2 * 2 * HR + 2304, 2, 2, NKV, NS)
        bank = s.banks()
        raw_in, w_in, turned, moved_a, moved_v, mm_done, hid_ready, out_done, dve = (
            s.sem(n) for n in ("raw_in", "w_in", "turned", "moved_a", "moved_v", "mm_done", "hid_ready", "out_done", "dve"))
        with nc.Block() as block:
            @block.sync
            def _(sp):
                sp.dma_start(raw, rows[0].rearrange("(n s) k g d -> n (s k g d)", s=16)).then_inc(raw_in, 16)
                sp.dma_start(w1, A["cmp_w1"].rearrange("k (t p) h -> p k t h", p=P)).then_inc(w_in, 16)
                sp.dma_start(w2, A["cmp_w2"].rearrange("k (m p) d -> p k m d", p=P)).then_inc(w_in, 16)

            @block.tensor
            def _(pe):
                pe.wait_ge(raw_in, 16)
                for kv in range(2):
                    for q in range(2):
                        for st in range(8 * q, 8 * q + 8):
                            for gp in range(2):
                                o = 512 * st + 256 * kv + P * gp
                                c = 64 * (st % 8) + NS * gp
                                ins = pe.transpose(bank[2 * kv + q][:, c:c + NS], raw[:, o:o + P], ident[0:NS, 0:NS])
                        ins.then_inc(turned, 1)
                pe.wait_ge(w_in, 32)
                pe.wait_ge(moved_a, 64)
                pe.wait_ge(moved_v, 64)
                for kv in range(2):
                    for m in range(2):
                        for t in range(16):
                            sh = 1 if t >= 8 else 0
                            ins = pe.matmul(bank[4 + 2 * kv + m][:, 0:NKV * 31], w1[:, kv, t, P * m:P * m + P],
                                            xt[:, kv, t % 8, :, sh:sh + 31], start=(t == 0), stop=(t == 15))
                        ins.then_inc(mm_done, 1)
                pe.wait_ge(hid_ready, 4)
                for g in range(NKV):
                    for m in range(2):
                        pe.matmul(bank[0][64 * (g % 2):64 * (g % 2) + 64, 32 * (g // 2):32 * (g // 2) + 31], w2[:, 0, m, :],
                                  hid[:, 0, m, g, 0:31], start=(m == 0), stop=(m == 1))
                for g in range(NKV):
                    for m in range(2):
                        ins = pe.matmul(bank[1][0:31, 64 * g:64 * g + 64], hid[:, 1, m, g, 0:31], w2[:, 1, m, :],
                                        start=(m == 0), stop=(m == 1))
                ins.then_inc(out_done, 1)

            def move(eng, copy, sem_, g2):
                for kv in range(2):
                    for q in range(2):
                        eng.wait_ge(turned, 2 * kv + q + 1)
                        for st in range(8 * q, 8 * q + 8):
                            for gp in range(2):
                                c = 64 * (st % 8) + NS * gp
                                copy(xt[64 * (st % 2):64 * (st % 2) + 64, kv, st // 2, 2 * gp + g2, :],
                                     bank[2 * kv + q][64 * g2:64 * g2 + 64, c:c + NS]).then_inc(sem_, 1)

            @block.scalar
            def _(act):
                move(act, nc.scalar.copy, moved_a, 0)
                for kv in range(2):
                    for m in range(2):
                        act.wait_ge(mm_done, 2 * kv + m + 1)
                        nc.scalar.activation(hid[:, kv, m, :, 0:31], bank[4 + 2 * kv + m][:, 0:NKV * 31].rearrange("p (g c) -> p g c", g=NKV),
                                             ACT.Gelu_apprx_tanh, bias=pe_bias[:, 2 * kv + m:2 * kv + m + 1]).then_inc(hid_ready, 1)

            @block.vector
            def _(v):
                move(v, v.tensor_copy, moved_v, 1)
                v.wait_ge(out_done, 1)
                v.tensor_copy(ckp[:, :, 0:31], bank[0][:, 0:64].rearrange("p (q c) -> p q c", q=2)[:, :, 0:31]).then_inc(dve, 1)
                v.tensor_copy(cvp[0:31, :], bank[1][0:31, 0:256]).then_inc(dve, 1)


def attention_masks(nc, R, cm, cma, cm01, nmask, wmask, hsum, forced):
    with Scope(nc, "masks") as s:
        ones = s.sb("ones", [P, P])
        pi, l_i, lf, li8, nm8 = s.sb("pi", [P, 1], I32), s.sb("l_i", [P, 1], I32), s.sb("lf", [P, 1]), s.sb("li8", [P, 8]), s.sb("nm8", [P, 8])
        qi, qf, cid, gl = s.sb("qi", [P, P], I32), s.sb("qf", [P, P]), s.sb("cid", [P, 1], I32), s.sb("gl", [P, 1])
        made, dve = s.sem("made"), s.sem("dve")
        with nc.Block() as block:
            @block.gpsimd
            def _(pool):
                pool.memset(ones[:, :], 0.0).then_inc(made, 1)
                pool.memset(cma, 0.0).then_inc(made, 1)
                pool.memset(cm01, 1.0).then_inc(made, 1)
                pool.iota(pi[:, :], pattern=[[0, 1]], base=0, channel_multiplier=1).then_inc(made, 1)
                pool.iota(li8[:, :], pattern=[[1, 8]], base=0, channel_multiplier=0, allow_small_or_imprecise_dtypes=True).then_inc(made, 1)
                pool.iota(qi[:, :], pattern=[[1, P]], base=0, channel_multiplier=0).then_inc(made, 1)
                pool.wait_ge(made, 6)
                pool.affine_select(out=cm, in_=ones[:, :], compare_op=ALU.is_ge, fill=NEG, base=0,
                                   pattern=[[-1, P]], channel_multiplier=1).then_inc(made, 1)
                pool.affine_select(out=cma, in_=cma, compare_op=ALU.is_ge, fill=NEG, base=-31,
                                   pattern=[[P, 4], [-16, 31]], channel_multiplier=1).then_inc(made, 1)
                pool.affine_select(out=cm01, in_=cm01, compare_op=ALU.is_ge, fill=0.0, base=-31,
                                   pattern=[[P, 4], [-16, 31]], channel_multiplier=1).then_inc(made, 1)

            @block.vector
            def _(v):
                link = Link(v, dve)
                v.wait_ge(made, 6)
                link(v.tensor_scalar(l_i[:, :], pi[:, :], 7, None, ALU.bitwise_and))
                link(v.tensor_copy(lf[:, :], l_i[:, :]))
                link(v.tensor_scalar(nm8[:, :], li8[:, :], lf[:, 0:1], NEG, ALU.is_gt, ALU.mult))
                link(v.tensor_scalar(wmask, li8[:, :], lf[:, 0:1], NEG, ALU.is_le, ALU.mult))
                link(v.memset(nmask, NEG))
                for b in range(DEC_B):
                    ins = v.tensor_copy(nmask[:, b, 8 * b:8 * b + 8], nm8[:, :])
                link(ins)
                link(v.tensor_scalar(qi[:, :], qi[:, :], 103, None, ALU.bitwise_and))
                link(v.tensor_scalar(cid[:, :], pi[:, :], 103, None, ALU.bitwise_and))
                link(v.tensor_copy(qf[:, :], qi[:, :]))
                link(v.tensor_copy(gl[:, :], cid[:, :]))
                link(v.tensor_scalar(hsum, qf[:, :], gl[:, 0:1], None, ALU.is_equal))
                link(v.memset(forced, 0.0))
                link(v.memset(forced[:, 0:1], 1e4))
                link(v.memset(forced[:, 64:65], 1e4))


def prompt_attention(nc, A, R, ident, ckp, cvp, cm, cma, cm01, kt_s, oT):
    with Scope(nc, "pa") as s:
        kv, q = R(KV_OFF, NT, 3, 512), R(Q_OFF, 8, TOK)
        gates = R(GT_OFF, NT, 16, 3)
        kt = R(A_FREE, 2, 2, SEQ)
        p_ = [R(A_FREE + 2048 + 1024 * i, 2, 512) for i in range(2)]
        pT = [R(A_FREE + 4096 + 1024 * i, 2, 512) for i in range(2)]
        o = R(A_FREE + 6144, 4, NH, HD)
        mx, cf = R(A_FREE + 10240, 2, 2), R(A_FREE + 10248, 2, 2)
        NSUM = 5
        sm = R(A_FREE + 13104, NSUM, 2)
        ob = R(A_FREE + 10256, 2, 2, HD)
        pc = R(A_FREE + 10512, NH, 32)
        pcT = R(A_FREE + 11024, NH, P)
        mc, sc = R(A_FREE + 13072, NH), R(A_FREE + 13088, NH)
        psS = [s.ctx.enter_context(nc.psum_tensor(f"pa_s{i}", [P, 2, 512], F32)) for i in range(2)]
        psT = [s.ctx.enter_context(nc.psum_tensor(f"pa_t{i}", [P, 512], F32)) for i in range(2)]
        psO = [s.ctx.enter_context(nc.psum_tensor(f"pa_o{i}", [P, 512], F32)) for i in range(2)]
        dve, k_turned, k_moved, s_done, c_exp_in, c_exp, c_ready, c_turned, c_moved, c_out, c_gated = (
            s.sem(n) for n in ("dve", "k_turned", "k_moved", "s_done", "c_exp_in", "c_exp", "c_ready", "c_turned", "c_moved", "c_out", "c_gated"))
        s_full, max_ready, p_ready, t_full, t_used, o_full, o_used, o_turned, o_moved = (
            s.sem(n) for n in ("s_full", "max_ready", "p_ready", "t_full", "t_used", "o_full", "o_used", "o_turned", "o_moved"))
        units = [(br, i, m, g2) for i in range(4) for br in range(2) for m in range(0, 8, 2) for g2 in range(2)]

        def head(m, g2):
            return (2 * (m // 4) + g2) * HPK + m % 4

        with nc.Block() as block:
            @block.tensor
            def _(pe):
                for j in range(4):
                    br, gp = j // 2, j % 2
                    for i in range(4):
                        ins = pe.transpose(psS[j // 2][:, j % 2, P * i:P * i + P], kv[:, i, 1 + br, P * gp:P * gp + P], ident[:, :])
                    ins.then_inc(k_turned, 1)
                for j in range(4):
                    br, gp = j // 2, j % 2
                    ins = pe.transpose(psO[0][:, 64 * j:64 * j + 64], kv[0:64, 4, 1 + br, P * gp:P * gp + P], ident[0:64, 0:64])
                ins.then_inc(k_turned, 1)
                for i in range(4):
                    if i == 0:
                        pe.wait_ge(k_moved, 5)
                    else:
                        pe.wait_ge(c_exp_in, i)
                    for m in range(8):
                        for g2 in range(2):
                            r = slice(64 * g2, 64 * g2 + 64)
                            ins = pe.matmul(psS[0][:, g2, 32 * m:32 * m + 31], q[r, m, P * i:P * i + P], ckp[r, m // 4, 0:31],
                                            start=True, stop=True)
                    ins.then_inc(s_done, 1)
                    pe.wait_ge(c_ready, i + 1)
                    for j in range(4):
                        if 4 * i + j >= 2:
                            pe.wait_ge(c_moved, 4 * i + j - 1)
                        for n in range(4):
                            ins = pe.transpose(psT[j % 2][0:31, P * n:P * n + P], pc[:, 4 * j + n, 0:31], ident[:, :])
                        ins.then_inc(c_turned, 1)
                    pe.wait_ge(c_moved, 4 * i + 4)
                    if i >= 1:
                        pe.wait_ge(c_gated, i)
                    for h in range(NH):
                        ins = pe.matmul(psO[h // 8][:, HD * (h % 8):HD * (h % 8) + HD], pcT[0:31, h, :],
                                        cvp[0:31, HD * (h // HPK):HD * (h // HPK) + HD], start=True, stop=True)
                    ins.then_inc(c_out, 1)

                def scores(u):
                    br, i, m, g2 = units[u]
                    r = slice(64 * g2, 64 * g2 + 64)
                    if u >= 2:
                        pe.wait_ge(p_ready, 2 * (u - 1))
                    n = P * (i + 1)
                    for e in range(2):
                        ins = pe.matmul(psS[u % 2][:, e, 0:n], q[r, m + e, P * i:P * i + P], kt[r, br, m // 4, 0:n], start=True, stop=True)
                    ins.then_inc(s_full, 1)

                def turn_p(u):
                    br, i, m, g2 = units[u]
                    pe.wait_ge(p_ready, 2 * u + 2)
                    for e in range(2):
                        if 2 * u + e >= 2:
                            pe.wait_ge(t_used, 2 * u + e - 1)
                        for k in range(i + 1):
                            ins = pe.transpose(psT[e][:, P * k:P * k + P], p_[u % 2][:, e, P * k:P * k + P], ident[:, :])
                        ins.then_inc(t_full, 1)

                def outputs(u):
                    br, i, m, g2 = units[u]
                    g = 2 * (m // 4) + g2
                    if u >= 2:
                        pe.wait_ge(o_used, u - 1)
                    for e in range(2):
                        pe.wait_ge(t_used, 2 * u + e + 1)
                        for k in range(i + 1):
                            ins = pe.matmul(psO[u % 2][:, HD * e:HD * e + HD], pT[u % 2][:, e, P * k:P * k + P],
                                            kv[:, k, 1 + br, 256 + HD * g:256 + HD * g + HD], start=(k == 0), stop=(k == i))
                    ins.then_inc(o_full, 1)

                pe.wait_ge(c_exp_in, 4)
                pe.wait_ge(c_gated, 4)
                scores(0)
                scores(1)
                for u in range(len(units)):
                    turn_p(u)
                    if u + 2 < len(units):
                        scores(u + 2)
                    outputs(u)
                pe.wait_ge(o_used, len(units))
                for i in range(4):
                    for h in range(2):
                        j = 2 * i + h
                        if j >= 2:
                            pe.wait_ge(o_moved, j - 1)
                        for k in range(4):
                            a = P * (4 * h + k)
                            ins = pe.transpose(psT[j % 2][:, P * k:P * k + P],
                                               o[:, i].rearrange("p h d -> p (h d)")[:, a:a + P], ident[:, :])
                        ins.then_inc(o_turned, 1)

            def turned_out(act, u):
                n = P * (units[u][1] + 1)
                for e in range(2):
                    act.wait_ge(t_full, 2 * u + e + 1)
                    if u >= 2:
                        act.wait_ge(o_full, u - 1)
                    nc.scalar.copy(pT[u % 2][:, e, 0:n], psT[e][:, 0:n]).then_inc(t_used, 1)

            @block.scalar
            def _(act):
                for i in range(4):
                    act.wait_ge(c_exp_in, i + 1)
                    nc.scalar.activation(pc[:, :, 0:31], pc[:, :, 0:31], ACT.Exp, scale=SCALE).then_inc(c_exp, 1)
                for u, (br, i, m, g2) in enumerate(units):
                    n = P * (i + 1)
                    act.wait_ge(max_ready, u + 1)
                    if u >= 2:
                        act.wait_ge(t_full, 2 * u - 2)
                    for e in range(2):
                        nc.scalar.activation(p_[u % 2][:, e, 0:n], psS[u % 2][:, e, 0:n], ACT.Exp, bias=mx[:, u % 2, e:e + 1],
                                             scale=SCALE, accum_out=sm[:, u % NSUM, e:e + 1]).then_inc(p_ready, 1)
                    if u >= 1:
                        turned_out(act, u - 1)
                turned_out(act, len(units) - 1)
                for j in range(8):
                    act.wait_ge(o_turned, j + 1)
                    nc.scalar.copy(oT[:, 4 * (j % 2):4 * (j % 2) + 4, P * (j // 2):P * (j // 2) + P],
                                   psT[j % 2][:, :].rearrange("p (k t) -> p k t", k=4)).then_inc(o_moved, 1)

            @block.vector
            def _(v):
                link = Link(v, dve)
                for j in range(4):
                    v.wait_ge(k_turned, j + 1)
                    v.tensor_copy(kt[:, j // 2, j % 2, :], psS[j // 2][:, j % 2, :]).then_inc(k_moved, 1)
                v.wait_ge(k_turned, 5)
                v.tensor_copy(kt_s.rearrange("p a b t -> p (a b t)"), psO[0][:, 0:256]).then_inc(k_moved, 1)
                for i in range(4):
                    v.wait_ge(s_done, i + 1)
                    if i >= 1:
                        v.wait_ge(c_turned, 4 * i)
                    for gp in range(2):
                        for g2 in range(2):
                            h = head(4 * gp, g2)
                            s31 = psS[0][:, g2, 0:256].rearrange("p (h c) -> p h c", h=8)[:, 4 * gp:4 * gp + 4, 0:31]
                            ins = v.tensor_tensor(pc[:, h:h + 4, 0:31], s31, bc(cma[:, i, :].unsqueeze(1), [P, 4, 31]), ALU.add)
                    link(ins)
                    link(v.tensor_reduce(mc, pc[:, :, 0:31], AX, ALU.max))
                    v.tensor_tensor(pc[:, :, 0:31], pc[:, :, 0:31], bc(mc.unsqueeze(2), [P, NH, 31]), ALU.subtract).then_inc(c_exp_in, 1)
                    v.wait_ge(c_exp, i + 1)
                    link(v.tensor_tensor(pc[:, :, 0:31], pc[:, :, 0:31], bc(cm01[:, i, :].unsqueeze(1), [P, NH, 31]), ALU.mult))
                    v.engine_nop().then_inc(c_ready, 1)
                    link(v.tensor_reduce(sc, pc[:, :, 0:31], AX, ALU.add))
                    link(v.tensor_scalar(sc, sc, TINY, None, ALU.max))
                    link(v.reciprocal(sc, sc))
                    link(v.tensor_tensor(sc, sc, gates[:, i, :, 0], ALU.mult))
                    for j in range(4):
                        v.wait_ge(c_turned, 4 * i + j + 1)
                        if j == 0 and i >= 1:
                            v.wait_ge(c_out, i)
                        v.tensor_copy(pcT[0:31, 4 * j:4 * j + 4, :], psT[j % 2][0:31, :].rearrange("p (h t) -> p h t", h=4)).then_inc(c_moved, 1)
                    v.wait_ge(c_out, i + 1)
                    for h in range(2):
                        ins = v.tensor_tensor(o[:, i, 8 * h:8 * h + 8, :], psO[h][:, :].rearrange("p (h d) -> p h d", h=8),
                                              bc(sc[:, 8 * h:8 * h + 8].unsqueeze(2), [P, 8, HD]), ALU.mult)
                    ins.then_inc(c_gated, 1)
                v.wait_ge(c_gated, 4)

                def merge(u):
                    br, i, m, g2 = units[u]
                    h = head(m, g2)
                    v.wait_ge(p_ready, 2 * u + 2)
                    link(v.reciprocal(cf[:, u % 2, :], sm[:, u % NSUM, :]))
                    link(v.tensor_tensor(cf[:, u % 2, :], cf[:, u % 2, :], gates[:, i, h:h + 2, 1 + br], ALU.mult))
                    v.wait_ge(o_full, u + 1)
                    link(v.tensor_tensor(ob[:, u % 2], psO[u % 2][:, 0:2 * HD].rearrange("p (e d) -> p e d", e=2),
                                         bc(cf[:, u % 2, :].unsqueeze(2), [P, 2, HD]), ALU.mult))
                    v.tensor_tensor(o[:, i, h:h + 2, :], o[:, i, h:h + 2, :], ob[:, u % 2], ALU.add).then_inc(o_used, 1)

                def prepare(u):
                    br, i, m, g2 = units[u]
                    n = P * (i + 1)
                    v.wait_ge(s_full, u + 1)
                    diag = psS[u % 2][:, :, P * i:n]
                    link(v.tensor_tensor(diag, diag, bc(cm.unsqueeze(1), [P, 2, P]), ALU.add))
                    if u >= 2:
                        v.wait_ge(p_ready, 2 * u - 2)
                    link(v.tensor_reduce(mx[:, u % 2, :], psS[u % 2][:, :, 0:n], AX, ALU.max))
                    v.tensor_scalar(mx[:, u % 2, :], mx[:, u % 2, :], -SCALE, None, ALU.mult).then_inc(max_ready, 1)

                prepare(0)
                prepare(1)
                for u in range(len(units)):
                    if u + 2 < len(units):
                        prepare(u + 2)
                    merge(u)


OT_OFF = KV_OFF
KV4_OFF = KV_OFF + 4 * 1536
QBD_OFF = XT_OFF + 1680
S_FREE = Q_OFF


def sample_queries(nc, R, gate_dram, gs):
    with Scope(nc, "sq") as s:
        q, qbd = R(Q_OFF, 8, TOK), R(QBD_OFF, DEC_B, 2, P)
        zeroed, done, g_in = s.sem("zeroed"), s.sem("done"), s.sem("g_in")
        with nc.Block() as block:
            @block.gpsimd
            def _(pool):
                pool.memset(qbd, 0.0).then_inc(zeroed, 1)

            @block.vector
            def _(v):
                v.wait_ge(zeroed, 1)
                for g in range(NKV):
                    gp, g2 = g // 2, g % 2
                    r = slice(64 * g2, 64 * g2 + 64)
                    dst = qbd[r, :, gp, 32 * g:32 * g + 32].rearrange("p b (n l) -> p b n l", n=HPK)
                    src = q[r, 4 * gp:4 * gp + 4, SEQ:TOK].rearrange("p n (b l) -> p b n l", b=DEC_B)
                    v.tensor_copy(dst, src).then_inc(done, 1)

            @block.sync
            def _(sp):
                for b in range(DEC_B):
                    src = gate_dram.rearrange("(b l) (h r) -> b h l r", b=DEC_B, r=3)[b]
                    sp.dma_start(gs[:, b, :], src).then_inc(g_in, 16)
                sp.wait_ge(g_in, 16 * DEC_B)


def sample_attention(nc, A, R, ident, idx_slc, ck_dram, cv_dram, kt_s, nmask, wmask, hsum, forced, gs, oT):
    with Scope(nc, "sa") as s:
        qbd, kv4 = R(QBD_OFF, DEC_B, 2, P), R(KV4_OFF, 3, 512)
        at = [S_FREE]

        def place(*shape, dt=F32):
            n = int(np.prod(shape))
            at[0] += n + n % 2
            return R(at[0] - n - n % 2, *shape, dt=dt)

        NJ = 8
        raw = [place(4, 512) for _ in range(NJ + 1)]
        sc = place(9 * 512 + 128)
        OLD, WIN = NJ * 512, NJ * 512 + 64
        kts = [place(2, 512) for _ in range(2)]
        pt = [place(512) for _ in range(2)]
        ptn = place(512)
        ck, cv = place(2, 256), place(2, 256)
        pc = place(256)
        qb = place(2, P)
        ps = place(66)
        sel = place(66)
        m8 = place(2, 8)
        tm, es = place(10), place(10)
        mxs, sms, cf = place(4), place(4), place(4)
        ob, obs = place(HD), place(DEC_B, 2, HD)
        idx = place(NJ, dt=I32)
        bank = s.banks()
        psK, psS, psT, O0, O1 = bank[0:2], bank[2:4], bank[4:6], bank[6], bank[7]
        names = ("idx_ready", "gather_go", "win_in", "ck_in", "cv_in", "dve", "qb_ready", "c_full", "cmax_ready", "c_exp", "p4_ready",
                 "hs_full", "k_turned", "k_moved_v", "k_moved_a", "s_full", "s_moved", "max_ready", "e_ready", "pn_ready",
                 "t_full", "t_moved_v", "t_moved_a", "v_done", "ob_ready", "ob_turned", "pad_ready", "own_wait")
        (idx_ready, gather_go, win_in, ck_in, cv_in, dve, qb_ready, c_full, cmax_ready, c_exp, p4_ready, hs_full, k_turned, k_moved_v,
         k_moved_a, s_full, s_moved, max_ready, e_ready, pn_ready, t_full, t_moved_v, t_moved_a, v_done, ob_ready,
         ob_turned, pad_ready, own_wait) = (s.sem(n) for n in names)
        raw_in = [s.sem(f"raw_in{j}") for j in range(NJ)]
        cache = A["cache_slc_kv"].rearrange("n (i s) k g d -> (n i) (s k g d)", s=4)
        ORDER = (1, 2, 3, 4, 5, 6, 7, 0, 8, 9)
        NO = len(ORDER)

        def samples(eng, body):
            body(0, True)
            with eng.Fori(1, DEC_B) as b:
                body(b, False)

        def at_b(x, b, n=1):
            return x[:, n * b:n * b + n] if isinstance(b, int) else x[:, bass.ds(n * b, n)]

        def turned_k(j):
            return kts[j % 2]

        with nc.Block() as block:
            @block.gpsimd
            def _(pool):
                def body(b, first):
                    if not first:
                        for j in range(NJ):
                            pool.wait_ge(raw_in[j], 16 * b)
                    pool.tensor_copy(idx, at_b(idx_slc, b, NJ)).then_inc(idx_ready, 1)
                    pool.wait_ge(idx_ready, b + 1)
                    for j in range(NJ):
                        if not first:
                            pool.wait_ge(v_done, NO * b - NO + ORDER.index(j + 1) + 1)
                            pool.sem_inc(gather_go, 1)
                        pool.indirect_dma_start(out=raw[j].rearrange("p s n -> p (s n)"), out_offset=None, in_=cache,
                                                in_offset=bass.IndirectOffsetOnAxis(ap=idx[:, j:j + 1], axis=0)).then_inc(raw_in[j], 16)
                samples(pool, body)

            @block.sync
            def _(sp):
                def body(b, first):
                    def row(x):
                        return x[b:b + 1] if isinstance(b, int) else x[bass.ds(b, 1)]
                    if not first:
                        sp.wait_ge(c_full, b)
                    sp.dma_start(ck.rearrange("p a n -> p (a n)"), row(ck_dram).rearrange("o p n -> p (o n)")).then_inc(ck_in, 16)
                    if not first:
                        sp.wait_ge(v_done, NO * b)
                    sp.dma_start(cv.rearrange("p a n -> p (a n)"), row(cv_dram).rearrange("o p n -> p (o n)")).then_inc(cv_in, 16)
                    sp.dma_start(raw[NJ].rearrange("p s n -> p (s n)"),
                                 row(A["cache_win_kv"]).rearrange("o (p s) k g d -> p (o s k g d)", s=4)).then_inc(win_in, 16)
                samples(sp, body)

            @block.tensor
            def _(pe):
                def body(b, first):
                    def turn(j):
                        pe.wait_ge(raw_in[j], 16 * b + 16) if j < NJ else pe.wait_ge(win_in, 16 * b + 16)
                        if not (first and j == 0):
                            pe.wait_ge(k_moved_v, 9 * b + j)
                            pe.wait_ge(k_moved_a, 9 * b + j)
                        for gp in range(2):
                            for r in range(4):
                                ins = pe.transpose(psK[gp][:, P * r:P * r + P], raw[j][:, r, P * gp:P * gp + P], ident[:, :])
                            ins.then_inc(k_turned, 1)

                    def scores(j):
                        pe.wait_ge(k_moved_v, 9 * b + j + 1)
                        pe.wait_ge(k_moved_a, 9 * b + j + 1)
                        if not (first and j < 2):
                            pe.wait_ge(s_moved, 9 * b + j - 1)
                        for gp in range(2):
                            ins = pe.matmul(psS[j % 2][:, :], qb[:, gp, :], turned_k(j)[:, gp, :], start=(gp == 0), stop=(gp == 1))
                        ins.then_inc(s_full, 1)

                    turn(0)
                    pe.wait_ge(qb_ready, b + 1)
                    pe.wait_ge(ck_in, 16 * b + 16)
                    if not first:
                        pe.wait_ge(ob_ready, b)
                    for gp in range(2):
                        ins = pe.matmul(O0[:, 0:255], qb[:, gp, :], ck[:, gp, 0:255], start=(gp == 0), stop=(gp == 1))
                    for br in range(2):
                        for gp in range(2):
                            ins = pe.matmul(O0[:, 320 + 64 * br:384 + 64 * br], qb[:, gp, :], kt_s[:, br, gp, :],
                                            start=(gp == 0), stop=(gp == 1))
                    ins.then_inc(c_full, 1)
                    turn(1)
                    scores(0)
                    pe.wait_ge(p4_ready, b + 1)
                    pe.matmul(O0[:, 256:320], hsum, ps[:, 0:64], start=True, stop=True).then_inc(hs_full, 1)
                    for j in range(1, 9):
                        if j < 8:
                            turn(j + 1)
                        scores(j)

                    def turn_p(n):
                        q = ORDER[n]
                        if q == 0:
                            pe.wait_ge(pn_ready, b + 1)
                            pe.wait_ge(e_ready, 9 * b + 9)
                        else:
                            pe.wait_ge(e_ready, 9 * b + q)
                        if n >= 2 or not first:
                            if n % 2 == 0:
                                pe.wait_ge(t_moved_v, 5 * b + n // 2)
                            else:
                                pe.wait_ge(t_moved_a, 5 * b + n // 2)
                        for r in range(4):
                            if q == 0 and r >= 2:
                                o = (OLD, WIN + 512)[r - 2]
                                ins = pe.transpose(psT[n % 2][0:64, P * r:P * r + P], sc[:, o:o + 64], ident[:, :])
                                continue
                            src = pc[:, P * r:P * r + P] if q == 0 else \
                                (sc[:, 512 * (q - 1) + P * r:512 * (q - 1) + P * r + P] if q < 9 else sc[:, WIN + P * r:WIN + P * r + P])
                            ins = pe.transpose(psT[n % 2][:, P * r:P * r + P], src, ident[:, :])
                        ins.then_inc(t_full, 1)

                    def values(n):
                        q = ORDER[n]
                        if n % 2 == 0:
                            pe.wait_ge(t_moved_v, 5 * b + n // 2 + 1)
                        else:
                            pe.wait_ge(t_moved_a, 5 * b + n // 2 + 1)
                        if q == 0:
                            pe.wait_ge(cv_in, 16 * b + 16)
                            for r in range(2):
                                ins = pe.matmul(O1[:, 0:256], ptn[:, P * r:P * r + P], cv[:, r, :], start=(r == 0), stop=(r == 1))
                            ins.then_inc(v_done, 1)
                            return
                        out = O0[:, 0:256] if q < 9 else O1[:, 256:512]
                        for r in range(4):
                            ins = pe.matmul(out, pt[n % 2][:, P * r:P * r + P], raw[q - 1][:, r, 256:512],
                                            start=(r == 0 and q in (1, 9)), stop=False, skip_group_check=True)
                        if q >= 8:
                            o = 256 if q == 8 else 384
                            ins = pe.matmul(out, ptn[0:64, o:o + P], kv4[0:64, 1 + (q == 9), 256:512], start=False, stop=True,
                                            skip_group_check=True)
                        ins.then_inc(v_done, 1)

                    turn_p(0)
                    for n in range(NO):
                        if n + 1 < NO:
                            turn_p(n + 1)
                        values(n)
                samples(pe, body)
                pe.wait_ge(ob_ready, DEC_B)
                for b in range(DEC_B):
                    ins = pe.transpose((O0, O1)[b // 4][:, P * (b % 4):P * (b % 4) + P], obs[:, b].rearrange("p e d -> p (e d)"), ident[:, :])
                ins.then_inc(ob_turned, 1)

            @block.scalar
            def _(act):
                def body(b, first):
                    def move_k(j):
                        act.wait_ge(k_turned, 18 * b + 2 * j + 2)
                        if not (first and j < 2):
                            act.wait_ge(s_full, 9 * b + j - 1)
                        nc.scalar.copy(turned_k(j)[:, 1, :], psK[1][:, :]).then_inc(k_moved_a, 1)

                    move_k(0)
                    act.wait_ge(cmax_ready, b + 1)
                    nc.scalar.activation(pc[:, 0:255], O0[:, 0:255], ACT.Exp, bias=mxs[:, 0:1], scale=SCALE,
                                         accum_out=sms[:, 0:1]).then_inc(c_exp, 1)
                    for j in range(1, 9):
                        move_k(j)

                    def exp(j):
                        act.wait_ge(max_ready, 2 * b + 1 if j < NJ else 2 * b + 2)
                        o, n = (512 * j, 512 + 64 * (j == NJ - 1)) if j < NJ else (WIN, 576)
                        w = 1 + (j == NJ)
                        nc.scalar.activation(sc[:, o:o + n], sc[:, o:o + n], ACT.Exp, bias=mxs[:, w:w + 1], scale=SCALE,
                                             accum_out=es[:, j:j + 1]).then_inc(e_ready, 1)

                    def move_p(n):
                        act.wait_ge(t_full, NO * b + n + 1)
                        if n >= 2 or not first:
                            act.wait_ge(v_done, NO * b + n - 1)
                        if ORDER[n] == 0:
                            nc.scalar.copy(ptn[:, 0:256], psT[1][:, 0:256])
                            nc.scalar.copy(ptn[0:64, 256:512], psT[1][0:64, 256:512]).then_inc(t_moved_a, 1)
                        else:
                            nc.scalar.copy(pt[1], psT[1][:, :]).then_inc(t_moved_a, 1)

                    for j in range(3):
                        exp(j)
                    for n in (1, 3, 5):
                        move_p(n)
                        exp(n + 2)
                        exp(n + 3)
                    move_p(7)
                    move_p(9)
                samples(act, body)

            @block.vector
            def _(v):
                NL = 24

                def body(b, first):
                    link = Link(v, dve, NL * b)
                    if not first:
                        v.wait_ge(s_full, 9 * b)
                    v.tensor_copy(qb.rearrange("p a n -> p (a n)"),
                                  (qbd[:, 0:1] if first else qbd[:, bass.ds(b, 1)]).rearrange("p o a n -> p (o a n)")).then_inc(qb_ready, 1)

                    def move_k(j):
                        v.wait_ge(k_turned, 18 * b + 2 * j + 1)
                        if not (first and j < 2):
                            v.wait_ge(s_full, 9 * b + j - 1)
                        v.tensor_copy(turned_k(j)[:, 0, :], psK[0][:, :]).then_inc(k_moved_v, 1)

                    move_k(0)
                    v.wait_ge(c_full, b + 1)
                    link(v.tensor_reduce(mxs[:, 0:1], O0[:, 0:255], AX, ALU.max))
                    v.tensor_scalar(mxs[:, 0:1], mxs[:, 0:1], -SCALE, None, ALU.mult).then_inc(cmax_ready, 1)
                    move_k(1)
                    v.wait_ge(c_exp, b + 1)
                    link(v.reciprocal(cf[:, 0:1], sms[:, 0:1]))
                    link(v.tensor_scalar(pc[:, 0:255], pc[:, 0:255], cf[:, 0:1], None, ALU.mult))
                    v.sem_inc(pn_ready, 1)
                    link(v.tensor_reduce(ps[:, 0:64], pc.rearrange("p (j c) -> p j c", c=4), AX, ALU.add))
                    spill = pc.rearrange("p (j c) -> p j c", c=4)[:, 0:63, 3]
                    v.tensor_tensor(ps[:, 1:64], ps[:, 1:64], spill, ALU.add).then_inc(p4_ready, 1)
                    v.wait_ge(hs_full, b + 1)
                    v.tensor_tensor(sel[:, 0:64], O0[:, 256:320], forced[:, 0:64], ALU.add)
                    link(v.tensor_copy(sel[:, 64:65], forced[:, 64:65]))
                    move_k(2)
                    for i in range(2):
                        v.sem_inc(own_wait, 1)
                        link(v.max(m8[:, i, :], sel[:, 0:65]))
                        v.sem_inc(own_wait, 1)
                        link(v.match_replace(sel[:, 0:65], m8[:, i, :], sel[:, 0:65], -1e9))
                    link(v.tensor_scalar(sel[:, 0:65], sel[:, 0:65], -1e9, NEG, ALU.not_equal, ALU.mult))
                    if not first:
                        v.wait_ge(t_full, NO * b)
                    nm = nmask[:, 0] if first else nmask[:, bass.ds(b, 1)].rearrange("p o n -> p (o n)")
                    v.tensor_tensor(sc[:, OLD:OLD + 64], O0[:, 320:384], nm, ALU.add)
                    link(v.tensor_tensor(sc[:, WIN + 512:WIN + 576], O0[:, 384:448], nm, ALU.add))
                    link(v.tensor_scalar(sc[:, OLD:OLD + 64], sc[:, OLD:OLD + 64], sel[:, 64:65], None, ALU.add))
                    for j in range(8):
                        v.wait_ge(s_full, 9 * b + j + 1)
                        m = bc(bc(sel[:, 8 * j:8 * j + 8].unsqueeze(2), [P, 8, 16]).unsqueeze(1), [P, 4, 8, 16])
                        v.tensor_tensor(sc[:, 512 * j:512 * j + 512].rearrange("p (r j i) -> p r j i", r=4, j=8),
                                        psS[j % 2][:, :].rearrange("p (r j i) -> p r j i", r=4, j=8), m, ALU.add).then_inc(s_moved, 1)
                        if 1 <= j < 7:
                            move_k(j + 2)
                        v.wait_ge(s_moved, 9 * b + j + 1)
                        n = 512 + 64 * (j == NJ - 1)
                        ins = v.tensor_reduce(tm[:, j:j + 1], sc[:, 512 * j:512 * j + n], AX, ALU.max)
                    link(ins)
                    link(v.tensor_reduce(mxs[:, 1:2], tm[:, 0:8], AX, ALU.max))
                    v.tensor_scalar(mxs[:, 1:2], mxs[:, 1:2], -SCALE, None, ALU.mult).then_inc(max_ready, 1)
                    v.wait_ge(s_full, 9 * b + 9)
                    v.tensor_copy(sc[:, WIN:WIN + 512], psS[0][:, :]).then_inc(s_moved, 1)
                    v.wait_ge(s_moved, 9 * b + 9)
                    w8 = sc[:, WIN:WIN + 512].rearrange("p (r q) -> p r q", r=4)[:, :, 0:2]
                    link(v.tensor_tensor(w8, w8, wmask.rearrange("p (q r) -> p r q", r=4), ALU.add))
                    link(v.tensor_reduce(mxs[:, 2:3], sc[:, WIN:WIN + 576], AX, ALU.max))
                    v.tensor_scalar(mxs[:, 2:3], mxs[:, 2:3], -SCALE, None, ALU.mult).then_inc(max_ready, 1)
                    for n in range(0, NO, 2):
                        v.wait_ge(t_full, NO * b + n + 1)
                        if n >= 2 or not first:
                            v.wait_ge(v_done, NO * b + n - 1)
                        v.tensor_copy(pt[0], psT[0][:, :]).then_inc(t_moved_v, 1)
                    link(v.memset(sms[:, 0:1], 1.0))
                    v.wait_ge(e_ready, 9 * b + 9)
                    link(v.tensor_reduce(sms[:, 1:2], es[:, 0:8], AX, ALU.add))
                    link(v.tensor_copy(sms[:, 2:3], es[:, 8:9]))
                    link(v.reciprocal(cf[:, 0:3], sms[:, 0:3]))
                    g3 = gs[:, 0] if first else gs[:, bass.ds(b, 1)].rearrange("p o n -> p (o n)")
                    link(v.tensor_tensor(cf[:, 0:3], cf[:, 0:3], g3, ALU.mult))
                    v.wait_ge(v_done, NO * b + NO)
                    for br, src in ((0, O1[:, 0:256]), (1, O0[:, 0:256]), (2, O1[:, 256:512])):
                        for g in range(NKV):
                            r = slice(32 * g, 32 * g + 32)
                            x = src[r, HD * g:HD * g + HD]
                            if br == 0:
                                ins = v.tensor_scalar(ob[r, :], x, cf[r, 0:1], None, ALU.mult)
                            elif br == 1:
                                ins = v.scalar_tensor_tensor(out=ob[r, :], in0=x, scalar=cf[r, 1:2], in1=ob[r, :], op0=ALU.mult, op1=ALU.add)
                            else:
                                for e in range(2):
                                    dst = obs[r, 0, e, :] if first else obs[r, bass.ds(b, 1), e, :].rearrange("p o d -> p (o d)")
                                    ins = v.scalar_tensor_tensor(out=dst, in0=x, scalar=cf[r, 2:3], in1=ob[r, :], op0=ALU.mult, op1=ALU.add)
                        link(ins)
                    v.sem_inc(ob_ready, 1)
                    used = link.count
                    assert used == NL, used
                v.memset(pc[:, 255:256], 0.0).then_inc(pad_ready, 1)
                v.wait_ge(pad_ready, 1)
                samples(v, body)
                v.wait_ge(ob_turned, 1)
                for b in range(DEC_B):
                    for e in range(2):
                        r = slice(64 * e, 64 * e + 64)
                        src = (O0, O1)[b // 4][r, P * (b % 4):P * (b % 4) + P].rearrange("p (m e l) -> p m e l", m=8, e=2)[:, :, e, :]
                        v.tensor_copy(oT[r, :, SEQ + 8 * b:SEQ + 8 * b + 8], src)


def attention_out(nc, A, R, x, oT):
    with Scope(nc, "ao") as s:
        w = R(A_FREE, KT, D)
        bank = s.banks()
        w_in, full, used = s.sem("w_in"), s.sem("full"), s.sem("used")
        with nc.Block() as block:
            @block.sync
            def _(sp):
                sp.dma_start(w, A["b_w_o"][0].rearrange("(k p) n -> p k n", p=P)).then_inc(w_in, 16)

            @block.tensor
            def _(pe):
                pe.wait_ge(w_in, 16)
                for i, (t0, n) in enumerate(TILES):
                    for h in range(2):
                        j = 2 * i + h
                        if j >= 8:
                            pe.wait_ge(used, j - 7)
                        for k in range(KT):
                            ins = pe.matmul(bank[j % 8][0:n, :], oT[:, k, t0:t0 + n], w[:, k, 512 * h:512 * h + 512],
                                            start=(k == 0), stop=(k == KT - 1))
                        ins.then_inc(full, 1)

            @block.vector
            def _(v):
                for i, (t0, n) in enumerate(TILES):
                    for h in range(2):
                        j = 2 * i + h
                        v.wait_ge(full, j + 1)
                        xs = x[0:n, i, 512 * h:512 * h + 512]
                        v.scalar_tensor_tensor(out=xs, in0=xs, scalar=ALPHA, in1=bank[j % 8][0:n, :], op0=ALU.mult, op1=ALU.add).then_inc(used, 1)


OUTS = {"y_prompt": [1, SEQ, D], "y_sample": [DEC_B, DEC_S, D], "h_last": [P, DEC_B + 1, SG],
        "p_cmp": [1, SEQ, 2, NKV, HD], "p_slc": [1, SEQ, 2, NKV, HD], "p_win": [1, SEQ, 2, NKV, HD],
        "s_cmp": [DEC_B, DEC_S, 2, NKV, HD], "s_slc": [DEC_B, DEC_S, 2, NKV, HD], "s_win": [DEC_B, SEQ, 2, NKV, HD]}


def build(nc, A, O):
    def dram(name, shape, dt=F32):
        return nc.dram_tensor(name, shape, dt).ap()

    Scope.spent = []
    with Scope(nc, "all") as s:
        ident, jmat = s.sb("ident", [P, P]), s.sb("jmat", [P, P])
        A["eps"] = s.sb("eps", [P, 1])
        idx_cmp, idx_slc = s.sb("idx_cmp", [P, 4 * DEC_B], I32), s.sb("idx_slc", [P, 8 * DEC_B], I32)
        pe_bias, gates_s = s.sb("pe_bias", [P, 4]), s.sb("gates_s", [P, DEC_B, 3])
        ck_dram, cv_dram = dram("ck", [DEC_B, P, 512]), dram("cv", [DEC_B, P, 512])
        y_rows = dram("y_rows", [NROW, D])
        constants(nc, ident, jmat, A["eps"])
        page_rows(nc, A, idx_cmp, idx_slc)
        compress_cache(nc, A, ident, idx_cmp, pe_bias, ck_dram, cv_dram, y_rows[NE * RB:NROW])
        recycle(nc)
        R = Region(s.sb("arena", [P, ARENA]))
        x = R(X_OFF, NT, D)

        u_dram, s5_dram = dram("u", [D, TOK]), dram("s5_y", [D, TOK])
        tab, bx1, bx2, cy1, cy2 = (R(S5_TAB, 20, 64), *[R(off, SG, SW) for off in (S5_X1, S5_X2, S5_Y1, S5_Y2)])
        toep, et, o = R(5376, SG, CH, SW), R(13568, SG, P), R(21760, SG, CH, SW)
        ho, hs = R(S5_X1, DEC_B + 1, SG), R(S5_X2 + 512, DEC_B, SG)
        s5_inputs(nc, A, R, ident, u_dram)
        s5_parameters(nc, A, ident, jmat, tab, bx1, bx2, cy1, cy2, R)
        s5_matrices(nc, A, R, ident, toep, et, o)
        s5_chunks(nc, A, R, toep, et, u_dram, hs)
        s5_scan(nc, R, jmat, hs, ho)
        s5_outputs(nc, R, o, s5_dram, ho, O["h_last"])
        glu(nc, A, R, x, u_dram, s5_dram)
        for layer in range(2):
            recycle(nc)
            if layer == 1:
                attention(nc, A, O, R, x, ident, idx_slc, pe_bias, gates_s, ck_dram, cv_dram, dram("gates", [DEC_B * DEC_S, NH * 3]))
                recycle(nc)
            x_dram, row_tok = dram(f"x{layer}", [TOK, D]), dram(f"row_tok{layer}", [NROW, 1], I32)
            weights = Weights(nc, A, R, layer)
            layer_norm(nc, A, R, f"ln_a{layer}", layer, 0, ident, x, x_dram=x_dram, weights=weights)
            route(nc, R, f"route{layer}", weights, row_tok)
            experts(nc, R, f"moe{layer}", ident, weights, x_dram, y_rows)
            more_experts(nc, A, R, f"more{layer}", layer, ident, weights, x_dram, y_rows)
            combine(nc, R, f"comb{layer}", x, y_rows)
            layer_norm(nc, A, R, f"ln_b{layer}", layer, 1, ident, x,
                       outs=(O["y_prompt"], O["y_sample"]) if layer == 1 else None, turn=(layer == 0))


def attention(nc, A, O, R, x, ident, idx_slc, pe_bias, gates_s, ck_dram, cv_dram, gate_dram):
    at = [XT_OFF]

    def place(*shape):
        at[0] += int(np.prod(shape))
        return R(at[0] - int(np.prod(shape)), *shape)

    projections(nc, A, R, [O[n] for n in ("p_cmp", "p_slc", "p_win", "s_cmp", "s_slc", "s_win")], gate_dram)
    ck_p, cv_p = place(2, 32), place(256)
    causal, seen, seen01 = place(P), place(4, NCMP_P), place(4, NCMP_P)
    new_mask, win_mask, head_sum, forced = place(DEC_B, 64), place(8), place(P), place(66)
    new_keys = place(2, 2, 64)
    compress_prompt(nc, A, R, ident, pe_bias, O["p_cmp"], ck_p, cv_p)
    attention_masks(nc, R, causal, seen, seen01, new_mask, win_mask, head_sum, forced)
    oT = R(OT_OFF, KT, TOK)
    prompt_attention(nc, A, R, ident, ck_p, cv_p, causal, seen, seen01, new_keys, oT)
    sample_queries(nc, R, gate_dram, gates_s)
    sample_attention(nc, A, R, ident, idx_slc, ck_dram, cv_dram, new_keys, new_mask, win_mask, head_sum, forced, gates_s, oT)
    attention_out(nc, A, R, x, oT)


def kernel(**inputs):
    import numpy as _np
    import concourse.bacc as _bacc
    from concourse import mybir as _mybir
    from concourse.bass_utils import run_bass_kernel_spmd as _run

    nc = _bacc.Bacc("TRN2", target_bir_lowering=False, num_devices=1)
    given = {n: _np.asarray(inputs[n]) for n in _INS}
    given["state_ssm"] = given["state_ssm"][0].transpose(3, 2, 0, 1).reshape(P, DEC_B, SG)
    given["a_d"] = given["a_d"].reshape(KT, P).T
    given["cmp_pe"] = given["cmp_pe"].reshape(2, 16, P).transpose(2, 0, 1)
    w = given["b_w_qg"][0]
    wq = w[:, :D].reshape(D, 2, 2, HPK, HD).transpose(0, 1, 3, 2, 4).reshape(D, D)
    given["b_w_qg"] = _np.concatenate([wq, w[:, D:]], axis=1)
    arrays, A, O = {}, {}, {}
    for n in _INS:
        a = _np.ascontiguousarray(given[n])
        arrays[f"in_{n}"] = a
        A[n] = nc.dram_tensor(f"in_{n}", a.shape, _mybir.dt.from_np(a.dtype), kind="ExternalInput").ap()
    for n, shape in OUTS.items():
        O[n] = nc.dram_tensor(f"out_{n}", shape, _mybir.dt.float32, kind="ExternalOutput").ap()
    build(nc, A, O)
    r = _run(nc, [arrays], core_ids=[0])
    got = {n: r.results[0][f"out_{n}"] for n in OUTS}
    h = got["h_last"]
    p_state = _np.ascontiguousarray(h[:, DEC_B].reshape(2, SP_, SG).transpose(2, 1, 0))[None, None]
    s_state = _np.ascontiguousarray(h[:, :DEC_B].reshape(2, SP_, DEC_B, SG).transpose(2, 3, 1, 0))[None]
    return (got["y_prompt"], got["y_sample"], p_state, got["p_cmp"], got["p_slc"], got["p_win"],
            s_state, got["s_cmp"], got["s_slc"], got["s_win"])
```
